# Optimizing a Trainium2 kernel written in Bass

```python
import numpy as np
import jax
import jax.numpy as jnp
from jax import lax
import math
import jax, jax.numpy as jnp

D_MODEL = 1024
BATCH = 1
SEQ = 256
DEPTH = 2

HEAD_DIM = 64
ROPE_THETA = 10000.0
NORM_EPS = 1e-6
NEG = -1e30
BRANCH_W = D_MODEL // 2
N_BRANCH = 4
NSA_HEADS = BRANCH_W // HEAD_DIM
NSA_KV = 2
NSA_R = NSA_HEADS // NSA_KV
CMP_LEN = 32
CMP_STRIDE = 16
CMP_HIDDEN = 256
SEL_LEN = 64
SEL_TOPK = 16
NSA_WINDOW = 512
SEL_Q_CHUNK = 32
FORCE_BONUS = 1e3
SWA_HEADS = BRANCH_W // HEAD_DIM
SWA_KV = 2
SWA_R = SWA_HEADS // SWA_KV
SWA_WINDOW = 128
Q_BLOCK = 128
CONV_CH = BRANCH_W
CONV_WIDTH = 31
POOL_CH = BRANCH_W
POOL_WINDOWS = (2, 4, 8, 16)
POOL_GROUPS = 4
POOL_GROUP_CH = POOL_CH // POOL_GROUPS
D_FF = ((8 * D_MODEL // 3) + 127) // 128 * 128
FFN_CONV_WIDTH = 3
IN_SIZES = (
    NSA_HEADS * HEAD_DIM,
    3 * 2 * NSA_KV * HEAD_DIM,
    3 * NSA_HEADS,
    SWA_HEADS * HEAD_DIM,
    2 * SWA_KV * HEAD_DIM,
    2 * CONV_CH,
    POOL_CH,
)
IN_COLS = sum(IN_SIZES)


def rms_norm(x, g):
    xf = x.astype(jnp.float32)
    y = xf * lax.rsqrt(jnp.mean(xf * xf, axis=-1, keepdims=True) + NORM_EPS)
    return (y * g.astype(jnp.float32)).astype(x.dtype)

def layer_norm(x, g, b):
    xf = x.astype(jnp.float32)
    mu = jnp.mean(xf, axis=-1, keepdims=True)
    var = jnp.mean(jnp.square(xf - mu), axis=-1, keepdims=True)
    y = (xf - mu) * lax.rsqrt(var + NORM_EPS)
    return (y * g.astype(jnp.float32) + b.astype(jnp.float32)).astype(x.dtype)

def rope_tables(seq):
    inv = 1.0 / (ROPE_THETA ** (jnp.arange(0, HEAD_DIM, 2, dtype=jnp.float32) / HEAD_DIM))
    ang = jnp.arange(seq, dtype=jnp.float32)[:, None] * inv[None, :]
    return jnp.cos(ang), jnp.sin(ang)

def apply_rope(x, cos, sin):
    shp = (1, x.shape[1]) + (1,) * (x.ndim - 3) + (HEAD_DIM // 2,)
    c, s = cos.reshape(shp), sin.reshape(shp)
    xf = x.astype(jnp.float32)
    x1, x2 = xf[..., : HEAD_DIM // 2], xf[..., HEAD_DIM // 2:]
    return jnp.concatenate([x1 * c - x2 * s, x2 * c + x1 * s], axis=-1).astype(x.dtype)

def causal_depthwise_conv(x, w, b):
    k, c = w.shape
    y = lax.conv_general_dilated(
        x, w[:, None, :].astype(x.dtype), window_strides=(1,), padding=[(k - 1, 0)],
        dimension_numbers=("NWC", "WIO", "NWC"), feature_group_count=c)
    return y + b.astype(x.dtype)

def masked_softmax(s, mask):
    p = jax.nn.softmax(jnp.where(mask, s, NEG), axis=-1)
    return jnp.where(mask, p, 0.0)

def banded_attention(q, k, v, window, sinks):
    bsz, seq, g, r, dk = q.shape
    span = window + Q_BLOCK
    k_pad = jnp.pad(k, ((0, 0), (window, 0), (0, 0), (0, 0)))
    v_pad = jnp.pad(v, ((0, 0), (window, 0), (0, 0), (0, 0)))
    scale = dk ** -0.5

    def block(i):
        start = i * Q_BLOCK
        qb = lax.dynamic_slice_in_dim(q, start, Q_BLOCK, axis=1)
        kb = lax.dynamic_slice_in_dim(k_pad, start, span, axis=1)
        vb = lax.dynamic_slice_in_dim(v_pad, start, span, axis=1)
        t = start + jnp.arange(Q_BLOCK)
        j = start - window + jnp.arange(span)
        mask = (j[None, :] <= t[:, None]) & (j[None, :] > t[:, None] - window) & (j[None, :] >= 0)
        mask = mask[None, None, None]
        s = jnp.einsum("bqgrd,bkgd->bgrqk", qb, kb, preferred_element_type=jnp.float32) * scale
        if sinks is None:
            p = masked_softmax(s, mask)
        else:
            sink = sinks.astype(jnp.float32).reshape(g, r)[None, :, :, None, None]
            s = jnp.where(mask, s, NEG)
            m = jnp.maximum(jnp.max(s, axis=-1, keepdims=True), sink)
            e = jnp.exp(s - m)
            p = e / (jnp.sum(e, axis=-1, keepdims=True) + jnp.exp(sink - m))
        return jnp.einsum("bgrqk,bkgd->bqgrd", p.astype(v.dtype), vb)

    out = lax.map(block, jnp.arange(seq // Q_BLOCK))
    return jnp.moveaxis(out, 0, 1).reshape(bsz, seq, g, r, dk)

def nsa_compress(k, pos, w1, w2):
    bsz, seq, g, dk = k.shape
    n_cmp = (seq - CMP_LEN) // CMP_STRIDE + 1
    idx = np.arange(n_cmp)[:, None] * CMP_STRIDE + np.arange(CMP_LEN)[None, :]
    blk = jnp.swapaxes(k[:, idx], 2, 3) + pos.astype(k.dtype)
    flat = blk.reshape(bsz, n_cmp, g, CMP_LEN * dk)
    return jax.nn.gelu(flat @ w1, approximate=True) @ w2

def nsa_compressed_attention(q, kc, vc):
    seq, n_cmp = q.shape[1], kc.shape[1]
    t = jnp.arange(seq)
    blk_end = jnp.arange(n_cmp) * CMP_STRIDE + CMP_LEN - 1
    mask = (blk_end[None, :] <= t[:, None])[None, :, None, None, :]
    s = jnp.einsum("bsgrd,bngd->bsgrn", q, kc, preferred_element_type=jnp.float32) * HEAD_DIM ** -0.5
    p = masked_softmax(s, mask)
    o = jnp.einsum("bsgrn,bngd->bsgrd", p.astype(vc.dtype), vc)
    return o, p

def nsa_select_blocks(p_cmp, seq):
    n_cmp = p_cmp.shape[-1]
    n_slc = seq // SEL_LEN
    i = jnp.arange(n_cmp)
    j = jnp.arange(n_slc)
    overlap = ((i[:, None] * CMP_STRIDE < (j[None, :] + 1) * SEL_LEN)
               & (i[:, None] * CMP_STRIDE + CMP_LEN > j[None, :] * SEL_LEN)).astype(jnp.float32)
    imp = jnp.einsum("bsgrn,nj->bsgj", p_cmp, overlap)
    cur = jnp.arange(seq) // SEL_LEN
    valid = (j[None, :] <= cur[:, None])[None, :, None, :]
    forced = ((j[None, :] == 0) | (j[None, :] == cur[:, None]) | (j[None, :] == cur[:, None] - 1))[None, :, None, :]
    score = jnp.where(valid, imp + jnp.where(forced, FORCE_BONUS, 0.0), -1.0)
    _, sel = lax.top_k(score, min(SEL_TOPK, n_slc))
    return sel

def nsa_selected_attention(q, k, v, sel):
    bsz, seq, g, r, dk = q.shape
    n_slc = seq // SEL_LEN
    n_top = sel.shape[-1]
    kb = k.reshape(bsz, n_slc, SEL_LEN, g, dk).transpose(0, 3, 1, 2, 4)
    vb = v.reshape(bsz, n_slc, SEL_LEN, g, dk).transpose(0, 3, 1, 2, 4)
    nc = seq // SEL_Q_CHUNK
    qc = jnp.moveaxis(q.reshape(bsz, nc, SEL_Q_CHUNK, g, r, dk), 1, 0)
    sc = jnp.moveaxis(sel.reshape(bsz, nc, SEL_Q_CHUNK, g, n_top), 1, 0)
    b_idx = jnp.arange(bsz)[:, None, None, None]
    g_idx = jnp.arange(g)[None, None, :, None]
    scale = dk ** -0.5

    def chunk(args):
        q_c, sel_c, c = args
        t = c * SEL_Q_CHUNK + jnp.arange(SEL_Q_CHUNK)
        kg = kb[b_idx, g_idx, sel_c]
        vg = vb[b_idx, g_idx, sel_c]
        s = jnp.einsum("bcgrd,bcgkld->bcgrkl", q_c, kg, preferred_element_type=jnp.float32) * scale
        kpos = sel_c[..., None] * SEL_LEN + jnp.arange(SEL_LEN)
        mask = (kpos <= t[None, :, None, None, None])[:, :, :, None]
        flat = (bsz, SEL_Q_CHUNK, g, r, n_top * SEL_LEN)
        p = masked_softmax(s.reshape(flat), mask.reshape(bsz, SEL_Q_CHUNK, g, 1, n_top * SEL_LEN)).reshape(s.shape)
        return jnp.einsum("bcgrkl,bcgkld->bcgrd", p.astype(vg.dtype), vg)

    out = lax.map(chunk, (qc, sc, jnp.arange(nc)))
    return jnp.moveaxis(out, 0, 1).reshape(bsz, seq, g, r, dk)

def conformer_conv(u, conv_w, conv_b, ln_g, ln_b):
    a, gte = jnp.split(u, 2, axis=-1)
    c = a * jax.nn.sigmoid(gte)
    c = causal_depthwise_conv(c, conv_w, conv_b)
    return jax.nn.silu(layer_norm(c, ln_g, ln_b))

def pool_mixer(u, w, scale):
    bsz, seq, _ = u.shape
    uf = u.reshape(bsz, seq, POOL_GROUPS, POOL_GROUP_CH).astype(jnp.float32)
    cs = jnp.pad(jnp.cumsum(uf, axis=1), ((0, 0), (1, 0), (0, 0), (0, 0)))
    t = jnp.arange(seq)[:, None]
    win = jnp.array(POOL_WINDOWS, dtype=jnp.int32)[None, :]
    lo = jnp.maximum(t + 1 - win, 0)
    g_idx = jnp.arange(POOL_GROUPS)[None, :]
    mean = (cs[:, 1:] - cs[:, lo, g_idx]) / (t + 1 - lo).astype(jnp.float32)[None, :, :, None]
    pooled = (mean - uf).astype(u.dtype)
    mixed = jnp.einsum("bsgc,gcd->bsgd", pooled, w)
    return mixed.reshape(bsz, seq, POOL_CH) * scale

def first_inputs(seed: int = 0) -> dict:
    key = jax.random.key(seed)
    ks = jax.random.split(key, 24)
    f32 = jnp.float32
    L = DEPTH

    def nrm(k, shape, scale):
        return jax.random.normal(k, shape, f32) * scale

    return {
        "x": nrm(ks[0], (BATCH, SEQ, D_MODEL), 1.0),
        "norm_mix_pre": 1.0 + nrm(ks[1], (L, D_MODEL), 0.05),
        "norm_mix_post": 1.0 + nrm(ks[2], (L, D_MODEL), 0.05),
        "norm_ffn_pre": 1.0 + nrm(ks[3], (L, D_MODEL), 0.05),
        "norm_ffn_post": 1.0 + nrm(ks[4], (L, D_MODEL), 0.05),
        "w_in": nrm(ks[5], (L, D_MODEL, IN_COLS), D_MODEL ** -0.5),
        "nsa_cmp_pos": nrm(ks[6], (L, 2, CMP_LEN, HEAD_DIM), 0.1),
        "nsa_cmp_w1": nrm(ks[7], (L, 2, CMP_LEN * HEAD_DIM, CMP_HIDDEN), (CMP_LEN * HEAD_DIM) ** -0.5),
        "nsa_cmp_w2": nrm(ks[8], (L, 2, CMP_HIDDEN, HEAD_DIM), CMP_HIDDEN ** -0.5),
        "swa_sinks": nrm(ks[9], (L, SWA_HEADS), 0.5),
        "conv_w": nrm(ks[10], (L, CONV_WIDTH, CONV_CH), CONV_WIDTH ** -0.5),
        "conv_b": nrm(ks[11], (L, CONV_CH), 0.01),
        "conv_ln_g": 1.0 + nrm(ks[12], (L, CONV_CH), 0.05),
        "conv_ln_b": nrm(ks[13], (L, CONV_CH), 0.01),
        "pool_w": nrm(ks[14], (L, POOL_GROUPS, POOL_GROUP_CH, POOL_GROUP_CH), POOL_GROUP_CH ** -0.5),
        "pool_scale": 1.0 + nrm(ks[15], (L, POOL_CH), 0.1),
        "w_branch": nrm(ks[16], (L, N_BRANCH, BRANCH_W, D_MODEL), BRANCH_W ** -0.5),
        "w_gate": nrm(ks[17], (L, D_MODEL, N_BRANCH * D_MODEL), D_MODEL ** -0.5),
        "w_o": nrm(ks[18], (L, D_MODEL, D_MODEL), D_MODEL ** -0.5),
        "ffn_w_up": nrm(ks[19], (L, D_MODEL, 2 * D_FF), D_MODEL ** -0.5),
        "ffn_conv_w": nrm(ks[20], (L, FFN_CONV_WIDTH, 2 * D_FF), FFN_CONV_WIDTH ** -0.5),
        "ffn_conv_b": nrm(ks[21], (L, 2 * D_FF), 0.01),
        "ffn_w_down": nrm(ks[22], (L, D_FF, D_MODEL), D_FF ** -0.5),
    }

def first_block(x, norm_mix_pre, norm_mix_post, norm_ffn_pre, norm_ffn_post, w_in,
              nsa_cmp_pos, nsa_cmp_w1, nsa_cmp_w2, swa_sinks, conv_w, conv_b, conv_ln_g,
              conv_ln_b, pool_w, pool_scale, w_branch, w_gate, w_o, ffn_w_up, ffn_conv_w,
              ffn_conv_b, ffn_w_down):
    bsz, seq, _ = x.shape
    cos, sin = rope_tables(seq)
    splits = np.cumsum(IN_SIZES)[:-1].tolist()
    for l in range(DEPTH):
        h = rms_norm(x, norm_mix_pre[l])
        proj = h @ w_in[l]
        a_q, a_kv, a_gate, d_q, d_kv, b_in, c_in = jnp.split(proj, splits, axis=-1)

        qa = a_q.reshape(bsz, seq, NSA_KV, NSA_R, HEAD_DIM)
        kv = a_kv.reshape(bsz, seq, 3, 2, NSA_KV, HEAD_DIM)
        k_cmp = nsa_compress(kv[:, :, 0, 0], nsa_cmp_pos[l, 0], nsa_cmp_w1[l, 0], nsa_cmp_w2[l, 0])
        v_cmp = nsa_compress(kv[:, :, 0, 1], nsa_cmp_pos[l, 1], nsa_cmp_w1[l, 1], nsa_cmp_w2[l, 1])
        o_cmp, p_cmp = nsa_compressed_attention(qa, k_cmp, v_cmp)
        sel = nsa_select_blocks(p_cmp, seq)
        qa_rot = apply_rope(qa, cos, sin)
        o_slc = nsa_selected_attention(qa_rot, apply_rope(kv[:, :, 1, 0], cos, sin), kv[:, :, 1, 1], sel)
        o_win = banded_attention(qa_rot, apply_rope(kv[:, :, 2, 0], cos, sin), kv[:, :, 2, 1], NSA_WINDOW, None)
        ga = jax.nn.sigmoid(a_gate).reshape(bsz, seq, 3, NSA_KV, NSA_R, 1)
        o_a = (ga[:, :, 0] * o_cmp + ga[:, :, 1] * o_slc + ga[:, :, 2] * o_win).reshape(bsz, seq, BRANCH_W)

        o_b = conformer_conv(b_in, conv_w[l], conv_b[l], conv_ln_g[l], conv_ln_b[l])

        o_c = pool_mixer(c_in, pool_w[l], pool_scale[l])

        qd = apply_rope(d_q.reshape(bsz, seq, SWA_KV, SWA_R, HEAD_DIM), cos, sin)
        kvd = d_kv.reshape(bsz, seq, 2, SWA_KV, HEAD_DIM)
        o_d = banded_attention(qd, apply_rope(kvd[:, :, 0], cos, sin), kvd[:, :, 1], SWA_WINDOW,
                               swa_sinks[l]).reshape(bsz, seq, BRANCH_W)

        branches = jnp.stack([o_a, o_b, o_c, o_d], axis=2)
        up = jnp.einsum("bsnc,ncd->bsnd", branches, w_branch[l])
        gates = jax.nn.sigmoid((h @ w_gate[l]).reshape(bsz, seq, N_BRANCH, D_MODEL))
        mix = jnp.einsum("bsnd,bsnd->bsd", gates, up) @ w_o[l]
        x = x + rms_norm(mix, norm_mix_post[l])

        hf = rms_norm(x, norm_ffn_pre[l])
        u = causal_depthwise_conv(hf @ ffn_w_up[l], ffn_conv_w[l], ffn_conv_b[l])
        gate, val = jnp.split(u, 2, axis=-1)
        f = (jax.nn.gelu(gate, approximate=True) * val) @ ffn_w_down[l]
        x = x + rms_norm(f, norm_ffn_post[l])
    return x


DEPTH_2 = 1

CTX_LEN = 256
GRID_W = 64

SSD_HEADS = 16
SSD_HEAD_DIM = 64
D_SSD = SSD_HEADS * SSD_HEAD_DIM
SSD_GROUPS = 2
SSD_HEADS_PER_GROUP = SSD_HEADS // SSD_GROUPS
D_STATE = 128
CONV_W = 5
CHUNK = 128
D_XBC = D_SSD + 2 * SSD_GROUPS * D_STATE

ATTN_Q_HEADS = 16
ATTN_KV_HEADS = 4
GQA_GROUP = ATTN_Q_HEADS // ATTN_KV_HEADS
D_ATTN = ATTN_Q_HEADS * HEAD_DIM

D_MIX = D_SSD + D_ATTN

OFF_Z = 0
OFF_Q = OFF_Z + D_SSD
OFF_XBC = OFF_Q + D_ATTN
OFF_DT = OFF_XBC + D_XBC
OFF_K = OFF_DT + 2 * SSD_HEADS
OFF_V = OFF_K + ATTN_KV_HEADS * HEAD_DIM
D_IN_PROJ = OFF_V + ATTN_KV_HEADS * HEAD_DIM

MOE_GROUPS = 4
EXPERTS_PER_GROUP = 4
N_EXPERTS = MOE_GROUPS * EXPERTS_PER_GROUP
TOP_K_IN_GROUP = 2
D_EXPERT = 256


F32 = jnp.float32

def layer_norm_2(x, g, b, eps=1e-5):
    xf = x.astype(F32)
    mu = jnp.mean(xf, -1, keepdims=True)
    var = jnp.mean(jnp.square(xf - mu), -1, keepdims=True)
    return ((xf - mu) * lax.rsqrt(var + eps) * g + b).astype(x.dtype)

def rms_norm_2(x, g, eps=1e-6):
    xf = x.astype(F32)
    return (xf * lax.rsqrt(jnp.mean(xf * xf, -1, keepdims=True) + eps) * g).astype(x.dtype)

def dwconv_silu(u, w, b):
    y = lax.conv_general_dilated(u, w[:, None, :], (1,), [(CONV_W // 2, CONV_W // 2)],
                                 dimension_numbers=('NWC', 'WIO', 'NWC'),
                                 feature_group_count=u.shape[-1])
    return jax.nn.silu(y + b)

def axial_rope_tables(n_rows):
    rows = jnp.broadcast_to(jnp.arange(n_rows, dtype=F32)[:, None], (n_rows, GRID_W)).reshape(-1)
    cols = jnp.broadcast_to(jnp.arange(GRID_W, dtype=F32)[None, :], (n_rows, GRID_W)).reshape(-1)
    axis_dim = HEAD_DIM // 2
    inv_freq = jnp.power(ROPE_THETA, -jnp.arange(0, axis_dim, 2, dtype=F32) / axis_dim)
    ang = jnp.concatenate([rows[:, None] * inv_freq, cols[:, None] * inv_freq], -1)
    return jnp.cos(ang), jnp.sin(ang)

def apply_rope_2(x, cos, sin):
    xf = x.astype(F32).reshape(*x.shape[:-1], HEAD_DIM // 2, 2)
    x0, x1 = xf[..., 0], xf[..., 1]
    c = cos[None, :, None, :]
    s = sin[None, :, None, :]
    out = jnp.stack([x0 * c - x1 * s, x0 * s + x1 * c], -1)
    return out.reshape(x.shape).astype(x.dtype)

def ssd_scan(xs, dt, A, Bm, Cm, h0, with_output):
    b, L = xs.shape[:2]
    nc = L // CHUNK
    G, R, P, N = SSD_GROUPS, SSD_HEADS_PER_GROUP, SSD_HEAD_DIM, D_STATE
    xdt = (xs.astype(F32) * dt[..., None]).reshape(b, nc, CHUNK, G, R, P)
    a_cs = jnp.cumsum((dt * A).reshape(b, nc, CHUNK, G, R), axis=2)
    Bc = Bm.astype(F32).reshape(b, nc, CHUNK, G, N)
    w_state = jnp.exp(a_cs[:, :, -1:] - a_cs)
    chunk_states = jnp.einsum('bcsgn,bcsgr,bcsgrp->bcgrpn', Bc, w_state, xdt)
    chunk_decay = jnp.exp(a_cs[:, :, -1])

    def carry_state(h, inp):
        s_c, d_c = inp
        return h * d_c[..., None, None] + s_c, h

    h_final, h_in = lax.scan(carry_state, h0,
                             (jnp.moveaxis(chunk_states, 1, 0), jnp.moveaxis(chunk_decay, 1, 0)))
    if not with_output:
        return h_final
    Cc = Cm.astype(F32).reshape(b, nc, CHUNK, G, N)
    diff = a_cs[:, :, :, None] - a_cs[:, :, None]
    lower = jnp.tril(jnp.ones((CHUNK, CHUNK), bool))[:, :, None, None]
    decay = jnp.where(lower, jnp.exp(jnp.where(lower, diff, 0.0)), 0.0)
    cb = jnp.einsum('bcqgn,bcsgn->bcqsg', Cc, Bc)
    y_diag = jnp.einsum('bcqsgr,bcsgrp->bcqgrp', cb[..., None] * decay, xdt)
    y_off = jnp.einsum('bcqgn,bcgrpn,bcqgr->bcqgrp', Cc, jnp.moveaxis(h_in, 0, 1), jnp.exp(a_cs))
    return (y_diag + y_off).reshape(b, L, G, R, P), h_final

def ssd_bidirectional(xs, Bm, Cm, dt, A, h0_f, h0_b, with_output):
    fl = lambda u: jnp.flip(u, axis=1)
    out_f = ssd_scan(xs, dt[:, :, 0], A[0], Bm, Cm, h0_f, with_output)
    out_b = ssd_scan(fl(xs), fl(dt[:, :, 1]), A[1], fl(Bm), fl(Cm), h0_b, with_output)
    return out_f, out_b

def ssd_prepare(xbc_raw, dt_raw, p):
    b, L, _ = xbc_raw.shape
    xbc = dwconv_silu(xbc_raw, p['conv_w'], p['conv_b'])
    gn = SSD_GROUPS * D_STATE
    xs = xbc[..., :D_SSD].reshape(b, L, SSD_GROUPS, SSD_HEADS_PER_GROUP, SSD_HEAD_DIM)
    Bm = xbc[..., D_SSD:D_SSD + gn].reshape(b, L, SSD_GROUPS, D_STATE)
    Cm = xbc[..., D_SSD + gn:].reshape(b, L, SSD_GROUPS, D_STATE)
    dt = jax.nn.softplus(dt_raw.astype(F32).reshape(b, L, 2, SSD_HEADS) + p['dt_bias'].astype(F32))
    dt = dt.reshape(b, L, 2, SSD_GROUPS, SSD_HEADS_PER_GROUP)
    A = -jnp.exp(p['a_log'].astype(F32)).reshape(2, SSD_GROUPS, SSD_HEADS_PER_GROUP)
    return xs, Bm, Cm, dt, A

def ssd_output(y_f, y_b, xs, z, p):
    b, L = z.shape[:2]
    skip = p['d_skip'].astype(F32).reshape(SSD_GROUPS, SSD_HEADS_PER_GROUP)[..., None]
    y = y_f + jnp.flip(y_b, axis=1) + xs.astype(F32) * skip
    y = y.reshape(b, L, D_SSD) * jax.nn.silu(z.astype(F32))
    yg = y.reshape(b, L, SSD_GROUPS, D_SSD // SSD_GROUPS)
    yg = yg * lax.rsqrt(jnp.mean(yg * yg, -1, keepdims=True) + 1e-6)
    return (yg.reshape(b, L, D_SSD) * p['ssd_norm_g']).astype(z.dtype)

def gqa_block_attention(q, k, v):
    b, L = q.shape[:2]
    nblk = L // Q_BLOCK
    qb = q.reshape(b, nblk, Q_BLOCK, ATTN_KV_HEADS, GQA_GROUP, HEAD_DIM).swapaxes(0, 1)
    scale = HEAD_DIM ** -0.5

    def one_block(q_blk):
        s = jnp.einsum('bqhgd,bkhd->bhgqk', q_blk, k, preferred_element_type=F32) * scale
        pr = jax.nn.softmax(s, axis=-1).astype(v.dtype)
        return jnp.einsum('bhgqk,bkhd->bqhgd', pr, v)

    o = lax.map(one_block, qb)
    return o.swapaxes(0, 1).reshape(b, L, D_ATTN)

def context_mixer(hc, p, with_output):
    b, S, _ = hc.shape
    side = hc @ p['w_in'][:, OFF_XBC:]
    xbc_raw = side[..., :OFF_DT - OFF_XBC]
    dt_raw = side[..., OFF_DT - OFF_XBC:OFF_K - OFF_XBC]
    k = rms_norm_2(side[..., OFF_K - OFF_XBC:OFF_V - OFF_XBC].reshape(b, S, ATTN_KV_HEADS, HEAD_DIM), p['k_norm_g'])
    v = side[..., OFF_V - OFF_XBC:].reshape(b, S, ATTN_KV_HEADS, HEAD_DIM)
    xs, Bm, Cm, dt, A = ssd_prepare(xbc_raw, dt_raw, p)
    h0 = jnp.zeros((b, SSD_GROUPS, SSD_HEADS_PER_GROUP, SSD_HEAD_DIM, D_STATE), F32)
    if not with_output:
        hf, hb = ssd_bidirectional(xs, Bm, Cm, dt, A, h0, h0, False)
        return (k, v, hf, hb), None
    (y_f, hf), (y_b, hb) = ssd_bidirectional(xs, Bm, Cm, dt, A, h0, h0, True)
    zq = hc @ p['w_in'][:, :OFF_XBC]
    z = zq[..., OFF_Z:OFF_Q]
    q = rms_norm_2(zq[..., OFF_Q:].reshape(b, S, ATTN_Q_HEADS, HEAD_DIM), p['q_norm_g'])
    y_ssd = ssd_output(y_f, y_b, xs, z, p)
    o = gqa_block_attention(q, k, v)
    return (k, v, hf, hb), jnp.concatenate([y_ssd, o], -1) @ p['w_out']

def latent_mixer(hx, ctx_side, p, cos, sin):
    b, L, _ = hx.shape
    k_ctx, v_ctx, hf_ctx, hb_ctx = ctx_side
    proj = hx @ p['w_in']
    z = proj[..., OFF_Z:OFF_Q]
    q = proj[..., OFF_Q:OFF_XBC].reshape(b, L, ATTN_Q_HEADS, HEAD_DIM)
    xbc_raw = proj[..., OFF_XBC:OFF_DT]
    dt_raw = proj[..., OFF_DT:OFF_K]
    k = proj[..., OFF_K:OFF_V].reshape(b, L, ATTN_KV_HEADS, HEAD_DIM)
    v = proj[..., OFF_V:].reshape(b, L, ATTN_KV_HEADS, HEAD_DIM)
    xs, Bm, Cm, dt, A = ssd_prepare(xbc_raw, dt_raw, p)
    (y_f, _), (y_b, _) = ssd_bidirectional(xs, Bm, Cm, dt, A, hf_ctx, hb_ctx, True)
    y_ssd = ssd_output(y_f, y_b, xs, z, p)
    q = apply_rope_2(rms_norm_2(q, p['q_norm_g']), cos, sin)
    k = apply_rope_2(rms_norm_2(k, p['k_norm_g']), cos, sin)
    o = gqa_block_attention(q, jnp.concatenate([k_ctx, k], axis=1), jnp.concatenate([v_ctx, v], axis=1))
    return jnp.concatenate([y_ssd, o], -1) @ p['w_out']

def hier_moe(h, p):
    b, L, d = h.shape
    t = h.reshape(-1, d)
    g_prob = jax.nn.softmax((t @ p['w_rg'] + p['b_rg']).astype(F32), axis=-1)
    g_val, g_idx = lax.top_k(g_prob, 1)
    e_logits = (t @ p['w_re'] + p['b_re']).astype(F32).reshape(-1, MOE_GROUPS, EXPERTS_PER_GROUP)
    e_sel = jnp.take_along_axis(e_logits, g_idx[:, :, None], axis=1)[:, 0]
    e_val, e_idx = lax.top_k(jax.nn.softmax(e_sel, axis=-1), TOP_K_IN_GROUP)
    e_val = e_val / jnp.sum(e_val, -1, keepdims=True)
    w_group = jnp.sum(jax.nn.one_hot(e_idx, EXPERTS_PER_GROUP, dtype=F32) * e_val[..., None], axis=1)
    combine = jax.nn.one_hot(g_idx[:, 0], MOE_GROUPS, dtype=F32)[:, :, None] * g_val[:, :, None] * w_group[:, None, :]
    combine = combine.reshape(-1, N_EXPERTS).astype(t.dtype)
    gate = jnp.einsum('td,edf->tef', t, p['w_gate'])
    up = jnp.einsum('td,edf->tef', t, p['w_up'])
    hid = jax.nn.silu(gate) * up * combine[..., None]
    return jnp.einsum('tef,efd->td', hid, p['w_down']).reshape(b, L, d)

def second_inputs(seed: int = 0) -> dict:
    key = jax.random.key(seed)
    ks = jax.random.split(key, 28)
    nrm = lambda k, shape, scale: jax.random.normal(k, shape, F32) * scale
    beta = (8.0 * DEPTH_2) ** -0.25
    dt0 = jnp.exp(jax.random.uniform(ks[9], (DEPTH_2, 2, SSD_HEADS), F32, math.log(1e-3), math.log(1e-1)))
    dt_bias = dt0 + jnp.log(-jnp.expm1(-dt0))
    a_log = jnp.log(jax.random.uniform(ks[10], (DEPTH_2, 2, SSD_HEADS), F32, 1.0, 16.0))
    return {
        'x': nrm(ks[0], (BATCH, SEQ, D_MODEL), 1.0),
        'c': nrm(ks[1], (BATCH, D_MODEL), 1.0),
        'ctx': nrm(ks[2], (BATCH, CTX_LEN, D_MODEL), 1.0),
        'c_ctx': nrm(ks[3], (D_MODEL,), 1.0),
        'w_mod': nrm(ks[4], (DEPTH_2, D_MODEL, 6 * D_MODEL), 0.5 * D_MODEL ** -0.5),
        'b_mod': nrm(ks[5], (DEPTH_2, 6 * D_MODEL), 0.02),
        'w_in': nrm(ks[6], (DEPTH_2, D_MODEL, D_IN_PROJ), D_MODEL ** -0.5),
        'conv_w': nrm(ks[7], (DEPTH_2, CONV_W, D_XBC), CONV_W ** -0.5),
        'conv_b': nrm(ks[8], (DEPTH_2, D_XBC), 0.02),
        'dt_bias': dt_bias,
        'a_log': a_log,
        'd_skip': 1.0 + nrm(ks[11], (DEPTH_2, SSD_HEADS), 0.05),
        'ssd_norm_g': 1.0 + nrm(ks[12], (DEPTH_2, D_SSD), 0.05),
        'q_norm_g': 1.0 + nrm(ks[13], (DEPTH_2, HEAD_DIM), 0.05),
        'k_norm_g': 1.0 + nrm(ks[14], (DEPTH_2, HEAD_DIM), 0.05),
        'w_out': nrm(ks[15], (DEPTH_2, D_MIX, D_MODEL), beta * D_MIX ** -0.5),
        'ln1_g': 1.0 + nrm(ks[16], (DEPTH_2, D_MODEL), 0.05),
        'ln1_b': nrm(ks[17], (DEPTH_2, D_MODEL), 0.02),
        'w_rg': nrm(ks[18], (DEPTH_2, D_MODEL, MOE_GROUPS), D_MODEL ** -0.5),
        'b_rg': nrm(ks[19], (DEPTH_2, MOE_GROUPS), 0.01),
        'w_re': nrm(ks[20], (DEPTH_2, D_MODEL, N_EXPERTS), D_MODEL ** -0.5),
        'b_re': nrm(ks[21], (DEPTH_2, N_EXPERTS), 0.01),
        'w_gate': nrm(ks[22], (DEPTH_2, N_EXPERTS, D_MODEL, D_EXPERT), D_MODEL ** -0.5),
        'w_up': nrm(ks[23], (DEPTH_2, N_EXPERTS, D_MODEL, D_EXPERT), D_MODEL ** -0.5),
        'w_down': nrm(ks[24], (DEPTH_2, N_EXPERTS, D_EXPERT, D_MODEL), beta * D_EXPERT ** -0.5),
        'ln2_g': 1.0 + nrm(ks[25], (DEPTH_2, D_MODEL), 0.05),
        'ln2_b': nrm(ks[26], (DEPTH_2, D_MODEL), 0.02),
    }

def second_block(x, c, ctx, c_ctx, w_mod, b_mod, w_in, conv_w, conv_b, dt_bias, a_log, d_skip, ssd_norm_g,
              q_norm_g, k_norm_g, w_out, ln1_g, ln1_b, w_rg, b_rg, w_re, b_re, w_gate, w_up, w_down,
              ln2_g, ln2_b):
    n_rows = x.shape[1] // GRID_W
    cos, sin = axial_rope_tables(n_rows)
    alpha = (2.0 * DEPTH_2) ** 0.25
    silu_c = jax.nn.silu(c)
    silu_cc = jax.nn.silu(c_ctx)
    for l in range(DEPTH_2):
        last = l == DEPTH_2 - 1
        p = {'w_in': w_in[l], 'conv_w': conv_w[l], 'conv_b': conv_b[l], 'dt_bias': dt_bias[l],
             'a_log': a_log[l], 'd_skip': d_skip[l], 'ssd_norm_g': ssd_norm_g[l], 'q_norm_g': q_norm_g[l],
             'k_norm_g': k_norm_g[l], 'w_out': w_out[l], 'w_rg': w_rg[l], 'b_rg': b_rg[l], 'w_re': w_re[l],
             'b_re': b_re[l], 'w_gate': w_gate[l], 'w_up': w_up[l], 'w_down': w_down[l]}
        sh_a, sc_a, g_a, sh_f, sc_f, g_f = [m[:, None, :] for m in jnp.split(silu_c @ w_mod[l] + b_mod[l], 6, axis=-1)]
        n_mod = 3 if last else 6
        mod_c = jnp.split(silu_cc @ w_mod[l][:, :n_mod * D_MODEL] + b_mod[l][:n_mod * D_MODEL], n_mod, axis=-1)
        hc = ctx * (1.0 + mod_c[1]) + mod_c[0]
        ctx_side, ctx_out = context_mixer(hc, p, not last)
        hx = x * (1.0 + sc_a) + sh_a
        x = layer_norm_2(alpha * x + g_a * latent_mixer(hx, ctx_side, p, cos, sin), ln1_g[l], ln1_b[l])
        x = layer_norm_2(alpha * x + g_f * hier_moe(x * (1.0 + sc_f) + sh_f, p), ln2_g[l], ln2_b[l])
        if not last:
            ctx = layer_norm_2(alpha * ctx + mod_c[2] * ctx_out, ln1_g[l], ln1_b[l])
            ctx = layer_norm_2(alpha * ctx + mod_c[5] * hier_moe(ctx * (1.0 + mod_c[4]) + mod_c[3], p),
                             ln2_g[l], ln2_b[l])
    return x


def setup_inputs(seed=0):
    out = dict(first_inputs(seed))
    for name, value in second_inputs(seed + 1).items():
        if name != "x":
            out[name + "_2"] = value
    return out


def reference(
    x, norm_mix_pre, norm_mix_post, norm_ffn_pre, norm_ffn_post, w_in, nsa_cmp_pos, nsa_cmp_w1,
    nsa_cmp_w2, swa_sinks, conv_w, conv_b, conv_ln_g, conv_ln_b, pool_w, pool_scale, w_branch,
    w_gate, w_o, ffn_w_up, ffn_conv_w, ffn_conv_b, ffn_w_down, c_2, ctx_2, c_ctx_2, w_mod_2,
    b_mod_2, w_in_2, conv_w_2, conv_b_2, dt_bias_2, a_log_2, d_skip_2, ssd_norm_g_2, q_norm_g_2,
    k_norm_g_2, w_out_2, ln1_g_2, ln1_b_2, w_rg_2, b_rg_2, w_re_2, b_re_2, w_gate_2, w_up_2,
    w_down_2, ln2_g_2, ln2_b_2,
):
    x = first_block(
        x, norm_mix_pre, norm_mix_post, norm_ffn_pre, norm_ffn_post, w_in, nsa_cmp_pos,
        nsa_cmp_w1, nsa_cmp_w2, swa_sinks, conv_w, conv_b, conv_ln_g, conv_ln_b, pool_w,
        pool_scale, w_branch, w_gate, w_o, ffn_w_up, ffn_conv_w, ffn_conv_b, ffn_w_down,
    )
    return second_block(
        x, c_2, ctx_2, c_ctx_2, w_mod_2, b_mod_2, w_in_2, conv_w_2, conv_b_2, dt_bias_2,
        a_log_2, d_skip_2, ssd_norm_g_2, q_norm_g_2, k_norm_g_2, w_out_2, ln1_g_2, ln1_b_2,
        w_rg_2, b_rg_2, w_re_2, b_re_2, w_gate_2, w_up_2, w_down_2, ln2_g_2, ln2_b_2,
    )


_drawn_inputs = setup_inputs


def setup_inputs(seed=0):
    import zlib

    import numpy as np

    out = dict(_drawn_inputs(seed))
    spreads = {}
    factors = {'swa_sinks': 4.641,
     'conv_b': 4.104,
     'conv_ln_b': 8.0,
     'ffn_conv_b': 4.75,
     'ctx_2': 8.0,
     'c_ctx_2': 7.734,
     'b_mod_2': 7.028,
     'conv_b_2': 8.0,
     'a_log_2': 3.998,
     'd_skip_2': 64.0,
     'ssd_norm_g_2': 28.351,
     'q_norm_g_2': 8.0,
     'k_norm_g_2': 8.0,
     'ln1_b_2': 2.768,
     'b_rg_2': 37.259,
     'b_re_2': 64.0,
     'ln2_b_2': 2.76}
    for name, (base, spread) in spreads.items():
        noise = np.random.default_rng([zlib.crc32(name.encode()), seed]).standard_normal(out[name].shape)
        drawn = base * np.exp(spread * noise) if base else spread * noise
        out[name] = jnp.asarray(drawn.astype(out[name].dtype))
    for name, factor in factors.items():
        out[name] = (out[name] * factor).astype(out[name].dtype)
    return out
```

```python
from contextlib import ExitStack

import numpy as np

import concourse.bass as bass
import concourse.mybir as mybir

F32 = mybir.dt.float32
ALU = mybir.AluOpType
ACT = mybir.ActivationFunctionType
AX_X = mybir.AxisListType.X

P = 128
T = 256
TT = T // P
D = 1024
KD = D // P
LAYERS = 2
DH = 64
BR = 512
NEG = -1e30
EPS = 1e-6
SLOTS = 4
CH = 2048
DFF = 2816
FB = DFF // P
TAPS = 31
CMP_N = 15
N_LAYER_CHUNKS = 80


def offsets(fields):
    at, out = 0, {}
    for name, width in fields:
        out[name] = (at, width)
        at += width
    return out, at


COLS, N_COLS = offsets([
    ("g_mix", KD), ("g_ffn", KD), ("pos", 32), ("w2", 256), ("conv_w", 4 * TAPS), ("conv_b", 4),
    ("ln_g", 4), ("ln_b", 4), ("pool_w", 512), ("pool_s", 4), ("fw", 2 * FB * 3), ("fb", 2 * FB),
    ("w_ga", KD * 24),
])
ROWS, N_ROWS = offsets([("mix_post", D), ("ffn_post", D), ("sinks", 8)])
CONST, N_CONST = offsets([
    ("ident", P), ("tri_u", P), ("tri_l", P), ("ones", P), ("full_causal", 2 * P), ("band", 2 * P),
    ("cmp_mask", 32), ("cmp_valid", 2), ("blk8", 8), ("rope", 192), ("axial", 192),
    ("pool_inv", 64), ("mhalf", 32), ("four", 4),
])


def constants():
    c = np.zeros((P, N_CONST), np.float32)

    def put(name, value):
        at, width = CONST[name]
        c[:, at:at + width] = np.asarray(value, np.float32).reshape(P, width)

    q = np.arange(P)
    later = q[:, None] >= q[None, :]
    causal = np.where(later, 0.0, NEG)
    put("ident", np.eye(P))
    put("tri_u", q[:, None] <= q[None, :])
    put("tri_l", later)
    put("ones", np.ones((P, P)))
    put("full_causal", np.concatenate([np.zeros((P, P)), causal], 1))
    put("band", np.concatenate([np.where(q[None, :] > q[:, None], 0.0, NEG), causal], 1))
    t = q[:, None] + P * np.arange(TT)[None, :]
    end = np.where(np.arange(16) < CMP_N, np.arange(16) * 16 + 31, 10 ** 9)
    put("cmp_mask", np.where(end[None, None, :] <= t[:, :, None], 0.0, NEG))
    put("cmp_valid", t >= 31)
    put("blk8", q[:, None] // 16 == np.arange(8)[None, :])
    inv = 1.0 / (10000.0 ** (np.arange(0, 64, 2, dtype=np.float32) / 64))
    ang = t[:, :, None].astype(np.float32) * inv.astype(np.float32)
    put("rope", np.stack([np.cos(ang), np.sin(ang), -np.sin(ang)], 1))
    inv = np.power(np.float32(10000.0), -np.arange(0, 32, 2, dtype=np.float32) / 32)
    ang = np.concatenate([(t // 64)[:, :, None] * inv, (t % 64)[:, :, None] * inv], -1).astype(np.float32)
    put("axial", np.stack([np.cos(ang), np.sin(ang), -np.sin(ang)], 1))
    put("pool_inv", np.broadcast_to(
        [[1.0 / min(w, i + 1) for i in range(16)] for w in (2, 4, 8, 16)], (P, 4, 16)))
    put("mhalf", np.full((P, 32), -0.5))
    put("four", np.broadcast_to([4.0, 3.0, 2.0, 1.0], (P, 4)))
    return c


REGION = {**{f"a{i}": (i * 512, 512) for i in range(4)}, "s": (2048, 1024), "t": (3072, 512), "u": (3584, 512)}


class Jobs:

    def __init__(self, psum, filled, drained, region=REGION, ring=4):
        self.psum, self.filled, self.drained, self.region, self.ring = psum, filled, drained, region, ring
        self.jobs, self.turn, self.sum, self.next = {}, {}, {}, 0

    def plan(self, name, region=None, drains=1):
        if region is None:
            region, self.next = f"a{self.next % self.ring}", self.next + 1
        before, turn = self.sum.get(region, 0), self.turn.get(region, 0)
        self.jobs[name] = (region, turn + 1, before, before + drains)
        self.turn[region], self.sum[region] = turn + 1, before + drains

    def out(self, name):
        at, width = self.region[self.jobs[name][0]]
        return self.psum[:, at:at + width]

    def claim(self, pe, name):
        region, _, before, _ = self.jobs[name]
        if before:
            pe.wait_ge(self.drained[region], before)

    def fill(self, ins, name):
        ins.then_inc(self.filled[self.jobs[name][0]], 1)

    def wait_filled(self, eng, name):
        region, turn, _, _ = self.jobs[name]
        eng.wait_ge(self.filled[region], turn)

    def drain(self, ins, name):
        ins.then_inc(self.drained[self.jobs[name][0]], 1)

    def wait_drained(self, eng, name):
        region, _, _, after = self.jobs[name]
        eng.wait_ge(self.drained[region], after)


class Signal:

    def __init__(self, sem):
        self.sem, self.n = sem, 0

    def up(self, ins):
        self.n += 1
        ins.then_inc(self.sem, 1)

    def here(self, eng, less=0):
        if self.n - less > 0:
            eng.wait_ge(self.sem, self.n - less)


def bc(ap, shape):
    return ap.to_broadcast(shape)


ATT = [("slc", 0, 0, 384), ("win", 0, 1, 640), ("swa", 1, 2, 896)]
ITEMS = [(a, t, g) for a in range(3) for t in range(TT) for g in range(2)]


def plan_layer(jobs):
    for c in range(2):
        for t in range(TT):
            jobs.plan(("ht", c, t))
    for w in ("kv", "kv2", "q", "dq"):
        for t in range(TT):
            jobs.plan((w, t))
    jobs.plan("ga")
    for t in range(TT):
        jobs.plan(("cd", t))
    for i in range(2):
        jobs.plan(("c", i))
    for t in range(TT):
        jobs.plan(("qT", t))
        jobs.plan(("rkT", t))
    for i in range(2):
        jobs.plan(("ba", i))
    for kv in range(2):
        jobs.plan(("hid", kv))
    for i in range(2):
        jobs.plan(("bg", i))
    jobs.plan("kc", drains=2)
    jobs.plan("vc")
    for t in range(TT):
        jobs.plan(("rqT", t))
        jobs.plan(("rdT", t))
    for i in range(2):
        jobs.plan(("pool", i), drains=2)
    for t in range(TT):
        jobs.plan(("cs", t))
    for t in range(TT):
        jobs.plan(("cpT", t), "t")
        jobs.plan(("co", t), "u")
    for a, t, g in ITEMS:
        jobs.plan(("S", a, t, g), "s")
        for kb in range(t + 1):
            jobs.plan(("PT", a, t, g, kb), "t")
        if g == 1:
            jobs.plan(("O", a, t), "u")
    for i in range(16):
        jobs.plan(("gate", i))
    for t in range(TT):
        jobs.plan(("convT", t))
    for t in range(TT):
        jobs.plan(("oaT", t))
        jobs.plan(("odT", t))
    for n in BRANCH_ORDER:
        for i in range(4):
            if (n, i) == (3, 2):
                for t in range(TT):
                    jobs.plan(("obT", t), drains=4)
            jobs.plan(("up", n, i))
    for c in range(2):
        for t in range(TT):
            jobs.plan(("wo", c, t), drains=2)
    for c in range(2):
        for t in range(TT):
            jobs.plan(("hf", c, t))
    for j in range(FB):
        jobs.plan(("ffn", j))
    for t in range(TT):
        for c in range(2):
            jobs.plan(("down", c, t), f"a{2 * t + c}", drains=2)


BRANCH_ORDER = (2, 0, 3, 1)


def layer_block(nc, l, mem, ring, landed, used, wts, psum, sems, cols_dram, rows_dram, loaded):
    filled = {r: sems(f"filled_{r}") for r in REGION}
    drained = {r: sems(f"drained_{r}") for r in REGION}
    jobs = Jobs(psum, filled, drained)
    plan_layer(jobs)

    squares = sems("squares")
    rstd_ready = sems("rstd_ready")
    normed = sems("normed")
    kd_ready = sems("kd_ready")
    roped = sems("roped")
    flat_ready = sems("flat_ready")
    sig_ready = sems("sig_ready")
    conv_done = sems("conv_done")
    stat_ready = sems("stat_ready")
    lnstd_ready = sems("lnstd_ready")
    pooled = sems("pooled")
    cmp_s = sems("cmp_s")
    cmp_e = sems("cmp_e")
    cmp_coef = sems("cmp_coef")
    masked = sems("masked")
    exped = sems("exped")
    tail_sent = sems("tail_sent")
    gates_ready = sems("gates_ready")
    o_ready = sems("o_ready")
    prod = sems("prod")
    mixed = sems("mixed")
    hid_ready = sems("hid_ready")
    ffn_init = sems("ffn_init")
    gelued = sems("gelued")
    f_ready = sems("f_ready")
    x_ready = sems("x_ready")
    params = sems("params")
    v_order, a_order, g_order = sems("v_order"), sems("a_order"), sems("g_order")

    x, tm, hT, proj, gates, qTs, rkT = (mem[k] for k in ("x", "tm", "hT", "proj", "gates", "qTs", "rkT"))
    kd = gates[:, 0:1024].rearrange("p (t m r d) -> p t m r d", t=2, m=4, r=2)
    flat = gates[:, 0:960].rearrange("p (m l n) -> p m l n", m=4, n=CMP_N)
    cdT = gates[:, 2048:3072].rearrange("p (m t) -> p m t", m=4)
    rtmp = gates[:, 3072:4480]
    rot = gates[:, 4480:7296].rearrange("p (t c) -> p t c", t=2)
    fT = gates[:, 0:FB * T].rearrange("p (j t) -> p j t", j=FB)
    oa, od = tm[:, 0, :].rearrange("p (t c) -> p t c", t=2), tm[:, 1, :].rearrange("p (t c) -> p t c", t=2)
    hq = [proj[:, 0, :], proj[:, 1, :]]
    ln_tm = proj[:, :, 1024:1536]
    sg = mem["sg"]
    hidk, hidv, kblk, vblk = mem["hidk"], mem["hidv"], mem["kblk"], mem["vblk"]
    sc, pt = mem["sc"], mem["pt"]
    small = mem["small"]
    brT, mixT, bglu, cpad, acc, tmp = (mem[k] for k in ("brT", "hT", "bglu", "cpad", "acc", "tmp"))
    cols, rows, const = mem["cols"], mem["rows"], mem["const"]

    def K(name, a=0, b=None):
        at, width = CONST[name]
        return const[:, at + a:at + (width if b is None else b)]

    def C(name, a=0, b=None):
        at, width = COLS[name]
        return cols[:, at + a:at + (width if b is None else b)]

    def R(name):
        at, width = ROWS[name]
        return rows[:, at:at + width]

    ident = K("ident")
    ga = small[:, 0:48].rearrange("p (t b h) -> p t b h", t=2, b=3)
    ss, rstd = small[:, 48:52], small[:, 52:56]
    ss4 = small[:, 56:60].rearrange("p (t c) -> p t c", t=2)
    nmax = small[:, 64:72]
    den, coef = small[:, 72:88].rearrange("p (b h) -> p b h", b=2), small[:, 88:104].rearrange("p (b h) -> p b h", b=2)
    stats, mv, lnstd = small[:, 104:116].rearrange("p (t s) -> p t s", t=2), small[:, 116:120].rearrange("p (t s) -> p t s", t=2), small[:, 120:122]
    cden = small[:, 128:144].rearrange("p (t h) -> p t h", t=2)
    cmax = small[:, 144:160].rearrange("p (t h) -> p t h", t=2)
    ccoef = small[:, 160:176].rearrange("p (t h) -> p t h", t=2)
    sinkv = small[:, 176:192].rearrange("p (b g j) -> p b g j", b=2, g=2)
    msq = small[:, 184:188]
    csc = mem["csc"]

    with nc.Block() as block:
        @block.sync
        def _(sp):
            with sp.Fori(0, N_LAYER_CHUNKS // SLOTS) as turn:
                for s in range(SLOTS):
                    sp.wait_ge(used, l * N_LAYER_CHUNKS + turn * SLOTS + (s + 1))
                    sp.dma_start(ring[:, s, :], wts[l * N_LAYER_CHUNKS + turn * SLOTS + (s + SLOTS)]).then_inc(landed[s], 16)

        @block.tensor
        def _(pe):
            state = {"chunk": 0, "owed": False}

            def next_chunk():
                c = state["chunk"]
                state["chunk"] += 1
                pe.wait_ge(landed[c % SLOTS], (l * (N_LAYER_CHUNKS // SLOTS) + (c // SLOTS + 1)) * 16)
                return ring[:, c % SLOTS, :]

            def done_with(ins):
                ins.then_inc(used, 1)

            def carry(ins):
                if state["owed"]:
                    ins.then_inc(used, 1)
                    state["owed"] = False

            def transpose4(name, blocks):
                jobs.claim(pe, name)
                out = jobs.out(name)
                for i, b in enumerate(blocks):
                    n = b.shape[1]
                    mm = pe.transpose(out[0:n, i * P:(i + 1) * P], b, ident)
                jobs.fill(mm, name)

            pe.wait_ge(loaded, 32)
            pe.wait_ge(params, 32)
            for c in range(2):
                for t in range(TT):
                    pe.wait_ge(normed, t + 1)
                    transpose4(("ht", c, t), [tm[:, t, (4 * c + i) * P:(4 * c + i + 1) * P] for i in range(4)])

            for w in ("kv", "kv2", "q", "dq"):
                for half in range(2):
                    chunk = next_chunk().rearrange("p (k n) -> p k n", k=4)
                    for t in range(TT):
                        if w == "kv":
                            jobs.wait_drained(pe, ("ht", half, t))
                        if half == 0:
                            jobs.claim(pe, (w, t))
                        for k in range(4):
                            mm = pe.matmul(jobs.out((w, t)), hT[:, 4 * half + k, t * P:(t + 1) * P], chunk[:, k, :],
                                           start=(half == 0 and k == 0), stop=(half == 1 and k == 3))
                            if k == 0:
                                carry(mm)
                        if half == 1 and t == 0:
                            jobs.fill(mm, (w, t))
                    if half == 0:
                        done_with(mm)
                    else:
                        jobs.fill(mm, (w, 1))
                        state["owed"] = True

            jobs.claim(pe, "ga")
            for t in range(TT):
                for k in range(KD):
                    mm = pe.matmul(jobs.out("ga")[:, 24 * t:24 * t + 24], hT[:, k, t * P:(t + 1) * P],
                                   C("w_ga", 24 * k, 24 * k + 24), start=(k == 0), stop=(k == KD - 1))
                    if k == 0:
                        carry(mm)
            jobs.fill(mm, "ga")

            def blocks_fm(name):
                chunk = next_chunk().rearrange("p (k m) -> p k m", k=KD)
                jobs.claim(pe, name)
                for b in range(2):
                    for k in range(KD):
                        mm = pe.matmul(jobs.out(name)[:, b * T:(b + 1) * T], chunk[:, k, b * P:(b + 1) * P], hT[:, k, :],
                                       start=(k == 0), stop=(k == KD - 1))
                        if k == 0:
                            carry(mm)
                jobs.fill(mm, name)
                return name

            def release(name):
                assert not state["owed"]
                state["owed"] = True

            for t in range(TT):
                pe.wait_ge(kd_ready, t + 1)
                transpose4(("cd", t), [kd[:, t, m, :, :].rearrange("p r d -> p (r d)") for m in range(4)])
            for i in range(2):
                release(blocks_fm(("c", i)))
            for t in range(TT):
                jobs.wait_drained(pe, ("q", t))
                transpose4(("qT", t), [proj[:, t, 1024 + i * P:1024 + (i + 1) * P] for i in range(4)])
                pe.wait_ge(roped, 3 * t + 1)
                transpose4(("rkT", t), [rot[:, t, i * P:(i + 1) * P] for i in range(3)])
            for i in range(2):
                release(blocks_fm(("ba", i)))

            for kv in range(2):
                for half in range(2):
                    chunk = next_chunk().rearrange("p (l h) -> p l h", l=8)
                    if half == 0:
                        jobs.claim(pe, ("hid", kv))
                        pe.wait_ge(flat_ready, 4 * kv + 4)
                    for ht in range(2):
                        out = jobs.out(("hid", kv))[:, (2 * half + ht) * 32:(2 * half + ht) * 32 + 30]
                        for lp in range(8):
                            mm = pe.matmul(out.rearrange("p (g n) -> p g n", g=2), chunk[:, lp, ht * P:(ht + 1) * P],
                                           flat[:, 2 * kv:2 * kv + 2, 8 * half + lp, :], start=(lp == 0), stop=(lp == 7))
                            if lp == 0:
                                carry(mm)
                    if half == 0:
                        done_with(mm)
                jobs.fill(mm, ("hid", kv))
                release(("hid", kv))
            for i in range(2):
                release(blocks_fm(("bg", i)))

            pe.wait_ge(hid_ready, 2)
            jobs.claim(pe, "kc")
            for g in range(2):
                for ht in range(2):
                    mm = pe.matmul(jobs.out("kc")[64 * g:64 * g + 64, 0:CMP_N], C("w2", 64 * ht, 64 * ht + 64),
                                   hidk[:, ht, g, 0:CMP_N], start=(ht == 0), stop=(ht == 1))
            jobs.fill(mm, "kc")
            pe.wait_ge(hid_ready, 4)
            jobs.claim(pe, "vc")
            for ht in range(2):
                mm = pe.matmul(jobs.out("vc")[:, 0:DH], hidv[:, ht, :], C("w2", 128 + 64 * ht, 128 + 64 * ht + 64),
                               start=(ht == 0), stop=(ht == 1))
            jobs.fill(mm, "vc")
            for t in range(TT):
                pe.wait_ge(roped, 3 * t + 2)
                transpose4(("rqT", t), [rot[:, t, 384 + i * P:384 + (i + 1) * P] for i in range(4)])
                pe.wait_ge(roped, 3 * t + 3)
                transpose4(("rdT", t), [rot[:, t, 896 + i * P:896 + (i + 1) * P] for i in range(4)])
            for i in range(2):
                jobs.claim(pe, ("pool", i))
                pe.wait_ge(pooled, 2 * i + 2)
                for b in range(2):
                    mm = pe.matmul(jobs.out(("pool", i))[:, b * T:(b + 1) * T], C("pool_w", (2 * i + b) * P, (2 * i + b + 1) * P),
                                   brT[:, 1, 2 * i + b, :], start=True, stop=True)
                jobs.fill(mm, ("pool", i))

            jobs.wait_drained(pe, "kc")
            for t in range(TT):
                jobs.wait_drained(pe, ("qT", t))
                jobs.claim(pe, ("cs", t))
                for j in range(4):
                    mm = pe.matmul(jobs.out(("cs", t))[:, 32 * j:32 * j + 32], qTs[:, 0, j, t * P:(t + 1) * P],
                                   kblk[:, :], start=True, stop=True)
                jobs.fill(mm, ("cs", t))

            gate_at = {"n": 0}

            def gate_chunks(n):
                for _ in range(n):
                    if gate_at["n"] < 16:
                        release(blocks_fm(("gate", gate_at["n"])))
                        gate_at["n"] += 1

            def cmp_out():
                for t in range(TT):
                    pe.wait_ge(cmp_e, t + 1)
                    transpose4(("cpT", t), [csc[:, t, :]])
                gate_chunks(1)
                jobs.wait_drained(pe, "vc")
                for t in range(TT):
                    jobs.wait_drained(pe, ("cpT", t))
                    jobs.claim(pe, ("co", t))
                    mm = pe.matmul(jobs.out(("co", t)), mem["cpT"][:, t, :], vblk[:, :], start=True, stop=True)
                    jobs.fill(mm, ("co", t))

            def scores(i):
                a, t, g = ITEMS[i]
                _, rq, rk, _ = ATT[a]
                name = ("S", a, t, g)
                if g == 0:
                    jobs.wait_drained(pe, ("rkT", t))
                    jobs.wait_drained(pe, (("rqT", "rdT")[rq], t))
                jobs.claim(pe, name)
                for j in range(4):
                    nk = (t + 1) * P
                    mm = pe.matmul(jobs.out(name)[:, j * T:j * T + nk], qTs[64 * g:64 * g + 64, 1 + rq, j, t * P:(t + 1) * P],
                                   rkT[64 * g:64 * g + 64, rk, 0:nk], start=True, stop=True)
                jobs.fill(mm, name)

            def turn_probs(i):
                a, t, g = ITEMS[i]
                pe.wait_ge(exped, 4 * i + 4)
                for kb in range(t + 1):
                    transpose4(("PT", a, t, g, kb), [sc[:, i % 2, j, kb * P:(kb + 1) * P] for j in range(4)])

            def values(i):
                a, t, g = ITEMS[i]
                v = ATT[a][3]
                if g == 0:
                    jobs.claim(pe, ("O", a, t))
                for kb in range(t + 1):
                    jobs.wait_drained(pe, ("PT", a, t, g, kb))
                for j in range(4):
                    for kb in range(t + 1):
                        mm = pe.matmul(jobs.out(("O", a, t))[:, (2 * j + g) * DH:(2 * j + g + 1) * DH], pt[:, i % 2, kb, j, :],
                                       proj[:, kb, v + DH * g:v + DH * g + DH], start=(kb == 0), stop=(kb == t))
                if g == 1:
                    jobs.fill(mm, ("O", a, t))

            for i in range(len(ITEMS) + 1):
                if i < len(ITEMS):
                    scores(i)
                gate_chunks(1)
                if i == 1:
                    cmp_out()
                if i >= 1:
                    turn_probs(i - 1)
                    gate_chunks(i % 3 == 0)
                    values(i - 1)
            gate_chunks(16)

            for t in range(TT):
                pe.wait_ge(conv_done, 4 * TAPS)
                transpose4(("convT", t), [acc[:, b, t * P:(t + 1) * P] for b in range(4)])
            for t in range(TT):
                pe.wait_ge(o_ready, t + 1)
                jobs.wait_drained(pe, ("O", 2, t))
                transpose4(("oaT", t), [oa[:, t, b * P:(b + 1) * P] for b in range(4)])
                transpose4(("odT", t), [od[:, t, b * P:(b + 1) * P] for b in range(4)])

            for n in BRANCH_ORDER:
                for half in range(2):
                    if n == 3 and half == 1:
                        for t in range(TT):
                            jobs.wait_drained(pe, ("convT", t))
                            transpose4(("obT", t), [ln_tm[:, t, b * P:(b + 1) * P] for b in range(4)])
                    chunk = next_chunk().rearrange("p (k n) -> p k n", k=4)
                    if half == 0:
                        for name in {0: [("oaT", 0), ("oaT", 1)], 3: [("odT", 0), ("odT", 1)], 2: [("pool", 0), ("pool", 1)],
                                     1: [("obT", 0), ("obT", 1)]}[n]:
                            jobs.wait_drained(pe, name)
                    for i in range(2):
                        name = ("up", n, 2 * half + i)
                        jobs.claim(pe, name)
                        for b in range(2):
                            for k in range(4):
                                mm = pe.matmul(jobs.out(name)[:, b * T:(b + 1) * T], chunk[:, k, (2 * i + b) * P:(2 * i + b + 1) * P],
                                               brT[:, n, k, :], start=(k == 0), stop=(k == 3))
                                if k == 0:
                                    carry(mm)
                        jobs.fill(mm, name)
                    release(name)

            def to_tokens(kind, c, half, t, chunk, src):
                name = (kind, c, t)
                if half == 0:
                    jobs.claim(pe, name)
                for k in range(4):
                    mm = pe.matmul(jobs.out(name), src[:, 4 * half + k, t * P:(t + 1) * P], chunk[:, k, :],
                                   start=(half == 0 and k == 0), stop=(half == 1 and k == 3))
                    if k == 0:
                        carry(mm)
                if half == 1:
                    jobs.fill(mm, name)
                return mm

            pe.wait_ge(mixed, 12)
            for c in range(2):
                for half in range(2):
                    chunk = next_chunk().rearrange("p (k n) -> p k n", k=4)
                    for t in range(TT):
                        mm = to_tokens("wo", c, half, t, chunk, mixT)
                    if half == 0:
                        done_with(mm)
                    else:
                        release(("wo", c, 1))

            for c in range(2):
                for t in range(TT):
                    pe.wait_ge(normed, TT + t + 1)
                    transpose4(("hf", c, t), [tm[:, t, (4 * c + i) * P:(4 * c + i + 1) * P] for i in range(4)])
            for c in range(2):
                for t in range(TT):
                    jobs.wait_drained(pe, ("hf", c, t))
            for j in range(FB):
                release(blocks_fm(("ffn", j)))
            for t in range(TT):
                for c in range(2):
                    jobs.claim(pe, ("down", c, t))
            for i in range(FB // 2):
                chunk = next_chunk().rearrange("p (k n) -> p k n", k=2)
                for k in range(2):
                    pe.wait_ge(f_ready, 2 * i + k + 1)
                    for t in range(TT):
                        for c in range(2):
                            name = ("down", c, t)
                            mm = pe.matmul(jobs.out(name), fT[:, 2 * i + k, t * P:(t + 1) * P], chunk[:, k, c * 512:(c + 1) * 512],
                                           start=(i == 0 and k == 0), stop=(2 * i + k == FB - 1))
                            if k == 0:
                                carry(mm)
                            if 2 * i + k == FB - 1:
                                jobs.fill(mm, name)
                if i < FB // 2 - 1:
                    done_with(mm)
            jobs.wait_filled(pe, ("down", 1, 1))
            pe.sem_inc(used, 1)
            next_chunk()
            pe.sem_inc(used, 1)
            assert state["chunk"] == N_LAYER_CHUNKS, state

        @block.scalar
        def _(act):
            order = Signal(a_order)

            def square(src, out, total, sig):
                act.activation(out, src, ACT.Square, accum_out=total).then_inc(sig, 1)

            act.dma_start(cols[:, :], cols_dram[l]).then_inc(params, 16)
            act.dma_start(rows[:, :], rows_dram[l].to_broadcast([P, N_ROWS])).then_inc(params, 16)
            act.wait_ge(loaded, 32)
            for t in range(TT):
                square(x[:, t, :], tm[:, t, :], ss[:, t:t + 1], squares)

            def copy_out(name, dst, src=None, scale=1.0, func=ACT.Copy):
                jobs.wait_filled(act, name)
                jobs.drain(act.activation(dst, jobs.out(name) if src is None else src, func, scale=scale), name)

            for w, at in (("kv", 0), ("kv2", 512), ("q", 1024), ("dq", 1536)):
                for t in range(TT):
                    copy_out((w, t), proj[:, t, at:at + 512])
            copy_out("ga", small[:, 0:48], jobs.out("ga")[:, 0:48], func=ACT.Sigmoid)
            for t in range(TT):
                copy_out(("cd", t), cdT[:, :, t * P:(t + 1) * P], jobs.out(("cd", t)).rearrange("p (m t) -> p m t", m=4))
            for i in range(2):
                copy_out(("c", i), cpad[:, 2 * i:2 * i + 2, 16:16 + T], jobs.out(("c", i)).rearrange("p (b t) -> p b t", b=2))
            for t in range(TT):
                copy_out(("qT", t), qTs[:, 0, :, t * P:(t + 1) * P], jobs.out(("qT", t)).rearrange("p (m t) -> p m t", m=4), 0.125)
            for i in range(2):
                copy_out(("ba", i), bglu[:, 2 * i:2 * i + 2, TAPS - 1:TAPS - 1 + T], jobs.out(("ba", i)).rearrange("p (b t) -> p b t", b=2))
            for ht in range(2):
                jobs.wait_drained(act, ("hid", 0))
                act.activation(hidk[:, ht, :, 0:CMP_N], mem["hsum"][:, 0, ht, 0:30].rearrange("p (g n) -> p g n", g=2),
                               ACT.Gelu_apprx_tanh).then_inc(hid_ready, 1)
            for ht in range(2):
                jobs.wait_drained(act, ("hid", 1))
                act.activation(hidv[:, ht, :].rearrange("p (j g n) -> p j g n", j=4, g=2)[:, :, :, 0:CMP_N],
                               bc(mem["hsum"][:, 1, ht, 0:30].rearrange("p (g n) -> p g n", g=2).unsqueeze(1), [P, 4, 2, CMP_N]),
                               ACT.Gelu_apprx_tanh).then_inc(hid_ready, 1)
            for i in range(2):
                copy_out(("bg", i), sg[:, i, :], func=ACT.Sigmoid)
            for t in range(TT):
                copy_out(("rqT", t), qTs[:, 1, :, t * P:(t + 1) * P], jobs.out(("rqT", t)).rearrange("p (m t) -> p m t", m=4), 0.125)
                copy_out(("rdT", t), qTs[:, 2, :, t * P:(t + 1) * P], jobs.out(("rdT", t)).rearrange("p (m t) -> p m t", m=4), 0.125)
            for i in range(2):
                jobs.wait_filled(act, ("pool", i))
                for b in range(2):
                    n = 2 * i + b
                    jobs.drain(act.activation(brT[:, 2, n, :], jobs.out(("pool", i))[:, b * T:(b + 1) * T], ACT.Copy,
                                              scale=C("pool_s", n, n + 1)), ("pool", i))

            gate_at = {"n": 0}

            def gate_out(n):
                for _ in range(n):
                    i = gate_at["n"]
                    if i < 16:
                        copy_out(("gate", i), gates[:, i * 512:(i + 1) * 512])
                        gate_at["n"] += 1

            def exps(i):
                a, t, g = ITEMS[i]
                act.wait_ge(masked, i + 1)
                if a == 2:
                    act.activation(sinkv[:, i // 2 % 2, g, :], sinkv[:, i // 2 % 2, g, :], ACT.Exp).then_inc(tail_sent, 1)
                for j in range(4):
                    b = den[:, (i // 2) % 2, 2 * j + g:2 * j + g + 1]
                    act.activation(sc[:, i % 2, j, 0:(t + 1) * P], sc[:, i % 2, j, 0:(t + 1) * P], ACT.Exp,
                                   bias=nmax[:, 4 * (i % 2) + j:4 * (i % 2) + j + 1], accum_out=b).then_inc(exped, 1)

            for t in range(TT):
                act.wait_ge(cmp_s, t + 1)
                act.activation(csc[:, t, :], csc[:, t, :], ACT.Exp).then_inc(cmp_e, 1)
            for i in range(len(ITEMS) + 1):
                if i == 1:
                    gate_out(1)
                    for t in range(TT):
                        copy_out(("cpT", t), mem["cpT"][:, t, :], jobs.out(("cpT", t))[:, 0:P])
                    gate_out(1)
                else:
                    gate_out(1)
                if i >= 1:
                    a, t, g = ITEMS[i - 1]
                    for kb in range(t + 1):
                        copy_out(("PT", a, t, g, kb), pt[:, (i - 1) % 2, kb, :, :], jobs.out(("PT", a, t, g, kb)).rearrange("p (j q) -> p j q", j=4))
                if i < len(ITEMS):
                    exps(i)
                if i >= 1:
                    gate_out(i % 3 == 0)
            gate_out(16)
            for n in BRANCH_ORDER:
                for i in range(4):
                    jobs.wait_drained(act, ("gate", 12 + i))
                act.activation(gates[:, n * 2048:(n + 1) * 2048], gates[:, n * 2048:(n + 1) * 2048], ACT.Sigmoid).then_inc(gates_ready, 1)
            for t in range(TT):
                copy_out(("oaT", t), brT[:, 0, :, t * P:(t + 1) * P], jobs.out(("oaT", t)).rearrange("p (m t) -> p m t", m=4))
                copy_out(("odT", t), brT[:, 3, :, t * P:(t + 1) * P], jobs.out(("odT", t)).rearrange("p (m t) -> p m t", m=4))
            for t in range(TT):
                jobs.wait_filled(act, ("obT", t))
                for b in range(4):
                    jobs.drain(act.activation(brT[:, 1, b, t * P:(t + 1) * P], jobs.out(("obT", t))[:, b * P:(b + 1) * P], ACT.Silu,
                                              scale=C("ln_g", b, b + 1), bias=C("ln_b", b, b + 1)), ("obT", t))

            def post(kind, c, t):
                name = (kind, c, t)
                jobs.wait_filled(act, name)
                jobs.drain(act.activation(tm[:, t, c * 512:(c + 1) * 512], jobs.out(name), ACT.Copy), name)
                region, _, before, _ = jobs.jobs[name]
                act.wait_ge(drained[region], before + 1)
                jobs.drain(act.activation(jobs.out(name), jobs.out(name), ACT.Square, accum_out=ss4[:, t, c:c + 1]), name)

            for c in range(2):
                for t in range(TT):
                    post("wo", c, t)
            for t in range(TT):
                act.wait_ge(x_ready, t + 1)
                square(x[:, t, :], tm[:, t, :], ss[:, t:t + 1], squares)

            for j in range(FB + 1):
                if j < FB:
                    jobs.wait_filled(act, ("ffn", j))
                    if j >= 4:
                        act.wait_ge(f_ready, j - 3)
                    u = hq[j % 2][:, (j // 2 % 2) * 512:(j // 2 % 2) * 512 + 512]
                    for b in range(2):
                        n = 2 * j + b
                        act.activation(u[:, b * T:(b + 1) * T], jobs.out(("ffn", j))[:, b * T:(b + 1) * T], ACT.Identity,
                                       scale=C("fw", 3 * n + 2, 3 * n + 3), bias=C("fb", n, n + 1)).then_inc(ffn_init, 1)
                if j >= 1:
                    u = hq[(j - 1) % 2][:, ((j - 1) // 2 % 2) * 512:((j - 1) // 2 % 2) * 512 + 512]
                    jobs.wait_drained(act, ("ffn", j - 1))
                    act.activation(u[:, 0:T], u[:, 0:T], ACT.Gelu_apprx_tanh).then_inc(gelued, 1)
            for t in range(TT):
                for c in range(2):
                    post("down", c, t)

        @block.vector
        def _(dve):
            order = Signal(v_order)
            conv = Signal(conv_done)

            def norm_tiles(first):
                for t in range(TT):
                    dve.wait_ge(rstd_ready, first)
                    dve.tensor_scalar(tm[:, t, :], x[:, t, :], rstd[:, t:t + 1], None, ALU.mult).then_inc(normed, 1)

            def scaled_turn(kind, g):
                for c in range(2):
                    for t in range(TT):
                        name = (kind, c, t)
                        jobs.wait_filled(dve, name)
                        jobs.drain(dve.tensor_tensor(
                            hT[:, 4 * c:4 * c + 4, t * P:(t + 1) * P], jobs.out(name).rearrange("p (m t) -> p m t", m=4),
                            bc(C(g, 4 * c, 4 * c + 4).unsqueeze(2), [P, 4, P]), ALU.mult), name)

            dve.wait_ge(params, 32)
            norm_tiles(1)
            scaled_turn("ht", "g_mix")

            def rope(dst, src, groups, t, at):
                n, width = groups
                h = width // 64
                tab = [K("rope", 64 * i + 32 * t, 64 * i + 32 * t + 32) for i in range(3)]
                tw = rtmp[:, at:at + n * width].rearrange("p (n h r d) -> p n h r d", n=n, r=2, d=32)
                order.up(dve.tensor_tensor(dst.rearrange("p n (h d) -> p n h d", d=32), src.rearrange("p n (h d) -> p n h d", d=32),
                                           bc(tab[0].unsqueeze(1).unsqueeze(1), [P, n, 2 * h, 32]), ALU.mult))
                halves = src.rearrange("p n (h r d) -> p n h r d", r=2, d=32)
                for r in range(2):
                    order.up(dve.tensor_tensor(tw[:, :, :, r, :], halves[:, :, :, 1 - r, :],
                                               bc(tab[2 - r].unsqueeze(1).unsqueeze(1), [P, n, h, 32]), ALU.mult))
                order.here(dve)
                dve.tensor_tensor(dst, dst, rtmp[:, at:at + n * width].rearrange("p (n c) -> p n c", n=n), ALU.add).then_inc(roped, 1)

            for t in range(TT):
                jobs.wait_drained(dve, ("kv", t))
                dve.tensor_copy(kd[:, t, :, :, :], bc(proj[:, t, 0:256].rearrange("p (m d) -> p m d", m=4).unsqueeze(2), [P, 4, 2, DH]))\
                   .then_inc(kd_ready, 1)
            for t in range(TT):
                jobs.wait_drained(dve, ("kv2", t))
                rope(rot[:, t, 0:384].rearrange("p (n c) -> p n c", n=3),
                     proj[:, t, 256:1024].rearrange("p (n c) -> p n c", n=3)[:, :, 0:P], (3, P), t, 0)
                jobs.wait_drained(dve, ("q", t))
                rope(rot[:, t, 384:896].rearrange("p (n c) -> p n c", n=1), proj[:, t, 1024:1536].rearrange("p (n c) -> p n c", n=1),
                     (1, 512), t, 384)
                jobs.wait_drained(dve, ("dq", t))
                rope(rot[:, t, 896:1408].rearrange("p (n c) -> p n c", n=1), proj[:, t, 1536:2048].rearrange("p (n c) -> p n c", n=1),
                     (1, 512), t, 896)
                if t == 0:
                    dve.wait_ge(roped, 3)
            for t in range(TT):
                jobs.wait_filled(dve, ("rkT", t))
                jobs.drain(dve.tensor_copy(rkT[:, :, t * P:(t + 1) * P], jobs.out(("rkT", t))[:, 0:384].rearrange("p (m t) -> p m t", m=3)), ("rkT", t))

            jobs.wait_drained(dve, ("c", 1))
            for g in range(4):
                src = cpad[:, g, :]
                bufs = [mem["psum_a"], mem["psum_b"]]
                for s in range(g + 1):
                    sh = 1 << s
                    lo = 2 * sh - 1
                    dst = bufs[s % 2][:, :]
                    order.up(dve.tensor_tensor(dst[:, lo:16 + T], src[:, lo:16 + T], src[:, lo - sh:16 + T - sh], ALU.add))
                    order.here(dve)
                    src = dst
                w = 2 << g
                out = brT[:, 1, g, :]
                order.up(dve.scalar_tensor_tensor(out=out, in0=src[:, 16:16 + T], scalar=1.0 / w, in1=cpad[:, g, 16:16 + T],
                                                  op0=ALU.mult, op1=ALU.subtract))
                order.here(dve)
                order.up(dve.tensor_tensor(out[:, 0:16], src[:, 16:32], K("pool_inv", 16 * g, 16 * g + 16), ALU.mult))
                order.here(dve)
                dve.tensor_tensor(out[:, 0:16], out[:, 0:16], cpad[:, g, 16:32], ALU.subtract).then_inc(pooled, 1)

            for kv in range(2):
                jobs.wait_filled(dve, ("hid", kv))
                h = jobs.out(("hid", kv))[:, 0:128].rearrange("p (a h n) -> p a h n", a=2, h=2)
                order.up(dve.tensor_copy(mem["hsum"][:, kv, :, 0:30], h[:, 0, :, 0:30]))
                order.here(dve)
                jobs.drain(dve.tensor_tensor(mem["hsum"][:, kv, :, 0:30], mem["hsum"][:, kv, :, 0:30], h[:, 1, :, 0:30], ALU.add), ("hid", kv))
            for i in range(2):
                jobs.wait_drained(dve, ("bg", i))
                jobs.wait_drained(dve, ("ba", i))
                order.up(dve.tensor_tensor(bglu[:, 2 * i:2 * i + 2, TAPS - 1:TAPS - 1 + T], bglu[:, 2 * i:2 * i + 2, TAPS - 1:TAPS - 1 + T],
                                           sg[:, i, :].rearrange("p (b t) -> p b t", b=2), ALU.mult))
            order.here(dve)

            conv_at = {"n": 0}

            def conv_steps(n):
                for _ in range(n):
                    i = conv_at["n"]
                    if i >= 4 * TAPS:
                        return
                    k, b = divmod(i, 4)
                    w = C("conv_w", TAPS * b + k, TAPS * b + k + 1)
                    if k == 0:
                        conv.up(dve.tensor_scalar(acc[:, b, :], bglu[:, b, 0:T], w, C("conv_b", b, b + 1), ALU.mult, ALU.add))
                    else:
                        conv.here(dve, less=3)
                        conv.up(dve.scalar_tensor_tensor(out=acc[:, b, :], in0=bglu[:, b, k:k + T], scalar=w, in1=acc[:, b, :],
                                                         op0=ALU.mult, op1=ALU.add))
                    conv_at["n"] += 1

            jobs.wait_filled(dve, "kc")
            for g in range(2):
                jobs.drain(dve.tensor_copy(kblk[64 * g:64 * g + 64, 16 * g:16 * g + CMP_N], jobs.out("kc")[64 * g:64 * g + 64, 0:CMP_N]), "kc")
            jobs.wait_filled(dve, "vc")
            jobs.drain(dve.tensor_tensor(vblk[:, :].rearrange("p (h d) -> p h d", h=8), bc(jobs.out("vc")[:, 0:DH].unsqueeze(1), [P, 8, DH]),
                                         bc(K("blk8").unsqueeze(2), [P, 8, DH]), ALU.mult), "vc")
            conv_steps(12)
            for t in range(TT):
                jobs.wait_filled(dve, ("cs", t))
                s3 = csc[:, t, :].rearrange("p (h n) -> p h n", h=8)
                jobs.drain(dve.tensor_tensor(s3, jobs.out(("cs", t))[:, 0:P].rearrange("p (h n) -> p h n", h=8),
                                             bc(K("cmp_mask", 16 * t, 16 * t + 16).unsqueeze(1), [P, 8, 16]), ALU.add), ("cs", t))
                jobs.wait_drained(dve, ("cs", t))
                order.up(dve.tensor_reduce(cmax[:, t, :], s3, AX_X, ALU.max))
                order.here(dve)
                dve.tensor_tensor(s3, s3, bc(cmax[:, t, :].unsqueeze(2), [P, 8, 16]), ALU.subtract).then_inc(cmp_s, 1)

            def mask(i):
                a, t, g = ITEMS[i]
                name, nk = ("S", a, t, g), (t + 1) * P
                if i >= 2:
                    for kb in range(ITEMS[i - 2][1] + 1):
                        jobs.wait_filled(dve, ("PT", *ITEMS[i - 2], kb))
                jobs.wait_filled(dve, name)
                m = K("band" if a == 2 else "full_causal", 2 * P - nk, 2 * P)
                s3 = sc[:, i % 2, :, 0:nk]
                jobs.drain(dve.tensor_tensor(s3, jobs.out(name).rearrange("p (j k) -> p j k", j=4)[:, :, 0:nk],
                                             bc(m.unsqueeze(1), [P, 4, nk]), ALU.add), name)
                jobs.wait_drained(dve, name)
                nm = nmax[:, 4 * (i % 2):4 * (i % 2) + 4]
                if a < 2:
                    dve.tensor_reduce(nm, s3, AX_X, ALU.max, negate=True).then_inc(masked, 1)
                    return
                sink = R("sinks").rearrange("p (j g) -> p j g", g=2)[:, :, g]
                order.up(dve.tensor_reduce(nm, s3, AX_X, ALU.max))
                order.here(dve)
                order.up(dve.tensor_tensor(nm, nm, sink, ALU.max))
                order.here(dve)
                order.up(dve.tensor_tensor(sinkv[:, i // 2 % 2, g, :], sink, nm, ALU.subtract))
                order.here(dve)
                dve.tensor_scalar(nm, nm, -1.0, None, ALU.mult).then_inc(masked, 1)

            def out_scale(i):
                a, t, g = ITEMS[i]
                d, c = den[:, (i // 2) % 2, :], coef[:, (i // 2) % 2, :]
                dve.wait_ge(exped, 4 * i + 4)
                if a == 2:
                    dve.wait_ge(tail_sent, 2 * t + 2)
                    order.up(dve.tensor_tensor(d.rearrange("p (j g) -> p g j", g=2), d.rearrange("p (j g) -> p g j", g=2),
                                               sinkv[:, i // 2 % 2, :, :], ALU.add))
                    order.here(dve)
                order.up(dve.reciprocal(c, d))
                order.here(dve)
                if a < 2:
                    order.up(dve.tensor_tensor(c, c, ga[:, t, 1 + a, :], ALU.mult))
                    order.here(dve)
                name = ("O", a, t)
                jobs.wait_filled(dve, name)
                o3 = jobs.out(name).rearrange("p (h d) -> p h d", h=8)
                cb = bc(c.unsqueeze(2), [P, 8, DH])
                if a == 2:
                    jobs.drain(dve.tensor_tensor(od[:, t, :].rearrange("p (h d) -> p h d", h=8), o3, cb, ALU.mult), name)
                    return
                tb = tmp[:, t, :]
                jobs.drain(dve.tensor_tensor(tb.rearrange("p (h d) -> p h d", h=8), o3, cb, ALU.mult), name)
                jobs.wait_drained(dve, name)
                add = dve.tensor_tensor(oa[:, t, :], oa[:, t, :], tb, ALU.add)
                if a == 1:
                    add.then_inc(o_ready, 1)
                else:
                    order.up(add)
                    order.here(dve)

            def cmp_scale():
                for t in range(TT):
                    dve.wait_ge(cmp_e, t + 1)
                    order.up(dve.tensor_reduce(cden[:, t, :], csc[:, t, :].rearrange("p (h n) -> p h n", h=8), AX_X, ALU.add))
                    order.here(dve)
                    order.up(dve.reciprocal(ccoef[:, t, :], cden[:, t, :]))
                    order.here(dve)
                    order.up(dve.scalar_tensor_tensor(out=ccoef[:, t, :], in0=ccoef[:, t, :], scalar=K("cmp_valid", t, t + 1),
                                                      in1=ga[:, t, 0, :], op0=ALU.mult, op1=ALU.mult))
                    order.here(dve)
                    jobs.wait_filled(dve, ("co", t))
                    jobs.drain(dve.tensor_tensor(oa[:, t, :].rearrange("p (h d) -> p h d", h=8),
                                                 jobs.out(("co", t)).rearrange("p (h d) -> p h d", h=8),
                                                 bc(ccoef[:, t, :].unsqueeze(2), [P, 8, DH]), ALU.mult), ("co", t))
                    jobs.wait_drained(dve, ("co", t))

            for i in range(len(ITEMS) + 1):
                if i < len(ITEMS):
                    mask(i)
                conv_steps(10)
                if i == 1:
                    cmp_scale()
                if i >= 1 and ITEMS[i - 1][2] == 1:
                    out_scale(i - 1)
            conv_steps(4 * TAPS)

            for t in range(TT):
                jobs.wait_filled(dve, ("convT", t))
                order.up(dve.bn_stats(stats[:, t, :], jobs.out(("convT", t))))
                order.here(dve)
                dve.bn_aggr(mv[:, t, :], stats[:, t, :]).then_inc(stat_ready, 1)
            for t in range(TT):
                dve.wait_ge(lnstd_ready, t + 1)
                jobs.drain(dve.tensor_scalar(ln_tm[:, t, :], jobs.out(("convT", t)), mv[:, t, 0:1], lnstd[:, t:t + 1],
                                             ALU.subtract, ALU.mult), ("convT", t))

            k = 0
            for bi, n in enumerate(BRANCH_ORDER):
                dve.wait_ge(gates_ready, bi + 1)
                for i in range(4):
                    name = ("up", n, i)
                    jobs.wait_filled(dve, name)
                    g2 = gates[:, n * 2048 + i * 512:n * 2048 + (i + 1) * 512]
                    if bi == 0:
                        dst = mixT[:, 2 * i:2 * i + 2, :].rearrange("p b t -> p (b t)")
                    else:
                        if k >= 2:
                            dve.wait_ge(mixed, k - 1)
                        dst = tmp[:, k % 2, :]
                        k += 1
                    jobs.drain(dve.tensor_tensor(dst, jobs.out(name), g2, ALU.mult), name)

            def residual(kind, g, first):
                for t in range(TT):
                    dve.wait_ge(rstd_ready, first)
                    for c in range(2):
                        jobs.wait_drained(dve, (kind, c, t))
                    order.up(dve.scalar_tensor_tensor(out=tm[:, t, :], in0=tm[:, t, :], scalar=rstd[:, 2 + t:3 + t], in1=R(g),
                                                      op0=ALU.mult, op1=ALU.mult))
                    order.here(dve)
                    dve.tensor_tensor(x[:, t, :], x[:, t, :], tm[:, t, :], ALU.add).then_inc(x_ready, 1)

            residual("wo", "mix_post", 2)
            dve.wait_ge(squares, 2 * TT)
            norm_tiles(3)
            scaled_turn("hf", "g_ffn")

            for j in range(FB):
                u = hq[j % 2][:, (j // 2 % 2) * 512:(j // 2 % 2) * 512 + 512]
                out = jobs.out(("ffn", j))
                for step in (1, 2):
                    for b in range(2):
                        n = 2 * j + b
                        w = C("fw", 3 * n + 2 - step, 3 * n + 3 - step)
                        if step == 1:
                            dve.wait_ge(ffn_init, 2 * j + 2)
                        else:
                            order.here(dve, less=1)
                        ins = dve.scalar_tensor_tensor(out=u[:, b * T + step:(b + 1) * T], in0=out[:, b * T:(b + 1) * T - step], scalar=w,
                                                       in1=u[:, b * T + step:(b + 1) * T], op0=ALU.mult, op1=ALU.add)
                        if step == 2 and b == 1:
                            jobs.drain(ins, ("ffn", j))
                        else:
                            order.up(ins)
            residual("down", "ffn_post", 4)

        @block.gpsimd
        def _(pool):
            order = Signal(g_order)

            def chain(ins):
                order.up(ins)
                order.here(pool)

            def inv_root(dst, total, n):
                chain(pool.tensor_scalar(msq[:, 0:2], total, 1.0 / n, EPS, ALU.mult, ALU.add))
                pool.tensor_tensor(dst, msq[:, 0:2], K("mhalf", 0, 2), ALU.pow).then_inc(rstd_ready, 1)

            pool.wait_ge(squares, TT)
            inv_root(rstd[:, 0:2], ss[:, 0:2], D)

            for t in range(TT):
                jobs.wait_drained(pool, ("cd", t))
            for m in range(4):
                kv = m // 2
                for par in range(2):
                    src = cdT[64 * par:64 * par + 64, m, :].rearrange("p (n r) -> p n r", r=16)
                    for half in range(2):
                        s = src[:, half:half + CMP_N, :].rearrange("p n (l r) -> p l n r", r=2)[:, :, :, par]
                        ps = C("pos", 16 * kv + 8 * half, 16 * kv + 8 * half + 8)[64 * par:64 * par + 64, :]
                        ins = pool.tensor_tensor(flat[64 * par:64 * par + 64, m, 8 * half:8 * half + 8, :], s,
                                                 bc(ps.unsqueeze(2), [64, 8, CMP_N]), ALU.add)
                        if half == 1:
                            ins.then_inc(flat_ready, 1)
                        else:
                            order.up(ins)
                order.here(pool)

            for t in range(TT):
                pool.wait_ge(stat_ready, t + 1)
                chain(pool.tensor_scalar(msq[:, 2:3], mv[:, t, 1:2], 1.0, EPS, ALU.mult, ALU.add))
                pool.tensor_tensor(lnstd[:, t:t + 1], msq[:, 2:3], K("mhalf", 0, 1), ALU.pow).then_inc(lnstd_ready, 1)
                pool.wait_ge(lnstd_ready, t + 1)

            k = 0
            for n in BRANCH_ORDER[1:]:
                for i in range(4):
                    jobs.wait_drained(pool, ("up", n, i))
                    if k >= 4:
                        pool.wait_ge(mixed, k - 3)
                    dst = mixT[:, 2 * i:2 * i + 2, :].rearrange("p b t -> p (b t)")
                    pool.tensor_tensor(dst, dst, tmp[:, k % 2, :], ALU.add).then_inc(mixed, 1)
                    k += 1

            def post(kind, turn):
                for c in range(2):
                    for t in range(TT):
                        jobs.wait_drained(pool, (kind, c, t))
                chain(pool.tensor_tensor(msq[:, 0:2], ss4[:, :, 0], ss4[:, :, 1], ALU.add))
                chain(pool.tensor_scalar(msq[:, 0:2], msq[:, 0:2], 1.0 / D, EPS, ALU.mult, ALU.add))
                pool.tensor_tensor(rstd[:, 2:4], msq[:, 0:2], K("mhalf", 0, 2), ALU.pow).then_inc(rstd_ready, 1)
                pool.wait_ge(rstd_ready, turn)

            post("wo", 2)
            pool.wait_ge(squares, 2 * TT)
            inv_root(rstd[:, 0:2], ss[:, 0:2], D)
            for j in range(FB):
                u = hq[j % 2][:, (j // 2 % 2) * 512:(j // 2 % 2) * 512 + 512]
                pool.wait_ge(gelued, j + 1)
                pool.tensor_tensor(fT[:, j, :], u[:, 0:T], u[:, T:2 * T], ALU.mult).then_inc(f_ready, 1)
            pool.wait_ge(rstd_ready, 3)
            post("down", 4)


HEADS = 16
MODS = 6 * KD
DX = 12
SEQ_TILES = 4
ALPHA = 2.0 ** 0.25
LN_EPS = 1e-5
EXPERTS = 16
EXPERT_STEP = 4
N_BLOCK2_CHUNKS = 24 + 2 + 6 + 4 + 4 + 8

COLS2, N_COLS2 = offsets([("b_mod", MODS), ("conv_w", 5 * DX), ("conv_b", DX), ("ssd_g", 8), ("c", 16), ("w_dt", KD * 32), ("w_r", KD * 20)])
ROWS2, N_ROWS2 = offsets([("ln1_g", D), ("ln1_b", D), ("ln2_g", D), ("ln2_b", D), ("dtb", 32), ("alog", 32), ("qn", DH), ("kn", DH),
                          ("br", 20), ("skip", 16)])
MEM2 = dict(
    hT=(KD, 512), xdt=(4, 1024), bcf=(4, 512), z=(TT, 1024), q=(TT, 1024), kv=(4, 512), xs=(4, 1024), bt=(4, 256),
    wx=(2, 1024), y=(2, 1024), kT=(2, 512), qT=(8, T), p=(2, 512), pt=(2, 512), m=(4, 512), cb=(2, 2, 2, P),
    cols2=(N_COLS2,), rows2=(N_ROWS2,), sm=(1200,), sm2=(950,), aT=(2, P), combT=(T,),
)
STATES = [(0, 0), (1, 0), (2, 0), (1, 1), (0, 1), (3, 1)]
UNITS = [(t, g, quad) for t in range(TT) for g in range(2) for quad in range(2)]
HEAD_ITEMS = [(t, b, g) for t in range(TT) for b in range(8) for g in range(2)]


def plan_block2(jobs):
    jobs.plan("mod")
    for s in range(2):
        for c in range(2):
            for t in range(TT):
                jobs.plan(("in", s, c, t))
    jobs.plan("dt")
    for i, r in zip(range(4), ("s0", "s1", "t", "u")):
        jobs.plan(("kv", i), r)
    for b in range(DX):
        jobs.plan(("xbc", b))
    jobs.plan("cum")
    for c in range(2):
        for t in range(TT):
            jobs.plan(("q", c, t))
    for c in range(2):
        for t in range(TT):
            jobs.plan(("z", c, t))
    jobs.plan("aT")
    for i in range(4):
        for half in range(2):
            jobs.plan(("xsT", i, half))
        jobs.plan(("bT", i))
    for i in range(2):
        jobs.plan(("kT", i))
    for t in range(TT):
        jobs.plan(("cb", t))
    for n in range(len(STATES)):
        for g in range(2):
            jobs.plan(("st", n, g), ("s0", "s1")[g])
    for t, g, quad in UNITS:
        for d in range(2):
            jobs.plan(("aq", t, g, quad, d))
        if quad == 1:
            jobs.plan(("yd", t, g), "a3")
            for d in range(2):
                jobs.plan(("yo", t, g, d), ("t", "u")[d])
    for t in range(TT):
        for h in range(2):
            jobs.plan(("qT", t, h))
    for n, (t, b, g) in enumerate(HEAD_ITEMS):
        jobs.plan(("S", n), ("s0", "s1")[n % 2])
        jobs.plan(("PT", n), ("t", "u")[n % 2])
        if b % 4 == 0 and g == 0:
            jobs.plan(("O", t, b // 4), "a3")
    for t in range(TT):
        for h in range(4):
            jobs.plan(("mixT", h, t))
    for v in range(2):
        for c in range(2):
            jobs.plan(("gB", v, c))
    for t in range(TT):
        for c in range(2):
            jobs.plan(("out", t, c), f"a{2 * t + c}")
    for c in range(2):
        for t in range(TT):
            jobs.plan(("hf", c, t), ("s0", "s1", "t", "u")[2 * c + t])
    jobs.plan("route", "s0")
    jobs.plan("combT", "s1")
    for i in range(8):
        jobs.plan(("combB", i), ("t", "u")[i % 2])


def block2(nc, mem, ring, landed, used, wts, psum, sems, cols_dram, rows_dram, ctx_dram, out_dram):
    region = {**{f"a{i}": (i * 512, 512) for i in range(4)}, "s0": (2048, 512), "s1": (2560, 512), "t": (3072, 512), "u": (3584, 512)}
    filled = {r: sems(f"filled2_{r}") for r in region}
    drained = {r: sems(f"drained2_{r}") for r in region}
    jobs = Jobs(psum, filled, drained, region, ring=3)
    plan_block2(jobs)

    params, ctx_in = sems("params2"), sems("ctx_in")
    silu_c = sems("silu_c")
    mod_ready = sems("mod_ready")
    shifted = sems("shifted")
    conv_init = sems("conv_init")
    xbc_ready = sems("xbc_ready")
    dt_neg, dt_exp, dt_u, dt_ln, dt_ready = (sems(n) for n in ("dt_neg", "dt_exp", "dt_u", "dt_ln", "dt_ready"))
    a_ready = sems("a_ready")
    decays = sems("decays")
    diff_ready = sems("diff_ready")
    dw_ready = sems("dw_ready")
    xw_ready = sems("xw_ready")
    h_ready = sems("h_ready")
    xdt_ready = sems("xdt_ready")
    skip_ready = sems("skip_ready")
    aq_diff = sems("aq_diff")
    aq_exp = sems("aq_exp")
    m_ready = sems("m_ready")
    y_sq = sems("y_sq")
    y_gated = sems("y_gated")
    y_std = sems("y_std")
    y_norm = sems("y_norm")
    qk_sum = sems("qk_sum")
    qk_std = sems("qk_std")
    qk_ready = sems("qk_ready")
    nmax_ready = sems("nmax_ready")
    pt_ready = sems("pt_ready")
    diag_ready = sems("diag_ready")
    ln_stat, ln_std, x_normed = sems("ln_stat"), sems("ln_std"), sems("x_normed")
    comb_ready = sems("comb_ready")
    r_logits, r_exp = sems("r_logits"), sems("r_exp")
    zero_ready = sems("zero_ready")
    silu_g = sems("silu_g")
    hid_raw = sems("hid_raw")
    hid_ready = sems("hid_ready2")
    hid_used = sems("hid_used")
    stored = sems("stored")
    m_used = sems("m_used")
    v_order, g_order, a_order = sems("v_order2"), sems("g_order2"), sems("a_order2")

    hT, xdt, bcf, z, q, kv, xs, bt, wx, y, kT, qT, p, pt, m, cb = (mem[k] for k in (
        "hT", "xdt", "bcf", "z", "q", "kv", "xs", "bt", "wx", "y", "kT", "qT", "p", "pt", "m", "cb"))
    x, const, cols, rows, sm = mem["x"], mem["const"], mem["cols2"], mem["rows2"], mem["sm"]
    xbc_xs = xdt[:, :, :].rearrange("p i (b t) -> p (i b) t", t=512)
    H = hT[:, :, :].rearrange("p k t -> p (k t)").rearrange("p (n c) -> p n c", c=1024)
    mixT = xdt[:, :, :].rearrange("p i (b t) -> p (i b) t", t=T)
    gB = z
    combB = xs[:, :, :].rearrange("p i (b t) -> p (i b) t", t=T)
    hfT = hT[:, :, 0:T]
    res = y
    ctx_tm = y

    at = [0]

    def small(n):
        at[0] += n
        return sm[:, at[0] - n:at[0]]

    modT = small(96).rearrange("p (b v) -> p b v", v=2)
    cvec = small(16)
    dtr, dt, dtA, tmp_a, tmp_b = (small(128).rearrange("p (i h) -> p i h", i=4) for _ in range(5))
    acs = small(256).rearrange("p (i h) -> p i h", i=4)
    expA = small(32)
    ssq, rq = small(16), small(16)
    assert at[0] <= 1200
    sm2 = mem["sm2"]
    at2 = [0]

    def small2(n):
        at2[0] += n
        return sm2[:, at2[0] - n:at2[0]]

    dec = small2(128).rearrange("p (i h) -> p i h", i=4)
    dw = small2(128).rearrange("p (i h) -> p i h", i=4)
    ea = small2(128).rearrange("p (i h) -> p i h", i=4)
    yss, yrs = small2(4), small2(4)
    kss, krs = small2(16), small2(16)
    qss, qrs = small2(32).rearrange("p (t h) -> p t h", t=2), small2(32).rearrange("p (t h) -> p t h", t=2)
    nm, dn, rden = small2(32), small2(32), small2(32)
    stats, mv, lstd, lms = small2(24).rearrange("p (t c s) -> p t c s", t=2, c=2), small2(4).rearrange("p (t s) -> p t s", t=2), small2(2), small2(2)
    lg = small2(40).rearrange("p (t n) -> p t n", t=2)
    gm, gs, gval = small2(2), small2(2), small2(2)
    goh = small2(8).rearrange("p (t g) -> p t g", t=2)
    r8a, r8b, es, pe_, oh1, oh2, pm, wgt = (small2(8).rearrange("p (t g) -> p t g", t=2) for _ in range(8))
    r2a, r2b, r2c = small2(2), small2(2), small2(2)
    r32 = small2(32).rearrange("p (t g e) -> p t g e", t=2, g=4)
    comb = small2(32).rearrange("p (t e) -> p t e", t=2)
    aT = mem["aT"]
    combT = mem["combT"]

    def K(name, a=0, b=None):
        o, width = CONST[name]
        return const[:, o + a:o + (width if b is None else b)]

    def C(name, a=0, b=None):
        o, width = COLS2[name]
        return cols[:, o + a:o + (width if b is None else b)]

    def R(name):
        o, width = ROWS2[name]
        return rows[:, o:o + width]

    ident = K("ident")
    first = LAYERS * N_LAYER_CHUNKS

    with nc.Block() as block:
        @block.sync
        def _(sp):
            sp.dma_start(ctx_tm[:, :, :], ctx_dram.rearrange("(t p) d -> p t d", p=P)).then_inc(ctx_in, 16)
            left = N_BLOCK2_CHUNKS + 3 * EXPERTS - SLOTS
            with sp.Fori(0, left // SLOTS) as turn:
                for s in range(SLOTS):
                    sp.wait_ge(used, turn * SLOTS + (first + s + 1))
                    sp.dma_start(ring[:, s, :], wts[turn * SLOTS + (first + s + SLOTS)]).then_inc(landed[s], 16)
            for t in range(TT):
                sp.wait_ge(x_normed, TT + t + 1)
                sp.dma_start(out_dram[t * P:(t + 1) * P, :], x[:, t, :]).then_inc(stored, 16)
            sp.wait_ge(stored, 16 * TT)

        @block.tensor
        def _(pe):
            state = {"chunk": first, "owed": False}

            def next_chunk():
                c = state["chunk"]
                state["chunk"] += 1
                pe.wait_ge(landed[c % SLOTS], (c // SLOTS + 1) * 16)
                return ring[:, c % SLOTS, :]

            def carry(ins):
                if state["owed"]:
                    ins.then_inc(used, 1)
                    state["owed"] = False

            def owe():
                assert not state["owed"]
                state["owed"] = True

            def transpose4(name, blocks, step=P):
                jobs.claim(pe, name)
                out = jobs.out(name)
                for i, b in enumerate(blocks):
                    mm = pe.transpose(out[0:b.shape[1], i * step:i * step + P], b, ident)
                    if i == 0 and len(blocks) > 1:
                        carry(mm)
                jobs.fill(mm, name)

            pe.wait_ge(silu_c, 1)
            jobs.claim(pe, "mod")
            for n in range(MODS // 2):
                chunk = next_chunk().rearrange("p (k m) -> p k m", k=KD)
                for b in range(2):
                    for k in range(KD):
                        mm = pe.matmul(jobs.out("mod")[:, (2 * n + b) * 2:(2 * n + b) * 2 + 2], chunk[:, k, b * P:(b + 1) * P],
                                       cvec[:, 2 * k:2 * k + 2], start=(k == 0), stop=(k == KD - 1))
                if n < MODS // 2 - 1:
                    mm.then_inc(used, 1)
            jobs.fill(mm, "mod")
            owe()

            for s in range(2):
                src = (ctx_tm, x)[s]
                if s == 0:
                    pe.wait_ge(ctx_in, 16)
                for c in range(2):
                    for t in range(TT):
                        transpose4(("in", s, c, t), [src[:, t, (4 * c + i) * P:(4 * c + i + 1) * P] for i in range(4)])
            pe.wait_ge(shifted, 8)
            jobs.claim(pe, "dt")
            for i in range(SEQ_TILES):
                for k in range(KD):
                    mm = pe.matmul(jobs.out("dt")[:, 32 * i:32 * i + 32], hT[:, k, i * P:(i + 1) * P], C("w_dt", 32 * k, 32 * k + 32),
                                   start=(k == 0), stop=(k == KD - 1))
            jobs.fill(mm, "dt")

            def tokens(kind, tiles, names):
                for half in range(2):
                    chunk = next_chunk().rearrange("p (k n) -> p k n", k=4)
                    for tile, name in zip(tiles, names):
                        if half == 0:
                            jobs.claim(pe, name)
                        for k in range(4):
                            mm = pe.matmul(jobs.out(name), hT[:, 4 * half + k, tile * P:(tile + 1) * P], chunk[:, k, :],
                                           start=(half == 0 and k == 0), stop=(half == 1 and k == 3))
                            if k == 0:
                                carry(mm)
                        if half == 1:
                            jobs.fill(mm, name)
                    if half == 0:
                        mm.then_inc(used, 1)
                    else:
                        owe()

            tokens("kv", range(SEQ_TILES), [("kv", i) for i in range(SEQ_TILES)])
            for b in range(DX):
                if b % 2 == 0:
                    chunk = next_chunk().rearrange("p (k m) -> p k m", k=KD)
                jobs.claim(pe, ("xbc", b))
                for k in range(KD):
                    mm = pe.matmul(jobs.out(("xbc", b)), chunk[:, k, b % 2 * P:(b % 2 + 1) * P], hT[:, k, :], start=(k == 0), stop=(k == KD - 1))
                    if k == 0:
                        carry(mm)
                jobs.fill(mm, ("xbc", b))
                if b % 2 == 1:
                    owe()

            pe.wait_ge(dt_ready, 1)
            jobs.claim(pe, "cum")
            for i in range(SEQ_TILES):
                out = jobs.out("cum")[:, 64 * i:64 * i + 64]
                mm = pe.matmul(out[:, 0:16], K("tri_u"), dtA[:, i, 0:16], start=True, stop=True)
                carry(mm)
                pe.matmul(out[:, 16:32], K("tri_l"), dtA[:, i, 16:32], start=True, stop=True)
                mm = pe.matmul(out[:, 32:64], K("ones"), dtA[:, i, :], start=True, stop=True)
            jobs.fill(mm, "cum")
            for c in range(2):
                tokens("q", (2, 3), [("q", c, t) for t in range(TT)])
            for c in range(2):
                tokens("z", (2, 3), [("z", c, t) for t in range(TT)])
            jobs.wait_drained(pe, "cum")
            transpose4("aT", [acs[:, 2 + t, 0:32] for t in range(TT)])

            pe.wait_ge(xbc_ready, DX)
            for i in range(SEQ_TILES):
                for half in range(2):
                    transpose4(("xsT", i, half), [xbc_xs[:, 4 * half + b, i * P:(i + 1) * P] for b in range(4)])
                transpose4(("bT", i), [bcf[:, g, i * P:(i + 1) * P] for g in range(2)])
            pe.wait_ge(qk_ready, 1)
            for b in range(2):
                transpose4(("kT", b), [kv[:, i, b * P:(b + 1) * P] for i in range(SEQ_TILES)])
            for t in range(TT):
                jobs.claim(pe, ("cb", t))
                for g in range(2):
                    mm = pe.matmul(jobs.out(("cb", t))[:, g * P:(g + 1) * P], bcf[:, g, (2 + t) * P:(3 + t) * P],
                                   bcf[:, 2 + g, (2 + t) * P:(3 + t) * P], start=True, stop=True)
                jobs.fill(mm, ("cb", t))
            for n, (i, d) in enumerate(STATES):
                pe.wait_ge(xw_ready, n + 1)
                jobs.wait_drained(pe, ("bT", i))
                for g in range(2):
                    jobs.claim(pe, ("st", n, g))
                    jobs.fill(pe.matmul(jobs.out(("st", n, g)), bt[:, i, g * P:(g + 1) * P], wx[:, n % 2, g * 512:(g + 1) * 512],
                                        start=True, stop=True), ("st", n, g))

            jobs.wait_drained(pe, "aT")

            def spread(t, g, quad):
                for d in range(2):
                    name = ("aq", t, g, quad, d)
                    jobs.claim(pe, name)
                    for h in range(4):
                        head = 16 * d + 8 * g + 4 * quad + h
                        mm = pe.matmul(jobs.out(name)[:, h * P:(h + 1) * P], bc(ident[0:32, head:head + 1], [32, P]), aT[0:32, t, :],
                                       start=True, stop=True)
                    jobs.fill(mm, name)

            pe.wait_ge(xdt_ready, 4)
            spread(*UNITS[0])
            for n, (t, g, quad) in enumerate(UNITS):
                if n + 1 < len(UNITS):
                    spread(*UNITS[n + 1])
                pe.wait_ge(m_ready, 2 * n + 2)
                if quad == 0:
                    jobs.claim(pe, ("yd", t, g))
                for h in range(4):
                    for d in range(2):
                        mm = pe.matmul(jobs.out(("yd", t, g))[:, (4 * quad + h) * DH:(4 * quad + h + 1) * DH],
                                       m[:, (2 * n + d) % 4, h * P:(h + 1) * P],
                                       xdt[:, 2 * t + d, (8 * g + 4 * quad + h) * DH:(8 * g + 4 * quad + h + 1) * DH],
                                       start=(d == 0), stop=(d == 1))
                if quad == 0:
                    mm.then_inc(m_used, 1)
                else:
                    jobs.fill(mm, ("yd", t, g))
                    pe.wait_ge(h_ready, 12)
                    for d in range(2):
                        jobs.claim(pe, ("yo", t, g, d))
                        mm = pe.matmul(jobs.out(("yo", t, g, d)), bcf[:, 2 + g, (2 + t) * P:(3 + t) * P],
                                       H[:, 2 * d + t, g * 512:(g + 1) * 512], start=True, stop=True)
                        jobs.fill(mm, ("yo", t, g, d))

            for t in range(TT):
                pe.wait_ge(qk_ready, 2 + t)
                for h in range(2):
                    transpose4(("qT", t, h), [q[:, t, (4 * h + b) * P:(4 * h + b + 1) * P] for b in range(4)])
            for b in range(2):
                jobs.wait_drained(pe, ("kT", b))

            def values(n):
                t, b, g = HEAD_ITEMS[n]
                if b % 4 == 0 and g == 0:
                    jobs.claim(pe, ("O", t, b // 4))
                jobs.wait_drained(pe, ("PT", n))
                for i in range(SEQ_TILES):
                    mm = pe.matmul(jobs.out(("O", t, b // 4))[:, (2 * (b % 4) + g) * DH:(2 * (b % 4) + g + 1) * DH],
                                   pt[:, n % 2, i * P:(i + 1) * P], kv[:, i, 256 + (2 * (b // 4) + g) * DH:256 + (2 * (b // 4) + g + 1) * DH],
                                   start=(i == 0), stop=(i == SEQ_TILES - 1))
                if b % 4 == 3 and g == 1:
                    jobs.fill(mm, ("O", t, b // 4))

            for n in range(len(HEAD_ITEMS) + 2):
                if n < len(HEAD_ITEMS):
                    t, b, g = HEAD_ITEMS[n]
                    if g == 0 and b % 4 == 0:
                        jobs.wait_drained(pe, ("qT", t, b // 4))
                    jobs.claim(pe, ("S", n))
                    jobs.fill(pe.matmul(jobs.out(("S", n)), qT[64 * g:64 * g + 64, b, t * P:(t + 1) * P], kT[64 * g:64 * g + 64, b // 4, :],
                                        start=True, stop=True), ("S", n))
                if n >= 1 and n - 1 < len(HEAD_ITEMS):
                    jobs.wait_drained(pe, ("S", n - 1))
                    transpose4(("PT", n - 1), [p[:, (n - 1) % 2, i * P:(i + 1) * P] for i in range(SEQ_TILES)])
                if n >= 2:
                    values(n - 2)

            for t in range(TT):
                for h in range(4):
                    if h == 0:
                        pe.wait_ge(y_norm, t + 1)
                    if h >= 2:
                        jobs.wait_drained(pe, ("O", t, h - 2))
                    src = y[:, t, :] if h < 2 else q[:, t, :]
                    transpose4(("mixT", h, t), [src[:, (4 * (h % 2) + b) * P:(4 * (h % 2) + b + 1) * P] for b in range(4)])
            for v in range(2):
                pe.wait_ge(diag_ready, v + 1)
                for c in range(2):
                    jobs.claim(pe, ("gB", v, c))
                    jobs.fill(pe.matmul(jobs.out(("gB", v, c)), K("ones"), wx[:, v, c * 512:(c + 1) * 512], start=True, stop=True), ("gB", v, c))
            for t in range(TT):
                for h in range(4):
                    jobs.wait_drained(pe, ("mixT", h, t))
                for c in range(2):
                    jobs.claim(pe, ("out", t, c))
            for i in range(8):
                chunk = next_chunk().rearrange("p (k n) -> p k n", k=2)
                for k in range(2):
                    for t in range(TT):
                        for c in range(2):
                            mm = pe.matmul(jobs.out(("out", t, c)), mixT[:, 2 * i + k, t * P:(t + 1) * P], chunk[:, k, c * 512:(c + 1) * 512],
                                           start=(i == 0 and k == 0), stop=(i == 7 and k == 1))
                            if k == 0:
                                carry(mm)
                            if i == 7 and k == 1:
                                jobs.fill(mm, ("out", t, c))
                if i < 7:
                    mm.then_inc(used, 1)
            owe()

            for c in range(2):
                for t in range(TT):
                    pe.wait_ge(x_normed, t + 1)
                    transpose4(("hf", c, t), [x[:, t, (4 * c + i) * P:(4 * c + i + 1) * P] for i in range(4)])
            pe.wait_ge(shifted, 12)
            jobs.claim(pe, "route")
            for t in range(TT):
                for k in range(KD):
                    mm = pe.matmul(jobs.out("route")[:, 20 * t:20 * t + 20], hfT[:, k, t * P:(t + 1) * P], C("w_r", 20 * k, 20 * k + 20),
                                   start=(k == 0), stop=(k == KD - 1))
            jobs.fill(mm, "route")
            pe.wait_ge(comb_ready, 1)
            transpose4("combT", [comb[:, t, :] for t in range(TT)])
            jobs.wait_drained(pe, "combT")
            for i in range(8):
                jobs.claim(pe, ("combB", i))
                for e in range(2):
                    mm = pe.matmul(jobs.out(("combB", i))[:, e * T:(e + 1) * T], bc(ident[0:16, 2 * i + e:2 * i + e + 1], [16, P]), combT[0:16, :],
                                   start=True, stop=True)
                jobs.fill(mm, ("combB", i))

            pe.wait_ge(zero_ready, 1)
            for r in range(4):
                pe.wait_ge(drained[f"a{r}"], jobs.sum[f"a{r}"])
                pe.matmul(psum[:, r * 512:(r + 1) * 512], m[:, 0, 0:P], m[:, 1, :], start=True, stop=False, skip_group_check=True)

            with pe.Fori(0, EXPERTS // EXPERT_STEP) as step:
                n_chunk = [state["chunk"]]

                def chunk_at(turn_chunks=3 * EXPERT_STEP):
                    c = n_chunk[0]
                    n_chunk[0] += 1
                    pe.wait_ge(landed[c % SLOTS], step * (turn_chunks // SLOTS * 16) + (c // SLOTS + 1) * 16)
                    return ring[:, c % SLOTS, :]

                def expert_in(e):
                    for part, r in enumerate((("s0", "s1"), ("t", "u"))[e % 2]):
                        chunk = chunk_at().rearrange("p (k m) -> p k m", k=KD)
                        pe.wait_ge(drained[r], step * 2 + (jobs.sum[r] + e // 2))
                        for b in range(2):
                            for k in range(KD):
                                mm = pe.matmul(psum[:, region[r][0] + b * T:region[r][0] + (b + 1) * T], chunk[:, k, b * P:(b + 1) * P],
                                               hfT[:, k, :], start=(k == 0), stop=(k == KD - 1))
                                if b == 0 and k == 0:
                                    carry(mm)
                        mm.then_inc(filled[r], 1)
                        owe()

                def expert_out(e):
                    chunk = chunk_at().rearrange("p (k n) -> p k n", k=2)
                    pe.wait_ge(hid_ready, step * EXPERT_STEP + (e + 1))
                    for k in range(2):
                        for t in range(TT):
                            for c in range(2):
                                mm = pe.matmul(psum[:, (2 * t + c) * 512:(2 * t + c + 1) * 512],
                                               m[:, 2 * (e % 2):2 * (e % 2) + 1, k * T + t * P:k * T + (t + 1) * P].rearrange("p a n -> p (a n)"),
                                               chunk[:, k, c * 512:(c + 1) * 512], start=False, stop=False, skip_group_check=True)
                                if k == 0 and t == 0 and c == 0:
                                    carry(mm)
                    mm.then_inc(hid_used, 1)
                    owe()

                expert_in(0)
                for e in range(EXPERT_STEP):
                    if e + 1 < EXPERT_STEP:
                        expert_in(e + 1)
                    expert_out(e)
                pe.wait_ge(hid_used, step * EXPERT_STEP + EXPERT_STEP)
                pe.sem_inc(used, 1)
                state["owed"] = False

        @block.scalar
        def _(act):
            order = Signal(a_order)

            def copy_out(name, dst, src=None, scale=1.0, func=ACT.Copy):
                jobs.wait_filled(act, name)
                jobs.drain(act.activation(dst, jobs.out(name) if src is None else src, func, scale=scale), name)

            act.dma_start(cols[:, :], cols_dram).then_inc(params, 16)
            act.dma_start(rows[:, :], rows_dram.to_broadcast([P, N_ROWS2])).then_inc(params, 16)
            act.wait_ge(params, 32)
            act.activation(cvec, C("c"), ACT.Silu).then_inc(silu_c, 1)
            for i in range(SEQ_TILES):
                copy_out(("kv", i), kv[:, i, :])
            for b in range(DX + 1):
                if b < DX:
                    jobs.wait_filled(act, ("xbc", b))
                    dst = xbc_xs[:, b, :] if b < 8 else bcf[:, b - 8, :]
                    act.activation(dst, jobs.out(("xbc", b)), ACT.Identity, scale=C("conv_w", 5 * b + 2, 5 * b + 3),
                                   bias=C("conv_b", b, b + 1)).then_inc(conv_init, 1)
                if b >= 1:
                    dst = xbc_xs[:, b - 1, :] if b - 1 < 8 else bcf[:, b - 9, :]
                    jobs.wait_drained(act, ("xbc", b - 1))
                    act.activation(dst, dst, ACT.Silu).then_inc(xbc_ready, 1)
            act.activation(expA, R("alog"), ACT.Exp).then_inc(a_ready, 1)
            act.wait_ge(dt_neg, 1)
            act.activation(tmp_b[:, :, :], tmp_b[:, :, :], ACT.Exp).then_inc(dt_exp, 1)
            act.wait_ge(dt_u, 1)
            act.activation(tmp_a[:, :, :], tmp_a[:, :, :], ACT.Ln).then_inc(dt_ln, 1)
            for c in range(2):
                for t in range(TT):
                    copy_out(("q", c, t), q[:, t, c * 512:(c + 1) * 512])
            for c in range(2):
                for t in range(TT):
                    copy_out(("z", c, t), z[:, t, c * 512:(c + 1) * 512], func=ACT.Silu)
            act.wait_ge(diff_ready, 1)
            act.activation(dec[:, :, :], acs[:, :, 32:64], ACT.Exp).then_inc(decays, 1)
            act.activation(ea[:, :, :], acs[:, :, 0:32], ACT.Exp).then_inc(decays, 1)
            act.activation(dw[:, :, :], dw[:, :, :], ACT.Exp).then_inc(decays, 1)
            copy_out("aT", aT[0:32, :, :], jobs.out("aT")[0:32, 0:2 * P].rearrange("p (t q) -> p t q", t=2))
            for i in range(SEQ_TILES):
                for half in range(2):
                    copy_out(("xsT", i, half), xs[:, i, half * 512:(half + 1) * 512])
                copy_out(("bT", i), bt[:, i, :], jobs.out(("bT", i))[:, 0:256])
            for b in range(2):
                copy_out(("kT", b), kT[:, b, :])

            for n in range(len(UNITS)):
                for d in range(2):
                    act.wait_ge(aq_diff, 2 * n + d + 1)
                    act.activation(m[:, (2 * n + d) % 4, :], m[:, (2 * n + d) % 4, :], ACT.Exp).then_inc(aq_exp, 1)
            for t in range(TT):
                for h in range(2):
                    copy_out(("qT", t, h), qT[:, 4 * h:4 * h + 4, t * P:(t + 1) * P], jobs.out(("qT", t, h)).rearrange("p (b t) -> p b t", b=4), 0.125)
            for n in range(len(HEAD_ITEMS) + 1):
                if n < len(HEAD_ITEMS):
                    if n >= 2:
                        jobs.wait_filled(act, ("PT", n - 2))
                    act.wait_ge(nmax_ready, n + 1)
                    name = ("S", n)
                    jobs.wait_filled(act, name)
                    jobs.drain(act.activation(p[:, n % 2, :], jobs.out(name), ACT.Exp, bias=nm[:, n:n + 1], accum_out=dn[:, n:n + 1]), name)
                if n >= 1 and (n - 1) % 2 == 0:
                    copy_out(("PT", n - 1), pt[:, (n - 1) % 2, :])
            for t in range(TT):
                act.wait_ge(y_gated, t + 1)
                if t:
                    act.wait_ge(y_sq, 2 * t)
                for g in range(2):
                    act.activation(wx[:, g, 0:512], y[:, t, g * 512:(g + 1) * 512], ACT.Square, accum_out=yss[:, 2 * t + g:2 * t + g + 1]).then_inc(y_sq, 1)
            for t in range(TT):
                for h in (2, 3):
                    copy_out(("mixT", h, t), mixT[:, 4 * h:4 * h + 4, t * P:(t + 1) * P], jobs.out(("mixT", h, t)).rearrange("p (b t) -> p b t", b=4))
            for v in range(2):
                for c in range(2):
                    copy_out(("gB", v, c), gB[:, v, c * 512:(c + 1) * 512])
            act.wait_ge(r_logits, 1)
            act.activation(r8a[:, :, :], r8a[:, :, :], ACT.Exp).then_inc(r_exp, 1)
            act.activation(es[:, :, :], es[:, :, :], ACT.Exp).then_inc(r_exp, 1)
            copy_out("combT", combT[0:16, :], jobs.out("combT")[0:16, 0:T])
            for i in range(8):
                copy_out(("combB", i), combB[:, 2 * i:2 * i + 2, :], jobs.out(("combB", i)).rearrange("p (e t) -> p e t", e=2))
            with act.Fori(0, EXPERTS // EXPERT_STEP) as step:
                for e in range(EXPERT_STEP):
                    r = ("s0", "t")[e % 2]
                    act.wait_ge(filled[r], step * 2 + (jobs.turn[r] + e // 2 + 1))
                    if e >= 2:
                        act.wait_ge(hid_raw, step * EXPERT_STEP + (e - 1))
                    act.activation(p[:, e % 2, :], psum[:, region[r][0]:region[r][0] + 512], ACT.Silu).then_inc(drained[r], 1)
                act.wait_ge(hid_raw, step * EXPERT_STEP + EXPERT_STEP)

        @block.vector
        def _(dve):
            order = Signal(v_order)

            def chain(ins):
                order.up(ins)
                order.here(dve)

            def tt(out, a, b, op):
                chain(dve.tensor_tensor(out, a, b, op))

            dve.wait_ge(params, 32)
            jobs.wait_filled(dve, "mod")
            jobs.drain(dve.tensor_tensor(modT[:, :, :], jobs.out("mod")[:, 0:96].rearrange("p (b v) -> p b v", v=2),
                                         bc(C("b_mod").unsqueeze(2), [P, MODS, 2]), ALU.add), "mod")
            jobs.wait_drained(dve, "mod")
            dve.tensor_scalar(modT[:, 8:16, :], modT[:, 8:16, :], 1.0, None, ALU.add).then_inc(mod_ready, 1)
            dve.tensor_scalar(modT[:, 32:40, :], modT[:, 32:40, :], 1.0, None, ALU.add).then_inc(mod_ready, 1)
            dve.wait_ge(mod_ready, 2)

            def scale_in(name, dst, block, v):
                jobs.wait_filled(dve, name)
                jobs.drain(dve.tensor_tensor(dst, jobs.out(name).rearrange("p (b t) -> p b t", b=4),
                                             bc(modT[:, block:block + 4, v:v + 1], [P, 4, P]), ALU.mult), name)

            for s in range(2):
                for c in range(2):
                    for t in range(TT):
                        scale_in(("in", s, c, t), hT[:, 4 * c:4 * c + 4, (2 * s + t) * P:(2 * s + t + 1) * P], 8 + 4 * c, 1 - s)
            jobs.wait_filled(dve, "dt")
            jobs.drain(dve.tensor_tensor(dtr[:, :, :], jobs.out("dt")[:, 0:128].rearrange("p (i h) -> p i h", i=4),
                                         bc(R("dtb").unsqueeze(1), [P, 4, 32]), ALU.add), "dt")
            jobs.wait_drained(dve, "dt")
            chain(dve.tensor_scalar(tmp_b[:, :, :], dtr[:, :, :], -1.0, None, ALU.mult))
            dve.tensor_tensor(tmp_b[:, :, :], tmp_b[:, :, :], dtr[:, :, :], ALU.min).then_inc(dt_neg, 1)

            def taps(b):
                dve.wait_ge(conv_init, b + 1)
                dst = (xbc_xs[:, b, :] if b < 8 else bcf[:, b - 8, :]).rearrange("p (s t) -> p s t", s=2)
                src = jobs.out(("xbc", b)).rearrange("p (s t) -> p s t", s=2)
                for n, k in enumerate((0, 1, 3, 4)):
                    sh = k - 2
                    lo, hi = max(0, -sh), T - max(0, sh)
                    ins = dve.scalar_tensor_tensor(out=dst[:, :, lo:hi], in0=src[:, :, lo + sh:hi + sh], scalar=C("conv_w", 5 * b + k, 5 * b + k + 1),
                                                   in1=dst[:, :, lo:hi], op0=ALU.mult, op1=ALU.add)
                    if n < 3:
                        chain(ins)
                    else:
                        jobs.drain(ins, ("xbc", b))

            for b in range(DX):
                taps(b)
            dve.wait_ge(dt_exp, 1)
            chain(dve.tensor_scalar(tmp_a[:, :, :], tmp_b[:, :, :], 1.0, None, ALU.add))
            chain(dve.tensor_scalar(dt[:, :, :], tmp_a[:, :, :], -1.0, None, ALU.add))
            chain(dve.tensor_scalar(dtA[:, :, :], dt[:, :, :], 0.0, None, ALU.is_equal))
            dve.tensor_tensor(dt[:, :, :], dt[:, :, :], dtA[:, :, :], ALU.add).then_inc(dt_u, 1)
            dve.wait_ge(dt_u, 1)
            chain(dve.reciprocal(dt[:, :, :], dt[:, :, :]))
            tt(dt[:, :, :], dt[:, :, :], tmp_b[:, :, :], ALU.mult)
            dve.wait_ge(dt_ln, 1)
            tt(tmp_a[:, :, :], tmp_a[:, :, :], dtA[:, :, :], ALU.add)
            tt(dt[:, :, :], dt[:, :, :], tmp_a[:, :, :], ALU.mult)
            chain(dve.scalar_tensor_tensor(out=dt[:, :, :], in0=dtr[:, :, :], scalar=0.0, in1=dt[:, :, :], op0=ALU.max, op1=ALU.add))
            dve.wait_ge(a_ready, 1)
            chain(dve.tensor_scalar(expA, expA, -1.0, None, ALU.mult))
            dve.tensor_tensor(dtA[:, :, :], dt[:, :, :], bc(expA.unsqueeze(1), [P, 4, 32]), ALU.mult).then_inc(dt_ready, 1)
            jobs.wait_filled(dve, "cum")
            jobs.drain(dve.tensor_copy(acs[:, :, :], jobs.out("cum")[:, 0:256].rearrange("p (i h) -> p i h", i=4)), "cum")
            jobs.wait_drained(dve, "cum")
            dve.tensor_tensor(dw[:, :, :], acs[:, :, 32:64], acs[:, :, 0:32], ALU.subtract).then_inc(diff_ready, 1)

            tmpw = m[:, 0:2, :].rearrange("p a n -> p (a n)")
            tmpv = m[:, 2:4, :].rearrange("p a n -> p (a n)")

            def head_norm(v, n_heads, ssum, rs, turn, g, tiles, tab):
                tn = len(tiles)
                w4 = tmpw.rearrange("p (t c) -> p t c", t=tn)
                tt(w4, v, v, ALU.mult)
                dve.tensor_reduce(ssum, w4.rearrange("p t (h d) -> p t h d", d=DH), AX_X, ALU.add).then_inc(qk_sum, 1)
                dve.wait_ge(qk_std, turn)
                for i in range(tn):
                    v3 = v[:, i, :].rearrange("p (h d) -> p h d", d=DH)
                    order.up(dve.tensor_tensor(v3, v3, bc(rs[:, i, :].unsqueeze(2), [P, n_heads, DH]), ALU.mult))
                order.here(dve)
                for i in range(tn):
                    v3 = v[:, i, :].rearrange("p (h d) -> p h d", d=DH)
                    order.up(dve.tensor_tensor(v3, v3, bc(g.unsqueeze(1), [P, n_heads, DH]), ALU.mult))
                order.here(dve)
                for i, tile in enumerate(tiles):
                    if tile is None:
                        continue
                    cos, sin, nsin = (K("axial", 64 * s + 32 * tile, 64 * s + 32 * tile + 32) for s in range(3))
                    v3 = v[:, i, :].rearrange("p (h d) -> p h d", d=32)
                    w3 = tmpw[:, 0:64 * n_heads].rearrange("p (h r d) -> p h r d", r=2, d=32)
                    v4 = v[:, i, :].rearrange("p (h r d) -> p h r d", r=2, d=32)
                    for r, tb in ((0, nsin), (1, sin)):
                        order.up(dve.tensor_tensor(w3[:, :, r, :], v4[:, :, 1 - r, :], bc(tb.unsqueeze(1), [P, n_heads, 32]), ALU.mult))
                    tt(tmpv[:, 0:64 * n_heads].rearrange("p (h d) -> p h d", d=32), v3, bc(cos.unsqueeze(1), [P, 2 * n_heads, 32]), ALU.mult)
                    tt(v[:, i, :], tmpw[:, 0:64 * n_heads], tmpv[:, 0:64 * n_heads], ALU.add)

            for i in range(SEQ_TILES):
                jobs.wait_drained(dve, ("kv", i))
            head_norm(kv[:, :, 0:256], 4, kss.rearrange("p (t h) -> p t h", t=4), krs.rearrange("p (t h) -> p t h", t=4), 1, R("kn"),
                      [None, None, 0, 1], None)
            dve.tensor_copy(kss[:, 0:1], krs[:, 0:1]).then_inc(qk_ready, 1)

            dve.wait_ge(decays, 3)
            dve.tensor_tensor(dw[:, :, :], dw[:, :, :], dt[:, :, :], ALU.mult).then_inc(dw_ready, 1)
            for t in range(TT):
                for c in range(2):
                    jobs.wait_drained(dve, ("q", c, t))
                head_norm(q[:, t:t + 1, :], 16, qss[:, t:t + 1, :], qrs[:, t:t + 1, :], 2 + t, R("qn"), [t], None)
                dve.tensor_copy(qss[:, t, 0:1], qrs[:, t, 0:1]).then_inc(qk_ready, 1)
            for t in range(TT):
                jobs.wait_filled(dve, ("cb", t))
                src = jobs.out(("cb", t))[:, 0:256].rearrange("p (g q) -> p g q", g=2)
                order.up(dve.tensor_tensor(cb[:, t, 0, :, :], src, bc(K("tri_u").unsqueeze(1), [P, 2, P]), ALU.mult))
                jobs.drain(dve.tensor_tensor(cb[:, t, 1, :, :], src, bc(K("tri_l").unsqueeze(1), [P, 2, P]), ALU.mult), ("cb", t))

            slot = {0: 0, 1: 0, 2: 1, 3: 3, 4: 3, 5: 2}
            prev = {1: 0, 2: 0, 4: 3, 5: 3}
            for n, (i, d) in enumerate(STATES):
                for g in range(2):
                    name = ("st", n, g)
                    dst = H[:, slot[n], g * 512:(g + 1) * 512]
                    jobs.wait_filled(dve, name)
                    if n in prev:
                        src = H[:, prev[n], g * 512:(g + 1) * 512].rearrange("p (h c) -> p h c", c=DH)
                        chain(dve.tensor_tensor(dst.rearrange("p (h c) -> p h c", c=DH), src,
                                                bc(dec[:, i, 16 * d + 8 * g:16 * d + 8 * g + 8].unsqueeze(2), [P, 8, DH]), ALU.mult))
                        jobs.drain(dve.tensor_tensor(dst, dst, jobs.out(name), ALU.add), name)
                    else:
                        jobs.drain(dve.tensor_copy(dst, jobs.out(name)), name)
                    jobs.wait_drained(dve, name)
                    dve.sem_inc(h_ready, 1)

            def decay_diffs(n):
                t, g, quad = UNITS[n]
                for d in range(2):
                    name = ("aq", t, g, quad, d)
                    if 2 * n + d >= 4:
                        if UNITS[n - 2][2] == 0:
                            dve.wait_ge(m_used, (n - 2) // 2 + 1)
                        else:
                            jobs.wait_filled(dve, ("yd", *UNITS[n - 2][:2]))
                    jobs.wait_filled(dve, name)
                    for h in range(4):
                        head = 16 * d + 8 * g + 4 * quad + h
                        ins = dve.tensor_scalar(m[:, (2 * n + d) % 4, h * P:(h + 1) * P], jobs.out(name)[:, h * P:(h + 1) * P],
                                                acs[:, 2 + t, head:head + 1], 0.0, ALU.subtract, ALU.min)
                        if h < 3:
                            order.up(ins)
                        else:
                            jobs.drain(ins, name)
                    jobs.wait_drained(dve, name)
                    dve.sem_inc(aq_diff, 1)

            def gather_y(t, g):
                yy = y[:, t, g * 512:(g + 1) * 512]
                if g == 0:
                    dve.wait_ge(skip_ready, t + 1)
                name = ("yd", t, g)
                jobs.wait_filled(dve, name)
                jobs.drain(dve.tensor_tensor(yy, jobs.out(name), yy, ALU.add), name)
                jobs.wait_drained(dve, name)
                for d in range(2):
                    name = ("yo", t, g, d)
                    jobs.wait_filled(dve, name)
                    tb = p[:, d, :]
                    jobs.drain(dve.tensor_tensor(tb.rearrange("p (h c) -> p h c", c=DH), jobs.out(name).rearrange("p (h c) -> p h c", c=DH),
                                                 bc(ea[:, 2 + t, 16 * d + 8 * g:16 * d + 8 * g + 8].unsqueeze(2), [P, 8, DH]), ALU.mult), name)
                    jobs.wait_drained(dve, name)
                    tt(yy, yy, tb, ALU.add)
                if g == 1:
                    for c in range(2):
                        jobs.wait_drained(dve, ("z", c, t))
                    dve.tensor_tensor(y[:, t, :], y[:, t, :], z[:, t, :], ALU.mult).then_inc(y_gated, 1)

            for n in range(len(UNITS) + 1):
                if n < len(UNITS):
                    decay_diffs(n)
                if n >= 1 and UNITS[n - 1][2] == 1:
                    gather_y(*UNITS[n - 1][:2])

            for n in range(len(HEAD_ITEMS) + 2):
                if n < len(HEAD_ITEMS):
                    jobs.wait_filled(dve, ("S", n))
                    dve.tensor_reduce(nm[:, n:n + 1], jobs.out(("S", n)), AX_X, ALU.max, negate=True).then_inc(nmax_ready, 1)
                if n >= 1 and (n - 1) % 2 == 1:
                    name = ("PT", n - 1)
                    jobs.wait_filled(dve, name)
                    jobs.drain(dve.tensor_copy(pt[:, (n - 1) % 2, :], jobs.out(name)), name)
                if n >= 2:
                    t, b, g = HEAD_ITEMS[n - 2]
                    if b % 4 == 3 and g == 1:
                        name = ("O", t, b // 4)
                        h0 = n - 2 - 7
                        jobs.wait_drained(dve, ("S", n - 2))
                        chain(dve.reciprocal(rden[:, h0:h0 + 8], dn[:, h0:h0 + 8]))
                        jobs.wait_filled(dve, name)
                        jobs.drain(dve.tensor_tensor(q[:, t, (b // 4) * 512:(b // 4 + 1) * 512].rearrange("p (h c) -> p h c", c=DH),
                                                     jobs.out(name).rearrange("p (h c) -> p h c", c=DH),
                                                     bc(rden[:, h0:h0 + 8].unsqueeze(2), [P, 8, DH]), ALU.mult), name)
            for t in range(TT):
                dve.wait_ge(y_std, t + 1)
                for g in range(2):
                    ins = dve.tensor_scalar(y[:, t, g * 512:(g + 1) * 512], y[:, t, g * 512:(g + 1) * 512], yrs[:, 2 * t + g:2 * t + g + 1], None, ALU.mult)
                    if g == 0:
                        order.up(ins)
                    else:
                        ins.then_inc(y_norm, 1)
            dve.wait_ge(y_sq, 4)
            for v, block in enumerate((16, 40)):
                for b in range(8):
                    ins = dve.tensor_scalar(wx[:, v, b * P:(b + 1) * P], ident, modT[:, block + b, 0:1], None, ALU.mult)
                    if b < 7:
                        order.up(ins)
                    else:
                        ins.then_inc(diag_ready, 1)
            for t in range(TT):
                for h in range(2):
                    name = ("mixT", h, t)
                    jobs.wait_filled(dve, name)
                    jobs.drain(dve.tensor_tensor(mixT[:, 4 * h:4 * h + 4, t * P:(t + 1) * P], jobs.out(name).rearrange("p (b t) -> p b t", b=4),
                                                 bc(C("ssd_g", 4 * h, 4 * h + 4).unsqueeze(2), [P, 4, P]), ALU.mult), name)

            def residual(v, which, sources):
                for t in range(TT):
                    for c in range(2):
                        cs = slice(c * 512, (c + 1) * 512)
                        wait, src, done = sources(t, c)
                        wait()
                        done(dve.tensor_tensor(res[:, t, cs], src, gB[:, v, cs], ALU.mult))
                        chain(dve.scalar_tensor_tensor(out=res[:, t, cs], in0=x[:, t, cs], scalar=ALPHA, in1=res[:, t, cs], op0=ALU.mult, op1=ALU.add))
                        chain(dve.bn_stats(stats[:, t, c, :], res[:, t, cs]))
                    dve.bn_aggr(mv[:, t, :], stats[:, t, :, :].rearrange("p c s -> p (c s)")).then_inc(ln_stat, 1)
                for t in range(TT):
                    dve.wait_ge(ln_std, v * TT + t + 1)
                    chain(dve.tensor_scalar(x[:, t, :], res[:, t, :], mv[:, t, 0:1], lstd[:, t:t + 1], ALU.subtract, ALU.mult))
                    tt(x[:, t, :], x[:, t, :], R(f"ln{v + 1}_g"), ALU.mult)
                    dve.tensor_tensor(x[:, t, :], x[:, t, :], R(f"ln{v + 1}_b"), ALU.add).then_inc(x_normed, 1)

            def out_source(t, c):
                name = ("out", t, c)

                def wait():
                    jobs.wait_filled(dve, name)

                def done(ins):
                    jobs.drain(ins, name)
                    jobs.wait_drained(dve, name)
                return wait, jobs.out(name), done

            for c in range(2):
                jobs.wait_drained(dve, ("gB", 1, c))
            residual(0, "out", out_source)
            for c in range(2):
                for t in range(TT):
                    scale_in(("hf", c, t), hT[:, 4 * c:4 * c + 4, t * P:(t + 1) * P], 32 + 4 * c, 0)

            jobs.wait_filled(dve, "route")
            jobs.drain(dve.tensor_tensor(lg[:, :, :], jobs.out("route")[:, 0:40].rearrange("p (t n) -> p t n", t=2),
                                         bc(R("br").unsqueeze(1), [P, 2, 20]), ALU.add), "route")
            jobs.wait_drained(dve, "route")
            four = bc(K("four").unsqueeze(1), [P, 2, 4])

            def first_max(oh, v, vmax, scratch):
                chain(dve.tensor_reduce(vmax, v, AX_X, ALU.max))
                tt(oh, v, bc(vmax.unsqueeze(2), [P, 2, 4]), ALU.is_equal)
                tt(oh, oh, four, ALU.mult)
                chain(dve.tensor_reduce(scratch, oh, AX_X, ALU.max))
                tt(oh, oh, bc(scratch.unsqueeze(2), [P, 2, 4]), ALU.is_equal)

            first_max(goh[:, :, :], lg[:, :, 0:4], gm, r2a)
            tt(r8a[:, :, :], lg[:, :, 0:4], bc(gm.unsqueeze(2), [P, 2, 4]), ALU.subtract)
            el = lg[:, :, 4:20].rearrange("p t (g e) -> p t g e", g=4)
            for t in range(TT):
                order.up(dve.tensor_tensor(r32[:, t, :, :], el[:, t, :, :], bc(goh[:, t, :].unsqueeze(2), [P, 4, 4]), ALU.mult))
            order.here(dve)
            chain(dve.tensor_reduce(es[:, :, :], r32[:, :, :, :].rearrange("p t g e -> p t e g"), AX_X, ALU.add))
            chain(dve.tensor_reduce(r2b, es[:, :, :], AX_X, ALU.max))
            dve.tensor_tensor(es[:, :, :], es[:, :, :], bc(r2b.unsqueeze(2), [P, 2, 4]), ALU.subtract).then_inc(r_logits, 1)
            dve.wait_ge(r_exp, 2)
            chain(dve.tensor_reduce(gs, r8a[:, :, :], AX_X, ALU.add))
            chain(dve.reciprocal(gval, gs))
            chain(dve.tensor_reduce(r2a, es[:, :, :], AX_X, ALU.add))
            chain(dve.reciprocal(r2b, r2a))
            tt(pe_[:, :, :], es[:, :, :], bc(r2b.unsqueeze(2), [P, 2, 4]), ALU.mult)
            first_max(oh1[:, :, :], pe_[:, :, :], r2a, r2c)
            chain(dve.scalar_tensor_tensor(out=pm[:, :, :], in0=oh1[:, :, :], scalar=-2.0, in1=pe_[:, :, :], op0=ALU.mult, op1=ALU.add))
            first_max(oh2[:, :, :], pm[:, :, :], r2b, r2c)
            tt(r2c, r2a, r2b, ALU.add)
            chain(dve.reciprocal(r2c, r2c))
            tt(r2c, r2c, gval, ALU.mult)
            tt(wgt[:, :, :], oh1[:, :, :], oh2[:, :, :], ALU.add)
            tt(wgt[:, :, :], wgt[:, :, :], pe_[:, :, :], ALU.mult)
            tt(wgt[:, :, :], wgt[:, :, :], bc(r2c.unsqueeze(2), [P, 2, 4]), ALU.mult)
            for t in range(TT):
                ins = dve.tensor_tensor(comb[:, t, :].rearrange("p (g e) -> p g e", g=4), bc(goh[:, t, :].unsqueeze(2), [P, 4, 4]),
                                        bc(wgt[:, t, :].unsqueeze(1), [P, 4, 4]), ALU.mult)
                if t == 0:
                    chain(ins)
                else:
                    ins.then_inc(comb_ready, 1)
            for i in range(8):
                jobs.wait_drained(dve, ("combB", i))
            with dve.Fori(0, EXPERTS // EXPERT_STEP) as step:
                for e in range(EXPERT_STEP):
                    g, u = (("s0", "s1"), ("t", "u"))[e % 2]
                    dve.wait_ge(filled[u], step * 2 + (jobs.turn[u] + e // 2 + 1))
                    dve.wait_ge(drained[g], step * 2 + (jobs.sum[g] + e // 2 + 1))
                    dve.tensor_tensor(p[:, e % 2, :], p[:, e % 2, :], psum[:, region[u][0]:region[u][0] + 512], ALU.mult).then_inc(drained[u], 1)
                    dve.wait_ge(drained[u], step * 2 + (jobs.sum[u] + e // 2 + 1))
                    if e >= 2:
                        dve.wait_ge(hid_used, step * EXPERT_STEP + (e - 1))
                    comb_e = combB[:, bass.ds(step * EXPERT_STEP + e, 1), :]
                    hid = m[:, 2 * (e % 2):2 * (e % 2) + 1, :].rearrange("p a (b t) -> p (a b) t", t=T)
                    dve.tensor_tensor(hid, p[:, e % 2, :].rearrange("p (b t) -> p b t", b=2), bc(comb_e, [P, 2, T]), ALU.mult).then_inc(hid_ready, 1)
                    dve.wait_ge(hid_ready, step * EXPERT_STEP + (e + 1))
                    dve.sem_inc(hid_raw, 1)
                dve.wait_ge(hid_used, step * EXPERT_STEP + EXPERT_STEP)

            def moe_source(t, c):
                def done(ins):
                    chain(ins)
                return (lambda: None), psum[:, (2 * t + c) * 512:(2 * t + c + 1) * 512], done

            residual(1, "moe", moe_source)

        @block.gpsimd
        def _(pool):
            order = Signal(g_order)

            def chain(ins):
                order.up(ins)
                order.here(pool)

            pool.wait_ge(params, 32)
            pool.wait_ge(mod_ready, 2)
            for s in range(2):
                for c in range(2):
                    for t in range(TT):
                        jobs.wait_drained(pool, ("in", s, c, t))
                        dst = hT[:, 4 * c:4 * c + 4, (2 * s + t) * P:(2 * s + t + 1) * P]
                        pool.tensor_tensor(dst, dst, bc(modT[:, 4 * c:4 * c + 4, 1 - s:2 - s], [P, 4, P]), ALU.add).then_inc(shifted, 1)

            def inv_roots(turn, dst, total, n, sig, eps=EPS, scratch=None):
                w = dst.shape[1]
                chain(pool.tensor_scalar(scratch[:, 0:w], total, 1.0 / n, eps, ALU.mult, ALU.add))
                pool.tensor_tensor(dst, scratch[:, 0:w], K("mhalf", 0, w), ALU.pow).then_inc(sig, 1)
                pool.wait_ge(sig, turn)

            pool.wait_ge(qk_sum, 1)
            inv_roots(1, krs, kss, DH, qk_std, scratch=ssq)
            for t in range(TT):
                pool.wait_ge(qk_sum, 2 + t)
                inv_roots(2 + t, qrs[:, t, :], qss[:, t, :], DH, qk_std, scratch=ssq)

            pool.wait_ge(dw_ready, 1)
            for n, (i, d) in enumerate(STATES):
                for half in range(2):
                    jobs.wait_drained(pool, ("xsT", i, half))
                if n >= 2:
                    for g in range(2):
                        jobs.wait_filled(pool, ("st", n - 2, g))
                pool.tensor_tensor(wx[:, n % 2, :].rearrange("p (h c) -> p h c", c=DH), xs[:, i, :].rearrange("p (h c) -> p h c", c=DH),
                                   bc(dw[:, i, 16 * d:16 * d + 16].unsqueeze(2), [P, 16, DH]), ALU.mult).then_inc(xw_ready, 1)
            for i in range(4):
                for half in range(2):
                    jobs.wait_filled(pool, ("xsT", i, half))
            for t in range(TT):
                for d in range(2):
                    pool.tensor_tensor(xdt[:, 2 * t + d, :].rearrange("p (h c) -> p h c", c=DH), xs[:, 2 + t, :].rearrange("p (h c) -> p h c", c=DH),
                                       bc(dt[:, 2 + t, 16 * d:16 * d + 16].unsqueeze(2), [P, 16, DH]), ALU.mult).then_inc(xdt_ready, 1)
                pool.tensor_tensor(y[:, t, :].rearrange("p (h c) -> p h c", c=DH), xs[:, 2 + t, :].rearrange("p (h c) -> p h c", c=DH),
                                   bc(R("skip").unsqueeze(2), [P, 16, DH]), ALU.mult).then_inc(skip_ready, 1)
            for t in range(TT):
                jobs.wait_drained(pool, ("cb", t))
            for n, (t, g, quad) in enumerate(UNITS):
                for d in range(2):
                    pool.wait_ge(aq_exp, 2 * n + d + 1)
                    m3 = m[:, (2 * n + d) % 4, :].rearrange("p (h q) -> p h q", h=4)
                    pool.tensor_tensor(m3, m3, bc(cb[:, t, d, g, :].unsqueeze(1), [P, 4, P]), ALU.mult).then_inc(m_ready, 1)
            for t in range(TT):
                pool.wait_ge(y_sq, 2 * t + 2)
                inv_roots(t + 1, yrs[:, 2 * t:2 * t + 2], yss[:, 2 * t:2 * t + 2], 512, y_std, scratch=ssq)

            def ln_roots(v):
                for t in range(TT):
                    pool.wait_ge(ln_stat, v * TT + t + 1)
                    chain(pool.tensor_scalar(lms[:, 0:1], mv[:, t, 1:2], 1.0, LN_EPS, ALU.mult, ALU.add))
                    pool.tensor_tensor(lstd[:, t:t + 1], lms[:, 0:1], K("mhalf", 0, 1), ALU.pow).then_inc(ln_std, 1)
                    pool.wait_ge(ln_std, v * TT + t + 1)

            ln_roots(0)
            for c in range(2):
                for t in range(TT):
                    jobs.wait_drained(pool, ("hf", c, t))
                    dst = hT[:, 4 * c:4 * c + 4, t * P:(t + 1) * P]
                    pool.tensor_tensor(dst, dst, bc(modT[:, 24 + 4 * c:28 + 4 * c, 0:1], [P, 4, P]), ALU.add).then_inc(shifted, 1)
            jobs.wait_filled(pool, ("yd", 1, 1))
            pool.memset(m[:, 0:2, :], 0.0).then_inc(zero_ready, 1)
            ln_roots(1)


MEM = dict(
    tm=(TT, D), hT=(KD, T), proj=(TT, 2048), gates=(8192,), qTs=(3, 4, T), rkT=(3, T), sg=(2, 512),
    hidk=(2, 2, 16), hidv=(2, P), kblk=(32,), vblk=(512,), sc=(2, 4, T), pt=(2, 2, 4, P), small=(192,),
    brT=(4, 4, T), bglu=(4, T + TAPS - 1), cpad=(4, 16 + T), acc=(4, T), tmp=(2, 512), psum_a=(16 + T,), psum_b=(16 + T,),
    csc=(2, P), cpT=(2, P), hsum=(2, 2, 32), cols=(N_COLS,), rows=(N_ROWS,),
)


def build_program(nc, x_in, ctx_in, weights, cols, rows, cols2, rows2, const, out):
    with ExitStack() as ctx:
        keep = dict(x=(TT, D), const=(N_CONST,))
        mem = {k: ctx.enter_context(nc.sbuf_tensor(f"sb_{k}", [P, *s], F32)) for k, s in keep.items()}
        ring = ctx.enter_context(nc.sbuf_tensor("ring", [P, SLOTS, CH], F32))
        psum = ctx.enter_context(nc.psum_tensor("psum", [P, 4096], F32))
        landed = [ctx.enter_context(nc.semaphore(f"landed_{s}")) for s in range(SLOTS)]
        used = ctx.enter_context(nc.semaphore("used"))
        loaded = ctx.enter_context(nc.semaphore("loaded"))
        zeroed = ctx.enter_context(nc.semaphore("zeroed"))

        with ExitStack() as first:
            mem1 = {**mem, **{k: first.enter_context(nc.sbuf_tensor(f"sb_{k}", [P, *s], F32)) for k, s in MEM.items()}}

            with nc.Block() as block:
                @block.sync
                def _(sp):
                    sp.dma_start(mem["x"][:, :, :], x_in.rearrange("(t p) d -> p t d", p=P)).then_inc(loaded, 16)
                    sp.dma_start(mem["const"][:, :], const).then_inc(loaded, 16)
                    for s in range(SLOTS):
                        sp.dma_start(ring[:, s, :], weights[s]).then_inc(landed[s], 16)

                @block.gpsimd
                def _(pool):
                    pool.memset(mem1["hidv"][:, :, :], 0.0).then_inc(zeroed, 1)
                    pool.memset(mem1["kblk"][:, :], 0.0).then_inc(zeroed, 1)
                    pool.memset(mem1["bglu"][:, :, 0:TAPS - 1], 0.0).then_inc(zeroed, 1)
                    pool.memset(mem1["cpad"][:, :, 0:16], 0.0).then_inc(zeroed, 1)
                    pool.wait_ge(zeroed, 4)

            layer_sems = []

            def sems(name):
                s = first.enter_context(nc.semaphore(name))
                layer_sems.append(s)
                return s

            with nc.Fori(0, LAYERS) as l:
                layer_block(nc, l, mem1, ring, landed, used, weights, psum, sems, cols, rows, loaded)
                nums = [s.num for s in layer_sems]
                assert nums == list(range(nums[0], nums[-1] + 1))
                nc.all_engine_barrier(sems_to_clear=range(nums[0], nums[-1] + 1))

        with ExitStack() as second:
            mem2 = {**mem, **{k: second.enter_context(nc.sbuf_tensor(f"sb2_{k}", [P, *s], F32)) for k, s in MEM2.items()}}

            def sems2(name):
                return second.enter_context(nc.semaphore(name))

            block2(nc, mem2, ring, landed, used, weights, psum, sems2, cols2, rows2, ctx_in, out)


HEADS_IN_PAIRS = [4 * g + j for j in range(4) for g in range(2)]


def pairs(a, width, axis=-1):
    idx = np.concatenate([np.arange(h * width, (h + 1) * width) for h in HEADS_IN_PAIRS])
    return np.take(a, idx, axis=axis)


def to_cols(v):
    return v.reshape(-1, P).T


def k_split(w):
    return w.reshape(2, 4, P, 512).transpose(0, 2, 1, 3).reshape(2, P, CH)


def n_split(w):
    return w.reshape(KD, P, -1, 256).transpose(2, 1, 0, 3).reshape(-1, P, CH)


def rows_split(w):
    return w.reshape(-1, 2, P, D).transpose(0, 2, 1, 3).reshape(-1, P, CH)


def layer_inputs(l, i):
    w = i["w_in"][l]
    kv = w[:, 512:1280]
    gate_val = i["ffn_w_up"][l].reshape(D, 2, FB, P).transpose(0, 2, 1, 3).reshape(D, 2 * DFF)
    br = i["w_branch"][l]
    br = {0: pairs(br[0], DH, 0), 1: br[1], 2: br[2], 3: pairs(br[3], DH, 0)}
    chunks = [
        k_split(kv[:, 0:512]), k_split(np.concatenate([kv[:, 512:768], w[:, 1816:2072]], 1)),
        k_split(pairs(w[:, 0:512], DH)), k_split(pairs(w[:, 1304:1816], DH)),
        n_split(w[:, 3096:3608]), n_split(w[:, 2072:2584]),
        i["nsa_cmp_w1"][l].reshape(2, 2, 8, P, 256).transpose(0, 1, 3, 2, 4).reshape(4, P, CH),
        n_split(w[:, 2584:3096]),
        n_split(i["w_gate"][l]),
        *[br[n].reshape(4, P, 2, 512).transpose(2, 1, 0, 3).reshape(2, P, CH) for n in BRANCH_ORDER],
        k_split(i["w_o"][l][:, 0:512]), k_split(i["w_o"][l][:, 512:1024]),
        n_split(gate_val), rows_split(i["ffn_w_down"][l]), np.zeros((1, P, CH), np.float32),
    ]
    pos = i["nsa_cmp_pos"][l].reshape(2, 16, 2, DH).transpose(2, 3, 0, 1).reshape(P, 32)
    w2 = i["nsa_cmp_w2"][l].reshape(2, 2, P, DH).transpose(2, 0, 1, 3).reshape(P, 256)
    fields = dict(
        g_mix=to_cols(i["norm_mix_pre"][l]), g_ffn=to_cols(i["norm_ffn_pre"][l]), pos=pos, w2=w2,
        conv_w=i["conv_w"][l].reshape(TAPS, 4, P).transpose(2, 1, 0), conv_b=to_cols(i["conv_b"][l]),
        ln_g=to_cols(i["conv_ln_g"][l]), ln_b=to_cols(i["conv_ln_b"][l]),
        pool_w=i["pool_w"][l].transpose(1, 0, 2), pool_s=to_cols(i["pool_scale"][l]),
        fw=i["ffn_conv_w"][l].reshape(3, 2, FB, P).transpose(3, 2, 1, 0),
        fb=i["ffn_conv_b"][l].reshape(2, FB, P).transpose(2, 1, 0),
        w_ga=w[:, 1280:1304].reshape(KD, P, 3, 2, 4).transpose(1, 0, 2, 4, 3),
    )
    packed = np.concatenate([fields[name].reshape(P, width) for name, (_, width) in COLS.items()], 1)
    row = np.concatenate([i["norm_mix_post"][l], i["norm_ffn_post"][l], pairs(i["swa_sinks"][l], 1)])
    return np.concatenate(chunks), packed, row[None, :]


def block2_inputs(i):
    pick = lambda a, idx, axis=-1: np.take(a, np.concatenate([np.atleast_1d(v) for v in idx]), axis=axis)
    inner = np.concatenate([np.arange(0, DH, 2), np.arange(1, DH, 2)])
    w = i["w_in_2"][0]
    k_cols = [3616 + h * DH + inner for h in range(4)]
    q_heads = [4 * (2 * (b // 4) + g) + b % 4 for b in range(8) for g in range(2)]
    q_cols = [1024 + h * DH + inner for h in q_heads]
    wo = i["w_out_2"][0]
    o_rows = [np.arange(1024)] + [1024 + h * DH + np.arange(DH) for h in q_heads]
    q = pick(w, q_cols)
    chunks = [n_split(i["w_mod_2"][0]), k_split(np.concatenate([pick(w, k_cols), w[:, 3872:4128]], 1)), n_split(w[:, 2048:3584]),
              k_split(q[:, 0:512]), k_split(q[:, 512:1024]), k_split(w[:, 0:512]), k_split(w[:, 512:1024]),
              rows_split(pick(wo, o_rows, 0))]
    for e0 in range(0, EXPERTS, EXPERT_STEP):
        gu = [[n_split(i[k][0, e]) for k in ("w_gate_2", "w_up_2")] for e in range(e0, e0 + EXPERT_STEP)]
        down = [rows_split(i["w_down_2"][0, e]) for e in range(e0, e0 + EXPERT_STEP)]
        chunks += [*gu[0], *gu[1], down[0], *gu[2], down[1], *gu[3], down[2], down[3]]
    k_pack = lambda a: a.reshape(KD, P, -1).transpose(1, 0, 2)
    fields = dict(
        b_mod=to_cols(i["b_mod_2"][0]), conv_w=i["conv_w_2"][0].reshape(5, DX, P).transpose(2, 1, 0), conv_b=to_cols(i["conv_b_2"][0]),
        ssd_g=to_cols(i["ssd_norm_g_2"][0]), c=np.stack([to_cols(i["c_2"][0]), to_cols(i["c_ctx_2"])], -1),
        w_dt=k_pack(w[:, 3584:3616]), w_r=k_pack(np.concatenate([i["w_rg_2"][0], i["w_re_2"][0]], 1)),
    )
    packed = np.concatenate([fields[name].reshape(P, width) for name, (_, width) in COLS2.items()], 1)
    row = np.concatenate([i["ln1_g_2"][0], i["ln1_b_2"][0], i["ln2_g_2"][0], i["ln2_b_2"][0], i["dt_bias_2"][0].reshape(-1),
                          i["a_log_2"][0].reshape(-1), i["q_norm_g_2"][0][inner], i["k_norm_g_2"][0][inner],
                          i["b_rg_2"][0], i["b_re_2"][0], i["d_skip_2"][0]])
    return np.concatenate(chunks), packed, row[None, :]


def lay_out(i):
    layers = [layer_inputs(l, i) for l in range(LAYERS)]
    chunks2, packed2, row2 = block2_inputs(i)
    return dict(
        x_in=i["x"][0], ctx_in=i["ctx_2"][0], weights=np.concatenate([layers[0][0], layers[1][0], chunks2]),
        cols=np.stack([v[1] for v in layers]), rows=np.stack([v[2] for v in layers]), cols2=packed2, rows2=row2, const=constants(),
    )


def kernel(**inputs):
    import concourse.bacc as bacc
    from concourse.bass_utils import run_bass_kernel_spmd

    arrays = {k: np.ascontiguousarray(v) for k, v in lay_out({k: np.asarray(v) for k, v in inputs.items()}).items()}
    nc = bacc.Bacc("TRN2", target_bir_lowering=False, num_devices=1)
    args = {k: nc.dram_tensor(k, v.shape, F32, kind="ExternalInput").ap() for k, v in arrays.items()}
    out = nc.dram_tensor("out", (T, D), F32, kind="ExternalOutput").ap()
    build_program(nc, out=out, **args)
    result = run_bass_kernel_spmd(nc, [arrays], core_ids=[0])
    return result.results[0]["out"].reshape(1, T, D)
```

```python
from contextlib import ExitStack

import numpy as np

import concourse.bass as bass
import concourse.mybir as mybir

F32 = mybir.dt.float32
F32R = mybir.dt.float32r
ALU = mybir.AluOpType
ACT = mybir.ActivationFunctionType
AX_X = mybir.AxisListType.X

P = 128
T = 256
TT = T // P
D = 1024
KD = D // P
LAYERS = 2
DH = 64
BR = 512
NEG = -1e30
EPS = 1e-6
SLOTS = 4
CH = 2048
DFF = 2816
FB = DFF // P
TAPS = 31
CMP_N = 15
N_LAYER_CHUNKS = 92
SPLITS = 3
FFN_CHUNKS = FB + FB // 2
MODS = 6 * KD
MOD_STEPS = MODS // (4 * LAYERS)


def offsets(fields):
    at, out = 0, {}
    for name, width in fields:
        out[name] = (at, width)
        at += width
    return out, at


COLS, N_COLS = offsets([
    ("g_mix", KD), ("g_ffn", KD), ("pos", 32), ("w2", 256), ("conv_w", 4 * TAPS), ("conv_b", 4),
    ("ln_g", 4), ("ln_b", 4), ("pool_w", 512), ("pool_s", 4), ("fw", 2 * FB * 3), ("fb", 2 * FB),
    ("w_ga", KD * 24),
])
ROWS, N_ROWS = offsets([("mix_post", D), ("ffn_post", D), ("sinks", 8)])
CONST, N_CONST = offsets([
    ("ident", P), ("tri_u", P), ("tri_l", P), ("ones", P), ("full_causal", 2 * P), ("band", 2 * P),
    ("cmp_mask", 32), ("cmp_valid", 2), ("blk8", 8), ("rope", 192), ("axial", 192),
    ("pool_inv", 64), ("mhalf", 32), ("four", 4),
])


def constants():
    c = np.zeros((P, N_CONST), np.float32)

    def put(name, value):
        at, width = CONST[name]
        c[:, at:at + width] = np.asarray(value, np.float32).reshape(P, width)

    q = np.arange(P)
    later = q[:, None] >= q[None, :]
    causal = np.where(later, 0.0, NEG)
    put("ident", np.eye(P))
    put("tri_u", q[:, None] <= q[None, :])
    put("tri_l", later)
    put("ones", np.ones((P, P)))
    put("full_causal", np.concatenate([np.zeros((P, P)), causal], 1))
    put("band", np.concatenate([np.where(q[None, :] > q[:, None], 0.0, NEG), causal], 1))
    t = q[:, None] + P * np.arange(TT)[None, :]
    end = np.where(np.arange(16) < CMP_N, np.arange(16) * 16 + 31, 10 ** 9)
    put("cmp_mask", np.where(end[None, None, :] <= t[:, :, None], 0.0, NEG))
    put("cmp_valid", t >= 31)
    put("blk8", q[:, None] // 16 == np.arange(8)[None, :])
    inv = 1.0 / (10000.0 ** (np.arange(0, 64, 2, dtype=np.float32) / 64))
    ang = t[:, :, None].astype(np.float32) * inv.astype(np.float32)
    put("rope", np.stack([np.cos(ang), np.sin(ang), -np.sin(ang)], 1))
    inv = np.power(np.float32(10000.0), -np.arange(0, 32, 2, dtype=np.float32) / 32)
    ang = np.concatenate([(t // 64)[:, :, None] * inv, (t % 64)[:, :, None] * inv], -1).astype(np.float32)
    put("axial", np.stack([np.cos(ang), np.sin(ang), -np.sin(ang)], 1))
    put("pool_inv", np.broadcast_to(
        [[1.0 / min(w, i + 1) for i in range(16)] for w in (2, 4, 8, 16)], (P, 4, 16)))
    put("mhalf", np.full((P, 32), -0.5))
    put("four", np.broadcast_to([4.0, 3.0, 2.0, 1.0], (P, 4)))
    return c


REGION = {**{f"a{i}": (i * 512, 512) for i in range(4)}, "s": (2048, 1024), "t": (3072, 512), "u": (3584, 512)}


class Jobs:

    def __init__(self, psum, filled, drained, region=REGION, ring=4):
        self.psum, self.filled, self.drained, self.region, self.ring = psum, filled, drained, region, ring
        self.jobs, self.turn, self.sum, self.next = {}, {}, {}, 0

    def plan(self, name, region=None, drains=1):
        if region is None:
            region, self.next = f"a{self.next % self.ring}", self.next + 1
        before, turn = self.sum.get(region, 0), self.turn.get(region, 0)
        self.jobs[name] = (region, turn + 1, before, before + drains)
        self.turn[region], self.sum[region] = turn + 1, before + drains

    def out(self, name):
        at, width = self.region[self.jobs[name][0]]
        return self.psum[:, at:at + width]

    def claim(self, pe, name):
        region, _, before, _ = self.jobs[name]
        if before:
            pe.wait_ge(self.drained[region], before)

    def fill(self, ins, name):
        ins.then_inc(self.filled[self.jobs[name][0]], 1)

    def wait_filled(self, eng, name):
        region, turn, _, _ = self.jobs[name]
        eng.wait_ge(self.filled[region], turn)

    def drain(self, ins, name):
        ins.then_inc(self.drained[self.jobs[name][0]], 1)

    def wait_drained(self, eng, name):
        region, _, _, after = self.jobs[name]
        eng.wait_ge(self.drained[region], after)


class Signal:

    def __init__(self, sem):
        self.sem, self.n = sem, 0

    def up(self, ins):
        self.n += 1
        ins.then_inc(self.sem, 1)

    def here(self, eng, less=0):
        if self.n - less > 0:
            eng.wait_ge(self.sem, self.n - less)


def bc(ap, shape):
    return ap.to_broadcast(shape)


ATT = [("slc", 0, 0, 384), ("win", 0, 1, 640), ("swa", 1, 2, 896)]
ITEMS = [(a, t, g) for a in range(3) for t in range(TT) for g in range(2)]


def plan_mods(jobs, steps):
    for i in steps:
        jobs.plan(("mod", i))
        if i - 1 in steps:
            jobs.plan(("modT", i - 1))


EARLY_MODS, LATE_MODS = range(0, 3), range(3, MOD_STEPS)


def plan_layer(jobs):
    plan_mods(jobs, EARLY_MODS)
    for c in range(2):
        for t in range(TT):
            jobs.plan(("ht", c, t))
    jobs.plan(("modT", EARLY_MODS[-1]))
    for w in ("kv", "kv2", "q", "dq"):
        for t in range(TT):
            jobs.plan((w, t))
    jobs.plan("ga")
    for t in range(TT):
        jobs.plan(("cd", t))
    for i in range(2):
        jobs.plan(("c", i))
    for t in range(TT):
        jobs.plan(("qT", t))
        jobs.plan(("rkT", t))
    for i in range(2):
        jobs.plan(("ba", i))
    for kv in range(2):
        jobs.plan(("hid", kv))
    for i in range(2):
        jobs.plan(("bg", i))
    jobs.plan("kc", drains=2)
    jobs.plan("vc")
    for t in range(TT):
        jobs.plan(("rqT", t))
        jobs.plan(("rdT", t))
    for i in range(2):
        jobs.plan(("pool", i), drains=2)
    for t in range(TT):
        jobs.plan(("cs", t))
    for t in range(TT):
        jobs.plan(("cpT", t), "t")
        jobs.plan(("co", t), "u")
    for a, t, g in ITEMS:
        jobs.plan(("S", a, t, g), "s")
        for kb in range(t + 1):
            jobs.plan(("PT", a, t, g, kb), "t")
        if g == 1:
            jobs.plan(("O", a, t), "u")
    for i in range(16):
        jobs.plan(("gate", i))
    for t in range(TT):
        jobs.plan(("convT", t))
    for t in range(TT):
        jobs.plan(("oaT", t))
        jobs.plan(("odT", t))
    for n in BRANCH_ORDER:
        for i in range(4):
            if (n, i) == (3, 2):
                for t in range(TT):
                    jobs.plan(("obT", t), drains=4)
            jobs.plan(("up", n, i))
    for c in range(2):
        for t in range(TT):
            jobs.plan(("wo", c, t), drains=2)
    plan_mods(jobs, LATE_MODS)
    for c in range(2):
        for t in range(TT):
            jobs.plan(("hf", c, t))
    jobs.plan(("modT", LATE_MODS[-1]))
    for j in range(FB):
        jobs.plan(("ffn", j))
    for t in range(TT):
        for c in range(2):
            jobs.plan(("down", c, t), f"a{2 * t + c}", drains=2)


BRANCH_ORDER = (2, 0, 3, 1)


def layer_block(nc, l, mem, ring, landed, used, wts, psum, sems, cols_dram, rows_dram, loaded):
    filled = {r: sems(f"filled_{r}") for r in REGION}
    drained = {r: sems(f"drained_{r}") for r in REGION}
    jobs = Jobs(psum, filled, drained)
    plan_layer(jobs)

    squares = sems("squares")
    rstd_ready = sems("rstd_ready")
    normed = sems("normed")
    kd_ready = sems("kd_ready")
    roped = sems("roped")
    flat_ready = sems("flat_ready")
    sig_ready = sems("sig_ready")
    conv_done = sems("conv_done")
    stat_ready = sems("stat_ready")
    lnstd_ready = sems("lnstd_ready")
    pooled = sems("pooled")
    cmp_s = sems("cmp_s")
    cmp_e = sems("cmp_e")
    cmp_coef = sems("cmp_coef")
    masked = sems("masked")
    exped = sems("exped")
    tail_sent = sems("tail_sent")
    gates_ready = sems("gates_ready")
    o_ready = sems("o_ready")
    prod = sems("prod")
    mixed = sems("mixed")
    hid_ready = sems("hid_ready")
    hi_ready = sems("hi_ready")
    lo_ready = sems("lo_ready")
    scaled, h_hi, h_lo = sems("scaled"), sems("h_hi"), sems("h_lo")
    f_part = sems("f_part")
    ffn_init = sems("ffn_init")
    gelued = sems("gelued")
    f_ready = sems("f_ready")
    x_ready = sems("x_ready")
    params = sems("params")
    v_order, a_order, g_order = sems("v_order"), sems("a_order"), sems("g_order")

    x, tm, hT, proj, gates, qTs, rkT = (mem[k] for k in ("x", "tm", "hT", "proj", "gates", "qTs", "rkT"))
    kd = gates[:, 0:1024].rearrange("p (t m r d) -> p t m r d", t=2, m=4, r=2)
    flat = gates[:, 0:960].rearrange("p (m l n) -> p m l n", m=4, n=CMP_N)
    cdT = gates[:, 2048:3072].rearrange("p (m t) -> p m t", m=4)
    rtmp = gates[:, 3072:4480]
    rot = gates[:, 4480:7296].rearrange("p (t c) -> p t c", t=2)
    hfT, fT, split, f32 = (mem[k] for k in ("hfT", "fT", "split", "f32"))
    hf32 = mem["hq"][:, :, 0:512]
    oa, od = tm[:, 0, :].rearrange("p (t c) -> p t c", t=2), tm[:, 1, :].rearrange("p (t c) -> p t c", t=2)
    hq = [mem["hq"][:, 0, :], mem["hq"][:, 1, :]]
    ln_tm = proj[:, :, 1024:1536]
    sg = mem["sg"]
    hidk, hidv, kblk, vblk = mem["hidk"], mem["hidv"], mem["kblk"], mem["vblk"]
    sc, pt = mem["sc"], mem["pt"]
    small = mem["small"]
    brT, mixT, bglu, cpad, acc, tmp = (mem[k] for k in ("brT", "hT", "bglu", "cpad", "acc", "tmp"))
    cols, rows, const = mem["cols"], mem["rows"], mem["const"]

    def K(name, a=0, b=None):
        at, width = CONST[name]
        return const[:, at + a:at + (width if b is None else b)]

    def C(name, a=0, b=None):
        at, width = COLS[name]
        return cols[:, at + a:at + (width if b is None else b)]

    def R(name):
        at, width = ROWS[name]
        return rows[:, at:at + width]

    ident = K("ident")
    ga = small[:, 0:48].rearrange("p (t b h) -> p t b h", t=2, b=3)
    ss, rstd = small[:, 48:52], small[:, 52:56]
    ss4 = small[:, 56:60].rearrange("p (t c) -> p t c", t=2)
    nmax = small[:, 64:72]
    den, coef = small[:, 72:88].rearrange("p (b h) -> p b h", b=2), small[:, 88:104].rearrange("p (b h) -> p b h", b=2)
    stats, mv, lnstd = small[:, 104:116].rearrange("p (t s) -> p t s", t=2), small[:, 116:120].rearrange("p (t s) -> p t s", t=2), small[:, 120:122]
    cden = small[:, 128:144].rearrange("p (t h) -> p t h", t=2)
    cmax = small[:, 144:160].rearrange("p (t h) -> p t h", t=2)
    ccoef = small[:, 160:176].rearrange("p (t h) -> p t h", t=2)
    sinkv = small[:, 176:192].rearrange("p (b g j) -> p b g j", b=2, g=2)
    msq = small[:, 184:188]
    csc = mem["csc"]

    first_split = N_LAYER_CHUNKS - 1 - FFN_CHUNKS

    def split_hi(act, n):
        c = first_split + n
        if n >= SPLITS:
            act.wait_ge(used[(c - SPLITS) % SLOTS], l * (N_LAYER_CHUNKS // SLOTS) + ((c - SPLITS) // SLOTS + 1))
        act.wait_ge(landed[c % SLOTS], (l * (N_LAYER_CHUNKS // SLOTS) + (c // SLOTS + 1)) * 16)
        act.activation(split[:, n % SPLITS, 0, :], ring[:, c % SLOTS, :], ACT.Copy).then_inc(hi_ready, 1)

    def split_lo(dve, n):
        c = first_split + n
        dve.wait_ge(hi_ready, n + 1)
        dve.tensor_tensor(split[:, n % SPLITS, 1, :], ring[:, c % SLOTS, :], split[:, n % SPLITS, 0, :].bitcast(F32), ALU.subtract)\
           .then_inc(lo_ready, 1)

    with nc.Block() as block:
        @block.sync
        def _(sp):
            with sp.Fori(0, N_LAYER_CHUNKS // SLOTS) as turn:
                for s in range(SLOTS):
                    sp.wait_ge(used[s], l * (N_LAYER_CHUNKS // SLOTS) + turn + 1)
                    sp.dma_start(ring[:, s, :], wts[l * N_LAYER_CHUNKS + turn * SLOTS + (s + SLOTS)]).then_inc(landed[s], 16)

        @block.tensor
        def _(pe):
            state = {"chunk": 0, "owed": None}

            def next_chunk():
                c = state["chunk"]
                state["chunk"] += 1
                pe.wait_ge(landed[c % SLOTS], (l * (N_LAYER_CHUNKS // SLOTS) + (c // SLOTS + 1)) * 16)
                return ring[:, c % SLOTS, :]

            def done_with(ins):
                ins.then_inc(used[(state["chunk"] - 1) % SLOTS], 1)

            def carry(ins):
                if state["owed"] is not None:
                    ins.then_inc(used[state["owed"]], 1)
                    state["owed"] = None

            def release(name):
                assert state["owed"] is None
                state["owed"] = (state["chunk"] - 1) % SLOTS

            def transpose4(name, blocks):
                jobs.claim(pe, name)
                out = jobs.out(name)
                for i, b in enumerate(blocks):
                    n = b.shape[1]
                    mm = pe.transpose(out[0:n, i * P:(i + 1) * P], b, ident)
                    if i == 0 and len(blocks) > 1:
                        carry(mm)
                jobs.fill(mm, name)

            def mod(i):
                name = ("mod", i)
                jobs.claim(pe, name)
                for half in range(2):
                    chunk = next_chunk().rearrange("p (k n) -> p k n", k=4)
                    for k in range(4):
                        mm = pe.matmul(jobs.out(name)[0:2, :], mem["cvec"][:, 2 * (4 * half + k):2 * (4 * half + k) + 2], chunk[:, k, :],
                                       start=(half == 0 and k == 0), stop=(half == 1 and k == 3))
                        if k == 0:
                            carry(mm)
                    if half == 0:
                        done_with(mm)
                jobs.fill(mm, name)
                release(name)

            def mod_turn(i):
                jobs.wait_drained(pe, ("mod", i))
                jobs.claim(pe, ("modT", i))
                for b in range(4):
                    mm = pe.matmul(jobs.out(("modT", i))[:, 2 * b:2 * b + 2], mem["mrow"][0:2, i % 2, b * P:(b + 1) * P], ident[0:2, 0:2],
                                   start=True, stop=True)
                    if b == 0:
                        carry(mm)
                jobs.fill(mm, ("modT", i))

            def mods(steps):
                for i in steps:
                    mod(i)
                    if i - 1 in steps:
                        mod_turn(i - 1)

            pe.wait_ge(loaded, 48)
            pe.wait_ge(params, 32)
            mods(EARLY_MODS)
            for c in range(2):
                for t in range(TT):
                    pe.wait_ge(normed, t + 1)
                    transpose4(("ht", c, t), [tm[:, t, (4 * c + i) * P:(4 * c + i + 1) * P] for i in range(4)])
            mod_turn(EARLY_MODS[-1])

            for w in ("kv", "kv2", "q", "dq"):
                for half in range(2):
                    chunk = next_chunk().rearrange("p (k n) -> p k n", k=4)
                    for t in range(TT):
                        if w == "kv":
                            jobs.wait_drained(pe, ("ht", half, t))
                        if half == 0:
                            jobs.claim(pe, (w, t))
                        for k in range(4):
                            mm = pe.matmul(jobs.out((w, t)), hT[:, 4 * half + k, t * P:(t + 1) * P], chunk[:, k, :],
                                           start=(half == 0 and k == 0), stop=(half == 1 and k == 3))
                            if k == 0:
                                carry(mm)
                        if half == 1 and t == 0:
                            jobs.fill(mm, (w, t))
                    if half == 0:
                        done_with(mm)
                    else:
                        jobs.fill(mm, (w, 1))
                        release(w)

            jobs.claim(pe, "ga")
            for t in range(TT):
                for k in range(KD):
                    mm = pe.matmul(jobs.out("ga")[:, 24 * t:24 * t + 24], hT[:, k, t * P:(t + 1) * P],
                                   C("w_ga", 24 * k, 24 * k + 24), start=(k == 0), stop=(k == KD - 1))
                    if k == 0:
                        carry(mm)
            jobs.fill(mm, "ga")

            def blocks_fm(name):
                chunk = next_chunk().rearrange("p (k m) -> p k m", k=KD)
                jobs.claim(pe, name)
                for b in range(2):
                    for k in range(KD):
                        mm = pe.matmul(jobs.out(name)[:, b * T:(b + 1) * T], chunk[:, k, b * P:(b + 1) * P], hT[:, k, :],
                                       start=(k == 0), stop=(k == KD - 1))
                        if k == 0:
                            carry(mm)
                jobs.fill(mm, name)
                return name


            for t in range(TT):
                pe.wait_ge(kd_ready, t + 1)
                transpose4(("cd", t), [kd[:, t, m, :, :].rearrange("p r d -> p (r d)") for m in range(4)])
            for i in range(2):
                release(blocks_fm(("c", i)))
            for t in range(TT):
                jobs.wait_drained(pe, ("q", t))
                transpose4(("qT", t), [proj[:, t, 1024 + i * P:1024 + (i + 1) * P] for i in range(4)])
                pe.wait_ge(roped, 3 * t + 1)
                transpose4(("rkT", t), [rot[:, t, i * P:(i + 1) * P] for i in range(3)])
            for i in range(2):
                release(blocks_fm(("ba", i)))

            for kv in range(2):
                for half in range(2):
                    chunk = next_chunk().rearrange("p (l h) -> p l h", l=8)
                    if half == 0:
                        jobs.claim(pe, ("hid", kv))
                        pe.wait_ge(flat_ready, 4 * kv + 4)
                    for ht in range(2):
                        out = jobs.out(("hid", kv))[:, (2 * half + ht) * 32:(2 * half + ht) * 32 + 30]
                        for lp in range(8):
                            mm = pe.matmul(out.rearrange("p (g n) -> p g n", g=2), chunk[:, lp, ht * P:(ht + 1) * P],
                                           flat[:, 2 * kv:2 * kv + 2, 8 * half + lp, :], start=(lp == 0), stop=(lp == 7))
                            if lp == 0:
                                carry(mm)
                    if half == 0:
                        done_with(mm)
                jobs.fill(mm, ("hid", kv))
                release(("hid", kv))
            for i in range(2):
                release(blocks_fm(("bg", i)))

            pe.wait_ge(hid_ready, 2)
            jobs.claim(pe, "kc")
            for g in range(2):
                for ht in range(2):
                    mm = pe.matmul(jobs.out("kc")[64 * g:64 * g + 64, 0:CMP_N], C("w2", 64 * ht, 64 * ht + 64),
                                   hidk[:, ht, g, 0:CMP_N], start=(ht == 0), stop=(ht == 1))
            jobs.fill(mm, "kc")
            pe.wait_ge(hid_ready, 4)
            jobs.claim(pe, "vc")
            for ht in range(2):
                mm = pe.matmul(jobs.out("vc")[:, 0:DH], hidv[:, ht, :], C("w2", 128 + 64 * ht, 128 + 64 * ht + 64),
                               start=(ht == 0), stop=(ht == 1))
            jobs.fill(mm, "vc")
            for t in range(TT):
                pe.wait_ge(roped, 3 * t + 2)
                transpose4(("rqT", t), [rot[:, t, 384 + i * P:384 + (i + 1) * P] for i in range(4)])
                pe.wait_ge(roped, 3 * t + 3)
                transpose4(("rdT", t), [rot[:, t, 896 + i * P:896 + (i + 1) * P] for i in range(4)])
            for i in range(2):
                jobs.claim(pe, ("pool", i))
                pe.wait_ge(pooled, 2 * i + 2)
                for b in range(2):
                    mm = pe.matmul(jobs.out(("pool", i))[:, b * T:(b + 1) * T], C("pool_w", (2 * i + b) * P, (2 * i + b + 1) * P),
                                   brT[:, 1, 2 * i + b, :], start=True, stop=True)
                jobs.fill(mm, ("pool", i))

            jobs.wait_drained(pe, "kc")
            for t in range(TT):
                jobs.wait_drained(pe, ("qT", t))
                jobs.claim(pe, ("cs", t))
                for j in range(4):
                    mm = pe.matmul(jobs.out(("cs", t))[:, 32 * j:32 * j + 32], qTs[:, 0, j, t * P:(t + 1) * P],
                                   kblk[:, :], start=True, stop=True)
                jobs.fill(mm, ("cs", t))

            gate_at = {"n": 0}

            def gate_chunks(n):
                for _ in range(n):
                    if gate_at["n"] < 16:
                        release(blocks_fm(("gate", gate_at["n"])))
                        gate_at["n"] += 1

            def cmp_out():
                for t in range(TT):
                    pe.wait_ge(cmp_e, t + 1)
                    transpose4(("cpT", t), [csc[:, t, :]])
                gate_chunks(1)
                jobs.wait_drained(pe, "vc")
                for t in range(TT):
                    jobs.wait_drained(pe, ("cpT", t))
                    jobs.claim(pe, ("co", t))
                    mm = pe.matmul(jobs.out(("co", t)), mem["cpT"][:, t, :], vblk[:, :], start=True, stop=True)
                    jobs.fill(mm, ("co", t))

            def scores(i):
                a, t, g = ITEMS[i]
                _, rq, rk, _ = ATT[a]
                name = ("S", a, t, g)
                if g == 0:
                    jobs.wait_drained(pe, ("rkT", t))
                    jobs.wait_drained(pe, (("rqT", "rdT")[rq], t))
                jobs.claim(pe, name)
                for j in range(4):
                    nk = (t + 1) * P
                    mm = pe.matmul(jobs.out(name)[:, j * T:j * T + nk], qTs[64 * g:64 * g + 64, 1 + rq, j, t * P:(t + 1) * P],
                                   rkT[64 * g:64 * g + 64, rk, 0:nk], start=True, stop=True)
                jobs.fill(mm, name)

            def turn_probs(i):
                a, t, g = ITEMS[i]
                pe.wait_ge(exped, 4 * i + 4)
                for kb in range(t + 1):
                    transpose4(("PT", a, t, g, kb), [sc[:, i % 2, j, kb * P:(kb + 1) * P] for j in range(4)])

            def values(i):
                a, t, g = ITEMS[i]
                v = ATT[a][3]
                if g == 0:
                    jobs.claim(pe, ("O", a, t))
                for kb in range(t + 1):
                    jobs.wait_drained(pe, ("PT", a, t, g, kb))
                for j in range(4):
                    for kb in range(t + 1):
                        mm = pe.matmul(jobs.out(("O", a, t))[:, (2 * j + g) * DH:(2 * j + g + 1) * DH], pt[:, i % 2, kb, j, :],
                                       proj[:, kb, v + DH * g:v + DH * g + DH], start=(kb == 0), stop=(kb == t))
                if g == 1:
                    jobs.fill(mm, ("O", a, t))

            for i in range(len(ITEMS) + 1):
                if i < len(ITEMS):
                    scores(i)
                gate_chunks(1)
                if i == 1:
                    cmp_out()
                if i >= 1:
                    turn_probs(i - 1)
                    gate_chunks(i % 3 == 0)
                    values(i - 1)
            gate_chunks(16)

            for t in range(TT):
                pe.wait_ge(conv_done, 4 * TAPS)
                transpose4(("convT", t), [acc[:, b, t * P:(t + 1) * P] for b in range(4)])
            for t in range(TT):
                pe.wait_ge(o_ready, t + 1)
                jobs.wait_drained(pe, ("O", 2, t))
                transpose4(("oaT", t), [oa[:, t, b * P:(b + 1) * P] for b in range(4)])
                transpose4(("odT", t), [od[:, t, b * P:(b + 1) * P] for b in range(4)])

            for n in BRANCH_ORDER:
                for half in range(2):
                    if n == 3 and half == 1:
                        for t in range(TT):
                            jobs.wait_drained(pe, ("convT", t))
                            transpose4(("obT", t), [ln_tm[:, t, b * P:(b + 1) * P] for b in range(4)])
                    chunk = next_chunk().rearrange("p (k n) -> p k n", k=4)
                    if half == 0:
                        for name in {0: [("oaT", 0), ("oaT", 1)], 3: [("odT", 0), ("odT", 1)], 2: [("pool", 0), ("pool", 1)],
                                     1: [("obT", 0), ("obT", 1)]}[n]:
                            jobs.wait_drained(pe, name)
                    for i in range(2):
                        name = ("up", n, 2 * half + i)
                        jobs.claim(pe, name)
                        for b in range(2):
                            for k in range(4):
                                mm = pe.matmul(jobs.out(name)[:, b * T:(b + 1) * T], chunk[:, k, (2 * i + b) * P:(2 * i + b + 1) * P],
                                               brT[:, n, k, :], start=(k == 0), stop=(k == 3))
                                if k == 0:
                                    carry(mm)
                        jobs.fill(mm, name)
                    release(name)

            def to_tokens(kind, c, half, t, chunk, src):
                name = (kind, c, t)
                if half == 0:
                    jobs.claim(pe, name)
                for k in range(4):
                    mm = pe.matmul(jobs.out(name), src[:, 4 * half + k, t * P:(t + 1) * P], chunk[:, k, :],
                                   start=(half == 0 and k == 0), stop=(half == 1 and k == 3))
                    if k == 0:
                        carry(mm)
                if half == 1:
                    jobs.fill(mm, name)
                return mm

            pe.wait_ge(mixed, 12)
            for c in range(2):
                for half in range(2):
                    chunk = next_chunk().rearrange("p (k n) -> p k n", k=4)
                    for t in range(TT):
                        mm = to_tokens("wo", c, half, t, chunk, mixT)
                    if half == 0:
                        done_with(mm)
                    else:
                        release(("wo", c, 1))

            mods(LATE_MODS)
            for c in range(2):
                for t in range(TT):
                    pe.wait_ge(normed, TT + t + 1)
                    transpose4(("hf", c, t), [tm[:, t, (4 * c + i) * P:(4 * c + i + 1) * P] for i in range(4)])
            mod_turn(LATE_MODS[-1])
            def next_split(n):
                assert state["chunk"] == first_split + n
                state["chunk"] += 1
                pe.wait_ge(lo_ready, n + 1)
                return split[:, n % SPLITS, 0, :], split[:, n % SPLITS, 1, :]

            pe.wait_ge(h_lo, 2 * TT)
            for j in range(FB):
                hi, lo = (part.rearrange("p (k m) -> p k m", k=KD) for part in next_split(j))
                jobs.claim(pe, ("ffn", j))
                for b in range(2):
                    out = jobs.out(("ffn", j))[:, b * T:(b + 1) * T]
                    for k in range(KD):
                        mm = pe.matmul(out, hi[:, k, b * P:(b + 1) * P], hfT[:, 0, k, :], start=(k == 0), stop=False)
                        if k == 0:
                            carry(mm)
                        pe.matmul(out, hi[:, k, b * P:(b + 1) * P], hfT[:, 1, k, :], start=False, stop=False)
                        mm = pe.matmul(out, lo[:, k, b * P:(b + 1) * P], hfT[:, 0, k, :], start=False, stop=(k == KD - 1))
                jobs.fill(mm, ("ffn", j))
                release(("ffn", j))
            for t in range(TT):
                for c in range(2):
                    jobs.claim(pe, ("down", c, t))
            for i in range(FB // 2):
                hi, lo = (part.rearrange("p (k n) -> p k n", k=2) for part in next_split(FB + i))
                for k in range(2):
                    n = 2 * i + k
                    pe.wait_ge(f_ready, n + 1)
                    for t in range(TT):
                        for c in range(2):
                            name, cs, ts = ("down", c, t), slice(c * 512, (c + 1) * 512), slice(t * P, (t + 1) * P)
                            mm = pe.matmul(jobs.out(name), fT[:, 0, n, ts], hi[:, k, cs], start=(n == 0), stop=False)
                            if k == 0:
                                carry(mm)
                            pe.matmul(jobs.out(name), fT[:, 0, n, ts], lo[:, k, cs], start=False, stop=False)
                            mm = pe.matmul(jobs.out(name), fT[:, 1, n, ts], hi[:, k, cs], start=False, stop=(n == FB - 1))
                            if n == FB - 1:
                                jobs.fill(mm, name)
                if i < FB // 2 - 1:
                    done_with(mm)
            jobs.wait_filled(pe, ("down", 1, 1))
            pe.sem_inc(used[(state["chunk"] - 1) % SLOTS], 1)
            next_chunk()
            pe.sem_inc(used[(state["chunk"] - 1) % SLOTS], 1)
            assert state["chunk"] == N_LAYER_CHUNKS, state

        @block.scalar
        def _(act):
            order = Signal(a_order)

            def square(src, out, total, sig):
                act.activation(out, src, ACT.Square, accum_out=total).then_inc(sig, 1)

            act.dma_start(cols[:, :], cols_dram[l]).then_inc(params, 16)
            act.dma_start(rows[:, :], rows_dram[l].to_broadcast([P, N_ROWS])).then_inc(params, 16)
            act.wait_ge(loaded, 48)
            for t in range(TT):
                square(x[:, t, :], tm[:, t, :], ss[:, t:t + 1], squares)

            def copy_out(name, dst, src=None, scale=1.0, func=ACT.Copy):
                jobs.wait_filled(act, name)
                jobs.drain(act.activation(dst, jobs.out(name) if src is None else src, func, scale=scale), name)

            def mods_out(steps):
                for i in steps:
                    if i >= 2:
                        jobs.wait_filled(act, ("modT", i - 2))
                    copy_out(("mod", i), mem["mrow"][0:2, i % 2, :], jobs.out(("mod", i))[0:2, :])

            mods_out(EARLY_MODS)
            for w, at in (("kv", 0), ("kv2", 512), ("q", 1024), ("dq", 1536)):
                for t in range(TT):
                    copy_out((w, t), proj[:, t, at:at + 512])
            copy_out("ga", small[:, 0:48], jobs.out("ga")[:, 0:48], func=ACT.Sigmoid)
            for t in range(TT):
                copy_out(("cd", t), cdT[:, :, t * P:(t + 1) * P], jobs.out(("cd", t)).rearrange("p (m t) -> p m t", m=4))
            for i in range(2):
                copy_out(("c", i), cpad[:, 2 * i:2 * i + 2, 16:16 + T], jobs.out(("c", i)).rearrange("p (b t) -> p b t", b=2))
            for t in range(TT):
                copy_out(("qT", t), qTs[:, 0, :, t * P:(t + 1) * P], jobs.out(("qT", t)).rearrange("p (m t) -> p m t", m=4), 0.125)
            for i in range(2):
                copy_out(("ba", i), bglu[:, 2 * i:2 * i + 2, TAPS - 1:TAPS - 1 + T], jobs.out(("ba", i)).rearrange("p (b t) -> p b t", b=2))
            for ht in range(2):
                jobs.wait_drained(act, ("hid", 0))
                act.activation(hidk[:, ht, :, 0:CMP_N], mem["hsum"][:, 0, ht, 0:30].rearrange("p (g n) -> p g n", g=2),
                               ACT.Gelu_apprx_tanh).then_inc(hid_ready, 1)
            for ht in range(2):
                jobs.wait_drained(act, ("hid", 1))
                act.activation(hidv[:, ht, :].rearrange("p (j g n) -> p j g n", j=4, g=2)[:, :, :, 0:CMP_N],
                               bc(mem["hsum"][:, 1, ht, 0:30].rearrange("p (g n) -> p g n", g=2).unsqueeze(1), [P, 4, 2, CMP_N]),
                               ACT.Gelu_apprx_tanh).then_inc(hid_ready, 1)
            for i in range(2):
                copy_out(("bg", i), sg[:, i, :], func=ACT.Sigmoid)
            for t in range(TT):
                copy_out(("rqT", t), qTs[:, 1, :, t * P:(t + 1) * P], jobs.out(("rqT", t)).rearrange("p (m t) -> p m t", m=4), 0.125)
                copy_out(("rdT", t), qTs[:, 2, :, t * P:(t + 1) * P], jobs.out(("rdT", t)).rearrange("p (m t) -> p m t", m=4), 0.125)
            for i in range(2):
                jobs.wait_filled(act, ("pool", i))
                for b in range(2):
                    n = 2 * i + b
                    jobs.drain(act.activation(brT[:, 2, n, :], jobs.out(("pool", i))[:, b * T:(b + 1) * T], ACT.Copy,
                                              scale=C("pool_s", n, n + 1)), ("pool", i))

            gate_at = {"n": 0}

            def gate_out(n):
                for _ in range(n):
                    i = gate_at["n"]
                    if i < 16:
                        copy_out(("gate", i), gates[:, i * 512:(i + 1) * 512])
                        gate_at["n"] += 1

            def exps(i):
                a, t, g = ITEMS[i]
                act.wait_ge(masked, i + 1)
                if a == 2:
                    act.activation(sinkv[:, i // 2 % 2, g, :], sinkv[:, i // 2 % 2, g, :], ACT.Exp).then_inc(tail_sent, 1)
                for j in range(4):
                    b = den[:, (i // 2) % 2, 2 * j + g:2 * j + g + 1]
                    act.activation(sc[:, i % 2, j, 0:(t + 1) * P], sc[:, i % 2, j, 0:(t + 1) * P], ACT.Exp,
                                   bias=nmax[:, 4 * (i % 2) + j:4 * (i % 2) + j + 1], accum_out=b).then_inc(exped, 1)

            for t in range(TT):
                act.wait_ge(cmp_s, t + 1)
                act.activation(csc[:, t, :], csc[:, t, :], ACT.Exp).then_inc(cmp_e, 1)
            for i in range(len(ITEMS) + 1):
                if i == 1:
                    gate_out(1)
                    for t in range(TT):
                        copy_out(("cpT", t), mem["cpT"][:, t, :], jobs.out(("cpT", t))[:, 0:P])
                    gate_out(1)
                else:
                    gate_out(1)
                if i >= 1:
                    a, t, g = ITEMS[i - 1]
                    for kb in range(t + 1):
                        copy_out(("PT", a, t, g, kb), pt[:, (i - 1) % 2, kb, :, :], jobs.out(("PT", a, t, g, kb)).rearrange("p (j q) -> p j q", j=4))
                if i < len(ITEMS):
                    exps(i)
                if i >= 1:
                    gate_out(i % 3 == 0)
            gate_out(16)
            for n in BRANCH_ORDER:
                for i in range(4):
                    jobs.wait_drained(act, ("gate", 12 + i))
                act.activation(gates[:, n * 2048:(n + 1) * 2048], gates[:, n * 2048:(n + 1) * 2048], ACT.Sigmoid).then_inc(gates_ready, 1)
            for t in range(TT):
                copy_out(("oaT", t), brT[:, 0, :, t * P:(t + 1) * P], jobs.out(("oaT", t)).rearrange("p (m t) -> p m t", m=4))
                copy_out(("odT", t), brT[:, 3, :, t * P:(t + 1) * P], jobs.out(("odT", t)).rearrange("p (m t) -> p m t", m=4))
            for t in range(TT):
                jobs.wait_filled(act, ("obT", t))
                for b in range(4):
                    jobs.drain(act.activation(brT[:, 1, b, t * P:(t + 1) * P], jobs.out(("obT", t))[:, b * P:(b + 1) * P], ACT.Silu,
                                              scale=C("ln_g", b, b + 1), bias=C("ln_b", b, b + 1)), ("obT", t))

            def post(kind, c, t):
                name = (kind, c, t)
                jobs.wait_filled(act, name)
                jobs.drain(act.activation(tm[:, t, c * 512:(c + 1) * 512], jobs.out(name), ACT.Copy), name)
                region, _, before, _ = jobs.jobs[name]
                act.wait_ge(drained[region], before + 1)
                jobs.drain(act.activation(jobs.out(name), jobs.out(name), ACT.Square, accum_out=ss4[:, t, c:c + 1]), name)

            for c in range(2):
                for t in range(TT):
                    post("wo", c, t)
            mods_out(LATE_MODS)
            split_hi(act, 0)
            for t in range(TT):
                act.wait_ge(x_ready, t + 1)
                square(x[:, t, :], tm[:, t, :], ss[:, t:t + 1], squares)
            split_hi(act, 1)
            for n, (c, t) in enumerate((c, t) for c in range(2) for t in range(TT)):
                act.wait_ge(scaled, n + 1)
                act.activation(hfT[:, 0, 4 * c:4 * c + 4, t * P:(t + 1) * P], hf32[:, n % 2, :].rearrange("p (m t) -> p m t", m=4),
                               ACT.Copy).then_inc(h_hi, 1)
            split_hi(act, 2)

            for j in range(FB + 1):
                if j < FB:
                    jobs.wait_filled(act, ("ffn", j))
                    if j >= 4:
                        act.wait_ge(f_ready, j - 3)
                    u = hq[j % 2][:, (j // 2 % 2) * 512:(j // 2 % 2) * 512 + 512]
                    for b in range(2):
                        n = 2 * j + b
                        act.activation(u[:, b * T:(b + 1) * T], jobs.out(("ffn", j))[:, b * T:(b + 1) * T], ACT.Identity,
                                       scale=C("fw", 3 * n + 2, 3 * n + 3), bias=C("fb", n, n + 1)).then_inc(ffn_init, 1)
                if j >= 1:
                    u = hq[(j - 1) % 2][:, ((j - 1) // 2 % 2) * 512:((j - 1) // 2 % 2) * 512 + 512]
                    jobs.wait_drained(act, ("ffn", j - 1))
                    act.activation(u[:, 0:T], u[:, 0:T], ACT.Gelu_apprx_tanh).then_inc(gelued, 1)
                if j < FB:
                    split_hi(act, j + SPLITS)
            for n in range(FB + SPLITS, FFN_CHUNKS):
                split_hi(act, n)
            for t in range(TT):
                for c in range(2):
                    post("down", c, t)

        @block.vector
        def _(dve):
            order = Signal(v_order)
            conv = Signal(conv_done)

            def norm_tiles(first):
                for t in range(TT):
                    dve.wait_ge(rstd_ready, first)
                    dve.tensor_scalar(tm[:, t, :], x[:, t, :], rstd[:, t:t + 1], None, ALU.mult).then_inc(normed, 1)

            def scaled_turn(kind, g):
                for c in range(2):
                    for t in range(TT):
                        name = (kind, c, t)
                        jobs.wait_filled(dve, name)
                        jobs.drain(dve.tensor_tensor(
                            hT[:, 4 * c:4 * c + 4, t * P:(t + 1) * P], jobs.out(name).rearrange("p (m t) -> p m t", m=4),
                            bc(C(g, 4 * c, 4 * c + 4).unsqueeze(2), [P, 4, P]), ALU.mult), name)

            def mods_in(steps):
                for i in steps:
                    name = ("modT", i)
                    at = l * (4 * MOD_STEPS) + 4 * i
                    jobs.wait_filled(dve, name)
                    jobs.drain(dve.tensor_tensor(mem["modT"][:, bass.ds(at, 4), :], jobs.out(name)[:, 0:8].rearrange("p (b v) -> p b v", v=2),
                                                 bc(mem["cond"][:, bass.ds(at + 16, 4)].unsqueeze(2), [P, 4, 2]), ALU.add), name)

            dve.wait_ge(params, 32)
            norm_tiles(1)
            mods_in(EARLY_MODS[:-1])
            scaled_turn("ht", "g_mix")
            mods_in(EARLY_MODS[-1:])

            def rope(dst, src, groups, t, at):
                n, width = groups
                h = width // 64
                tab = [K("rope", 64 * i + 32 * t, 64 * i + 32 * t + 32) for i in range(3)]
                tw = rtmp[:, at:at + n * width].rearrange("p (n h r d) -> p n h r d", n=n, r=2, d=32)
                order.up(dve.tensor_tensor(dst.rearrange("p n (h d) -> p n h d", d=32), src.rearrange("p n (h d) -> p n h d", d=32),
                                           bc(tab[0].unsqueeze(1).unsqueeze(1), [P, n, 2 * h, 32]), ALU.mult))
                halves = src.rearrange("p n (h r d) -> p n h r d", r=2, d=32)
                for r in range(2):
                    order.up(dve.tensor_tensor(tw[:, :, :, r, :], halves[:, :, :, 1 - r, :],
                                               bc(tab[2 - r].unsqueeze(1).unsqueeze(1), [P, n, h, 32]), ALU.mult))
                order.here(dve)
                dve.tensor_tensor(dst, dst, rtmp[:, at:at + n * width].rearrange("p (n c) -> p n c", n=n), ALU.add).then_inc(roped, 1)

            for t in range(TT):
                jobs.wait_drained(dve, ("kv", t))
                dve.tensor_copy(kd[:, t, :, :, :], bc(proj[:, t, 0:256].rearrange("p (m d) -> p m d", m=4).unsqueeze(2), [P, 4, 2, DH]))\
                   .then_inc(kd_ready, 1)
            for t in range(TT):
                jobs.wait_drained(dve, ("kv2", t))
                rope(rot[:, t, 0:384].rearrange("p (n c) -> p n c", n=3),
                     proj[:, t, 256:1024].rearrange("p (n c) -> p n c", n=3)[:, :, 0:P], (3, P), t, 0)
                jobs.wait_drained(dve, ("q", t))
                rope(rot[:, t, 384:896].rearrange("p (n c) -> p n c", n=1), proj[:, t, 1024:1536].rearrange("p (n c) -> p n c", n=1),
                     (1, 512), t, 384)
                jobs.wait_drained(dve, ("dq", t))
                rope(rot[:, t, 896:1408].rearrange("p (n c) -> p n c", n=1), proj[:, t, 1536:2048].rearrange("p (n c) -> p n c", n=1),
                     (1, 512), t, 896)
                if t == 0:
                    dve.wait_ge(roped, 3)
            for t in range(TT):
                jobs.wait_filled(dve, ("rkT", t))
                jobs.drain(dve.tensor_copy(rkT[:, :, t * P:(t + 1) * P], jobs.out(("rkT", t))[:, 0:384].rearrange("p (m t) -> p m t", m=3)), ("rkT", t))

            jobs.wait_drained(dve, ("c", 1))
            for g in range(4):
                src = cpad[:, g, :]
                bufs = [mem["psum_a"], mem["psum_b"]]
                for s in range(g + 1):
                    sh = 1 << s
                    lo = 2 * sh - 1
                    dst = bufs[s % 2][:, :]
                    order.up(dve.tensor_tensor(dst[:, lo:16 + T], src[:, lo:16 + T], src[:, lo - sh:16 + T - sh], ALU.add))
                    order.here(dve)
                    src = dst
                w = 2 << g
                out = brT[:, 1, g, :]
                order.up(dve.scalar_tensor_tensor(out=out, in0=src[:, 16:16 + T], scalar=1.0 / w, in1=cpad[:, g, 16:16 + T],
                                                  op0=ALU.mult, op1=ALU.subtract))
                order.here(dve)
                order.up(dve.tensor_tensor(out[:, 0:16], src[:, 16:32], K("pool_inv", 16 * g, 16 * g + 16), ALU.mult))
                order.here(dve)
                dve.tensor_tensor(out[:, 0:16], out[:, 0:16], cpad[:, g, 16:32], ALU.subtract).then_inc(pooled, 1)

            for kv in range(2):
                jobs.wait_filled(dve, ("hid", kv))
                h = jobs.out(("hid", kv))[:, 0:128].rearrange("p (a h n) -> p a h n", a=2, h=2)
                order.up(dve.tensor_copy(mem["hsum"][:, kv, :, 0:30], h[:, 0, :, 0:30]))
                order.here(dve)
                jobs.drain(dve.tensor_tensor(mem["hsum"][:, kv, :, 0:30], mem["hsum"][:, kv, :, 0:30], h[:, 1, :, 0:30], ALU.add), ("hid", kv))
            for i in range(2):
                jobs.wait_drained(dve, ("bg", i))
                jobs.wait_drained(dve, ("ba", i))
                order.up(dve.tensor_tensor(bglu[:, 2 * i:2 * i + 2, TAPS - 1:TAPS - 1 + T], bglu[:, 2 * i:2 * i + 2, TAPS - 1:TAPS - 1 + T],
                                           sg[:, i, :].rearrange("p (b t) -> p b t", b=2), ALU.mult))
            order.here(dve)

            conv_at = {"n": 0}

            def conv_steps(n):
                for _ in range(n):
                    i = conv_at["n"]
                    if i >= 4 * TAPS:
                        return
                    k, b = divmod(i, 4)
                    w = C("conv_w", TAPS * b + k, TAPS * b + k + 1)
                    if k == 0:
                        conv.up(dve.tensor_scalar(acc[:, b, :], bglu[:, b, 0:T], w, C("conv_b", b, b + 1), ALU.mult, ALU.add))
                    else:
                        conv.here(dve, less=3)
                        conv.up(dve.scalar_tensor_tensor(out=acc[:, b, :], in0=bglu[:, b, k:k + T], scalar=w, in1=acc[:, b, :],
                                                         op0=ALU.mult, op1=ALU.add))
                    conv_at["n"] += 1

            jobs.wait_filled(dve, "kc")
            for g in range(2):
                jobs.drain(dve.tensor_copy(kblk[64 * g:64 * g + 64, 16 * g:16 * g + CMP_N], jobs.out("kc")[64 * g:64 * g + 64, 0:CMP_N]), "kc")
            jobs.wait_filled(dve, "vc")
            jobs.drain(dve.tensor_tensor(vblk[:, :].rearrange("p (h d) -> p h d", h=8), bc(jobs.out("vc")[:, 0:DH].unsqueeze(1), [P, 8, DH]),
                                         bc(K("blk8").unsqueeze(2), [P, 8, DH]), ALU.mult), "vc")
            conv_steps(12)
            for t in range(TT):
                jobs.wait_filled(dve, ("cs", t))
                s3 = csc[:, t, :].rearrange("p (h n) -> p h n", h=8)
                jobs.drain(dve.tensor_tensor(s3, jobs.out(("cs", t))[:, 0:P].rearrange("p (h n) -> p h n", h=8),
                                             bc(K("cmp_mask", 16 * t, 16 * t + 16).unsqueeze(1), [P, 8, 16]), ALU.add), ("cs", t))
                jobs.wait_drained(dve, ("cs", t))
                order.up(dve.tensor_reduce(cmax[:, t, :], s3, AX_X, ALU.max))
                order.here(dve)
                dve.tensor_tensor(s3, s3, bc(cmax[:, t, :].unsqueeze(2), [P, 8, 16]), ALU.subtract).then_inc(cmp_s, 1)

            def mask(i):
                a, t, g = ITEMS[i]
                name, nk = ("S", a, t, g), (t + 1) * P
                if i >= 2:
                    for kb in range(ITEMS[i - 2][1] + 1):
                        jobs.wait_filled(dve, ("PT", *ITEMS[i - 2], kb))
                jobs.wait_filled(dve, name)
                m = K("band" if a == 2 else "full_causal", 2 * P - nk, 2 * P)
                s3 = sc[:, i % 2, :, 0:nk]
                jobs.drain(dve.tensor_tensor(s3, jobs.out(name).rearrange("p (j k) -> p j k", j=4)[:, :, 0:nk],
                                             bc(m.unsqueeze(1), [P, 4, nk]), ALU.add), name)
                jobs.wait_drained(dve, name)
                nm = nmax[:, 4 * (i % 2):4 * (i % 2) + 4]
                if a < 2:
                    dve.tensor_reduce(nm, s3, AX_X, ALU.max, negate=True).then_inc(masked, 1)
                    return
                sink = R("sinks").rearrange("p (j g) -> p j g", g=2)[:, :, g]
                order.up(dve.tensor_reduce(nm, s3, AX_X, ALU.max))
                order.here(dve)
                order.up(dve.tensor_tensor(nm, nm, sink, ALU.max))
                order.here(dve)
                order.up(dve.tensor_tensor(sinkv[:, i // 2 % 2, g, :], sink, nm, ALU.subtract))
                order.here(dve)
                dve.tensor_scalar(nm, nm, -1.0, None, ALU.mult).then_inc(masked, 1)

            def out_scale(i):
                a, t, g = ITEMS[i]
                d, c = den[:, (i // 2) % 2, :], coef[:, (i // 2) % 2, :]
                dve.wait_ge(exped, 4 * i + 4)
                if a == 2:
                    dve.wait_ge(tail_sent, 2 * t + 2)
                    order.up(dve.tensor_tensor(d.rearrange("p (j g) -> p g j", g=2), d.rearrange("p (j g) -> p g j", g=2),
                                               sinkv[:, i // 2 % 2, :, :], ALU.add))
                    order.here(dve)
                order.up(dve.reciprocal(c, d))
                order.here(dve)
                if a < 2:
                    order.up(dve.tensor_tensor(c, c, ga[:, t, 1 + a, :], ALU.mult))
                    order.here(dve)
                name = ("O", a, t)
                jobs.wait_filled(dve, name)
                o3 = jobs.out(name).rearrange("p (h d) -> p h d", h=8)
                cb = bc(c.unsqueeze(2), [P, 8, DH])
                if a == 2:
                    jobs.drain(dve.tensor_tensor(od[:, t, :].rearrange("p (h d) -> p h d", h=8), o3, cb, ALU.mult), name)
                    return
                tb = tmp[:, t, :]
                jobs.drain(dve.tensor_tensor(tb.rearrange("p (h d) -> p h d", h=8), o3, cb, ALU.mult), name)
                jobs.wait_drained(dve, name)
                add = dve.tensor_tensor(oa[:, t, :], oa[:, t, :], tb, ALU.add)
                if a == 1:
                    add.then_inc(o_ready, 1)
                else:
                    order.up(add)
                    order.here(dve)

            def cmp_scale():
                for t in range(TT):
                    dve.wait_ge(cmp_e, t + 1)
                    order.up(dve.tensor_reduce(cden[:, t, :], csc[:, t, :].rearrange("p (h n) -> p h n", h=8), AX_X, ALU.add))
                    order.here(dve)
                    order.up(dve.reciprocal(ccoef[:, t, :], cden[:, t, :]))
                    order.here(dve)
                    order.up(dve.scalar_tensor_tensor(out=ccoef[:, t, :], in0=ccoef[:, t, :], scalar=K("cmp_valid", t, t + 1),
                                                      in1=ga[:, t, 0, :], op0=ALU.mult, op1=ALU.mult))
                    order.here(dve)
                    jobs.wait_filled(dve, ("co", t))
                    jobs.drain(dve.tensor_tensor(oa[:, t, :].rearrange("p (h d) -> p h d", h=8),
                                                 jobs.out(("co", t)).rearrange("p (h d) -> p h d", h=8),
                                                 bc(ccoef[:, t, :].unsqueeze(2), [P, 8, DH]), ALU.mult), ("co", t))
                    jobs.wait_drained(dve, ("co", t))

            for i in range(len(ITEMS) + 1):
                if i < len(ITEMS):
                    mask(i)
                conv_steps(10)
                if i == 1:
                    cmp_scale()
                if i >= 1 and ITEMS[i - 1][2] == 1:
                    out_scale(i - 1)
            conv_steps(4 * TAPS)

            for t in range(TT):
                jobs.wait_filled(dve, ("convT", t))
                order.up(dve.bn_stats(stats[:, t, :], jobs.out(("convT", t))))
                order.here(dve)
                dve.bn_aggr(mv[:, t, :], stats[:, t, :]).then_inc(stat_ready, 1)
            for t in range(TT):
                dve.wait_ge(lnstd_ready, t + 1)
                jobs.drain(dve.tensor_scalar(ln_tm[:, t, :], jobs.out(("convT", t)), mv[:, t, 0:1], lnstd[:, t:t + 1],
                                             ALU.subtract, ALU.mult), ("convT", t))

            k = 0
            for bi, n in enumerate(BRANCH_ORDER):
                dve.wait_ge(gates_ready, bi + 1)
                for i in range(4):
                    name = ("up", n, i)
                    jobs.wait_filled(dve, name)
                    g2 = gates[:, n * 2048 + i * 512:n * 2048 + (i + 1) * 512]
                    if bi == 0:
                        dst = mixT[:, 2 * i:2 * i + 2, :].rearrange("p b t -> p (b t)")
                    else:
                        if k >= 2:
                            dve.wait_ge(mixed, k - 1)
                        dst = tmp[:, k % 2, :]
                        k += 1
                    jobs.drain(dve.tensor_tensor(dst, jobs.out(name), g2, ALU.mult), name)

            def residual(kind, g, first):
                for t in range(TT):
                    dve.wait_ge(rstd_ready, first)
                    for c in range(2):
                        jobs.wait_drained(dve, (kind, c, t))
                    order.up(dve.scalar_tensor_tensor(out=tm[:, t, :], in0=tm[:, t, :], scalar=rstd[:, 2 + t:3 + t], in1=R(g),
                                                      op0=ALU.mult, op1=ALU.mult))
                    order.here(dve)
                    dve.tensor_tensor(x[:, t, :], x[:, t, :], tm[:, t, :], ALU.add).then_inc(x_ready, 1)

            residual("wo", "mix_post", 2)
            mods_in(LATE_MODS[:-1])
            split_lo(dve, 0)
            dve.wait_ge(squares, 2 * TT)
            norm_tiles(3)
            split_lo(dve, 1)

            def low_part(n):
                c, t = divmod(n, TT)
                dve.wait_ge(h_hi, n + 1)
                part = hfT[:, :, 4 * c:4 * c + 4, t * P:(t + 1) * P]
                dve.tensor_tensor(part[:, 1, :, :], hf32[:, n % 2, :].rearrange("p (m t) -> p m t", m=4), part[:, 0, :, :].bitcast(F32),
                                  ALU.subtract).then_inc(h_lo, 1)

            for n in range(2 * TT + 1):
                if n < 2 * TT:
                    c, t = divmod(n, TT)
                    name = ("hf", c, t)
                    if n >= 2:
                        dve.wait_ge(h_lo, n - 1)
                    jobs.wait_filled(dve, name)
                    jobs.drain(dve.tensor_tensor(hf32[:, n % 2, :].rearrange("p (m t) -> p m t", m=4), jobs.out(name).rearrange("p (m t) -> p m t", m=4),
                                                 bc(C("g_ffn", 4 * c, 4 * c + 4).unsqueeze(2), [P, 4, P]), ALU.mult), name)
                    jobs.wait_drained(dve, name)
                    dve.sem_inc(scaled, 1)
                if n >= 1:
                    low_part(n - 1)
            split_lo(dve, 2)
            mods_in(LATE_MODS[-1:])

            for j in range(FB):
                u = hq[j % 2][:, (j // 2 % 2) * 512:(j // 2 % 2) * 512 + 512]
                out = jobs.out(("ffn", j))
                for step in (1, 2):
                    for b in range(2):
                        n = 2 * j + b
                        w = C("fw", 3 * n + 2 - step, 3 * n + 3 - step)
                        if step == 1:
                            dve.wait_ge(ffn_init, 2 * j + 2)
                        else:
                            order.here(dve, less=1)
                        ins = dve.scalar_tensor_tensor(out=u[:, b * T + step:(b + 1) * T], in0=out[:, b * T:(b + 1) * T - step], scalar=w,
                                                       in1=u[:, b * T + step:(b + 1) * T], op0=ALU.mult, op1=ALU.add)
                        if step == 2 and b == 1:
                            jobs.drain(ins, ("ffn", j))
                        else:
                            order.up(ins)
                split_lo(dve, j + SPLITS)
            for n in range(FB + SPLITS, FFN_CHUNKS):
                split_lo(dve, n)
            residual("down", "ffn_post", 4)

        @block.gpsimd
        def _(pool):
            order = Signal(g_order)

            def chain(ins):
                order.up(ins)
                order.here(pool)

            def inv_root(dst, total, n):
                chain(pool.tensor_scalar(msq[:, 0:2], total, 1.0 / n, EPS, ALU.mult, ALU.add))
                pool.tensor_tensor(dst, msq[:, 0:2], K("mhalf", 0, 2), ALU.pow).then_inc(rstd_ready, 1)

            pool.wait_ge(squares, TT)
            inv_root(rstd[:, 0:2], ss[:, 0:2], D)

            for t in range(TT):
                jobs.wait_drained(pool, ("cd", t))
            for m in range(4):
                kv = m // 2
                for par in range(2):
                    src = cdT[64 * par:64 * par + 64, m, :].rearrange("p (n r) -> p n r", r=16)
                    for half in range(2):
                        s = src[:, half:half + CMP_N, :].rearrange("p n (l r) -> p l n r", r=2)[:, :, :, par]
                        ps = C("pos", 16 * kv + 8 * half, 16 * kv + 8 * half + 8)[64 * par:64 * par + 64, :]
                        ins = pool.tensor_tensor(flat[64 * par:64 * par + 64, m, 8 * half:8 * half + 8, :], s,
                                                 bc(ps.unsqueeze(2), [64, 8, CMP_N]), ALU.add)
                        if half == 1:
                            ins.then_inc(flat_ready, 1)
                        else:
                            order.up(ins)
                order.here(pool)

            for t in range(TT):
                pool.wait_ge(stat_ready, t + 1)
                chain(pool.tensor_scalar(msq[:, 2:3], mv[:, t, 1:2], 1.0, EPS, ALU.mult, ALU.add))
                pool.tensor_tensor(lnstd[:, t:t + 1], msq[:, 2:3], K("mhalf", 0, 1), ALU.pow).then_inc(lnstd_ready, 1)
                pool.wait_ge(lnstd_ready, t + 1)

            k = 0
            for n in BRANCH_ORDER[1:]:
                for i in range(4):
                    jobs.wait_drained(pool, ("up", n, i))
                    if k >= 4:
                        pool.wait_ge(mixed, k - 3)
                    dst = mixT[:, 2 * i:2 * i + 2, :].rearrange("p b t -> p (b t)")
                    pool.tensor_tensor(dst, dst, tmp[:, k % 2, :], ALU.add).then_inc(mixed, 1)
                    k += 1

            def post(kind, turn):
                for c in range(2):
                    for t in range(TT):
                        jobs.wait_drained(pool, (kind, c, t))
                chain(pool.tensor_tensor(msq[:, 0:2], ss4[:, :, 0], ss4[:, :, 1], ALU.add))
                chain(pool.tensor_scalar(msq[:, 0:2], msq[:, 0:2], 1.0 / D, EPS, ALU.mult, ALU.add))
                pool.tensor_tensor(rstd[:, 2:4], msq[:, 0:2], K("mhalf", 0, 2), ALU.pow).then_inc(rstd_ready, 1)
                pool.wait_ge(rstd_ready, turn)

            post("wo", 2)
            pool.wait_ge(squares, 2 * TT)
            inv_root(rstd[:, 0:2], ss[:, 0:2], D)
            for j in range(FB):
                u = hq[j % 2][:, (j // 2 % 2) * 512:(j // 2 % 2) * 512 + 512]
                pool.wait_ge(gelued, j + 1)
                if j:
                    pool.wait_ge(f_ready, j)
                pool.tensor_tensor(f32[:, :], u[:, 0:T], u[:, T:2 * T], ALU.mult).then_inc(f_part, 1)
                pool.wait_ge(f_part, 2 * j + 1)
                pool.tensor_copy(fT[:, 0, j, :], f32[:, :]).then_inc(f_part, 1)
                pool.wait_ge(f_part, 2 * j + 2)
                pool.tensor_tensor(fT[:, 1, j, :], f32[:, :], fT[:, 0, j, :].bitcast(F32), ALU.subtract).then_inc(f_ready, 1)
            pool.wait_ge(rstd_ready, 3)
            post("down", 4)


HEADS = 16
DX = 12
SEQ_TILES = 4
ALPHA = 2.0 ** 0.25
LN_EPS = 1e-5
EXPERTS = 16
EXPERT_STEP = 4
N_BLOCK2_CHUNKS = 2 + 6 + 4 + 4 + 8

COLS2, N_COLS2 = offsets([("conv_w", 5 * DX), ("conv_b", DX), ("ssd_g", 8), ("w_dt", KD * 32), ("w_r", KD * 20)])
ROWS2, N_ROWS2 = offsets([("ln1_g", D), ("ln1_b", D), ("ln2_g", D), ("ln2_b", D), ("dtb", 32), ("alog", 32), ("qn", DH), ("kn", DH),
                          ("br", 20), ("skip", 16)])
MEM2 = dict(z=(TT, 1024), y=(2, 1024), cols2=(N_COLS2,), rows2=(N_ROWS2,), sm=(960,), sm2=(950,), aT=(2, P), combT=(T,))
MEM2_MIX = dict(
    hT=(KD, 512), bcf=(4, 512), xs=(4, 1024), kv=(4, 512), xdt=(4, 1024), wx=(2, 1024), q=(TT, 1024), bt=(4, 256),
    kT=(2, 512), qT=(8, T), p=(2, 512), pt=(2, 512), m=(4, 512), cb=(2, 2, 2, P),
)
MEM2_MOE_SPLIT = dict(split=(SPLITS, 2, CH), hfS=(2, KD, T), hidS=(2, 2, 512))
MEM2_MOE = dict(combB=(EXPERTS, T), pe=(2, 512), hid=(2, 512), hf=(KD, T))
STATES = [(0, 0), (1, 0), (2, 0), (1, 1), (0, 1), (3, 1)]
UNITS = [(t, g, quad) for t in range(TT) for g in range(2) for quad in range(2)]
HEAD_ITEMS = [(t, b, g) for t in range(TT) for b in range(8) for g in range(2)]


def plan_block2(jobs):
    for s in range(2):
        for c in range(2):
            for t in range(TT):
                jobs.plan(("in", s, c, t))
    jobs.plan("dt")
    for i, r in zip(range(4), ("s0", "s1", "t", "u")):
        jobs.plan(("kv", i), r)
    for b in range(DX):
        jobs.plan(("xbc", b))
    jobs.plan("cum")
    for c in range(2):
        for t in range(TT):
            jobs.plan(("q", c, t))
    for c in range(2):
        for t in range(TT):
            jobs.plan(("z", c, t))
    jobs.plan("aT")
    for i in range(4):
        for half in range(2):
            jobs.plan(("xsT", i, half))
        jobs.plan(("bT", i))
    for i in range(2):
        jobs.plan(("kT", i))
    for t in range(TT):
        jobs.plan(("cb", t))
    for n in range(len(STATES)):
        for g in range(2):
            jobs.plan(("st", n, g), ("s0", "s1")[g])
    for t, g, quad in UNITS:
        for d in range(2):
            jobs.plan(("aq", t, g, quad, d))
        if quad == 1:
            jobs.plan(("yd", t, g), "a3")
            for d in range(2):
                jobs.plan(("yo", t, g, d), ("t", "u")[d])
    for t in range(TT):
        for h in range(2):
            jobs.plan(("qT", t, h))
    for n, (t, b, g) in enumerate(HEAD_ITEMS):
        jobs.plan(("S", n), ("s0", "s1")[n % 2])
        jobs.plan(("PT", n), ("t", "u")[n % 2])
        if b % 4 == 0 and g == 0:
            jobs.plan(("O", t, b // 4), "a3")
    for t in range(TT):
        for h in range(4):
            jobs.plan(("mixT", h, t))
    for v in range(2):
        for c in range(2):
            jobs.plan(("gB", v, c))
    for t in range(TT):
        for c in range(2):
            jobs.plan(("out", t, c), f"a{2 * t + c}")
    for c in range(2):
        for t in range(TT):
            jobs.plan(("hf", c, t), ("s0", "s1", "t", "u")[2 * c + t])
    jobs.plan("route", "s0")
    for e in range(EXPERT_STEP):
        if e == 2:
            jobs.plan("combT", "s0")
            for i in range(8):
                jobs.plan(("combB", i), ("s0", "s1")[i % 2])
        for part, r in zip("GU", expert_regions(e)):
            jobs.plan((part, e), r)


def expert_regions(e):
    return ("s0", "s1") if e % 2 == 0 else ("t", "u")


MOE_ORDER = [("G", 0), ("U", 0), ("G", 1), ("U", 1), ("D", 0), ("G", 2), ("U", 2), ("D", 1), ("G", 3), ("U", 3), ("D", 2), ("D", 3)]


def block2(nc, mem, ring, landed, used, wts, psum, sems, cols_dram, rows_dram, ctx_dram, out_dram):
    region = {**{f"a{i}": (i * 512, 512) for i in range(4)}, "s0": (2048, 512), "s1": (2560, 512), "t": (3072, 512), "u": (3584, 512)}
    filled = {r: sems(f"filled2_{r}") for r in region}
    drained = {r: sems(f"drained2_{r}") for r in region}
    jobs = Jobs(psum, filled, drained, region, ring=3)
    plan_block2(jobs)

    params, ctx_in = sems("params2"), sems("ctx_in")
    mod_ready = sems("mod_ready")
    shifted = sems("shifted")
    conv_init = sems("conv_init")
    xbc_ready = sems("xbc_ready")
    dt_neg, dt_exp, dt_u, dt_ln, dt_ready = (sems(n) for n in ("dt_neg", "dt_exp", "dt_u", "dt_ln", "dt_ready"))
    a_ready = sems("a_ready")
    decays = sems("decays")
    diff_ready = sems("diff_ready")
    dw_ready = sems("dw_ready")
    xw_ready = sems("xw_ready")
    h_ready = sems("h_ready")
    xdt_ready = sems("xdt_ready")
    skip_ready = sems("skip_ready")
    aq_diff = sems("aq_diff")
    aq_exp = sems("aq_exp")
    m_ready = sems("m_ready")
    y_sq = sems("y_sq")
    y_gated = sems("y_gated")
    y_std = sems("y_std")
    y_norm = sems("y_norm")
    qk_sum = sems("qk_sum")
    qk_std = sems("qk_std")
    qk_ready = sems("qk_ready")
    nmax_ready = sems("nmax_ready")
    pt_ready = sems("pt_ready")
    diag_ready = sems("diag_ready")
    ln_stat, ln_std, x_normed = sems("ln_stat"), sems("ln_std"), sems("x_normed")
    comb_ready = sems("comb_ready")
    r_logits, r_exp = sems("r_logits"), sems("r_exp")
    zero_ready = sems("zero_ready")
    silu_g = sems("silu_g")
    hi_ready = sems("hi_ready2")
    lo_ready = sems("lo_ready2")
    h_hi, h_lo = sems("h_hi2"), sems("h_lo2")
    hid_raw = sems("hid_raw")
    hid_hi = sems("hid_hi")
    hid_ready = sems("hid_ready2")
    hid_used = sems("hid_used")
    stored = sems("stored")
    m_used = sems("m_used")
    v_order, g_order, a_order = sems("v_order2"), sems("g_order2"), sems("a_order2")

    split, hfS, hidS, combB, gated, hid, hf = (mem[k] for k in ("split", "hfS", "hidS", "combB", "pe", "hid", "hf"))
    hT, xdt, bcf, z, q, kv, xs, bt, wx, y, kT, qT, p, pt, m, cb = (mem[k] for k in (
        "hT", "xdt", "bcf", "z", "q", "kv", "xs", "bt", "wx", "y", "kT", "qT", "p", "pt", "m", "cb"))
    x, const, cols, rows, sm = mem["x"], mem["const"], mem["cols2"], mem["rows2"], mem["sm"]
    xbc_xs = xdt[:, :, :].rearrange("p i (b t) -> p (i b) t", t=512)
    H = hT[:, :, :].rearrange("p k t -> p (k t)").rearrange("p (n c) -> p n c", c=1024)
    mixT = xdt[:, :, :].rearrange("p i (b t) -> p (i b) t", t=T)
    gB = z
    res = y
    ctx_tm = y

    at = [0]

    def small(n):
        at[0] += n
        return sm[:, at[0] - n:at[0]]

    modT = mem["modT"]
    dtr, dt, dtA, tmp_a, tmp_b = (small(128).rearrange("p (i h) -> p i h", i=4) for _ in range(5))
    acs = small(256).rearrange("p (i h) -> p i h", i=4)
    expA = small(32)
    ssq, rq = small(16), small(16)
    assert at[0] <= 960
    sm2 = mem["sm2"]
    at2 = [0]

    def small2(n):
        at2[0] += n
        return sm2[:, at2[0] - n:at2[0]]

    dec = small2(128).rearrange("p (i h) -> p i h", i=4)
    dw = small2(128).rearrange("p (i h) -> p i h", i=4)
    ea = small2(128).rearrange("p (i h) -> p i h", i=4)
    yss, yrs = small2(4), small2(4)
    kss, krs = small2(16), small2(16)
    qss, qrs = small2(32).rearrange("p (t h) -> p t h", t=2), small2(32).rearrange("p (t h) -> p t h", t=2)
    nm, dn, rden = small2(32), small2(32), small2(32)
    stats, mv, lstd, lms = small2(24).rearrange("p (t c s) -> p t c s", t=2, c=2), small2(4).rearrange("p (t s) -> p t s", t=2), small2(2), small2(2)
    lg = small2(40).rearrange("p (t n) -> p t n", t=2)
    gm, gs, gval = small2(2), small2(2), small2(2)
    goh = small2(8).rearrange("p (t g) -> p t g", t=2)
    r8a, r8b, es, pe_, oh1, oh2, pm, wgt = (small2(8).rearrange("p (t g) -> p t g", t=2) for _ in range(8))
    r2a, r2b, r2c = small2(2), small2(2), small2(2)
    r32 = small2(32).rearrange("p (t g e) -> p t g e", t=2, g=4)
    comb = small2(32).rearrange("p (t e) -> p t e", t=2)
    aT = mem["aT"]
    combT = mem["combT"]

    def K(name, a=0, b=None):
        o, width = CONST[name]
        return const[:, o + a:o + (width if b is None else b)]

    def C(name, a=0, b=None):
        o, width = COLS2[name]
        return cols[:, o + a:o + (width if b is None else b)]

    def R(name):
        o, width = ROWS2[name]
        return rows[:, o:o + width]

    ident = K("ident")
    first = LAYERS * N_LAYER_CHUNKS
    first_moe = first + N_BLOCK2_CHUNKS
    turns = len(MOE_ORDER) // SLOTS

    def wait_expert(eng, step, part, e, what):
        r = expert_regions(e)["GU".index(part)]
        _, turn, free, done = jobs.jobs[(part, e)]
        sem = filled[r] if what == "filled" else drained[r]
        peeled = {"claim": free, "filled": turn, "drained": done}[what]
        later = {"claim": jobs.sum[r] - 2 + e // 2, "filled": jobs.turn[r] - 1 + e // 2, "drained": jobs.sum[r] - 1 + e // 2}[what]
        eng.wait_ge(sem, peeled if isinstance(step, int) else step * 2 + later)

    def expert_bank(part, e):
        at, width = region[expert_regions(e)["GU".index(part)]]
        return psum[:, at:at + width]

    def split_hi(act, step, n):
        c = first_moe + n
        act.wait_ge(used[(c - SPLITS) % SLOTS], step * turns + ((c - SPLITS) // SLOTS + 1))
        act.wait_ge(landed[c % SLOTS], step * (turns * 16) + (c // SLOTS + 1) * 16)
        act.activation(split[:, n % SPLITS, 0, :], ring[:, c % SLOTS, :], ACT.Copy).then_inc(hi_ready, 1)

    def split_lo(dve, step, n):
        dve.wait_ge(hi_ready, step * len(MOE_ORDER) + (n + 1))
        dve.tensor_tensor(split[:, n % SPLITS, 1, :], ring[:, (first_moe + n) % SLOTS, :], split[:, n % SPLITS, 0, :].bitcast(F32),
                          ALU.subtract).then_inc(lo_ready, 1)

    with nc.Block() as block:
        @block.sync
        def _(sp):
            sp.dma_start(ctx_tm[:, :, :], ctx_dram.rearrange("(t p) d -> p t d", p=P)).then_inc(ctx_in, 16)
            left = N_BLOCK2_CHUNKS + 3 * EXPERTS - SLOTS
            with sp.Fori(0, left // SLOTS) as turn:
                for s in range(SLOTS):
                    sp.wait_ge(used[s], turn + (first // SLOTS + 1))
                    sp.dma_start(ring[:, s, :], wts[turn * SLOTS + (first + s + SLOTS)]).then_inc(landed[s], 16)
            for t in range(TT):
                sp.wait_ge(x_normed, TT + t + 1)
                sp.dma_start(out_dram[t * P:(t + 1) * P, :], x[:, t, :]).then_inc(stored, 16)
            sp.wait_ge(stored, 16 * TT)

        @block.tensor
        def _(pe):
            state = {"chunk": first, "owed": None}

            def next_chunk():
                c = state["chunk"]
                state["chunk"] += 1
                pe.wait_ge(landed[c % SLOTS], (c // SLOTS + 1) * 16)
                return ring[:, c % SLOTS, :]

            def carry(ins):
                if state["owed"] is not None:
                    ins.then_inc(used[state["owed"]], 1)
                    state["owed"] = None

            def done_with(ins):
                ins.then_inc(used[(state["chunk"] - 1) % SLOTS], 1)

            def owe():
                assert state["owed"] is None
                state["owed"] = (state["chunk"] - 1) % SLOTS

            def transpose4(name, blocks, step=P):
                jobs.claim(pe, name)
                out = jobs.out(name)
                for i, b in enumerate(blocks):
                    mm = pe.transpose(out[0:b.shape[1], i * step:i * step + P], b, ident)
                    if i == 0 and len(blocks) > 1:
                        carry(mm)
                jobs.fill(mm, name)

            for s in range(2):
                src = (ctx_tm, x)[s]
                if s == 0:
                    pe.wait_ge(ctx_in, 16)
                for c in range(2):
                    for t in range(TT):
                        transpose4(("in", s, c, t), [src[:, t, (4 * c + i) * P:(4 * c + i + 1) * P] for i in range(4)])
            pe.wait_ge(shifted, 8)
            jobs.claim(pe, "dt")
            for i in range(SEQ_TILES):
                for k in range(KD):
                    mm = pe.matmul(jobs.out("dt")[:, 32 * i:32 * i + 32], hT[:, k, i * P:(i + 1) * P], C("w_dt", 32 * k, 32 * k + 32),
                                   start=(k == 0), stop=(k == KD - 1))
            jobs.fill(mm, "dt")

            def tokens(kind, tiles, names):
                for half in range(2):
                    chunk = next_chunk().rearrange("p (k n) -> p k n", k=4)
                    for tile, name in zip(tiles, names):
                        if half == 0:
                            jobs.claim(pe, name)
                        for k in range(4):
                            mm = pe.matmul(jobs.out(name), hT[:, 4 * half + k, tile * P:(tile + 1) * P], chunk[:, k, :],
                                           start=(half == 0 and k == 0), stop=(half == 1 and k == 3))
                            if k == 0:
                                carry(mm)
                        if half == 1:
                            jobs.fill(mm, name)
                    if half == 0:
                        done_with(mm)
                    else:
                        owe()

            tokens("kv", range(SEQ_TILES), [("kv", i) for i in range(SEQ_TILES)])
            for b in range(DX):
                if b % 2 == 0:
                    chunk = next_chunk().rearrange("p (k m) -> p k m", k=KD)
                jobs.claim(pe, ("xbc", b))
                for k in range(KD):
                    mm = pe.matmul(jobs.out(("xbc", b)), chunk[:, k, b % 2 * P:(b % 2 + 1) * P], hT[:, k, :], start=(k == 0), stop=(k == KD - 1))
                    if k == 0:
                        carry(mm)
                jobs.fill(mm, ("xbc", b))
                if b % 2 == 1:
                    owe()

            pe.wait_ge(dt_ready, 1)
            jobs.claim(pe, "cum")
            for i in range(SEQ_TILES):
                out = jobs.out("cum")[:, 64 * i:64 * i + 64]
                mm = pe.matmul(out[:, 0:16], K("tri_u"), dtA[:, i, 0:16], start=True, stop=True)
                carry(mm)
                pe.matmul(out[:, 16:32], K("tri_l"), dtA[:, i, 16:32], start=True, stop=True)
                mm = pe.matmul(out[:, 32:64], K("ones"), dtA[:, i, :], start=True, stop=True)
            jobs.fill(mm, "cum")
            for c in range(2):
                tokens("q", (2, 3), [("q", c, t) for t in range(TT)])
            for c in range(2):
                tokens("z", (2, 3), [("z", c, t) for t in range(TT)])
            jobs.wait_drained(pe, "cum")
            transpose4("aT", [acs[:, 2 + t, 0:32] for t in range(TT)])

            pe.wait_ge(xbc_ready, DX)
            for i in range(SEQ_TILES):
                for half in range(2):
                    transpose4(("xsT", i, half), [xbc_xs[:, 4 * half + b, i * P:(i + 1) * P] for b in range(4)])
                transpose4(("bT", i), [bcf[:, g, i * P:(i + 1) * P] for g in range(2)])
            pe.wait_ge(qk_ready, 1)
            for b in range(2):
                transpose4(("kT", b), [kv[:, i, b * P:(b + 1) * P] for i in range(SEQ_TILES)])
            for t in range(TT):
                jobs.claim(pe, ("cb", t))
                for g in range(2):
                    mm = pe.matmul(jobs.out(("cb", t))[:, g * P:(g + 1) * P], bcf[:, g, (2 + t) * P:(3 + t) * P],
                                   bcf[:, 2 + g, (2 + t) * P:(3 + t) * P], start=True, stop=True)
                jobs.fill(mm, ("cb", t))
            for n, (i, d) in enumerate(STATES):
                pe.wait_ge(xw_ready, n + 1)
                jobs.wait_drained(pe, ("bT", i))
                for g in range(2):
                    jobs.claim(pe, ("st", n, g))
                    jobs.fill(pe.matmul(jobs.out(("st", n, g)), bt[:, i, g * P:(g + 1) * P], wx[:, n % 2, g * 512:(g + 1) * 512],
                                        start=True, stop=True), ("st", n, g))

            jobs.wait_drained(pe, "aT")

            def spread(t, g, quad):
                for d in range(2):
                    name = ("aq", t, g, quad, d)
                    jobs.claim(pe, name)
                    for h in range(4):
                        head = 16 * d + 8 * g + 4 * quad + h
                        mm = pe.matmul(jobs.out(name)[:, h * P:(h + 1) * P], bc(ident[0:32, head:head + 1], [32, P]), aT[0:32, t, :],
                                       start=True, stop=True)
                    jobs.fill(mm, name)

            pe.wait_ge(xdt_ready, 4)
            spread(*UNITS[0])
            for n, (t, g, quad) in enumerate(UNITS):
                if n + 1 < len(UNITS):
                    spread(*UNITS[n + 1])
                pe.wait_ge(m_ready, 2 * n + 2)
                if quad == 0:
                    jobs.claim(pe, ("yd", t, g))
                for h in range(4):
                    for d in range(2):
                        mm = pe.matmul(jobs.out(("yd", t, g))[:, (4 * quad + h) * DH:(4 * quad + h + 1) * DH],
                                       m[:, (2 * n + d) % 4, h * P:(h + 1) * P],
                                       xdt[:, 2 * t + d, (8 * g + 4 * quad + h) * DH:(8 * g + 4 * quad + h + 1) * DH],
                                       start=(d == 0), stop=(d == 1))
                if quad == 0:
                    mm.then_inc(m_used, 1)
                else:
                    jobs.fill(mm, ("yd", t, g))
                    pe.wait_ge(h_ready, 12)
                    for d in range(2):
                        jobs.claim(pe, ("yo", t, g, d))
                        mm = pe.matmul(jobs.out(("yo", t, g, d)), bcf[:, 2 + g, (2 + t) * P:(3 + t) * P],
                                       H[:, 2 * d + t, g * 512:(g + 1) * 512], start=True, stop=True)
                        jobs.fill(mm, ("yo", t, g, d))

            for t in range(TT):
                pe.wait_ge(qk_ready, 2 + t)
                for h in range(2):
                    transpose4(("qT", t, h), [q[:, t, (4 * h + b) * P:(4 * h + b + 1) * P] for b in range(4)])
            for b in range(2):
                jobs.wait_drained(pe, ("kT", b))

            def values(n):
                t, b, g = HEAD_ITEMS[n]
                if b % 4 == 0 and g == 0:
                    jobs.claim(pe, ("O", t, b // 4))
                jobs.wait_drained(pe, ("PT", n))
                for i in range(SEQ_TILES):
                    mm = pe.matmul(jobs.out(("O", t, b // 4))[:, (2 * (b % 4) + g) * DH:(2 * (b % 4) + g + 1) * DH],
                                   pt[:, n % 2, i * P:(i + 1) * P], kv[:, i, 256 + (2 * (b // 4) + g) * DH:256 + (2 * (b // 4) + g + 1) * DH],
                                   start=(i == 0), stop=(i == SEQ_TILES - 1))
                if b % 4 == 3 and g == 1:
                    jobs.fill(mm, ("O", t, b // 4))

            for n in range(len(HEAD_ITEMS) + 2):
                if n < len(HEAD_ITEMS):
                    t, b, g = HEAD_ITEMS[n]
                    if g == 0 and b % 4 == 0:
                        jobs.wait_drained(pe, ("qT", t, b // 4))
                    jobs.claim(pe, ("S", n))
                    jobs.fill(pe.matmul(jobs.out(("S", n)), qT[64 * g:64 * g + 64, b, t * P:(t + 1) * P], kT[64 * g:64 * g + 64, b // 4, :],
                                        start=True, stop=True), ("S", n))
                if n >= 1 and n - 1 < len(HEAD_ITEMS):
                    jobs.wait_drained(pe, ("S", n - 1))
                    transpose4(("PT", n - 1), [p[:, (n - 1) % 2, i * P:(i + 1) * P] for i in range(SEQ_TILES)])
                if n >= 2:
                    values(n - 2)

            for t in range(TT):
                for h in range(4):
                    if h == 0:
                        pe.wait_ge(y_norm, t + 1)
                    if h >= 2:
                        jobs.wait_drained(pe, ("O", t, h - 2))
                    src = y[:, t, :] if h < 2 else q[:, t, :]
                    transpose4(("mixT", h, t), [src[:, (4 * (h % 2) + b) * P:(4 * (h % 2) + b + 1) * P] for b in range(4)])
            for v in range(2):
                pe.wait_ge(diag_ready, v + 1)
                for c in range(2):
                    jobs.claim(pe, ("gB", v, c))
                    jobs.fill(pe.matmul(jobs.out(("gB", v, c)), K("ones"), wx[:, v, c * 512:(c + 1) * 512], start=True, stop=True), ("gB", v, c))
            for t in range(TT):
                for h in range(4):
                    jobs.wait_drained(pe, ("mixT", h, t))
                for c in range(2):
                    jobs.claim(pe, ("out", t, c))
            for i in range(8):
                chunk = next_chunk().rearrange("p (k n) -> p k n", k=2)
                for k in range(2):
                    for t in range(TT):
                        for c in range(2):
                            mm = pe.matmul(jobs.out(("out", t, c)), mixT[:, 2 * i + k, t * P:(t + 1) * P], chunk[:, k, c * 512:(c + 1) * 512],
                                           start=(i == 0 and k == 0), stop=(i == 7 and k == 1))
                            if k == 0:
                                carry(mm)
                            if i == 7 and k == 1:
                                jobs.fill(mm, ("out", t, c))
                if i < 7:
                    done_with(mm)
            jobs.wait_filled(pe, ("out", 1, 1))
            pe.sem_inc(used[(state["chunk"] - 1) % SLOTS], 1)

            for c in range(2):
                for t in range(TT):
                    pe.wait_ge(x_normed, t + 1)
                    transpose4(("hf", c, t), [x[:, t, (4 * c + i) * P:(4 * c + i + 1) * P] for i in range(4)])
            pe.wait_ge(shifted, 12)
            jobs.claim(pe, "route")
            for t in range(TT):
                for k in range(KD):
                    mm = pe.matmul(jobs.out("route")[:, 20 * t:20 * t + 20], hf[:, k, t * P:(t + 1) * P], C("w_r", 20 * k, 20 * k + 20),
                                   start=(k == 0), stop=(k == KD - 1))
            jobs.fill(mm, "route")
            pe.wait_ge(h_lo, 4)
            pe.sem_inc(hid_used, 2)

            def parts(step, n):
                pe.wait_ge(lo_ready, step * len(MOE_ORDER) + (n + 1))
                return split[:, n % SPLITS, 0, :], split[:, n % SPLITS, 1, :]

            def expert_in(step, n):
                part, e = MOE_ORDER[n]
                hi, lo = (w.rearrange("p (k m) -> p k m", k=KD) for w in parts(step, n))
                wait_expert(pe, step, part, e, "claim")
                for b in range(2):
                    out = expert_bank(part, e)[:, b * T:(b + 1) * T]
                    for k in range(KD):
                        mm = pe.matmul(out, hi[:, k, b * P:(b + 1) * P], hfS[:, 0, k, :], start=(k == 0), stop=False)
                        if b == 0 and k == 0:
                            carry(mm)
                        pe.matmul(out, hi[:, k, b * P:(b + 1) * P], hfS[:, 1, k, :], start=False, stop=False)
                        mm = pe.matmul(out, lo[:, k, b * P:(b + 1) * P], hfS[:, 0, k, :], start=False, stop=(k == KD - 1))
                mm.then_inc(filled[expert_regions(e)["GU".index(part)]], 1)
                state["owed"] = (first_moe + n) % SLOTS

            def expert_out(step, n):
                _, e = MOE_ORDER[n]
                hi, lo = (w.rearrange("p (k n) -> p k n", k=2) for w in parts(step, n))
                pe.wait_ge(hid_ready, step * EXPERT_STEP + (e + 3))
                for k in range(2):
                    for t in range(TT):
                        h_hi_, h_lo_ = (hidS[:, e % 2, w, k * T + t * P:k * T + (t + 1) * P] for w in range(2))
                        for c in range(2):
                            out, cs = psum[:, (2 * t + c) * 512:(2 * t + c + 1) * 512], slice(c * 512, (c + 1) * 512)
                            mm = pe.matmul(out, h_hi_, hi[:, k, cs], start=False, stop=False, skip_group_check=True)
                            if k == 0 and t == 0 and c == 0:
                                carry(mm)
                            pe.matmul(out, h_hi_, lo[:, k, cs], start=False, stop=False, skip_group_check=True)
                            mm = pe.matmul(out, h_lo_, hi[:, k, cs], start=False, stop=False, skip_group_check=True)
                mm.then_inc(hid_used, 1)
                state["owed"] = (first_moe + n) % SLOTS

            def experts(step):
                for n, (part, e) in enumerate(MOE_ORDER):
                    if isinstance(step, int) and n == 4:
                        weights_of_tokens()
                    if part == "D":
                        expert_out(step, n)
                    else:
                        expert_in(step, n)
                pe.wait_ge(hid_used, step * EXPERT_STEP + (EXPERT_STEP + 2))
                pe.sem_inc(used[state["owed"]], 1)
                state["owed"] = None

            def weights_of_tokens():
                pe.wait_ge(comb_ready, 1)
                transpose4("combT", [comb[:, t, :] for t in range(TT)])
                jobs.wait_drained(pe, "combT")
                for i in range(8):
                    jobs.claim(pe, ("combB", i))
                    for e in range(2):
                        mm = pe.matmul(jobs.out(("combB", i))[:, e * T:(e + 1) * T], bc(ident[0:16, 2 * i + e:2 * i + e + 1], [16, P]),
                                       combT[0:16, :], start=True, stop=True)
                    jobs.fill(mm, ("combB", i))

            pe.wait_ge(zero_ready, 1)
            for r in range(4):
                pe.wait_ge(drained[f"a{r}"], jobs.sum[f"a{r}"])
                pe.matmul(psum[:, r * 512:(r + 1) * 512], hid[:, 0, 0:P], hid[:, 1, :], start=True, stop=False, skip_group_check=True)
            experts(0)
            with pe.Fori(1, EXPERTS // EXPERT_STEP) as step:
                experts(step)

        @block.scalar
        def _(act):
            order = Signal(a_order)

            def copy_out(name, dst, src=None, scale=1.0, func=ACT.Copy):
                jobs.wait_filled(act, name)
                jobs.drain(act.activation(dst, jobs.out(name) if src is None else src, func, scale=scale), name)

            act.dma_start(cols[:, :], cols_dram).then_inc(params, 16)
            act.dma_start(rows[:, :], rows_dram.to_broadcast([P, N_ROWS2])).then_inc(params, 16)
            act.wait_ge(params, 32)
            for i in range(SEQ_TILES):
                copy_out(("kv", i), kv[:, i, :])
            for b in range(DX + 1):
                if b < DX:
                    jobs.wait_filled(act, ("xbc", b))
                    dst = xbc_xs[:, b, :] if b < 8 else bcf[:, b - 8, :]
                    act.activation(dst, jobs.out(("xbc", b)), ACT.Identity, scale=C("conv_w", 5 * b + 2, 5 * b + 3),
                                   bias=C("conv_b", b, b + 1)).then_inc(conv_init, 1)
                if b >= 1:
                    dst = xbc_xs[:, b - 1, :] if b - 1 < 8 else bcf[:, b - 9, :]
                    jobs.wait_drained(act, ("xbc", b - 1))
                    act.activation(dst, dst, ACT.Silu).then_inc(xbc_ready, 1)
            act.activation(expA, R("alog"), ACT.Exp).then_inc(a_ready, 1)
            act.wait_ge(dt_neg, 1)
            act.activation(tmp_b[:, :, :], tmp_b[:, :, :], ACT.Exp).then_inc(dt_exp, 1)
            act.wait_ge(dt_u, 1)
            act.activation(tmp_a[:, :, :], tmp_a[:, :, :], ACT.Ln).then_inc(dt_ln, 1)
            for c in range(2):
                for t in range(TT):
                    copy_out(("q", c, t), q[:, t, c * 512:(c + 1) * 512])
            for c in range(2):
                for t in range(TT):
                    copy_out(("z", c, t), z[:, t, c * 512:(c + 1) * 512], func=ACT.Silu)
            act.wait_ge(diff_ready, 1)
            act.activation(dec[:, :, :], acs[:, :, 32:64], ACT.Exp).then_inc(decays, 1)
            act.activation(ea[:, :, :], acs[:, :, 0:32], ACT.Exp).then_inc(decays, 1)
            act.activation(dw[:, :, :], dw[:, :, :], ACT.Exp).then_inc(decays, 1)
            copy_out("aT", aT[0:32, :, :], jobs.out("aT")[0:32, 0:2 * P].rearrange("p (t q) -> p t q", t=2))
            for i in range(SEQ_TILES):
                for half in range(2):
                    copy_out(("xsT", i, half), xs[:, i, half * 512:(half + 1) * 512])
                copy_out(("bT", i), bt[:, i, :], jobs.out(("bT", i))[:, 0:256])
            for b in range(2):
                copy_out(("kT", b), kT[:, b, :])

            for n in range(len(UNITS)):
                for d in range(2):
                    act.wait_ge(aq_diff, 2 * n + d + 1)
                    act.activation(m[:, (2 * n + d) % 4, :], m[:, (2 * n + d) % 4, :], ACT.Exp).then_inc(aq_exp, 1)
            for t in range(TT):
                for h in range(2):
                    copy_out(("qT", t, h), qT[:, 4 * h:4 * h + 4, t * P:(t + 1) * P], jobs.out(("qT", t, h)).rearrange("p (b t) -> p b t", b=4), 0.125)
            for n in range(len(HEAD_ITEMS) + 1):
                if n < len(HEAD_ITEMS):
                    if n >= 2:
                        jobs.wait_filled(act, ("PT", n - 2))
                    act.wait_ge(nmax_ready, n + 1)
                    name = ("S", n)
                    jobs.wait_filled(act, name)
                    jobs.drain(act.activation(p[:, n % 2, :], jobs.out(name), ACT.Exp, bias=nm[:, n:n + 1], accum_out=dn[:, n:n + 1]), name)
                if n >= 1 and (n - 1) % 2 == 0:
                    copy_out(("PT", n - 1), pt[:, (n - 1) % 2, :])
            for t in range(TT):
                act.wait_ge(y_gated, t + 1)
                if t:
                    act.wait_ge(y_sq, 2 * t)
                for g in range(2):
                    act.activation(wx[:, g, 0:512], y[:, t, g * 512:(g + 1) * 512], ACT.Square, accum_out=yss[:, 2 * t + g:2 * t + g + 1]).then_inc(y_sq, 1)
            for t in range(TT):
                for h in (2, 3):
                    copy_out(("mixT", h, t), mixT[:, 4 * h:4 * h + 4, t * P:(t + 1) * P], jobs.out(("mixT", h, t)).rearrange("p (b t) -> p b t", b=4))
            for v in range(2):
                for c in range(2):
                    copy_out(("gB", v, c), gB[:, v, c * 512:(c + 1) * 512])
            split_hi(act, 0, 0)
            split_hi(act, 0, 1)
            for n in range(4):
                c, t = divmod(n, TT)
                act.wait_ge(shifted, 8 + n + 1)
                act.activation(hfS[:, 0, 4 * c:4 * c + 4, t * P:(t + 1) * P], hf[:, 4 * c:4 * c + 4, t * P:(t + 1) * P], ACT.Copy).then_inc(h_hi, 1)
            split_hi(act, 0, 2)

            def silu(step, e):
                wait_expert(act, step, "G", e, "filled")
                act.wait_ge(hid_raw, step * EXPERT_STEP + (e + 1))
                act.activation(gated[:, e % 2, :], expert_bank("G", e), ACT.Silu).then_inc(drained[expert_regions(e)[0]], 1)

            def hidden_hi(step, e):
                act.wait_ge(hid_raw, step * EXPERT_STEP + (e + 3))
                act.wait_ge(hid_used, step * EXPERT_STEP + (e + 1))
                act.activation(hidS[:, e % 2, 0, :], hid[:, e % 2, :], ACT.Copy).then_inc(hid_hi, 1)

            act.wait_ge(r_logits, 1)
            act.activation(r8a[:, :, :], r8a[:, :, :], ACT.Exp).then_inc(r_exp, 1)
            act.activation(es[:, :, :], es[:, :, :], ACT.Exp).then_inc(r_exp, 1)
            split_hi(act, 0, 3)
            silu(0, 0)
            split_hi(act, 0, 4)
            split_hi(act, 0, 5)
            silu(0, 1)
            split_hi(act, 0, 6)
            copy_out("combT", combT[0:16, :], jobs.out("combT")[0:16, 0:T])
            for i in range(8):
                copy_out(("combB", i), combB[:, 2 * i:2 * i + 2, :], jobs.out(("combB", i)).rearrange("p (e t) -> p e t", e=2))
            hidden_hi(0, 0)
            hidden_hi(0, 1)

            def last_two(step):
                split_hi(act, step, 7)
                silu(step, 2)
                split_hi(act, step, 8)
                hidden_hi(step, 2)
                split_hi(act, step, 9)
                split_hi(act, step, 10)
                silu(step, 3)
                split_hi(act, step, 11)
                hidden_hi(step, 3)

            last_two(0)
            with act.Fori(1, EXPERTS // EXPERT_STEP) as step:
                for n in range(3):
                    split_hi(act, step, n)
                silu(step, 0)
                split_hi(act, step, 3)
                hidden_hi(step, 0)
                split_hi(act, step, 4)
                silu(step, 1)
                split_hi(act, step, 5)
                hidden_hi(step, 1)
                split_hi(act, step, 6)
                last_two(step)

        @block.vector
        def _(dve):
            order = Signal(v_order)

            def chain(ins):
                order.up(ins)
                order.here(dve)

            def tt(out, a, b, op):
                chain(dve.tensor_tensor(out, a, b, op))

            dve.wait_ge(params, 32)
            dve.tensor_scalar(modT[:, 8:16, :], modT[:, 8:16, :], 1.0, None, ALU.add).then_inc(mod_ready, 1)
            dve.tensor_scalar(modT[:, 32:40, :], modT[:, 32:40, :], 1.0, None, ALU.add).then_inc(mod_ready, 1)
            dve.wait_ge(mod_ready, 2)

            def scale_in(name, dst, block, v):
                jobs.wait_filled(dve, name)
                jobs.drain(dve.tensor_tensor(dst, jobs.out(name).rearrange("p (b t) -> p b t", b=4),
                                             bc(modT[:, block:block + 4, v:v + 1], [P, 4, P]), ALU.mult), name)

            for s in range(2):
                for c in range(2):
                    for t in range(TT):
                        scale_in(("in", s, c, t), hT[:, 4 * c:4 * c + 4, (2 * s + t) * P:(2 * s + t + 1) * P], 8 + 4 * c, 1 - s)
            jobs.wait_filled(dve, "dt")
            jobs.drain(dve.tensor_tensor(dtr[:, :, :], jobs.out("dt")[:, 0:128].rearrange("p (i h) -> p i h", i=4),
                                         bc(R("dtb").unsqueeze(1), [P, 4, 32]), ALU.add), "dt")
            jobs.wait_drained(dve, "dt")
            chain(dve.tensor_scalar(tmp_b[:, :, :], dtr[:, :, :], -1.0, None, ALU.mult))
            dve.tensor_tensor(tmp_b[:, :, :], tmp_b[:, :, :], dtr[:, :, :], ALU.min).then_inc(dt_neg, 1)

            def taps(b):
                dve.wait_ge(conv_init, b + 1)
                dst = (xbc_xs[:, b, :] if b < 8 else bcf[:, b - 8, :]).rearrange("p (s t) -> p s t", s=2)
                src = jobs.out(("xbc", b)).rearrange("p (s t) -> p s t", s=2)
                for n, k in enumerate((0, 1, 3, 4)):
                    sh = k - 2
                    lo, hi = max(0, -sh), T - max(0, sh)
                    ins = dve.scalar_tensor_tensor(out=dst[:, :, lo:hi], in0=src[:, :, lo + sh:hi + sh], scalar=C("conv_w", 5 * b + k, 5 * b + k + 1),
                                                   in1=dst[:, :, lo:hi], op0=ALU.mult, op1=ALU.add)
                    if n < 3:
                        chain(ins)
                    else:
                        jobs.drain(ins, ("xbc", b))

            for b in range(DX):
                taps(b)
            dve.wait_ge(dt_exp, 1)
            chain(dve.tensor_scalar(tmp_a[:, :, :], tmp_b[:, :, :], 1.0, None, ALU.add))
            chain(dve.tensor_scalar(dt[:, :, :], tmp_a[:, :, :], -1.0, None, ALU.add))
            chain(dve.tensor_scalar(dtA[:, :, :], dt[:, :, :], 0.0, None, ALU.is_equal))
            dve.tensor_tensor(dt[:, :, :], dt[:, :, :], dtA[:, :, :], ALU.add).then_inc(dt_u, 1)
            dve.wait_ge(dt_u, 1)
            chain(dve.reciprocal(dt[:, :, :], dt[:, :, :]))
            tt(dt[:, :, :], dt[:, :, :], tmp_b[:, :, :], ALU.mult)
            dve.wait_ge(dt_ln, 1)
            tt(tmp_a[:, :, :], tmp_a[:, :, :], dtA[:, :, :], ALU.add)
            tt(dt[:, :, :], dt[:, :, :], tmp_a[:, :, :], ALU.mult)
            chain(dve.scalar_tensor_tensor(out=dt[:, :, :], in0=dtr[:, :, :], scalar=0.0, in1=dt[:, :, :], op0=ALU.max, op1=ALU.add))
            dve.wait_ge(a_ready, 1)
            chain(dve.tensor_scalar(expA, expA, -1.0, None, ALU.mult))
            dve.tensor_tensor(dtA[:, :, :], dt[:, :, :], bc(expA.unsqueeze(1), [P, 4, 32]), ALU.mult).then_inc(dt_ready, 1)
            jobs.wait_filled(dve, "cum")
            jobs.drain(dve.tensor_copy(acs[:, :, :], jobs.out("cum")[:, 0:256].rearrange("p (i h) -> p i h", i=4)), "cum")
            jobs.wait_drained(dve, "cum")
            dve.tensor_tensor(dw[:, :, :], acs[:, :, 32:64], acs[:, :, 0:32], ALU.subtract).then_inc(diff_ready, 1)

            tmpw = m[:, 0:2, :].rearrange("p a n -> p (a n)")
            tmpv = m[:, 2:4, :].rearrange("p a n -> p (a n)")

            def head_norm(v, n_heads, ssum, rs, turn, g, tiles, tab):
                tn = len(tiles)
                w4 = tmpw.rearrange("p (t c) -> p t c", t=tn)
                tt(w4, v, v, ALU.mult)
                dve.tensor_reduce(ssum, w4.rearrange("p t (h d) -> p t h d", d=DH), AX_X, ALU.add).then_inc(qk_sum, 1)
                dve.wait_ge(qk_std, turn)
                for i in range(tn):
                    v3 = v[:, i, :].rearrange("p (h d) -> p h d", d=DH)
                    order.up(dve.tensor_tensor(v3, v3, bc(rs[:, i, :].unsqueeze(2), [P, n_heads, DH]), ALU.mult))
                order.here(dve)
                for i in range(tn):
                    v3 = v[:, i, :].rearrange("p (h d) -> p h d", d=DH)
                    order.up(dve.tensor_tensor(v3, v3, bc(g.unsqueeze(1), [P, n_heads, DH]), ALU.mult))
                order.here(dve)
                for i, tile in enumerate(tiles):
                    if tile is None:
                        continue
                    cos, sin, nsin = (K("axial", 64 * s + 32 * tile, 64 * s + 32 * tile + 32) for s in range(3))
                    v3 = v[:, i, :].rearrange("p (h d) -> p h d", d=32)
                    w3 = tmpw[:, 0:64 * n_heads].rearrange("p (h r d) -> p h r d", r=2, d=32)
                    v4 = v[:, i, :].rearrange("p (h r d) -> p h r d", r=2, d=32)
                    for r, tb in ((0, nsin), (1, sin)):
                        order.up(dve.tensor_tensor(w3[:, :, r, :], v4[:, :, 1 - r, :], bc(tb.unsqueeze(1), [P, n_heads, 32]), ALU.mult))
                    tt(tmpv[:, 0:64 * n_heads].rearrange("p (h d) -> p h d", d=32), v3, bc(cos.unsqueeze(1), [P, 2 * n_heads, 32]), ALU.mult)
                    tt(v[:, i, :], tmpw[:, 0:64 * n_heads], tmpv[:, 0:64 * n_heads], ALU.add)

            for i in range(SEQ_TILES):
                jobs.wait_drained(dve, ("kv", i))
            head_norm(kv[:, :, 0:256], 4, kss.rearrange("p (t h) -> p t h", t=4), krs.rearrange("p (t h) -> p t h", t=4), 1, R("kn"),
                      [None, None, 0, 1], None)
            dve.tensor_copy(kss[:, 0:1], krs[:, 0:1]).then_inc(qk_ready, 1)

            dve.wait_ge(decays, 3)
            dve.tensor_tensor(dw[:, :, :], dw[:, :, :], dt[:, :, :], ALU.mult).then_inc(dw_ready, 1)
            for t in range(TT):
                for c in range(2):
                    jobs.wait_drained(dve, ("q", c, t))
                head_norm(q[:, t:t + 1, :], 16, qss[:, t:t + 1, :], qrs[:, t:t + 1, :], 2 + t, R("qn"), [t], None)
                dve.tensor_copy(qss[:, t, 0:1], qrs[:, t, 0:1]).then_inc(qk_ready, 1)
            for t in range(TT):
                jobs.wait_filled(dve, ("cb", t))
                src = jobs.out(("cb", t))[:, 0:256].rearrange("p (g q) -> p g q", g=2)
                order.up(dve.tensor_tensor(cb[:, t, 0, :, :], src, bc(K("tri_u").unsqueeze(1), [P, 2, P]), ALU.mult))
                jobs.drain(dve.tensor_tensor(cb[:, t, 1, :, :], src, bc(K("tri_l").unsqueeze(1), [P, 2, P]), ALU.mult), ("cb", t))

            slot = {0: 0, 1: 0, 2: 1, 3: 3, 4: 3, 5: 2}
            prev = {1: 0, 2: 0, 4: 3, 5: 3}
            for n, (i, d) in enumerate(STATES):
                for g in range(2):
                    name = ("st", n, g)
                    dst = H[:, slot[n], g * 512:(g + 1) * 512]
                    jobs.wait_filled(dve, name)
                    if n in prev:
                        src = H[:, prev[n], g * 512:(g + 1) * 512].rearrange("p (h c) -> p h c", c=DH)
                        chain(dve.tensor_tensor(dst.rearrange("p (h c) -> p h c", c=DH), src,
                                                bc(dec[:, i, 16 * d + 8 * g:16 * d + 8 * g + 8].unsqueeze(2), [P, 8, DH]), ALU.mult))
                        jobs.drain(dve.tensor_tensor(dst, dst, jobs.out(name), ALU.add), name)
                    else:
                        jobs.drain(dve.tensor_copy(dst, jobs.out(name)), name)
                    jobs.wait_drained(dve, name)
                    dve.sem_inc(h_ready, 1)

            def decay_diffs(n):
                t, g, quad = UNITS[n]
                for d in range(2):
                    name = ("aq", t, g, quad, d)
                    if 2 * n + d >= 4:
                        if UNITS[n - 2][2] == 0:
                            dve.wait_ge(m_used, (n - 2) // 2 + 1)
                        else:
                            jobs.wait_filled(dve, ("yd", *UNITS[n - 2][:2]))
                    jobs.wait_filled(dve, name)
                    for h in range(4):
                        head = 16 * d + 8 * g + 4 * quad + h
                        ins = dve.tensor_scalar(m[:, (2 * n + d) % 4, h * P:(h + 1) * P], jobs.out(name)[:, h * P:(h + 1) * P],
                                                acs[:, 2 + t, head:head + 1], 0.0, ALU.subtract, ALU.min)
                        if h < 3:
                            order.up(ins)
                        else:
                            jobs.drain(ins, name)
                    jobs.wait_drained(dve, name)
                    dve.sem_inc(aq_diff, 1)

            def gather_y(t, g):
                yy = y[:, t, g * 512:(g + 1) * 512]
                if g == 0:
                    dve.wait_ge(skip_ready, t + 1)
                name = ("yd", t, g)
                jobs.wait_filled(dve, name)
                jobs.drain(dve.tensor_tensor(yy, jobs.out(name), yy, ALU.add), name)
                jobs.wait_drained(dve, name)
                for d in range(2):
                    name = ("yo", t, g, d)
                    jobs.wait_filled(dve, name)
                    tb = p[:, d, :]
                    jobs.drain(dve.tensor_tensor(tb.rearrange("p (h c) -> p h c", c=DH), jobs.out(name).rearrange("p (h c) -> p h c", c=DH),
                                                 bc(ea[:, 2 + t, 16 * d + 8 * g:16 * d + 8 * g + 8].unsqueeze(2), [P, 8, DH]), ALU.mult), name)
                    jobs.wait_drained(dve, name)
                    tt(yy, yy, tb, ALU.add)
                if g == 1:
                    for c in range(2):
                        jobs.wait_drained(dve, ("z", c, t))
                    dve.tensor_tensor(y[:, t, :], y[:, t, :], z[:, t, :], ALU.mult).then_inc(y_gated, 1)

            for n in range(len(UNITS) + 1):
                if n < len(UNITS):
                    decay_diffs(n)
                if n >= 1 and UNITS[n - 1][2] == 1:
                    gather_y(*UNITS[n - 1][:2])

            for n in range(len(HEAD_ITEMS) + 2):
                if n < len(HEAD_ITEMS):
                    jobs.wait_filled(dve, ("S", n))
                    dve.tensor_reduce(nm[:, n:n + 1], jobs.out(("S", n)), AX_X, ALU.max, negate=True).then_inc(nmax_ready, 1)
                if n >= 1 and (n - 1) % 2 == 1:
                    name = ("PT", n - 1)
                    jobs.wait_filled(dve, name)
                    jobs.drain(dve.tensor_copy(pt[:, (n - 1) % 2, :], jobs.out(name)), name)
                if n >= 2:
                    t, b, g = HEAD_ITEMS[n - 2]
                    if b % 4 == 3 and g == 1:
                        name = ("O", t, b // 4)
                        h0 = n - 2 - 7
                        jobs.wait_drained(dve, ("S", n - 2))
                        chain(dve.reciprocal(rden[:, h0:h0 + 8], dn[:, h0:h0 + 8]))
                        jobs.wait_filled(dve, name)
                        jobs.drain(dve.tensor_tensor(q[:, t, (b // 4) * 512:(b // 4 + 1) * 512].rearrange("p (h c) -> p h c", c=DH),
                                                     jobs.out(name).rearrange("p (h c) -> p h c", c=DH),
                                                     bc(rden[:, h0:h0 + 8].unsqueeze(2), [P, 8, DH]), ALU.mult), name)
            for t in range(TT):
                dve.wait_ge(y_std, t + 1)
                for g in range(2):
                    ins = dve.tensor_scalar(y[:, t, g * 512:(g + 1) * 512], y[:, t, g * 512:(g + 1) * 512], yrs[:, 2 * t + g:2 * t + g + 1], None, ALU.mult)
                    if g == 0:
                        order.up(ins)
                    else:
                        ins.then_inc(y_norm, 1)
            dve.wait_ge(y_sq, 4)
            for v, block in enumerate((16, 40)):
                for b in range(8):
                    ins = dve.tensor_scalar(wx[:, v, b * P:(b + 1) * P], ident, modT[:, block + b, 0:1], None, ALU.mult)
                    if b < 7:
                        order.up(ins)
                    else:
                        ins.then_inc(diag_ready, 1)
            for t in range(TT):
                for h in range(2):
                    name = ("mixT", h, t)
                    jobs.wait_filled(dve, name)
                    jobs.drain(dve.tensor_tensor(mixT[:, 4 * h:4 * h + 4, t * P:(t + 1) * P], jobs.out(name).rearrange("p (b t) -> p b t", b=4),
                                                 bc(C("ssd_g", 4 * h, 4 * h + 4).unsqueeze(2), [P, 4, P]), ALU.mult), name)

            def residual(v, which, sources):
                for t in range(TT):
                    for c in range(2):
                        cs = slice(c * 512, (c + 1) * 512)
                        wait, src, done = sources(t, c)
                        wait()
                        done(dve.tensor_tensor(res[:, t, cs], src, gB[:, v, cs], ALU.mult))
                        chain(dve.scalar_tensor_tensor(out=res[:, t, cs], in0=x[:, t, cs], scalar=ALPHA, in1=res[:, t, cs], op0=ALU.mult, op1=ALU.add))
                        chain(dve.bn_stats(stats[:, t, c, :], res[:, t, cs]))
                    dve.bn_aggr(mv[:, t, :], stats[:, t, :, :].rearrange("p c s -> p (c s)")).then_inc(ln_stat, 1)
                for t in range(TT):
                    dve.wait_ge(ln_std, v * TT + t + 1)
                    chain(dve.tensor_scalar(x[:, t, :], res[:, t, :], mv[:, t, 0:1], lstd[:, t:t + 1], ALU.subtract, ALU.mult))
                    tt(x[:, t, :], x[:, t, :], R(f"ln{v + 1}_g"), ALU.mult)
                    dve.tensor_tensor(x[:, t, :], x[:, t, :], R(f"ln{v + 1}_b"), ALU.add).then_inc(x_normed, 1)

            def out_source(t, c):
                name = ("out", t, c)

                def wait():
                    jobs.wait_filled(dve, name)

                def done(ins):
                    jobs.drain(ins, name)
                    jobs.wait_drained(dve, name)
                return wait, jobs.out(name), done

            for c in range(2):
                jobs.wait_drained(dve, ("gB", 1, c))
            residual(0, "out", out_source)
            for v in range(2):
                split_lo(dve, 0, v)
            for n in range(4):
                c, t = divmod(n, TT)
                scale_in(("hf", c, t), hf[:, 4 * c:4 * c + 4, t * P:(t + 1) * P], 32 + 4 * c, 0)
            for n in range(4):
                c, t = divmod(n, TT)
                dve.wait_ge(h_hi, n + 1)
                part = hfS[:, :, 4 * c:4 * c + 4, t * P:(t + 1) * P]
                dve.tensor_tensor(part[:, 1, :, :], hf[:, 4 * c:4 * c + 4, t * P:(t + 1) * P], part[:, 0, :, :].bitcast(F32),
                                  ALU.subtract).then_inc(h_lo, 1)
            dve.sem_inc(hid_raw, 2)
            dve.sem_inc(hid_hi, 2)
            dve.sem_inc(hid_ready, 2)
            split_lo(dve, 0, 2)

            jobs.wait_filled(dve, "route")
            jobs.drain(dve.tensor_tensor(lg[:, :, :], jobs.out("route")[:, 0:40].rearrange("p (t n) -> p t n", t=2),
                                         bc(R("br").unsqueeze(1), [P, 2, 20]), ALU.add), "route")
            jobs.wait_drained(dve, "route")
            four = bc(K("four").unsqueeze(1), [P, 2, 4])

            def first_max(oh, v, vmax, scratch):
                chain(dve.tensor_reduce(vmax, v, AX_X, ALU.max))
                tt(oh, v, bc(vmax.unsqueeze(2), [P, 2, 4]), ALU.is_equal)
                tt(oh, oh, four, ALU.mult)
                chain(dve.tensor_reduce(scratch, oh, AX_X, ALU.max))
                tt(oh, oh, bc(scratch.unsqueeze(2), [P, 2, 4]), ALU.is_equal)

            first_max(goh[:, :, :], lg[:, :, 0:4], gm, r2a)
            tt(r8a[:, :, :], lg[:, :, 0:4], bc(gm.unsqueeze(2), [P, 2, 4]), ALU.subtract)
            el = lg[:, :, 4:20].rearrange("p t (g e) -> p t g e", g=4)
            for t in range(TT):
                order.up(dve.tensor_tensor(r32[:, t, :, :], el[:, t, :, :], bc(goh[:, t, :].unsqueeze(2), [P, 4, 4]), ALU.mult))
            order.here(dve)
            chain(dve.tensor_reduce(es[:, :, :], r32[:, :, :, :].rearrange("p t g e -> p t e g"), AX_X, ALU.add))
            chain(dve.tensor_reduce(r2b, es[:, :, :], AX_X, ALU.max))
            dve.tensor_tensor(es[:, :, :], es[:, :, :], bc(r2b.unsqueeze(2), [P, 2, 4]), ALU.subtract).then_inc(r_logits, 1)
            split_lo(dve, 0, 3)
            dve.wait_ge(r_exp, 2)
            chain(dve.tensor_reduce(gs, r8a[:, :, :], AX_X, ALU.add))
            chain(dve.reciprocal(gval, gs))
            chain(dve.tensor_reduce(r2a, es[:, :, :], AX_X, ALU.add))
            chain(dve.reciprocal(r2b, r2a))
            tt(pe_[:, :, :], es[:, :, :], bc(r2b.unsqueeze(2), [P, 2, 4]), ALU.mult)
            first_max(oh1[:, :, :], pe_[:, :, :], r2a, r2c)
            chain(dve.scalar_tensor_tensor(out=pm[:, :, :], in0=oh1[:, :, :], scalar=-2.0, in1=pe_[:, :, :], op0=ALU.mult, op1=ALU.add))
            first_max(oh2[:, :, :], pm[:, :, :], r2b, r2c)
            tt(r2c, r2a, r2b, ALU.add)
            chain(dve.reciprocal(r2c, r2c))
            tt(r2c, r2c, gval, ALU.mult)
            tt(wgt[:, :, :], oh1[:, :, :], oh2[:, :, :], ALU.add)
            tt(wgt[:, :, :], wgt[:, :, :], pe_[:, :, :], ALU.mult)
            tt(wgt[:, :, :], wgt[:, :, :], bc(r2c.unsqueeze(2), [P, 2, 4]), ALU.mult)
            for t in range(TT):
                ins = dve.tensor_tensor(comb[:, t, :].rearrange("p (g e) -> p g e", g=4), bc(goh[:, t, :].unsqueeze(2), [P, 4, 4]),
                                        bc(wgt[:, t, :].unsqueeze(1), [P, 4, 4]), ALU.mult)
                if t == 0:
                    chain(ins)
                else:
                    ins.then_inc(comb_ready, 1)

            def times_up(step, e):
                wait_expert(dve, step, "U", e, "filled")
                wait_expert(dve, step, "G", e, "drained")
                dve.tensor_tensor(gated[:, e % 2, :], gated[:, e % 2, :], expert_bank("U", e), ALU.mult).then_inc(drained[expert_regions(e)[1]], 1)

            def weight(step, e):
                wait_expert(dve, step, "U", e, "drained")
                dve.wait_ge(hid_ready, step * EXPERT_STEP + (e + 1))
                comb_e = combB[:, bass.ds(step * EXPERT_STEP + e, 1), :]
                dve.tensor_tensor(hid[:, e % 2, :].rearrange("p (b t) -> p b t", b=2), gated[:, e % 2, :].rearrange("p (b t) -> p b t", b=2),
                                  bc(comb_e, [P, 2, T]), ALU.mult).then_inc(hid_raw, 1)

            def hidden_lo(step, e):
                dve.wait_ge(hid_hi, step * EXPERT_STEP + (e + 3))
                dve.tensor_tensor(hidS[:, e % 2, 1, :], hid[:, e % 2, :], hidS[:, e % 2, 0, :].bitcast(F32), ALU.subtract).then_inc(hid_ready, 1)

            def last_two(step):
                split_lo(dve, step, 7)
                split_lo(dve, step, 8)
                times_up(step, 2)
                weight(step, 2)
                hidden_lo(step, 2)
                split_lo(dve, step, 9)
                split_lo(dve, step, 10)
                split_lo(dve, step, 11)
                times_up(step, 3)
                weight(step, 3)
                hidden_lo(step, 3)

            times_up(0, 0)
            split_lo(dve, 0, 4)
            split_lo(dve, 0, 5)
            times_up(0, 1)
            split_lo(dve, 0, 6)
            for i in range(8):
                jobs.wait_drained(dve, ("combB", i))
            for e in range(2):
                weight(0, e)
                hidden_lo(0, e)
            last_two(0)
            with dve.Fori(1, EXPERTS // EXPERT_STEP) as step:
                for n in range(4):
                    split_lo(dve, step, n)
                times_up(step, 0)
                weight(step, 0)
                hidden_lo(step, 0)
                split_lo(dve, step, 4)
                split_lo(dve, step, 5)
                times_up(step, 1)
                weight(step, 1)
                hidden_lo(step, 1)
                split_lo(dve, step, 6)
                last_two(step)
            dve.wait_ge(hid_used, EXPERTS + 2)

            def moe_source(t, c):
                def done(ins):
                    chain(ins)
                return (lambda: None), psum[:, (2 * t + c) * 512:(2 * t + c + 1) * 512], done

            residual(1, "moe", moe_source)

        @block.gpsimd
        def _(pool):
            order = Signal(g_order)

            def chain(ins):
                order.up(ins)
                order.here(pool)

            pool.wait_ge(params, 32)
            pool.wait_ge(mod_ready, 2)
            for s in range(2):
                for c in range(2):
                    for t in range(TT):
                        jobs.wait_drained(pool, ("in", s, c, t))
                        dst = hT[:, 4 * c:4 * c + 4, (2 * s + t) * P:(2 * s + t + 1) * P]
                        pool.tensor_tensor(dst, dst, bc(modT[:, 4 * c:4 * c + 4, 1 - s:2 - s], [P, 4, P]), ALU.add).then_inc(shifted, 1)

            def inv_roots(turn, dst, total, n, sig, eps=EPS, scratch=None):
                w = dst.shape[1]
                chain(pool.tensor_scalar(scratch[:, 0:w], total, 1.0 / n, eps, ALU.mult, ALU.add))
                pool.tensor_tensor(dst, scratch[:, 0:w], K("mhalf", 0, w), ALU.pow).then_inc(sig, 1)
                pool.wait_ge(sig, turn)

            pool.wait_ge(qk_sum, 1)
            inv_roots(1, krs, kss, DH, qk_std, scratch=ssq)
            for t in range(TT):
                pool.wait_ge(qk_sum, 2 + t)
                inv_roots(2 + t, qrs[:, t, :], qss[:, t, :], DH, qk_std, scratch=ssq)

            pool.wait_ge(dw_ready, 1)
            for n, (i, d) in enumerate(STATES):
                for half in range(2):
                    jobs.wait_drained(pool, ("xsT", i, half))
                if n >= 2:
                    for g in range(2):
                        jobs.wait_filled(pool, ("st", n - 2, g))
                pool.tensor_tensor(wx[:, n % 2, :].rearrange("p (h c) -> p h c", c=DH), xs[:, i, :].rearrange("p (h c) -> p h c", c=DH),
                                   bc(dw[:, i, 16 * d:16 * d + 16].unsqueeze(2), [P, 16, DH]), ALU.mult).then_inc(xw_ready, 1)
            for i in range(4):
                for half in range(2):
                    jobs.wait_filled(pool, ("xsT", i, half))
            for t in range(TT):
                for d in range(2):
                    pool.tensor_tensor(xdt[:, 2 * t + d, :].rearrange("p (h c) -> p h c", c=DH), xs[:, 2 + t, :].rearrange("p (h c) -> p h c", c=DH),
                                       bc(dt[:, 2 + t, 16 * d:16 * d + 16].unsqueeze(2), [P, 16, DH]), ALU.mult).then_inc(xdt_ready, 1)
                pool.tensor_tensor(y[:, t, :].rearrange("p (h c) -> p h c", c=DH), xs[:, 2 + t, :].rearrange("p (h c) -> p h c", c=DH),
                                   bc(R("skip").unsqueeze(2), [P, 16, DH]), ALU.mult).then_inc(skip_ready, 1)
            for t in range(TT):
                jobs.wait_drained(pool, ("cb", t))
            for n, (t, g, quad) in enumerate(UNITS):
                for d in range(2):
                    pool.wait_ge(aq_exp, 2 * n + d + 1)
                    m3 = m[:, (2 * n + d) % 4, :].rearrange("p (h q) -> p h q", h=4)
                    pool.tensor_tensor(m3, m3, bc(cb[:, t, d, g, :].unsqueeze(1), [P, 4, P]), ALU.mult).then_inc(m_ready, 1)
            for t in range(TT):
                pool.wait_ge(y_sq, 2 * t + 2)
                inv_roots(t + 1, yrs[:, 2 * t:2 * t + 2], yss[:, 2 * t:2 * t + 2], 512, y_std, scratch=ssq)

            def ln_roots(v):
                for t in range(TT):
                    pool.wait_ge(ln_stat, v * TT + t + 1)
                    chain(pool.tensor_scalar(lms[:, 0:1], mv[:, t, 1:2], 1.0, LN_EPS, ALU.mult, ALU.add))
                    pool.tensor_tensor(lstd[:, t:t + 1], lms[:, 0:1], K("mhalf", 0, 1), ALU.pow).then_inc(ln_std, 1)
                    pool.wait_ge(ln_std, v * TT + t + 1)

            ln_roots(0)
            for c in range(2):
                for t in range(TT):
                    jobs.wait_drained(pool, ("hf", c, t))
                    dst = hf[:, 4 * c:4 * c + 4, t * P:(t + 1) * P]
                    pool.tensor_tensor(dst, dst, bc(modT[:, 24 + 4 * c:28 + 4 * c, 0:1], [P, 4, P]), ALU.add).then_inc(shifted, 1)
            pool.memset(hid[:, :, :], 0.0).then_inc(zero_ready, 1)
            ln_roots(1)


MEM = dict(
    tm=(TT, D), hT=(KD, T), small=(192,), mrow=(2, 512), cols=(N_COLS,), rows=(N_ROWS,),
    kblk=(32,), hidv=(2, P), bglu=(4, T + TAPS - 1), cpad=(4, 16 + T),
)
MEM_MIX = dict(
    gates=(8192,), brT=(4, 4, T), qTs=(3, 4, T), proj=(TT, 2048), rkT=(3, T), sg=(2, 512),
    hidk=(2, 2, 16), vblk=(512,), sc=(2, 4, T), pt=(2, 2, 4, P),
    acc=(4, T), tmp=(2, 512), psum_a=(16 + T,), psum_b=(16 + T,), csc=(2, P), cpT=(2, P), hsum=(2, 2, 32),
)
MEM_FFN = dict(hq=(2, 1024), f32=(T,))
MEM_FFN_SPLIT = dict(split=(SPLITS, 2, CH), hfT=(2, KD, T), fT=(2, FB, T))


def build_program(nc, x_in, ctx_in, cond, weights, cols, rows, cols2, rows2, const, out):
    with ExitStack() as ctx:
        keep = dict(x=(TT, D), const=(N_CONST,), cond=(16 + MODS,), cvec=(16,), modT=(MODS, 2))
        mem = {k: ctx.enter_context(nc.sbuf_tensor(f"sb_{k}", [P, *s], F32)) for k, s in keep.items()}
        ring = ctx.enter_context(nc.sbuf_tensor("ring", [P, SLOTS, CH], F32))
        psum = ctx.enter_context(nc.psum_tensor("psum", [P, 4096], F32))
        landed = [ctx.enter_context(nc.semaphore(f"landed_{s}")) for s in range(SLOTS)]
        used = [ctx.enter_context(nc.semaphore(f"used_{s}")) for s in range(SLOTS)]
        loaded = ctx.enter_context(nc.semaphore("loaded"))
        zeroed = ctx.enter_context(nc.semaphore("zeroed"))

        with ExitStack() as first:
            mem1 = {**mem, **{k: first.enter_context(nc.sbuf_tensor(f"sb_{k}", [P, *s], F32)) for k, s in MEM.items()}}
            with ExitStack() as phase:
                for k, s in MEM_MIX.items():
                    mem1[k] = phase.enter_context(nc.sbuf_tensor(f"sb_{k}", [P, *s], F32))
            for fields, dtype in ((MEM_FFN_SPLIT, F32R), (MEM_FFN, F32)):
                for k, s in fields.items():
                    mem1[k] = first.enter_context(nc.sbuf_tensor(f"sb_{k}", [P, *s], dtype))

            with nc.Block() as block:
                @block.sync
                def _(sp):
                    sp.dma_start(mem["cond"][:, :], cond).then_inc(loaded, 16)
                    sp.dma_start(mem["x"][:, :, :], x_in.rearrange("(t p) d -> p t d", p=P)).then_inc(loaded, 16)
                    sp.dma_start(mem["const"][:, :], const).then_inc(loaded, 16)
                    for s in range(SLOTS):
                        sp.dma_start(ring[:, s, :], weights[s]).then_inc(landed[s], 16)

                @block.scalar
                def _(act):
                    act.wait_ge(loaded, 48)
                    act.activation(mem["cvec"][:, :], mem["cond"][:, 0:16], ACT.Silu).then_inc(zeroed, 1)

                @block.gpsimd
                def _(pool):
                    pool.memset(mem1["hidv"][:, :, :], 0.0).then_inc(zeroed, 1)
                    pool.memset(mem1["kblk"][:, :], 0.0).then_inc(zeroed, 1)
                    pool.memset(mem1["bglu"][:, :, 0:TAPS - 1], 0.0).then_inc(zeroed, 1)
                    pool.memset(mem1["cpad"][:, :, 0:16], 0.0).then_inc(zeroed, 1)
                    pool.wait_ge(zeroed, 5)

            layer_sems = []

            def sems(name):
                s = first.enter_context(nc.semaphore(name))
                layer_sems.append(s)
                return s

            with nc.Fori(0, LAYERS) as l:
                layer_block(nc, l, mem1, ring, landed, used, weights, psum, sems, cols, rows, loaded)
                nums = [s.num for s in layer_sems]
                assert nums == list(range(nums[0], nums[-1] + 1))
                nc.all_engine_barrier(sems_to_clear=range(nums[0], nums[-1] + 1))

        with ExitStack() as second:
            mem2 = {**mem, **{k: second.enter_context(nc.sbuf_tensor(f"sb2_{k}", [P, *s], F32)) for k, s in MEM2.items()}}
            with ExitStack() as phase:
                for k, s in MEM2_MIX.items():
                    mem2[k] = phase.enter_context(nc.sbuf_tensor(f"sb2_{k}", [P, *s], F32))
            for fields, dtype in ((MEM2_MOE_SPLIT, F32R), (MEM2_MOE, F32)):
                for k, s in fields.items():
                    mem2[k] = second.enter_context(nc.sbuf_tensor(f"sb2_{k}", [P, *s], dtype))

            def sems2(name):
                return second.enter_context(nc.semaphore(name))

            block2(nc, mem2, ring, landed, used, weights, psum, sems2, cols2, rows2, ctx_in, out)


HEADS_IN_PAIRS = [4 * g + j for j in range(4) for g in range(2)]


def pairs(a, width, axis=-1):
    idx = np.concatenate([np.arange(h * width, (h + 1) * width) for h in HEADS_IN_PAIRS])
    return np.take(a, idx, axis=axis)


def to_cols(v):
    return v.reshape(-1, P).T


def k_split(w):
    return w.reshape(2, 4, P, 512).transpose(0, 2, 1, 3).reshape(2, P, CH)


def n_split(w):
    return w.reshape(KD, P, -1, 256).transpose(2, 1, 0, 3).reshape(-1, P, CH)


def rows_split(w):
    return w.reshape(-1, 2, P, D).transpose(0, 2, 1, 3).reshape(-1, P, CH)


def layer_inputs(l, i):
    mod = [k_split(i["w_mod_2"][0][:, (l * MOD_STEPS + j) * 512:(l * MOD_STEPS + j + 1) * 512]) for j in range(MOD_STEPS)]
    w = i["w_in"][l]
    kv = w[:, 512:1280]
    gate_val = i["ffn_w_up"][l].reshape(D, 2, FB, P).transpose(0, 2, 1, 3).reshape(D, 2 * DFF)
    br = i["w_branch"][l]
    br = {0: pairs(br[0], DH, 0), 1: br[1], 2: br[2], 3: pairs(br[3], DH, 0)}
    chunks = [
        *(mod[j] for j in EARLY_MODS), k_split(kv[:, 0:512]), k_split(np.concatenate([kv[:, 512:768], w[:, 1816:2072]], 1)),
        k_split(pairs(w[:, 0:512], DH)), k_split(pairs(w[:, 1304:1816], DH)),
        n_split(w[:, 3096:3608]), n_split(w[:, 2072:2584]),
        i["nsa_cmp_w1"][l].reshape(2, 2, 8, P, 256).transpose(0, 1, 3, 2, 4).reshape(4, P, CH),
        n_split(w[:, 2584:3096]),
        n_split(i["w_gate"][l]),
        *[br[n].reshape(4, P, 2, 512).transpose(2, 1, 0, 3).reshape(2, P, CH) for n in BRANCH_ORDER],
        k_split(i["w_o"][l][:, 0:512]), k_split(i["w_o"][l][:, 512:1024]), *(mod[j] for j in LATE_MODS),
        n_split(gate_val), rows_split(i["ffn_w_down"][l]), np.zeros((1, P, CH), np.float32),
    ]
    pos = i["nsa_cmp_pos"][l].reshape(2, 16, 2, DH).transpose(2, 3, 0, 1).reshape(P, 32)
    w2 = i["nsa_cmp_w2"][l].reshape(2, 2, P, DH).transpose(2, 0, 1, 3).reshape(P, 256)
    fields = dict(
        g_mix=to_cols(i["norm_mix_pre"][l]), g_ffn=to_cols(i["norm_ffn_pre"][l]), pos=pos, w2=w2,
        conv_w=i["conv_w"][l].reshape(TAPS, 4, P).transpose(2, 1, 0), conv_b=to_cols(i["conv_b"][l]),
        ln_g=to_cols(i["conv_ln_g"][l]), ln_b=to_cols(i["conv_ln_b"][l]),
        pool_w=i["pool_w"][l].transpose(1, 0, 2), pool_s=to_cols(i["pool_scale"][l]),
        fw=i["ffn_conv_w"][l].reshape(3, 2, FB, P).transpose(3, 2, 1, 0),
        fb=i["ffn_conv_b"][l].reshape(2, FB, P).transpose(2, 1, 0),
        w_ga=w[:, 1280:1304].reshape(KD, P, 3, 2, 4).transpose(1, 0, 2, 4, 3),
    )
    packed = np.concatenate([fields[name].reshape(P, width) for name, (_, width) in COLS.items()], 1)
    row = np.concatenate([i["norm_mix_post"][l], i["norm_ffn_post"][l], pairs(i["swa_sinks"][l], 1)])
    return np.concatenate(chunks), packed, row[None, :]


def block2_inputs(i):
    pick = lambda a, idx, axis=-1: np.take(a, np.concatenate([np.atleast_1d(v) for v in idx]), axis=axis)
    inner = np.concatenate([np.arange(0, DH, 2), np.arange(1, DH, 2)])
    w = i["w_in_2"][0]
    k_cols = [3616 + h * DH + inner for h in range(4)]
    q_heads = [4 * (2 * (b // 4) + g) + b % 4 for b in range(8) for g in range(2)]
    q_cols = [1024 + h * DH + inner for h in q_heads]
    wo = i["w_out_2"][0]
    o_rows = [np.arange(1024)] + [1024 + h * DH + np.arange(DH) for h in q_heads]
    q = pick(w, q_cols)
    chunks = [k_split(np.concatenate([pick(w, k_cols), w[:, 3872:4128]], 1)), n_split(w[:, 2048:3584]),
              k_split(q[:, 0:512]), k_split(q[:, 512:1024]), k_split(w[:, 0:512]), k_split(w[:, 512:1024]),
              rows_split(pick(wo, o_rows, 0))]
    for e0 in range(0, EXPERTS, EXPERT_STEP):
        gu = [[n_split(i[k][0, e]) for k in ("w_gate_2", "w_up_2")] for e in range(e0, e0 + EXPERT_STEP)]
        down = [rows_split(i["w_down_2"][0, e]) for e in range(e0, e0 + EXPERT_STEP)]
        chunks += [*gu[0], *gu[1], down[0], *gu[2], down[1], *gu[3], down[2], down[3]]
    k_pack = lambda a: a.reshape(KD, P, -1).transpose(1, 0, 2)
    fields = dict(
        conv_w=i["conv_w_2"][0].reshape(5, DX, P).transpose(2, 1, 0), conv_b=to_cols(i["conv_b_2"][0]),
        ssd_g=to_cols(i["ssd_norm_g_2"][0]),
        w_dt=k_pack(w[:, 3584:3616]), w_r=k_pack(np.concatenate([i["w_rg_2"][0], i["w_re_2"][0]], 1)),
    )
    packed = np.concatenate([fields[name].reshape(P, width) for name, (_, width) in COLS2.items()], 1)
    row = np.concatenate([i["ln1_g_2"][0], i["ln1_b_2"][0], i["ln2_g_2"][0], i["ln2_b_2"][0], i["dt_bias_2"][0].reshape(-1),
                          i["a_log_2"][0].reshape(-1), i["q_norm_g_2"][0][inner], i["k_norm_g_2"][0][inner],
                          i["b_rg_2"][0], i["b_re_2"][0], i["d_skip_2"][0]])
    return np.concatenate(chunks), packed, row[None, :]


def lay_out(i):
    layers = [layer_inputs(l, i) for l in range(LAYERS)]
    chunks2, packed2, row2 = block2_inputs(i)
    return dict(
        cond=np.concatenate([np.stack([to_cols(i["c_2"][0]), to_cols(i["c_ctx_2"])], -1).reshape(P, 16), to_cols(i["b_mod_2"][0])], 1),
        x_in=i["x"][0], ctx_in=i["ctx_2"][0], weights=np.concatenate([layers[0][0], layers[1][0], chunks2]),
        cols=np.stack([v[1] for v in layers]), rows=np.stack([v[2] for v in layers]), cols2=packed2, rows2=row2, const=constants(),
    )


def kernel(**inputs):
    import concourse.bacc as bacc
    from concourse.bass_utils import run_bass_kernel_spmd

    arrays = {k: np.ascontiguousarray(v) for k, v in lay_out({k: np.asarray(v) for k, v in inputs.items()}).items()}
    nc = bacc.Bacc("TRN2", target_bir_lowering=False, num_devices=1)
    args = {k: nc.dram_tensor(k, v.shape, F32, kind="ExternalInput").ap() for k, v in arrays.items()}
    out = nc.dram_tensor("out", (T, D), F32, kind="ExternalOutput").ap()
    build_program(nc, out=out, **args)
    result = run_bass_kernel_spmd(nc, [arrays], core_ids=[0])
    return result.results[0]["out"].reshape(1, T, D)
```

```python
from contextlib import ExitStack

import numpy as np

import concourse.bass as bass
import concourse.mybir as mybir

F32 = mybir.dt.float32
F32R = mybir.dt.float32r
ALU = mybir.AluOpType
ACT = mybir.ActivationFunctionType
AX_X = mybir.AxisListType.X

P = 128
T = 256
TT = T // P
D = 1024
KD = D // P
LAYERS = 2
DH = 64
BR = 512
NEG = -1e30
EPS = 1e-6
SLOTS = 4
CH = 2048
DFF = 2816
FB = DFF // P
TAPS = 31
CMP_N = 15
N_LAYER_CHUNKS = 92
SPLITS = 3
FFN_CHUNKS = FB + FB // 2
MODS = 6 * KD
MOD_STEPS = MODS // (4 * LAYERS)


def offsets(fields):
    at, out = 0, {}
    for name, width in fields:
        out[name] = (at, width)
        at += width
    return out, at


COLS, N_COLS = offsets([
    ("g_mix", KD), ("g_ffn", KD), ("pos", 32), ("w2", 256), ("conv_w", 4 * TAPS), ("conv_b", 4),
    ("ln_g", 4), ("ln_b", 4), ("pool_w", 512), ("pool_s", 4), ("fw", 2 * FB * 3), ("fb", 2 * FB),
    ("w_ga", KD * 24),
])
ROWS, N_ROWS = offsets([("mix_post", D), ("ffn_post", D), ("sinks", 8)])
CONST, N_CONST = offsets([
    ("ident", P), ("tri_u", P), ("tri_l", P), ("ones", P), ("full_causal", 2 * P), ("band", 2 * P),
    ("cmp_mask", 32), ("cmp_valid", 2), ("blk8", 8), ("rope", 192), ("axial", 192),
    ("pool_inv", 64), ("mhalf", 32), ("four", 4),
])


def constants():
    c = np.zeros((P, N_CONST), np.float32)

    def put(name, value):
        at, width = CONST[name]
        c[:, at:at + width] = np.asarray(value, np.float32).reshape(P, width)

    q = np.arange(P)
    later = q[:, None] >= q[None, :]
    causal = np.where(later, 0.0, NEG)
    put("ident", np.eye(P))
    put("tri_u", q[:, None] <= q[None, :])
    put("tri_l", later)
    put("ones", np.ones((P, P)))
    put("full_causal", np.concatenate([np.zeros((P, P)), causal], 1))
    put("band", np.concatenate([np.where(q[None, :] > q[:, None], 0.0, NEG), causal], 1))
    t = q[:, None] + P * np.arange(TT)[None, :]
    end = np.where(np.arange(16) < CMP_N, np.arange(16) * 16 + 31, 10 ** 9)
    put("cmp_mask", np.where(end[None, None, :] <= t[:, :, None], 0.0, NEG))
    put("cmp_valid", t >= 31)
    put("blk8", q[:, None] // 16 == np.arange(8)[None, :])
    inv = 1.0 / (10000.0 ** (np.arange(0, 64, 2, dtype=np.float32) / 64))
    ang = t[:, :, None].astype(np.float32) * inv.astype(np.float32)
    put("rope", np.stack([np.cos(ang), np.sin(ang), -np.sin(ang)], 1))
    inv = np.power(np.float32(10000.0), -np.arange(0, 32, 2, dtype=np.float32) / 32)
    ang = np.concatenate([(t // 64)[:, :, None] * inv, (t % 64)[:, :, None] * inv], -1).astype(np.float32)
    put("axial", np.stack([np.cos(ang), np.sin(ang), -np.sin(ang)], 1))
    put("pool_inv", np.broadcast_to(
        [[1.0 / min(w, i + 1) for i in range(16)] for w in (2, 4, 8, 16)], (P, 4, 16)))
    put("mhalf", np.full((P, 32), -0.5))
    put("four", np.broadcast_to([4.0, 3.0, 2.0, 1.0], (P, 4)))
    return c


REGION = {**{f"a{i}": (i * 512, 512) for i in range(4)}, "s": (2048, 1024), "t": (3072, 512), "u": (3584, 512)}


class Jobs:

    def __init__(self, psum, filled, drained, region=REGION, ring=4):
        self.psum, self.filled, self.drained, self.region, self.ring = psum, filled, drained, region, ring
        self.jobs, self.turn, self.sum, self.next = {}, {}, {}, 0

    def plan(self, name, region=None, drains=1):
        if region is None:
            region, self.next = f"a{self.next % self.ring}", self.next + 1
        before, turn = self.sum.get(region, 0), self.turn.get(region, 0)
        self.jobs[name] = (region, turn + 1, before, before + drains)
        self.turn[region], self.sum[region] = turn + 1, before + drains

    def out(self, name):
        at, width = self.region[self.jobs[name][0]]
        return self.psum[:, at:at + width]

    def claim(self, pe, name):
        region, _, before, _ = self.jobs[name]
        if before:
            pe.wait_ge(self.drained[region], before)

    def fill(self, ins, name):
        ins.then_inc(self.filled[self.jobs[name][0]], 1)

    def wait_filled(self, eng, name):
        region, turn, _, _ = self.jobs[name]
        eng.wait_ge(self.filled[region], turn)

    def drain(self, ins, name):
        ins.then_inc(self.drained[self.jobs[name][0]], 1)

    def wait_drained(self, eng, name):
        region, _, _, after = self.jobs[name]
        eng.wait_ge(self.drained[region], after)


class Signal:

    def __init__(self, sem):
        self.sem, self.n = sem, 0

    def up(self, ins):
        self.n += 1
        ins.then_inc(self.sem, 1)

    def here(self, eng, less=0):
        if self.n - less > 0:
            eng.wait_ge(self.sem, self.n - less)


def bc(ap, shape):
    return ap.to_broadcast(shape)


ATT = [("slc", 0, 0, 384), ("win", 0, 1, 640), ("swa", 1, 2, 896)]
ITEMS = [(a, t, g) for t in range(TT) for a in range(3) for g in range(2)]


def plan_mods(jobs, steps):
    for i in steps:
        jobs.plan(("mod", i))
        if i - 1 in steps:
            jobs.plan(("modT", i - 1))


EARLY_MODS, LATE_MODS, END_MODS = range(0, 2), range(2, 5), range(5, MOD_STEPS)


def plan_layer(jobs):
    plan_mods(jobs, EARLY_MODS)
    for c in range(2):
        for t in range(TT):
            jobs.plan(("ht", c, t))
    jobs.plan(("modT", EARLY_MODS[-1]))
    for w in ("kv", "kv2", "q", "dq"):
        for t in range(TT):
            jobs.plan((w, t))
    jobs.plan("ga")
    for t in range(TT):
        jobs.plan(("cd", t))
    for i in range(2):
        jobs.plan(("c", i))
    for t in range(TT):
        jobs.plan(("qT", t))
        jobs.plan(("rkT", t))
    for i in range(2):
        jobs.plan(("ba", i))
    for kv in range(2):
        jobs.plan(("hid", kv))
    jobs.plan(("bg", 0))
    for kv in range(2):
        jobs.plan(("hidT", kv), drains=2)
    jobs.plan(("bg", 1))
    jobs.plan("kc", drains=2)
    jobs.plan("vc")
    for t in range(TT):
        jobs.plan(("rqT", t))
        jobs.plan(("rdT", t))
    for i in range(2):
        jobs.plan(("pool", i), drains=4)
    for t in range(TT):
        jobs.plan(("cs", t))
    for t in range(TT):
        jobs.plan(("cpT", t), "t")
    for a, t, g in ITEMS:
        jobs.plan(("S", a, t, g), "s")
        for kb in range(t + 1):
            jobs.plan(("PT", a, t, g, kb), "t")
        if g == 1 and a >= 1:
            jobs.plan(("O", a, t), "u", drains=2)
    for i in range(16):
        jobs.plan(("gate", i))
    for t in range(TT):
        jobs.plan(("convT", t))
    for n in BRANCH_ORDER:
        for i in range(4):
            if (n, i) == (3, 2):
                for t in range(TT):
                    jobs.plan(("obT", t), drains=4)
            jobs.plan(("up", n, i))
    for c in range(2):
        for t in range(TT):
            jobs.plan(("wo", c, t), drains=2)
    plan_mods(jobs, LATE_MODS)
    for c in range(2):
        for t in range(TT):
            jobs.plan(("hf", c, t))
    jobs.plan(("modT", LATE_MODS[-1]))
    for j in range(FB):
        jobs.plan(("ffn", j))
    for t in range(TT):
        for c in range(2):
            jobs.plan(("down", c, t), f"a{2 * t + c}", drains=2)
    for i in END_MODS:
        jobs.plan(("mod", i), "t")
        jobs.plan(("modT", i), "u")


BRANCH_ORDER = (2, 0, 3, 1)


def layer_block(nc, l, mem, ring, landed, used, wts, psum, sems, cols_dram, rows_dram, loaded):
    filled = {r: sems(f"filled_{r}") for r in REGION}
    drained = {r: sems(f"drained_{r}") for r in REGION}
    jobs = Jobs(psum, filled, drained)
    plan_layer(jobs)

    squares = sems("squares")
    rstd_ready = sems("rstd_ready")
    normed = sems("normed")
    kd_ready = sems("kd_ready")
    roped = sems("roped")
    flat_ready = sems("flat_ready")
    conv_done = sems("conv_done")
    stat_ready = sems("stat_ready")
    lnstd_ready = sems("lnstd_ready")
    pooled = sems("pooled")
    cmp_s = sems("cmp_s")
    cmp_e = sems("cmp_e")
    cmp_p = sems("cmp_p")
    weighed = sems("weighed")
    masked = sems("masked")
    exped = sems("exped")
    tail_sent = sems("tail_sent")
    gates_ready = sems("gates_ready")
    mixed = sems("mixed")
    ob_hi, ob_lo = sems("ob_hi"), sems("ob_lo")
    mix_hi, mix_lo = sems("mix_hi"), sems("mix_lo")
    hi_ready = sems("hi_ready")
    lo_ready = sems("lo_ready")
    scaled, h_hi, h_lo = sems("scaled"), sems("h_hi"), sems("h_lo")
    f_part = sems("f_part")
    ffn_init = sems("ffn_init")
    gelued = sems("gelued")
    f_ready = sems("f_ready")
    x_ready = sems("x_ready")
    params = sems("params")
    v_order, a_order, g_order = sems("v_order"), sems("a_order"), sems("g_order")

    x, tm, hT, proj, gates, qTs, rkT = (mem[k] for k in ("x", "tm", "hT", "proj", "gates", "qTs", "rkT"))
    kd = gates[:, 0:1024].rearrange("p (t m r d) -> p t m r d", t=2, m=4, r=2)
    flat = gates[:, 0:960].rearrange("p (v l g n) -> p v l g n", v=2, g=2, n=CMP_N)
    cdT = gates[:, 2048:3072].rearrange("p (m t) -> p m t", m=4)
    rtmp = gates[:, 3072:4480]
    rot = gates[:, 4480:7296].rearrange("p (t c) -> p t c", t=2)
    hfT, fT, split, f32 = (mem[k] for k in ("hfT", "fT", "split", "f32"))
    hf32 = mem["hq"][:, :, 0:512]
    hq = [mem["hq"][:, 0, :], mem["hq"][:, 1, :]]
    hidk, hidv, kblk, vblk = mem["hidk"], mem["hidv"], mem["kblk"], mem["vblk"]
    sc, pt = mem["sc"], mem["pt"]
    pt_flat = pt[:, :, :, :, :].rearrange("p b k j q -> p (b k j q)")
    ln_tm = pt_flat[:, 0:1024].rearrange("p (t c) -> p t c", t=2)
    bufs = [pt_flat[:, 0:16 + T], pt_flat[:, 512:512 + 16 + T]]
    hsum = pt_flat[:, 1024:1024 + 2 * T].rearrange("p (v t) -> p v t", v=2)
    sg = sc[:, :, :, :].rearrange("p b j k -> p (b j k)")[:, 0:1024].rearrange("p (i c) -> p i c", i=2)
    pooled_in = mem["tmp"][:, :, :].rearrange("p i c -> p (i c)").rearrange("p (g t) -> p g t", g=4)
    small = mem["small"]
    mixT, bglu, cpad, acc, tmp, mixS, split2 = (mem[k] for k in ("hT", "bglu", "cpad", "acc", "tmp", "mixS", "split2"))
    brS = {n: mem["brS"][:, :, i, :, :] for i, n in enumerate((0, 2, 3))}
    brS[1] = mem["br1"]
    cols, rows, const = mem["cols"], mem["rows"], mem["const"]

    def K(name, a=0, b=None):
        at, width = CONST[name]
        return const[:, at + a:at + (width if b is None else b)]

    def C(name, a=0, b=None):
        at, width = COLS[name]
        return cols[:, at + a:at + (width if b is None else b)]

    def R(name):
        at, width = ROWS[name]
        return rows[:, at:at + width]

    ident = K("ident")
    ga = small[:, 0:48].rearrange("p (t b h) -> p t b h", t=2, b=3)
    ss, rstd = small[:, 48:52], small[:, 52:56]
    ss4 = small[:, 56:60].rearrange("p (t c) -> p t c", t=2)
    nmax = small[:, 64:72]
    den, coef = small[:, 72:80].rearrange("p (b j) -> p b j", b=2), small[:, 88:96].rearrange("p (b j) -> p b j", b=2)
    stats, mv, lnstd = small[:, 104:116].rearrange("p (t s) -> p t s", t=2), small[:, 116:120].rearrange("p (t s) -> p t s", t=2), small[:, 120:122]
    cden = small[:, 128:144].rearrange("p (t h) -> p t h", t=2)
    cmax = small[:, 144:160].rearrange("p (t h) -> p t h", t=2)
    ccoef = small[:, 160:176].rearrange("p (t h) -> p t h", t=2)
    sinkv = small[:, 192:200].rearrange("p (b j) -> p b j", b=2)
    msq = small[:, 184:188]
    csc = mem["csc"]

    n_up = 12
    first_ffn = N_LAYER_CHUNKS - 1 - 2 * len(END_MODS) - FFN_CHUNKS
    first_up = first_ffn - 2 * len(LATE_MODS) - n_up

    def split_slot(n):
        if n < n_up:
            return first_up + n, split2[:, n % 2, :, :], 2
        return first_ffn + n - n_up, split[:, (n - n_up) % SPLITS, :, :], SPLITS

    def split_hi(act, n):
        c, slot, turns = split_slot(n)
        if turns <= n < n_up or n >= n_up + turns:
            act.wait_ge(used[(c - turns) % SLOTS], l * (N_LAYER_CHUNKS // SLOTS) + ((c - turns) // SLOTS + 1))
        act.wait_ge(landed[c % SLOTS], (l * (N_LAYER_CHUNKS // SLOTS) + (c // SLOTS + 1)) * 16)
        act.activation(slot[:, 0, :], ring[:, c % SLOTS, :], ACT.Copy).then_inc(hi_ready, 1)

    def split_lo(dve, n):
        c, slot, _ = split_slot(n)
        dve.wait_ge(hi_ready, n + 1)
        dve.tensor_tensor(slot[:, 1, :], ring[:, c % SLOTS, :], slot[:, 0, :].bitcast(F32), ALU.subtract).then_inc(lo_ready, 1)

    with nc.Block() as block:
        @block.sync
        def _(sp):
            with sp.Fori(0, N_LAYER_CHUNKS // SLOTS) as turn:
                for s in range(SLOTS):
                    sp.wait_ge(used[s], l * (N_LAYER_CHUNKS // SLOTS) + turn + 1)
                    sp.dma_start(ring[:, s, :], wts[l * N_LAYER_CHUNKS + turn * SLOTS + (s + SLOTS)]).then_inc(landed[s], 16)

        @block.tensor
        def _(pe):
            state = {"chunk": 0, "owed": None}

            def next_chunk():
                c = state["chunk"]
                state["chunk"] += 1
                pe.wait_ge(landed[c % SLOTS], (l * (N_LAYER_CHUNKS // SLOTS) + (c // SLOTS + 1)) * 16)
                return ring[:, c % SLOTS, :]

            def done_with(ins):
                ins.then_inc(used[(state["chunk"] - 1) % SLOTS], 1)

            def carry(ins):
                if state["owed"] is not None:
                    ins.then_inc(used[state["owed"]], 1)
                    state["owed"] = None

            def release(name):
                assert state["owed"] is None
                state["owed"] = (state["chunk"] - 1) % SLOTS

            def transpose4(name, blocks):
                jobs.claim(pe, name)
                out = jobs.out(name)
                for i, b in enumerate(blocks):
                    n = b.shape[1]
                    mm = pe.transpose(out[0:n, i * P:(i + 1) * P], b, ident)
                    if i == 0 and len(blocks) > 1:
                        carry(mm)
                jobs.fill(mm, name)

            def mod(i):
                name = ("mod", i)
                jobs.claim(pe, name)
                for half in range(2):
                    chunk = next_chunk().rearrange("p (k n) -> p k n", k=4)
                    for k in range(4):
                        mm = pe.matmul(jobs.out(name)[0:2, :], mem["cvec"][:, 2 * (4 * half + k):2 * (4 * half + k) + 2], chunk[:, k, :],
                                       start=(half == 0 and k == 0), stop=(half == 1 and k == 3))
                        if k == 0:
                            carry(mm)
                    if half == 0:
                        done_with(mm)
                jobs.fill(mm, name)
                release(name)

            def mod_turn(i):
                jobs.wait_drained(pe, ("mod", i))
                if i == 0:
                    pe.wait_ge(loaded, 32)
                jobs.claim(pe, ("modT", i))
                for b in range(4):
                    mm = pe.matmul(jobs.out(("modT", i))[:, 2 * b:2 * b + 2], mem["mrow"][0:2, i % 2, b * P:(b + 1) * P], ident[0:2, 0:2],
                                   start=True, stop=True)
                    if b == 0:
                        carry(mm)
                jobs.fill(mm, ("modT", i))

            def mods(steps):
                for i in steps:
                    mod(i)
                    if i - 1 in steps:
                        mod_turn(i - 1)

            mods(EARLY_MODS)
            pe.wait_ge(loaded, 32)
            for c in range(2):
                for t in range(TT):
                    pe.wait_ge(normed, t + 1)
                    transpose4(("ht", c, t), [tm[:, t, (4 * c + i) * P:(4 * c + i + 1) * P] for i in range(4)])
            mod_turn(EARLY_MODS[-1])

            for w in ("kv", "kv2", "q", "dq"):
                for half in range(2):
                    chunk = next_chunk().rearrange("p (k n) -> p k n", k=4)
                    for t in range(TT):
                        if w == "kv":
                            jobs.wait_drained(pe, ("ht", half, t))
                        if half == 0:
                            jobs.claim(pe, (w, t))
                        for k in range(4):
                            mm = pe.matmul(jobs.out((w, t)), hT[:, 4 * half + k, t * P:(t + 1) * P], chunk[:, k, :],
                                           start=(half == 0 and k == 0), stop=(half == 1 and k == 3))
                            if k == 0:
                                carry(mm)
                        if half == 1 and t == 0:
                            jobs.fill(mm, (w, t))
                    if half == 0:
                        done_with(mm)
                    else:
                        jobs.fill(mm, (w, 1))
                        release(w)

            jobs.claim(pe, "ga")
            for t in range(TT):
                for k in range(KD):
                    mm = pe.matmul(jobs.out("ga")[:, 24 * t:24 * t + 24], hT[:, k, t * P:(t + 1) * P],
                                   C("w_ga", 24 * k, 24 * k + 24), start=(k == 0), stop=(k == KD - 1))
                    if k == 0:
                        carry(mm)
            jobs.fill(mm, "ga")

            def blocks_fm(name):
                chunk = next_chunk().rearrange("p (k m) -> p k m", k=KD)
                jobs.claim(pe, name)
                for b in range(2):
                    for k in range(KD):
                        mm = pe.matmul(jobs.out(name)[:, b * T:(b + 1) * T], chunk[:, k, b * P:(b + 1) * P], hT[:, k, :],
                                       start=(k == 0), stop=(k == KD - 1))
                        if k == 0:
                            carry(mm)
                jobs.fill(mm, name)
                return name


            for t in range(TT):
                pe.wait_ge(kd_ready, t + 1)
                transpose4(("cd", t), [kd[:, t, m, :, :].rearrange("p r d -> p (r d)") for m in range(4)])
            for i in range(2):
                release(blocks_fm(("c", i)))
            for t in range(TT):
                jobs.wait_drained(pe, ("q", t))
                transpose4(("qT", t), [proj[:, t, 1024 + i * P:1024 + (i + 1) * P] for i in range(4)])
                pe.wait_ge(roped, 3 * t + 1)
                transpose4(("rkT", t), [rot[:, t, i * P:(i + 1) * P] for i in range(3)])
            for i in range(2):
                release(blocks_fm(("ba", i)))

            for kv in range(2):
                for half in range(2):
                    chunk = next_chunk().rearrange("p (l h) -> p l h", l=8)
                    if half == 0:
                        jobs.claim(pe, ("hid", kv))
                        pe.wait_ge(flat_ready, 4 * kv + 4)
                    for lp in range(8):
                        mm = pe.matmul(jobs.out(("hid", kv))[0:2 * CMP_N, 0:T], flat[:, kv, 8 * half + lp, :, :].rearrange("p g n -> p (g n)"),
                                       chunk[:, lp, :], start=(half == 0 and lp == 0), stop=(half == 1 and lp == 7))
                        if lp == 0:
                            carry(mm)
                    if half == 0:
                        done_with(mm)
                jobs.fill(mm, ("hid", kv))
                release(("hid", kv))
            release(blocks_fm(("bg", 0)))
            for kv in range(2):
                jobs.wait_drained(pe, ("hid", kv))
                jobs.claim(pe, ("hidT", kv))
                for ht in range(2):
                    mm = pe.matmul(jobs.out(("hidT", kv))[:, 32 * ht:32 * ht + 2 * CMP_N], hsum[0:2 * CMP_N, kv, ht * P:(ht + 1) * P],
                                   ident[0:2 * CMP_N, 0:2 * CMP_N], start=True, stop=True)
                    if ht == 0:
                        carry(mm)
                jobs.fill(mm, ("hidT", kv))
            release(blocks_fm(("bg", 1)))

            jobs.wait_drained(pe, ("hidT", 0))
            jobs.claim(pe, "kc")
            for g in range(2):
                for ht in range(2):
                    mm = pe.matmul(jobs.out("kc")[64 * g:64 * g + 64, 0:CMP_N], C("w2", 64 * ht, 64 * ht + 64),
                                   hidk[:, ht, g, 0:CMP_N], start=(ht == 0), stop=(ht == 1))
            jobs.fill(mm, "kc")
            jobs.wait_drained(pe, ("hidT", 1))
            jobs.claim(pe, "vc")
            for ht in range(2):
                mm = pe.matmul(jobs.out("vc")[:, 0:DH], hidv[:, ht, :], C("w2", 128 + 64 * ht, 128 + 64 * ht + 64),
                               start=(ht == 0), stop=(ht == 1))
            jobs.fill(mm, "vc")
            for t in range(TT):
                pe.wait_ge(roped, 3 * t + 2)
                transpose4(("rqT", t), [rot[:, t, 384 + i * P:384 + (i + 1) * P] for i in range(4)])
                pe.wait_ge(roped, 3 * t + 3)
                transpose4(("rdT", t), [rot[:, t, 896 + i * P:896 + (i + 1) * P] for i in range(4)])
            for i in range(2):
                jobs.claim(pe, ("pool", i))
                pe.wait_ge(pooled, 2 * i + 2)
                for b in range(2):
                    mm = pe.matmul(jobs.out(("pool", i))[:, b * T:(b + 1) * T], C("pool_w", (2 * i + b) * P, (2 * i + b + 1) * P),
                                   pooled_in[:, 2 * i + b, :], start=True, stop=True)
                jobs.fill(mm, ("pool", i))

            jobs.wait_drained(pe, "kc")
            for t in range(TT):
                jobs.wait_drained(pe, ("qT", t))
                jobs.claim(pe, ("cs", t))
                for j in range(4):
                    mm = pe.matmul(jobs.out(("cs", t))[:, 32 * j:32 * j + 32], qTs[:, 0, j, t * P:(t + 1) * P],
                                   kblk[:, :], start=True, stop=True)
                jobs.fill(mm, ("cs", t))

            gate_at = {"n": 0}

            def gate_chunks(n):
                for _ in range(n):
                    if gate_at["n"] < 16:
                        release(blocks_fm(("gate", gate_at["n"])))
                        gate_at["n"] += 1

            def cmp_out():
                for t in range(TT):
                    pe.wait_ge(cmp_p, t + 1)
                    transpose4(("cpT", t), [csc[:, t, :]])
                gate_chunks(1)

            def scores(i):
                a, t, g = ITEMS[i]
                _, rq, rk, _ = ATT[a]
                name = ("S", a, t, g)
                if g == 0:
                    jobs.wait_drained(pe, ("rkT", t))
                    jobs.wait_drained(pe, (("rqT", "rdT")[rq], t))
                jobs.claim(pe, name)
                for j in range(4):
                    nk = (t + 1) * P
                    mm = pe.matmul(jobs.out(name)[:, j * T:j * T + nk], qTs[64 * g:64 * g + 64, 1 + rq, j, t * P:(t + 1) * P],
                                   rkT[64 * g:64 * g + 64, rk, 0:nk], start=True, stop=True)
                jobs.fill(mm, name)

            def turn_probs(i):
                a, t, g = ITEMS[i]
                pe.wait_ge(weighed, i + 1)
                for kb in range(t + 1):
                    transpose4(("PT", a, t, g, kb), [sc[:, i % 2, j, kb * P:(kb + 1) * P] for j in range(4)])

            def values(i):
                a, t, g = ITEMS[i]
                v = ATT[a][3]
                name = ("O", max(a, 1), t)
                if a != 1 and g == 0:
                    jobs.claim(pe, name)
                if (a, g) == (0, 0):
                    jobs.wait_drained(pe, "vc")
                    jobs.wait_drained(pe, ("cpT", t))
                    for j in range(4):
                        pe.matmul(jobs.out(name)[:, j * P:(j + 1) * P], vblk[:, j * P:(j + 1) * P], mem["cpT"][:, t, :], start=(j == 0), stop=False,
                                  skip_group_check=True)
                for kb in range(t + 1):
                    jobs.wait_drained(pe, ("PT", a, t, g, kb))
                    mm = pe.matmul(jobs.out(name)[64 * g:64 * g + 64, :], proj[:, kb, v + DH * g:v + DH * g + DH],
                                   pt[:, i % 2, kb, :, :].rearrange("p j q -> p (j q)"), start=(a == 2 and kb == 0), stop=(a > 0 and kb == t),
                                   skip_group_check=True)
                if a > 0 and g == 1:
                    jobs.fill(mm, name)

            for i in range(len(ITEMS) + 1):
                if i < len(ITEMS):
                    scores(i)
                gate_chunks(i < len(ITEMS))
                if i == 1:
                    cmp_out()
                if i >= 1:
                    turn_probs(i - 1)
                    gate_chunks(i in (3, 6))
                    values(i - 1)
            gate_chunks(16)

            for t in range(TT):
                pe.wait_ge(conv_done, 4 * TAPS)
                transpose4(("convT", t), [acc[:, b, t * P:(t + 1) * P] for b in range(4)])

            def next_split(n):
                c, slot, _ = split_slot(n)
                assert state["chunk"] == c, (state, c)
                state["chunk"] += 1
                pe.wait_ge(lo_ready, n + 1)
                return slot[:, 0, :], slot[:, 1, :]

            for bi, n in enumerate(BRANCH_ORDER):
                for half in range(2):
                    if n == 3 and half == 1:
                        for t in range(TT):
                            jobs.wait_drained(pe, ("convT", t))
                            transpose4(("obT", t), [ln_tm[:, t, b * P:(b + 1) * P] for b in range(4)])
                    hi, lo = (part.rearrange("p (k n) -> p k n", k=4) for part in next_split(2 * bi + half))
                    if half == 0:
                        if n == 1:
                            pe.wait_ge(ob_lo, TT)
                        for name in {0: [("O", 1, 0), ("O", 1, 1)], 3: [("O", 2, 0), ("O", 2, 1)], 2: [("pool", 0), ("pool", 1)],
                                     1: []}[n]:
                            jobs.wait_drained(pe, name)
                    for i in range(2):
                        name = ("up", n, 2 * half + i)
                        jobs.claim(pe, name)
                        for b in range(2):
                            out, fs = jobs.out(name)[:, b * T:(b + 1) * T], slice((2 * i + b) * P, (2 * i + b + 1) * P)
                            for k in range(4):
                                mm = pe.matmul(out, hi[:, k, fs], brS[n][:, 0, k, :], start=(k == 0), stop=False)
                                if k == 0:
                                    carry(mm)
                                pe.matmul(out, hi[:, k, fs], brS[n][:, 1, k, :], start=False, stop=False)
                                mm = pe.matmul(out, lo[:, k, fs], brS[n][:, 0, k, :], start=False, stop=(k == 3))
                        jobs.fill(mm, name)
                    release(name)

            for c in range(2):
                for half in range(2):
                    hi, lo = (part.rearrange("p (k n) -> p k n", k=4) for part in next_split(8 + 2 * c + half))
                    for i in range(2):
                        pe.wait_ge(mix_lo, 2 * half + i + 1)
                    for t in range(TT):
                        name, ts = ("wo", c, t), slice(t * P, (t + 1) * P)
                        if half == 0:
                            jobs.claim(pe, name)
                        for k in range(4):
                            kk = 4 * half + k
                            mm = pe.matmul(jobs.out(name), mixS[:, 0, kk, ts], hi[:, k, :], start=(kk == 0), stop=False)
                            if k == 0:
                                carry(mm)
                            pe.matmul(jobs.out(name), mixS[:, 0, kk, ts], lo[:, k, :], start=False, stop=False)
                            mm = pe.matmul(jobs.out(name), mixS[:, 1, kk, ts], hi[:, k, :], start=False, stop=(kk == KD - 1))
                        if half == 1:
                            jobs.fill(mm, name)
                    if half == 0:
                        done_with(mm)
                    else:
                        release(("wo", c, 1))

            mods(LATE_MODS)
            for c in range(2):
                for t in range(TT):
                    pe.wait_ge(normed, TT + t + 1)
                    transpose4(("hf", c, t), [tm[:, t, (4 * c + i) * P:(4 * c + i + 1) * P] for i in range(4)])
            mod_turn(LATE_MODS[-1])
            pe.wait_ge(h_lo, 2 * TT)
            for j in range(FB):
                hi, lo = (part.rearrange("p (k m) -> p k m", k=KD) for part in next_split(n_up + j))
                jobs.claim(pe, ("ffn", j))
                for b in range(2):
                    out = jobs.out(("ffn", j))[:, b * T:(b + 1) * T]
                    for k in range(KD):
                        mm = pe.matmul(out, hi[:, k, b * P:(b + 1) * P], hfT[:, 0, k, :], start=(k == 0), stop=False)
                        if k == 0:
                            carry(mm)
                        pe.matmul(out, hi[:, k, b * P:(b + 1) * P], hfT[:, 1, k, :], start=False, stop=False)
                        mm = pe.matmul(out, lo[:, k, b * P:(b + 1) * P], hfT[:, 0, k, :], start=False, stop=(k == KD - 1))
                jobs.fill(mm, ("ffn", j))
                release(("ffn", j))
            for t in range(TT):
                for c in range(2):
                    jobs.claim(pe, ("down", c, t))
            for i in range(FB // 2):
                hi, lo = (part.rearrange("p (k n) -> p k n", k=2) for part in next_split(n_up + FB + i))
                for k in range(2):
                    n = 2 * i + k
                    pe.wait_ge(f_ready, n + 1)
                    for t in range(TT):
                        for c in range(2):
                            name, cs, ts = ("down", c, t), slice(c * 512, (c + 1) * 512), slice(t * P, (t + 1) * P)
                            mm = pe.matmul(jobs.out(name), fT[:, 0, n, ts], hi[:, k, cs], start=(n == 0), stop=False)
                            if k == 0:
                                carry(mm)
                            pe.matmul(jobs.out(name), fT[:, 0, n, ts], lo[:, k, cs], start=False, stop=False)
                            mm = pe.matmul(jobs.out(name), fT[:, 1, n, ts], hi[:, k, cs], start=False, stop=(n == FB - 1))
                            if n == FB - 1:
                                jobs.fill(mm, name)
                if i < FB // 2 - 1:
                    done_with(mm)
            release(("down", 1, 1))
            for i in END_MODS:
                mod(i)
                mod_turn(i)
            next_chunk()
            pe.sem_inc(used[(state["chunk"] - 1) % SLOTS], 1)
            assert state["chunk"] == N_LAYER_CHUNKS, state

        @block.scalar
        def _(act):
            order = Signal(a_order)

            def square(src, out, total, sig):
                act.activation(out, src, ACT.Square, accum_out=total).then_inc(sig, 1)

            act.dma_start(cols[:, :], cols_dram[l]).then_inc(params, 16)
            act.dma_start(rows[:, :], rows_dram[l].to_broadcast([P, N_ROWS])).then_inc(params, 16)
            act.wait_ge(loaded, 32)
            for t in range(TT):
                square(x[:, t, :], tm[:, t, :], ss[:, t:t + 1], squares)

            def copy_out(name, dst, src=None, scale=1.0, func=ACT.Copy):
                jobs.wait_filled(act, name)
                jobs.drain(act.activation(dst, jobs.out(name) if src is None else src, func, scale=scale), name)

            def mods_out(steps):
                for i in steps:
                    if i >= 2:
                        jobs.wait_filled(act, ("modT", i - 2))
                    copy_out(("mod", i), mem["mrow"][0:2, i % 2, :], jobs.out(("mod", i))[0:2, :])

            mods_out(EARLY_MODS)
            for w, at in (("kv", 0), ("kv2", 512), ("q", 1024), ("dq", 1536)):
                for t in range(TT):
                    copy_out((w, t), proj[:, t, at:at + 512])
            copy_out("ga", small[:, 0:48], jobs.out("ga")[:, 0:48], func=ACT.Sigmoid)
            for t in range(TT):
                copy_out(("cd", t), cdT[:, :, t * P:(t + 1) * P], jobs.out(("cd", t)).rearrange("p (m t) -> p m t", m=4))
            for i in range(2):
                copy_out(("c", i), cpad[:, 2 * i:2 * i + 2, 16:16 + T], jobs.out(("c", i)).rearrange("p (b t) -> p b t", b=2))
            for t in range(TT):
                copy_out(("qT", t), qTs[:, 0, :, t * P:(t + 1) * P], jobs.out(("qT", t)).rearrange("p (m t) -> p m t", m=4), 0.125)
            for i in range(2):
                copy_out(("ba", i), bglu[:, 2 * i:2 * i + 2, TAPS - 1:TAPS - 1 + T], jobs.out(("ba", i)).rearrange("p (b t) -> p b t", b=2))
            for kv in range(2):
                copy_out(("hid", kv), hsum[0:2 * CMP_N, kv, :], jobs.out(("hid", kv))[0:2 * CMP_N, 0:T], func=ACT.Gelu_apprx_tanh)
            for i in range(2):
                copy_out(("bg", i), sg[:, i, :], func=ACT.Sigmoid)
            for t in range(TT):
                copy_out(("rqT", t), qTs[:, 1, :, t * P:(t + 1) * P], jobs.out(("rqT", t)).rearrange("p (m t) -> p m t", m=4), 0.125)
                copy_out(("rdT", t), qTs[:, 2, :, t * P:(t + 1) * P], jobs.out(("rdT", t)).rearrange("p (m t) -> p m t", m=4), 0.125)
            for i in range(2):
                jobs.wait_filled(act, ("pool", i))
                for b in range(2):
                    n = 2 * i + b
                    jobs.drain(act.activation(brS[2][:, 0, n, :], jobs.out(("pool", i))[:, b * T:(b + 1) * T], ACT.Copy,
                                              scale=C("pool_s", n, n + 1)), ("pool", i))

            gate_at = {"n": 0}

            def gate_out(n):
                for _ in range(n):
                    i = gate_at["n"]
                    if i < 16:
                        copy_out(("gate", i), gates[:, i * 512:(i + 1) * 512])
                        gate_at["n"] += 1

            def exps(i):
                a, t, g = ITEMS[i]
                act.wait_ge(masked, i + 1)
                if a == 2:
                    act.activation(sinkv[:, i % 2, :], sinkv[:, i % 2, :], ACT.Exp).then_inc(tail_sent, 1)
                for j in range(4):
                    b = den[:, i % 2, j:j + 1]
                    act.activation(sc[:, i % 2, j, 0:(t + 1) * P], sc[:, i % 2, j, 0:(t + 1) * P], ACT.Exp,
                                   bias=nmax[:, 4 * (i % 2) + j:4 * (i % 2) + j + 1], accum_out=b).then_inc(exped, 1)

            for t in range(TT):
                act.wait_ge(cmp_s, t + 1)
                act.activation(csc[:, t, :], csc[:, t, :], ACT.Exp).then_inc(cmp_e, 1)
            def out_copy(i):
                a, t, g = ITEMS[i]
                if a > 0 and g == 1:
                    copy_out(("O", a, t), brS[(0, 0, 3)[a]][:, 0, :, t * P:(t + 1) * P], jobs.out(("O", a, t)).rearrange("p (m t) -> p m t", m=4))

            for i in range(len(ITEMS) + 1):
                if i >= 2:
                    out_copy(i - 2)
                if i == 1:
                    gate_out(1)
                    for t in range(TT):
                        copy_out(("cpT", t), mem["cpT"][:, t, :], jobs.out(("cpT", t))[:, 0:P])
                    gate_out(1)
                else:
                    gate_out(i < len(ITEMS))
                if i >= 1:
                    a, t, g = ITEMS[i - 1]
                    for kb in range(t + 1):
                        copy_out(("PT", a, t, g, kb), pt[:, (i - 1) % 2, kb, :, :], jobs.out(("PT", a, t, g, kb)).rearrange("p (j q) -> p j q", j=4))
                if i < len(ITEMS):
                    exps(i)
                if i >= 1:
                    gate_out(i in (3, 6))
            out_copy(len(ITEMS) - 1)
            split_hi(act, 0)
            gate_out(16)

            def open_gates(n):
                for i in range(4):
                    jobs.wait_drained(act, ("gate", 4 * n + i))
                act.activation(gates[:, n * 2048:(n + 1) * 2048], gates[:, n * 2048:(n + 1) * 2048], ACT.Sigmoid).then_inc(gates_ready, 1)

            open_gates(BRANCH_ORDER[0])
            split_hi(act, 1)
            open_gates(BRANCH_ORDER[1])
            split_hi(act, 2)
            open_gates(BRANCH_ORDER[2])
            split_hi(act, 3)
            open_gates(BRANCH_ORDER[3])
            split_hi(act, 4)
            split_hi(act, 5)
            for t in range(TT):
                jobs.wait_filled(act, ("obT", t))
                for b in range(4):
                    jobs.drain(act.activation(acc[:, b, t * P:(t + 1) * P], jobs.out(("obT", t))[:, b * P:(b + 1) * P], ACT.Silu,
                                              scale=C("ln_g", b, b + 1), bias=C("ln_b", b, b + 1)), ("obT", t))
                jobs.wait_drained(act, ("obT", t))
                act.activation(brS[1][:, 0, :, t * P:(t + 1) * P], acc[:, :, t * P:(t + 1) * P], ACT.Copy).then_inc(ob_hi, 1)
            split_hi(act, 6)
            split_hi(act, 7)
            split_hi(act, 8)
            for i in range(4):
                act.wait_ge(mixed, 9 + i)
                act.activation(mixS[:, 0, 2 * i:2 * i + 2, :], mixT[:, 2 * i:2 * i + 2, :], ACT.Copy).then_inc(mix_hi, 1)
            for n in range(9, n_up):
                split_hi(act, n)

            def post(kind, c, t):
                name = (kind, c, t)
                jobs.wait_filled(act, name)
                jobs.drain(act.activation(tm[:, t, c * 512:(c + 1) * 512], jobs.out(name), ACT.Copy), name)
                region, _, before, _ = jobs.jobs[name]
                act.wait_ge(drained[region], before + 1)
                jobs.drain(act.activation(jobs.out(name), jobs.out(name), ACT.Square, accum_out=ss4[:, t, c:c + 1]), name)

            for c in range(2):
                for t in range(TT):
                    post("wo", c, t)
            mods_out(LATE_MODS)
            split_hi(act, n_up)
            for t in range(TT):
                act.wait_ge(x_ready, t + 1)
                square(x[:, t, :], tm[:, t, :], ss[:, t:t + 1], squares)
            split_hi(act, n_up + 1)
            for n, (c, t) in enumerate((c, t) for c in range(2) for t in range(TT)):
                act.wait_ge(scaled, n + 1)
                act.activation(hfT[:, 0, 4 * c:4 * c + 4, t * P:(t + 1) * P], hf32[:, n % 2, :].rearrange("p (m t) -> p m t", m=4),
                               ACT.Copy).then_inc(h_hi, 1)
            split_hi(act, n_up + 2)

            for j in range(FB + 1):
                if j < FB:
                    jobs.wait_filled(act, ("ffn", j))
                    if j >= 4:
                        act.wait_ge(f_ready, j - 3)
                    u = hq[j % 2][:, (j // 2 % 2) * 512:(j // 2 % 2) * 512 + 512]
                    for b in range(2):
                        n = 2 * j + b
                        act.activation(u[:, b * T:(b + 1) * T], jobs.out(("ffn", j))[:, b * T:(b + 1) * T], ACT.Identity,
                                       scale=C("fw", 3 * n + 2, 3 * n + 3), bias=C("fb", n, n + 1)).then_inc(ffn_init, 1)
                if j >= 1:
                    u = hq[(j - 1) % 2][:, ((j - 1) // 2 % 2) * 512:((j - 1) // 2 % 2) * 512 + 512]
                    jobs.wait_drained(act, ("ffn", j - 1))
                    act.activation(u[:, 0:T], u[:, 0:T], ACT.Gelu_apprx_tanh).then_inc(gelued, 1)
                if j < FB:
                    split_hi(act, n_up + j + SPLITS)
            for n in range(FB + SPLITS, FFN_CHUNKS):
                split_hi(act, n_up + n)
            for t in range(TT):
                for c in range(2):
                    post("down", c, t)
            mods_out(END_MODS)

        @block.vector
        def _(dve):
            order = Signal(v_order)
            conv = Signal(conv_done)

            def norm_tiles(first):
                for t in range(TT):
                    dve.wait_ge(rstd_ready, first)
                    dve.tensor_scalar(tm[:, t, :], x[:, t, :], rstd[:, t:t + 1], None, ALU.mult).then_inc(normed, 1)

            def scaled_turn(kind, g):
                for c in range(2):
                    for t in range(TT):
                        name = (kind, c, t)
                        jobs.wait_filled(dve, name)
                        jobs.drain(dve.tensor_tensor(
                            hT[:, 4 * c:4 * c + 4, t * P:(t + 1) * P], jobs.out(name).rearrange("p (m t) -> p m t", m=4),
                            bc(C(g, 4 * c, 4 * c + 4).unsqueeze(2), [P, 4, P]), ALU.mult), name)

            def mods_in(steps):
                for i in steps:
                    name = ("modT", i)
                    at = l * (4 * MOD_STEPS) + 4 * i
                    jobs.wait_filled(dve, name)
                    jobs.drain(dve.tensor_tensor(mem["modT"][:, bass.ds(at, 4), :], jobs.out(name)[:, 0:8].rearrange("p (b v) -> p b v", v=2),
                                                 bc(mem["cond"][:, bass.ds(at + 16, 4)].unsqueeze(2), [P, 4, 2]), ALU.add), name)

            dve.wait_ge(params, 32)
            norm_tiles(1)
            mods_in(EARLY_MODS[:-1])
            scaled_turn("ht", "g_mix")
            mods_in(EARLY_MODS[-1:])

            def rope(dst, src, groups, t, at):
                n, width = groups
                h = width // 64
                tab = [K("rope", 64 * i + 32 * t, 64 * i + 32 * t + 32) for i in range(3)]
                tw = rtmp[:, at:at + n * width].rearrange("p (n h r d) -> p n h r d", n=n, r=2, d=32)
                order.up(dve.tensor_tensor(dst.rearrange("p n (h d) -> p n h d", d=32), src.rearrange("p n (h d) -> p n h d", d=32),
                                           bc(tab[0].unsqueeze(1).unsqueeze(1), [P, n, 2 * h, 32]), ALU.mult))
                halves = src.rearrange("p n (h r d) -> p n h r d", r=2, d=32)
                for r in range(2):
                    order.up(dve.tensor_tensor(tw[:, :, :, r, :], halves[:, :, :, 1 - r, :],
                                               bc(tab[2 - r].unsqueeze(1).unsqueeze(1), [P, n, h, 32]), ALU.mult))
                order.here(dve)
                dve.tensor_tensor(dst, dst, rtmp[:, at:at + n * width].rearrange("p (n c) -> p n c", n=n), ALU.add).then_inc(roped, 1)

            for t in range(TT):
                jobs.wait_drained(dve, ("kv", t))
                dve.tensor_copy(kd[:, t, :, :, :], bc(proj[:, t, 0:256].rearrange("p (m d) -> p m d", m=4).unsqueeze(2), [P, 4, 2, DH]))\
                   .then_inc(kd_ready, 1)
            for t in range(TT):
                jobs.wait_drained(dve, ("kv2", t))
                rope(rot[:, t, 0:384].rearrange("p (n c) -> p n c", n=3),
                     proj[:, t, 256:1024].rearrange("p (n c) -> p n c", n=3)[:, :, 0:P], (3, P), t, 0)
                jobs.wait_drained(dve, ("q", t))
                rope(rot[:, t, 384:896].rearrange("p (n c) -> p n c", n=1), proj[:, t, 1024:1536].rearrange("p (n c) -> p n c", n=1),
                     (1, 512), t, 384)
                jobs.wait_drained(dve, ("dq", t))
                rope(rot[:, t, 896:1408].rearrange("p (n c) -> p n c", n=1), proj[:, t, 1536:2048].rearrange("p (n c) -> p n c", n=1),
                     (1, 512), t, 896)
                if t == 0:
                    dve.wait_ge(roped, 3)
            for t in range(TT):
                jobs.wait_filled(dve, ("rkT", t))
                jobs.drain(dve.tensor_copy(rkT[:, :, t * P:(t + 1) * P], jobs.out(("rkT", t))[:, 0:384].rearrange("p (m t) -> p m t", m=3)), ("rkT", t))

            jobs.wait_drained(dve, ("c", 1))
            for g in range(4):
                src = cpad[:, g, :]
                for s in range(g + 1):
                    sh = 1 << s
                    lo = 2 * sh - 1
                    dst = bufs[s % 2]
                    order.up(dve.tensor_tensor(dst[:, lo:16 + T], src[:, lo:16 + T], src[:, lo - sh:16 + T - sh], ALU.add))
                    order.here(dve)
                    src = dst
                w = 2 << g
                out = pooled_in[:, g, :]
                order.up(dve.scalar_tensor_tensor(out=out, in0=src[:, 16:16 + T], scalar=1.0 / w, in1=cpad[:, g, 16:16 + T],
                                                  op0=ALU.mult, op1=ALU.subtract))
                order.here(dve)
                order.up(dve.tensor_tensor(out[:, 0:16], src[:, 16:32], K("pool_inv", 16 * g, 16 * g + 16), ALU.mult))
                order.here(dve)
                dve.tensor_tensor(out[:, 0:16], out[:, 0:16], cpad[:, g, 16:32], ALU.subtract).then_inc(pooled, 1)

            for kv in range(2):
                jobs.wait_filled(dve, ("hidT", kv))
                for ht in range(2):
                    src = jobs.out(("hidT", kv))[:, 32 * ht:32 * ht + 2 * CMP_N].rearrange("p (g n) -> p g n", g=2)
                    if kv == 0:
                        ins = dve.tensor_copy(hidk[:, ht, :, 0:CMP_N], src)
                    else:
                        ins = dve.tensor_copy(hidv[:, ht, :].rearrange("p (j g n) -> p j g n", j=4, g=2)[:, :, :, 0:CMP_N],
                                              bc(src.unsqueeze(1), [P, 4, 2, CMP_N]))
                    jobs.drain(ins, ("hidT", kv))
            for i in range(2):
                jobs.wait_drained(dve, ("bg", i))
                jobs.wait_drained(dve, ("ba", i))
                order.up(dve.tensor_tensor(bglu[:, 2 * i:2 * i + 2, TAPS - 1:TAPS - 1 + T], bglu[:, 2 * i:2 * i + 2, TAPS - 1:TAPS - 1 + T],
                                           sg[:, i, :].rearrange("p (b t) -> p b t", b=2), ALU.mult))
            order.here(dve)

            conv_at = {"n": 0}

            def conv_steps(n):
                for _ in range(n):
                    i = conv_at["n"]
                    if i >= 4 * TAPS:
                        return
                    k, b = divmod(i, 4)
                    w = C("conv_w", TAPS * b + k, TAPS * b + k + 1)
                    if k == 0:
                        conv.up(dve.tensor_scalar(acc[:, b, :], bglu[:, b, 0:T], w, C("conv_b", b, b + 1), ALU.mult, ALU.add))
                    else:
                        conv.here(dve, less=3)
                        conv.up(dve.scalar_tensor_tensor(out=acc[:, b, :], in0=bglu[:, b, k:k + T], scalar=w, in1=acc[:, b, :],
                                                         op0=ALU.mult, op1=ALU.add))
                    conv_at["n"] += 1

            jobs.wait_filled(dve, "kc")
            for g in range(2):
                jobs.drain(dve.tensor_copy(kblk[64 * g:64 * g + 64, 16 * g:16 * g + CMP_N], jobs.out("kc")[64 * g:64 * g + 64, 0:CMP_N]), "kc")
            jobs.wait_filled(dve, "vc")
            jobs.drain(dve.tensor_tensor(vblk[:, :].rearrange("p (h d) -> p h d", h=8), bc(jobs.out("vc")[:, 0:DH].unsqueeze(1), [P, 8, DH]),
                                         bc(K("blk8").unsqueeze(2), [P, 8, DH]), ALU.mult), "vc")
            conv_steps(12)
            for i in range(2):
                region, _, before, _ = jobs.jobs[("pool", i)]
                dve.wait_ge(drained[region], before + 2)
                for b in range(2):
                    n = 2 * i + b
                    jobs.drain(dve.scalar_tensor_tensor(out=brS[2][:, 1, n, :], in0=jobs.out(("pool", i))[:, b * T:(b + 1) * T],
                                                        scalar=C("pool_s", n, n + 1), in1=brS[2][:, 0, n, :].bitcast(F32),
                                                        op0=ALU.mult, op1=ALU.subtract), ("pool", i))
            for t in range(TT):
                jobs.wait_filled(dve, ("cs", t))
                s3 = csc[:, t, :].rearrange("p (h n) -> p h n", h=8)
                jobs.drain(dve.tensor_tensor(s3, jobs.out(("cs", t))[:, 0:P].rearrange("p (h n) -> p h n", h=8),
                                             bc(K("cmp_mask", 16 * t, 16 * t + 16).unsqueeze(1), [P, 8, 16]), ALU.add), ("cs", t))
                jobs.wait_drained(dve, ("cs", t))
                order.up(dve.tensor_reduce(cmax[:, t, :], s3, AX_X, ALU.max))
                order.here(dve)
                dve.tensor_tensor(s3, s3, bc(cmax[:, t, :].unsqueeze(2), [P, 8, 16]), ALU.subtract).then_inc(cmp_s, 1)

            def mask(i):
                a, t, g = ITEMS[i]
                name, nk = ("S", a, t, g), (t + 1) * P
                if i >= 2:
                    for kb in range(ITEMS[i - 2][1] + 1):
                        jobs.wait_filled(dve, ("PT", *ITEMS[i - 2], kb))
                jobs.wait_filled(dve, name)
                m = K("band" if a == 2 else "full_causal", 2 * P - nk, 2 * P)
                s3 = sc[:, i % 2, :, 0:nk]
                jobs.drain(dve.tensor_tensor(s3, jobs.out(name).rearrange("p (j k) -> p j k", j=4)[:, :, 0:nk],
                                             bc(m.unsqueeze(1), [P, 4, nk]), ALU.add), name)
                jobs.wait_drained(dve, name)
                nm = nmax[:, 4 * (i % 2):4 * (i % 2) + 4]
                if a < 2:
                    dve.tensor_reduce(nm, s3, AX_X, ALU.max, negate=True).then_inc(masked, 1)
                    return
                sink = R("sinks").rearrange("p (j g) -> p j g", g=2)[:, :, g]
                order.up(dve.tensor_reduce(nm, s3, AX_X, ALU.max))
                order.here(dve)
                order.up(dve.tensor_tensor(nm, nm, sink, ALU.max))
                order.here(dve)
                order.up(dve.tensor_tensor(sinkv[:, i % 2, :], sink, nm, ALU.subtract))
                order.here(dve)
                dve.tensor_scalar(nm, nm, -1.0, None, ALU.mult).then_inc(masked, 1)

            sinks_seen = Signal(tail_sent)

            def weigh(i):
                a, t, g = ITEMS[i]
                d, c = den[:, i % 2, :], coef[:, i % 2, :]
                dve.wait_ge(exped, 4 * i + 4)
                if a == 2:
                    sinks_seen.n += 1
                    sinks_seen.here(dve)
                    order.up(dve.tensor_tensor(d, d, sinkv[:, i % 2, :], ALU.add))
                    order.here(dve)
                order.up(dve.reciprocal(c, d))
                order.here(dve)
                if a < 2:
                    order.up(dve.tensor_tensor(c, c, ga[:, t, 1 + a, :].rearrange("p (j g) -> p j g", g=2)[:, :, g], ALU.mult))
                    order.here(dve)
                nk = (t + 1) * P
                dve.tensor_tensor(sc[:, i % 2, :, 0:nk], sc[:, i % 2, :, 0:nk], bc(c.unsqueeze(2), [P, 4, nk]), ALU.mult).then_inc(weighed, 1)

            def cmp_weigh():
                for t in range(TT):
                    dve.wait_ge(cmp_e, t + 1)
                    order.up(dve.tensor_reduce(cden[:, t, :], csc[:, t, :].rearrange("p (h n) -> p h n", h=8), AX_X, ALU.add))
                    order.here(dve)
                    order.up(dve.reciprocal(ccoef[:, t, :], cden[:, t, :]))
                    order.here(dve)
                    order.up(dve.scalar_tensor_tensor(out=ccoef[:, t, :], in0=ccoef[:, t, :], scalar=K("cmp_valid", t, t + 1),
                                                      in1=ga[:, t, 0, :], op0=ALU.mult, op1=ALU.mult))
                    order.here(dve)
                    s3 = csc[:, t, :].rearrange("p (h n) -> p h n", h=8)
                    dve.tensor_tensor(s3, s3, bc(ccoef[:, t, :].unsqueeze(2), [P, 8, 16]), ALU.mult).then_inc(cmp_p, 1)

            def out_low(i):
                a, t, g = ITEMS[i]
                if a > 0 and g == 1:
                    region, _, before, _ = jobs.jobs[("O", a, t)]
                    part = brS[(0, 0, 3)[a]][:, :, :, t * P:(t + 1) * P]
                    dve.wait_ge(drained[region], before + 1)
                    jobs.drain(dve.tensor_tensor(part[:, 1, :, :], jobs.out(("O", a, t)).rearrange("p (m t) -> p m t", m=4),
                                                 part[:, 0, :, :].bitcast(F32), ALU.subtract), ("O", a, t))

            for i in range(len(ITEMS) + 1):
                if i < len(ITEMS):
                    mask(i)
                if i == 0:
                    cmp_weigh()
                if i >= 1:
                    weigh(i - 1)
                if i >= 2:
                    out_low(i - 2)
                conv_steps(10)
            out_low(len(ITEMS) - 1)
            split_lo(dve, 0)
            conv_steps(4 * TAPS)

            for t in range(TT):
                jobs.wait_filled(dve, ("convT", t))
                order.up(dve.bn_stats(stats[:, t, :], jobs.out(("convT", t))))
                order.here(dve)
                dve.bn_aggr(mv[:, t, :], stats[:, t, :]).then_inc(stat_ready, 1)
            for t in range(TT):
                dve.wait_ge(lnstd_ready, t + 1)
                jobs.drain(dve.tensor_scalar(ln_tm[:, t, :], jobs.out(("convT", t)), mv[:, t, 0:1], lnstd[:, t:t + 1],
                                             ALU.subtract, ALU.mult), ("convT", t))

            split_lo(dve, 1)
            k = 0
            for bi, n in enumerate(BRANCH_ORDER):
                dve.wait_ge(gates_ready, bi + 1)
                for i in range(4):
                    name = ("up", n, i)
                    jobs.wait_filled(dve, name)
                    g2 = gates[:, n * 2048 + i * 512:n * 2048 + (i + 1) * 512]
                    if bi == 0:
                        dst = mixT[:, 2 * i:2 * i + 2, :].rearrange("p b t -> p (b t)")
                    else:
                        if k >= 2:
                            dve.wait_ge(mixed, k - 1)
                        dst = tmp[:, k % 2, :]
                        k += 1
                    jobs.drain(dve.tensor_tensor(dst, jobs.out(name), g2, ALU.mult), name)
                    if i % 2 == 1:
                        chunk = 2 * bi + i // 2
                        if chunk == 4:
                            for t in range(TT):
                                dve.wait_ge(ob_hi, t + 1)
                                part = brS[1][:, :, :, t * P:(t + 1) * P]
                                dve.tensor_tensor(part[:, 1, :, :], acc[:, :, t * P:(t + 1) * P], part[:, 0, :, :].bitcast(F32),
                                                  ALU.subtract).then_inc(ob_lo, 1)
                        if chunk < 7:
                            split_lo(dve, chunk + 2)
            for i in range(4):
                dve.wait_ge(mix_hi, i + 1)
                dve.tensor_tensor(mixS[:, 1, 2 * i:2 * i + 2, :], mixT[:, 2 * i:2 * i + 2, :], mixS[:, 0, 2 * i:2 * i + 2, :].bitcast(F32),
                                  ALU.subtract).then_inc(mix_lo, 1)
            for n in range(9, n_up):
                split_lo(dve, n)

            def residual(kind, g, first):
                for t in range(TT):
                    dve.wait_ge(rstd_ready, first)
                    for c in range(2):
                        jobs.wait_drained(dve, (kind, c, t))
                    order.up(dve.scalar_tensor_tensor(out=tm[:, t, :], in0=tm[:, t, :], scalar=rstd[:, 2 + t:3 + t], in1=R(g),
                                                      op0=ALU.mult, op1=ALU.mult))
                    order.here(dve)
                    dve.tensor_tensor(x[:, t, :], x[:, t, :], tm[:, t, :], ALU.add).then_inc(x_ready, 1)

            residual("wo", "mix_post", 2)
            mods_in(LATE_MODS[:-1])
            split_lo(dve, n_up)
            dve.wait_ge(squares, 2 * TT)
            norm_tiles(3)
            split_lo(dve, n_up + 1)

            def low_part(n):
                c, t = divmod(n, TT)
                dve.wait_ge(h_hi, n + 1)
                part = hfT[:, :, 4 * c:4 * c + 4, t * P:(t + 1) * P]
                dve.tensor_tensor(part[:, 1, :, :], hf32[:, n % 2, :].rearrange("p (m t) -> p m t", m=4), part[:, 0, :, :].bitcast(F32),
                                  ALU.subtract).then_inc(h_lo, 1)

            for n in range(2 * TT + 1):
                if n < 2 * TT:
                    c, t = divmod(n, TT)
                    name = ("hf", c, t)
                    if n >= 2:
                        dve.wait_ge(h_lo, n - 1)
                    jobs.wait_filled(dve, name)
                    jobs.drain(dve.tensor_tensor(hf32[:, n % 2, :].rearrange("p (m t) -> p m t", m=4), jobs.out(name).rearrange("p (m t) -> p m t", m=4),
                                                 bc(C("g_ffn", 4 * c, 4 * c + 4).unsqueeze(2), [P, 4, P]), ALU.mult), name)
                    jobs.wait_drained(dve, name)
                    dve.sem_inc(scaled, 1)
                if n >= 1:
                    low_part(n - 1)
            split_lo(dve, n_up + 2)
            mods_in(LATE_MODS[-1:])

            for j in range(FB):
                u = hq[j % 2][:, (j // 2 % 2) * 512:(j // 2 % 2) * 512 + 512]
                out = jobs.out(("ffn", j))
                for step in (1, 2):
                    for b in range(2):
                        n = 2 * j + b
                        w = C("fw", 3 * n + 2 - step, 3 * n + 3 - step)
                        if step == 1:
                            dve.wait_ge(ffn_init, 2 * j + 2)
                        else:
                            order.here(dve, less=1)
                        ins = dve.scalar_tensor_tensor(out=u[:, b * T + step:(b + 1) * T], in0=out[:, b * T:(b + 1) * T - step], scalar=w,
                                                       in1=u[:, b * T + step:(b + 1) * T], op0=ALU.mult, op1=ALU.add)
                        if step == 2 and b == 1:
                            jobs.drain(ins, ("ffn", j))
                        else:
                            order.up(ins)
                split_lo(dve, n_up + j + SPLITS)
            for n in range(FB + SPLITS, FFN_CHUNKS):
                split_lo(dve, n_up + n)
            residual("down", "ffn_post", 4)
            mods_in(END_MODS)

        @block.gpsimd
        def _(pool):
            order = Signal(g_order)

            def chain(ins):
                order.up(ins)
                order.here(pool)

            def inv_root(dst, total, n):
                chain(pool.tensor_scalar(msq[:, 0:2], total, 1.0 / n, EPS, ALU.mult, ALU.add))
                pool.tensor_tensor(dst, msq[:, 0:2], K("mhalf", 0, 2), ALU.pow).then_inc(rstd_ready, 1)

            pool.wait_ge(squares, TT)
            inv_root(rstd[:, 0:2], ss[:, 0:2], D)

            for t in range(TT):
                jobs.wait_drained(pool, ("cd", t))
            for m in range(4):
                kv = m // 2
                for par in range(2):
                    src = cdT[64 * par:64 * par + 64, m, :].rearrange("p (n r) -> p n r", r=16)
                    for half in range(2):
                        s = src[:, half:half + CMP_N, :].rearrange("p n (l r) -> p l n r", r=2)[:, :, :, par]
                        ps = C("pos", 16 * kv + 8 * half, 16 * kv + 8 * half + 8)[64 * par:64 * par + 64, :]
                        ins = pool.tensor_tensor(flat[64 * par:64 * par + 64, kv, 8 * half:8 * half + 8, m % 2, :], s,
                                                 bc(ps.unsqueeze(2), [64, 8, CMP_N]), ALU.add)
                        if half == 1:
                            ins.then_inc(flat_ready, 1)
                        else:
                            order.up(ins)
                order.here(pool)

            for t in range(TT):
                pool.wait_ge(stat_ready, t + 1)
                chain(pool.tensor_scalar(msq[:, 2:3], mv[:, t, 1:2], 1.0, EPS, ALU.mult, ALU.add))
                pool.tensor_tensor(lnstd[:, t:t + 1], msq[:, 2:3], K("mhalf", 0, 1), ALU.pow).then_inc(lnstd_ready, 1)
                pool.wait_ge(lnstd_ready, t + 1)

            k = 0
            for n in BRANCH_ORDER[1:]:
                for i in range(4):
                    jobs.wait_drained(pool, ("up", n, i))
                    if k >= 4:
                        pool.wait_ge(mixed, k - 3)
                    dst = mixT[:, 2 * i:2 * i + 2, :].rearrange("p b t -> p (b t)")
                    pool.tensor_tensor(dst, dst, tmp[:, k % 2, :], ALU.add).then_inc(mixed, 1)
                    k += 1

            def post(kind, turn):
                for c in range(2):
                    for t in range(TT):
                        jobs.wait_drained(pool, (kind, c, t))
                chain(pool.tensor_tensor(msq[:, 0:2], ss4[:, :, 0], ss4[:, :, 1], ALU.add))
                chain(pool.tensor_scalar(msq[:, 0:2], msq[:, 0:2], 1.0 / D, EPS, ALU.mult, ALU.add))
                pool.tensor_tensor(rstd[:, 2:4], msq[:, 0:2], K("mhalf", 0, 2), ALU.pow).then_inc(rstd_ready, 1)
                pool.wait_ge(rstd_ready, turn)

            post("wo", 2)
            pool.wait_ge(squares, 2 * TT)
            inv_root(rstd[:, 0:2], ss[:, 0:2], D)
            for j in range(FB):
                u = hq[j % 2][:, (j // 2 % 2) * 512:(j // 2 % 2) * 512 + 512]
                pool.wait_ge(gelued, j + 1)
                if j:
                    pool.wait_ge(f_ready, j)
                pool.tensor_tensor(f32[:, :], u[:, 0:T], u[:, T:2 * T], ALU.mult).then_inc(f_part, 1)
                pool.wait_ge(f_part, 2 * j + 1)
                pool.tensor_copy(fT[:, 0, j, :], f32[:, :]).then_inc(f_part, 1)
                pool.wait_ge(f_part, 2 * j + 2)
                pool.tensor_tensor(fT[:, 1, j, :], f32[:, :], fT[:, 0, j, :].bitcast(F32), ALU.subtract).then_inc(f_ready, 1)
            pool.wait_ge(rstd_ready, 3)
            post("down", 4)


HEADS = 16
DX = 12
SEQ_TILES = 4
ALPHA = 2.0 ** 0.25
LN_EPS = 1e-5
EXPERTS = 16
EXPERT_STEP = 4
N_BLOCK2_CHUNKS = 2 + 6 + 4 + 4 + 8

COLS2, N_COLS2 = offsets([("conv_w", 5 * DX), ("conv_b", DX), ("ssd_g", 8), ("w_dt", KD * 32), ("w_r", KD * 20)])
ROWS2, N_ROWS2 = offsets([("ln1_g", D), ("ln1_b", D), ("ln2_g", D), ("ln2_b", D), ("dtb", 32), ("alog", 32), ("qn", DH), ("kn", DH),
                          ("br", 20), ("skip", 16)])
MEM2 = dict(z=(TT, 1024), y=(2, 1024), cols2=(N_COLS2,), rows2=(N_ROWS2,), sm=(960,), sm2=(950,), aT=(2, P), combT=(T,))
MEM2_MIX = dict(
    hT=(KD, 512), bcf=(4, 512), xs=(4, 1024), kv=(4, 512), xdt=(4, 1024), wx=(2, 1024), q=(TT, 1024), bt=(4, 256),
    kT=(2, 512), probs=(4, 1024), m=(4, 512), cb=(2, 2, 2, P),
)
MEM2_MOE_SPLIT = dict(split=(SPLITS, 2, CH), hfS=(2, KD, T), hidS=(2, 2, 512))
MEM2_MOE = dict(combB=(EXPERTS, T), pe=(2, 512), hid=(2, 512), hf=(KD, T))
STATES = [(0, 0), (1, 0), (2, 0), (1, 1), (0, 1), (3, 1)]
UNITS = [(t, g, quad) for t in range(TT) for g in range(2) for quad in range(2)]
HEAD_ITEMS = [(t, b, g) for t in range(TT) for b in range(8) for g in range(2)]


def plan_block2(jobs):
    for s in (1, 0):
        for c in range(2):
            for t in range(TT):
                jobs.plan(("in", s, c, t))
        if s == 1:
            for c in range(2):
                for t in range(TT):
                    jobs.plan(("q", c, t))
    jobs.plan("dt")
    for i, r in zip(range(4), ("s0", "s1", "t", "u")):
        jobs.plan(("kv", i), r)
    for b in range(DX):
        jobs.plan(("xbc", b))
    jobs.plan("cum")
    jobs.plan("aT")
    for i in range(4):
        for half in range(2):
            jobs.plan(("xsT", i, half))
        jobs.plan(("bT", i))
    for t in range(TT):
        jobs.plan(("z", 0, t))
    for i in range(2):
        jobs.plan(("kT", i))
    for t in range(TT):
        jobs.plan(("cb", t))
    for n in range(len(STATES)):
        for g in range(2):
            jobs.plan(("st", n, g), ("s0", "s1")[g])
    for t in range(TT):
        jobs.plan(("z", 1, t), ("s0", "s1")[t])
    for t, g, quad in UNITS:
        for d in range(2):
            jobs.plan(("aq", t, g, quad, d))
        if quad == 1:
            jobs.plan(("yd", t, g), "a3")
            for d in range(2):
                jobs.plan(("yo", t, g, d), ("t", "u")[d])
    for t in range(TT):
        for h in range(2):
            jobs.plan(("qT", t, h))
    for n, (t, b, g) in enumerate(HEAD_ITEMS):
        jobs.plan(("S", n), ("s0", "s1")[n % 2])
        jobs.plan(("PT", n), ("t", "u")[n % 2])
        if b % 4 == 0 and g == 0:
            jobs.plan(("O", t, b // 4), ("a3", "a2")[b // 4])
    for t in range(TT):
        for h in range(4):
            jobs.plan(("mixT", h, t))
    for v in range(2):
        for c in range(2):
            jobs.plan(("gB", v, c))
    for t in range(TT):
        for c in range(2):
            jobs.plan(("out", t, c), f"a{2 * t + c}")
    for c in range(2):
        for t in range(TT):
            jobs.plan(("hf", c, t), ("s0", "s1", "t", "u")[2 * c + t])
    jobs.plan("route", "s0")
    for e in range(EXPERT_STEP):
        if e == 2:
            jobs.plan("combT", "s0")
            for i in range(8):
                jobs.plan(("combB", i), ("s0", "s1")[i % 2])
        for part, r in zip("GU", expert_regions(e)):
            jobs.plan((part, e), r)


def expert_regions(e):
    return ("s0", "s1") if e % 2 == 0 else ("t", "u")


MOE_ORDER = [("G", 0), ("U", 0), ("G", 1), ("U", 1), ("D", 0), ("G", 2), ("U", 2), ("D", 1), ("G", 3), ("U", 3), ("D", 2), ("D", 3)]


def block2(nc, mem, ring, landed, used, wts, psum, sems, cols_dram, rows_dram, ctx_dram, out_dram):
    region = {**{f"a{i}": (i * 512, 512) for i in range(4)}, "s0": (2048, 512), "s1": (2560, 512), "t": (3072, 512), "u": (3584, 512)}
    filled = {r: sems(f"filled2_{r}") for r in region}
    drained = {r: sems(f"drained2_{r}") for r in region}
    jobs = Jobs(psum, filled, drained, region, ring=3)
    plan_block2(jobs)

    params, ln_rows, ctx_in = sems("params2"), sems("ln_rows"), sems("ctx_in")
    mod_ready = sems("mod_ready")
    shifted = sems("shifted")
    conv_init = sems("conv_init")
    xbc_ready = sems("xbc_ready")
    dt_neg, dt_exp, dt_u, dt_ln, dt_ready = (sems(n) for n in ("dt_neg", "dt_exp", "dt_u", "dt_ln", "dt_ready"))
    a_ready = sems("a_ready")
    decays = sems("decays")
    diff_ready = sems("diff_ready")
    dw_ready = sems("dw_ready")
    xw_ready = sems("xw_ready")
    h_ready = sems("h_ready")
    xdt_ready = sems("xdt_ready")
    skip_ready = sems("skip_ready")
    aq_diff = sems("aq_diff")
    aq_exp = sems("aq_exp")
    m_ready = sems("m_ready")
    y_sq = sems("y_sq")
    y_gated = sems("y_gated")
    y_std = sems("y_std")
    y_norm = sems("y_norm")
    qk_sum = sems("qk_sum")
    qk_std = sems("qk_std")
    qk_ready = sems("qk_ready")
    nmax_ready = sems("nmax_ready")
    diag_ready = sems("diag_ready")
    ln_stat, ln_std, x_normed = sems("ln_stat"), sems("ln_std"), sems("x_normed")
    comb_ready = sems("comb_ready")
    r_logits, r_exp = sems("r_logits"), sems("r_exp")
    hi_ready = sems("hi_ready2")
    lo_ready = sems("lo_ready2")
    h_hi, h_lo = sems("h_hi2"), sems("h_lo2")
    hid_raw = sems("hid_raw")
    hid_hi = sems("hid_hi")
    hid_ready = sems("hid_ready2")
    hid_used = sems("hid_used")
    stored = sems("stored")
    m_used = sems("m_used")
    v_order, g_order, a_order = sems("v_order2"), sems("g_order2"), sems("a_order2")

    split, hfS, hidS, combB, gated, hid, hf = (mem[k] for k in ("split", "hfS", "hidS", "combB", "pe", "hid", "hf"))
    H = mem["probs"]
    qT = H[:, 0:2, :].rearrange("p a (b t) -> p (a b) t", t=T)
    p, pt = (H[:, i, :].rearrange("p (b k) -> p b k", b=2) for i in (2, 3))
    hT, xdt, bcf, z, q, kv, xs, bt, wx, y, kT, m, cb = (mem[k] for k in (
        "hT", "xdt", "bcf", "z", "q", "kv", "xs", "bt", "wx", "y", "kT", "m", "cb"))
    x, const, cols, rows, sm = mem["x"], mem["const"], mem["cols2"], mem["rows2"], mem["sm"]
    xbc_xs = xdt[:, :, :].rearrange("p i (b t) -> p (i b) t", t=512)
    mixT = xdt[:, :, :].rearrange("p i (b t) -> p (i b) t", t=T)
    gB = z
    res = y
    ctx_tm = y

    at = [0]

    def small(n):
        at[0] += n
        return sm[:, at[0] - n:at[0]]

    modT = mem["modT"]
    dtr, dt, dtA, tmp_a, tmp_b = (small(128).rearrange("p (i h) -> p i h", i=4) for _ in range(5))
    acs = small(256).rearrange("p (i h) -> p i h", i=4)
    expA = small(32)
    ssq, rq = small(16), small(16)
    assert at[0] <= 960
    sm2 = mem["sm2"]
    at2 = [0]

    def small2(n):
        at2[0] += n
        return sm2[:, at2[0] - n:at2[0]]

    dec = small2(128).rearrange("p (i h) -> p i h", i=4)
    dw = small2(128).rearrange("p (i h) -> p i h", i=4)
    ea = small2(128).rearrange("p (i h) -> p i h", i=4)
    yss, yrs = small2(4), small2(4)
    kss, krs = small2(16), small2(16)
    qss, qrs = small2(32).rearrange("p (t h) -> p t h", t=2), small2(32).rearrange("p (t h) -> p t h", t=2)
    nm, dn, rden = small2(32), small2(32), small2(32)
    stats, mv, lstd, lms = small2(24).rearrange("p (t c s) -> p t c s", t=2, c=2), small2(4).rearrange("p (t s) -> p t s", t=2), small2(2), small2(2)
    lg = small2(40).rearrange("p (t n) -> p t n", t=2)
    gm, gs, gval = small2(2), small2(2), small2(2)
    goh = small2(8).rearrange("p (t g) -> p t g", t=2)
    r8a, r8b, es, pe_, oh1, oh2, pm, wgt = (small2(8).rearrange("p (t g) -> p t g", t=2) for _ in range(8))
    r2a, r2b, r2c = small2(2), small2(2), small2(2)
    r32 = small2(32).rearrange("p (t g e) -> p t g e", t=2, g=4)
    comb = small2(32).rearrange("p (t e) -> p t e", t=2)
    aT = mem["aT"]
    combT = mem["combT"]

    def K(name, a=0, b=None):
        o, width = CONST[name]
        return const[:, o + a:o + (width if b is None else b)]

    def C(name, a=0, b=None):
        o, width = COLS2[name]
        return cols[:, o + a:o + (width if b is None else b)]

    def R(name):
        o, width = ROWS2[name]
        return rows[:, o:o + width]

    ident = K("ident")
    first = LAYERS * N_LAYER_CHUNKS
    first_moe = first + N_BLOCK2_CHUNKS
    turns = len(MOE_ORDER) // SLOTS

    def wait_expert(eng, step, part, e, what):
        r = expert_regions(e)["GU".index(part)]
        _, turn, free, done = jobs.jobs[(part, e)]
        sem = filled[r] if what == "filled" else drained[r]
        peeled = {"claim": free, "filled": turn, "drained": done}[what]
        later = {"claim": jobs.sum[r] - 2 + e // 2, "filled": jobs.turn[r] - 1 + e // 2, "drained": jobs.sum[r] - 1 + e // 2}[what]
        eng.wait_ge(sem, peeled if isinstance(step, int) else step * 2 + later)

    def expert_bank(part, e):
        at, width = region[expert_regions(e)["GU".index(part)]]
        return psum[:, at:at + width]

    def split_hi(act, step, n):
        c = first_moe + n
        act.wait_ge(used[(c - SPLITS) % SLOTS], step * turns + ((c - SPLITS) // SLOTS + 1))
        act.wait_ge(landed[c % SLOTS], step * (turns * 16) + (c // SLOTS + 1) * 16)
        act.activation(split[:, n % SPLITS, 0, :], ring[:, c % SLOTS, :], ACT.Copy).then_inc(hi_ready, 1)

    def split_lo(dve, step, n):
        dve.wait_ge(hi_ready, step * len(MOE_ORDER) + (n + 1))
        dve.tensor_tensor(split[:, n % SPLITS, 1, :], ring[:, (first_moe + n) % SLOTS, :], split[:, n % SPLITS, 0, :].bitcast(F32),
                          ALU.subtract).then_inc(lo_ready, 1)

    with nc.Block() as block:
        @block.sync
        def _(sp):
            sp.dma_start(ctx_tm[:, :, :], ctx_dram.rearrange("(t p) d -> p t d", p=P)).then_inc(ctx_in, 16)
            left = N_BLOCK2_CHUNKS + 3 * EXPERTS - SLOTS
            with sp.Fori(0, left // SLOTS) as turn:
                for s in range(SLOTS):
                    sp.wait_ge(used[s], turn + (first // SLOTS + 1))
                    sp.dma_start(ring[:, s, :], wts[turn * SLOTS + (first + s + SLOTS)]).then_inc(landed[s], 16)
            for t in range(TT):
                sp.wait_ge(x_normed, TT + t + 1)
                sp.dma_start(out_dram[t * P:(t + 1) * P, :], x[:, t, :]).then_inc(stored, 16)
            sp.wait_ge(stored, 16 * TT)

        @block.tensor
        def _(pe):
            state = {"chunk": first, "owed": None}

            def next_chunk():
                c = state["chunk"]
                state["chunk"] += 1
                pe.wait_ge(landed[c % SLOTS], (c // SLOTS + 1) * 16)
                return ring[:, c % SLOTS, :]

            def carry(ins):
                if state["owed"] is not None:
                    ins.then_inc(used[state["owed"]], 1)
                    state["owed"] = None

            def done_with(ins):
                ins.then_inc(used[(state["chunk"] - 1) % SLOTS], 1)

            def owe():
                assert state["owed"] is None
                state["owed"] = (state["chunk"] - 1) % SLOTS

            def transpose4(name, blocks, step=P):
                jobs.claim(pe, name)
                out = jobs.out(name)
                for i, b in enumerate(blocks):
                    mm = pe.transpose(out[0:b.shape[1], i * step:i * step + P], b, ident)
                    if i == 0 and len(blocks) > 1:
                        carry(mm)
                jobs.fill(mm, name)

            def tokens(kind, tiles, names, halves=(0, 1)):
                for half in halves:
                    chunk = next_chunk().rearrange("p (k n) -> p k n", k=4)
                    for tile, name in zip(tiles, names):
                        if half == 0:
                            jobs.claim(pe, name)
                        for k in range(4):
                            mm = pe.matmul(jobs.out(name), hT[:, 4 * half + k, tile * P:(tile + 1) * P], chunk[:, k, :],
                                           start=(half == 0 and k == 0), stop=(half == 1 and k == 3))
                            if k == 0:
                                carry(mm)
                        if half == 1:
                            jobs.fill(mm, name)
                    if half == 0:
                        done_with(mm)
                    else:
                        owe()

            for s in (1, 0):
                src = (ctx_tm, x)[s]
                if s == 0:
                    pe.wait_ge(ctx_in, 16)
                for c in range(2):
                    for t in range(TT):
                        transpose4(("in", s, c, t), [src[:, t, (4 * c + i) * P:(4 * c + i + 1) * P] for i in range(4)])
                if s == 1:
                    pe.wait_ge(shifted, 4)
                    for c in range(2):
                        tokens("q", (2, 3), [("q", c, t) for t in range(TT)])
            pe.wait_ge(params, 32)
            jobs.claim(pe, "dt")
            for i in (2, 3, 0, 1):
                if i == 0:
                    pe.wait_ge(shifted, 8)
                for k in range(KD):
                    mm = pe.matmul(jobs.out("dt")[:, 32 * i:32 * i + 32], hT[:, k, i * P:(i + 1) * P], C("w_dt", 32 * k, 32 * k + 32),
                                   start=(k == 0), stop=(k == KD - 1))
                    if k == 0:
                        carry(mm)
            jobs.fill(mm, "dt")

            tokens("kv", range(SEQ_TILES), [("kv", i) for i in range(SEQ_TILES)])
            for b in range(DX):
                if b % 2 == 0:
                    chunk = next_chunk().rearrange("p (k m) -> p k m", k=KD)
                jobs.claim(pe, ("xbc", b))
                for k in range(KD):
                    mm = pe.matmul(jobs.out(("xbc", b)), chunk[:, k, b % 2 * P:(b % 2 + 1) * P], hT[:, k, :], start=(k == 0), stop=(k == KD - 1))
                    if k == 0:
                        carry(mm)
                jobs.fill(mm, ("xbc", b))
                if b % 2 == 1:
                    owe()

            pe.wait_ge(dt_ready, 1)
            jobs.claim(pe, "cum")
            for i in range(SEQ_TILES):
                out = jobs.out("cum")[:, 64 * i:64 * i + 64]
                mm = pe.matmul(out[:, 0:16], K("tri_u"), dtA[:, i, 0:16], start=True, stop=True)
                carry(mm)
                pe.matmul(out[:, 16:32], K("tri_l"), dtA[:, i, 16:32], start=True, stop=True)
                mm = pe.matmul(out[:, 32:64], K("ones"), dtA[:, i, :], start=True, stop=True)
            jobs.fill(mm, "cum")
            jobs.wait_drained(pe, "cum")
            transpose4("aT", [acs[:, 2 + t, 0:32] for t in range(TT)])

            pe.wait_ge(xbc_ready, DX)
            for i in range(SEQ_TILES):
                for half in range(2):
                    transpose4(("xsT", i, half), [xbc_xs[:, 4 * half + b, i * P:(i + 1) * P] for b in range(4)])
                transpose4(("bT", i), [bcf[:, g, i * P:(i + 1) * P] for g in range(2)])
            tokens("z", (2, 3), [("z", 0, t) for t in range(TT)])
            pe.wait_ge(qk_ready, 1)
            for b in range(2):
                transpose4(("kT", b), [kv[:, i, b * P:(b + 1) * P] for i in range(SEQ_TILES)])
            for t in range(TT):
                jobs.claim(pe, ("cb", t))
                for g in range(2):
                    mm = pe.matmul(jobs.out(("cb", t))[:, g * P:(g + 1) * P], bcf[:, g, (2 + t) * P:(3 + t) * P],
                                   bcf[:, 2 + g, (2 + t) * P:(3 + t) * P], start=True, stop=True)
                jobs.fill(mm, ("cb", t))
            for n, (i, d) in enumerate(STATES):
                pe.wait_ge(xw_ready, n + 1)
                jobs.wait_drained(pe, ("bT", i))
                for g in range(2):
                    jobs.claim(pe, ("st", n, g))
                    jobs.fill(pe.matmul(jobs.out(("st", n, g)), bt[:, i, g * P:(g + 1) * P], wx[:, n % 2, g * 512:(g + 1) * 512],
                                        start=True, stop=True), ("st", n, g))

            jobs.wait_drained(pe, "aT")

            def spread(t, g, quad):
                for d in range(2):
                    name = ("aq", t, g, quad, d)
                    jobs.claim(pe, name)
                    for h in range(4):
                        head = 16 * d + 8 * g + 4 * quad + h
                        mm = pe.matmul(jobs.out(name)[:, h * P:(h + 1) * P], bc(ident[0:32, head:head + 1], [32, P]), aT[0:32, t, :],
                                       start=True, stop=True)
                        if h == 0:
                            carry(mm)
                    jobs.fill(mm, name)

            pe.wait_ge(xdt_ready, 4)
            spread(*UNITS[0])
            for n, (t, g, quad) in enumerate(UNITS):
                if n + 1 < len(UNITS):
                    spread(*UNITS[n + 1])
                if n in (0, 1):
                    tokens("z", (2, 3), [("z", 1, t) for t in range(TT)], halves=(n,))
                pe.wait_ge(m_ready, 2 * n + 2)
                if quad == 0:
                    jobs.claim(pe, ("yd", t, g))
                for h in range(4):
                    for d in range(2):
                        mm = pe.matmul(jobs.out(("yd", t, g))[:, (4 * quad + h) * DH:(4 * quad + h + 1) * DH],
                                       m[:, (2 * n + d) % 4, h * P:(h + 1) * P],
                                       xdt[:, 2 * t + d, (8 * g + 4 * quad + h) * DH:(8 * g + 4 * quad + h + 1) * DH],
                                       start=(d == 0), stop=(d == 1))
                if quad == 0:
                    mm.then_inc(m_used, 1)
                else:
                    jobs.fill(mm, ("yd", t, g))
                    pe.wait_ge(h_ready, 12)
                    for d in range(2):
                        jobs.claim(pe, ("yo", t, g, d))
                        mm = pe.matmul(jobs.out(("yo", t, g, d)), bcf[:, 2 + g, (2 + t) * P:(3 + t) * P],
                                       H[:, 2 * d + t, g * 512:(g + 1) * 512], start=True, stop=True)
                        jobs.fill(mm, ("yo", t, g, d))

            for t in range(TT):
                pe.wait_ge(qk_ready, 2 + t)
                for h in range(2):
                    transpose4(("qT", t, h), [q[:, t, (4 * h + b) * P:(4 * h + b + 1) * P] for b in range(4)])
            for b in range(2):
                jobs.wait_drained(pe, ("kT", b))

            def values(n):
                t, b, g = HEAD_ITEMS[n]
                if b % 4 == 0 and g == 0:
                    jobs.claim(pe, ("O", t, b // 4))
                jobs.wait_drained(pe, ("PT", n))
                for i in range(SEQ_TILES):
                    mm = pe.matmul(jobs.out(("O", t, b // 4))[:, (2 * (b % 4) + g) * DH:(2 * (b % 4) + g + 1) * DH],
                                   pt[:, n % 2, i * P:(i + 1) * P], kv[:, i, 256 + (2 * (b // 4) + g) * DH:256 + (2 * (b // 4) + g + 1) * DH],
                                   start=(i == 0), stop=(i == SEQ_TILES - 1))
                if b % 4 == 3 and g == 1:
                    jobs.fill(mm, ("O", t, b // 4))

            def head_scores(n):
                t, b, g = HEAD_ITEMS[n]
                if g == 0 and b % 4 == 0:
                    jobs.wait_drained(pe, ("qT", t, b // 4))
                jobs.claim(pe, ("S", n))
                jobs.fill(pe.matmul(jobs.out(("S", n)), qT[64 * g:64 * g + 64, b, t * P:(t + 1) * P], kT[64 * g:64 * g + 64, b // 4, :],
                                    start=True, stop=True), ("S", n))

            head_scores(0)
            head_scores(1)
            for n in range(len(HEAD_ITEMS) + 1):
                if n < len(HEAD_ITEMS):
                    jobs.wait_drained(pe, ("S", n))
                    transpose4(("PT", n), [p[:, n % 2, i * P:(i + 1) * P] for i in range(SEQ_TILES)])
                if n + 2 < len(HEAD_ITEMS):
                    head_scores(n + 2)
                if n >= 1:
                    values(n - 1)

            for t in range(TT):
                for h in range(4):
                    if h == 0:
                        pe.wait_ge(y_norm, t + 1)
                    if h >= 2:
                        jobs.wait_drained(pe, ("O", t, h - 2))
                    src = y[:, t, :] if h < 2 else q[:, t, :]
                    transpose4(("mixT", h, t), [src[:, (4 * (h % 2) + b) * P:(4 * (h % 2) + b + 1) * P] for b in range(4)])
            for v in range(2):
                pe.wait_ge(diag_ready, v + 1)
                for c in range(2):
                    jobs.claim(pe, ("gB", v, c))
                    jobs.fill(pe.matmul(jobs.out(("gB", v, c)), K("ones"), wx[:, v, c * 512:(c + 1) * 512], start=True, stop=True), ("gB", v, c))
            for t in range(TT):
                for h in range(4):
                    jobs.wait_drained(pe, ("mixT", h, t))
                for c in range(2):
                    jobs.claim(pe, ("out", t, c))
            for i in range(8):
                chunk = next_chunk().rearrange("p (k n) -> p k n", k=2)
                for k in range(2):
                    for t in range(TT):
                        for c in range(2):
                            mm = pe.matmul(jobs.out(("out", t, c)), mixT[:, 2 * i + k, t * P:(t + 1) * P], chunk[:, k, c * 512:(c + 1) * 512],
                                           start=(i == 0 and k == 0), stop=(i == 7 and k == 1))
                            if k == 0:
                                carry(mm)
                            if i == 7 and k == 1:
                                jobs.fill(mm, ("out", t, c))
                if i < 7:
                    done_with(mm)
            jobs.wait_filled(pe, ("out", 1, 1))
            pe.sem_inc(used[(state["chunk"] - 1) % SLOTS], 1)

            for c in range(2):
                for t in range(TT):
                    pe.wait_ge(x_normed, t + 1)
                    transpose4(("hf", c, t), [x[:, t, (4 * c + i) * P:(4 * c + i + 1) * P] for i in range(4)])
            pe.wait_ge(shifted, 12)
            jobs.claim(pe, "route")
            for t in range(TT):
                for k in range(KD):
                    mm = pe.matmul(jobs.out("route")[:, 20 * t:20 * t + 20], hf[:, k, t * P:(t + 1) * P], C("w_r", 20 * k, 20 * k + 20),
                                   start=(k == 0), stop=(k == KD - 1))
            jobs.fill(mm, "route")
            pe.wait_ge(h_lo, 4)
            pe.sem_inc(hid_used, 2)

            def parts(step, n):
                pe.wait_ge(lo_ready, step * len(MOE_ORDER) + (n + 1))
                return split[:, n % SPLITS, 0, :], split[:, n % SPLITS, 1, :]

            def expert_in(step, n):
                part, e = MOE_ORDER[n]
                hi, lo = (w.rearrange("p (k m) -> p k m", k=KD) for w in parts(step, n))
                wait_expert(pe, step, part, e, "claim")
                for b in range(2):
                    out = expert_bank(part, e)[:, b * T:(b + 1) * T]
                    for k in range(KD):
                        mm = pe.matmul(out, hi[:, k, b * P:(b + 1) * P], hfS[:, 0, k, :], start=(k == 0), stop=False)
                        if b == 0 and k == 0:
                            carry(mm)
                        pe.matmul(out, hi[:, k, b * P:(b + 1) * P], hfS[:, 1, k, :], start=False, stop=False)
                        mm = pe.matmul(out, lo[:, k, b * P:(b + 1) * P], hfS[:, 0, k, :], start=False, stop=(k == KD - 1))
                mm.then_inc(filled[expert_regions(e)["GU".index(part)]], 1)
                state["owed"] = (first_moe + n) % SLOTS

            def expert_out(step, n):
                _, e = MOE_ORDER[n]
                hi, lo = (w.rearrange("p (k n) -> p k n", k=2) for w in parts(step, n))
                pe.wait_ge(hid_ready, step * EXPERT_STEP + (e + 3))
                for k in range(2):
                    for t in range(TT):
                        h_hi_, h_lo_ = (hidS[:, e % 2, w, k * T + t * P:k * T + (t + 1) * P] for w in range(2))
                        for c in range(2):
                            out, cs = psum[:, (2 * t + c) * 512:(2 * t + c + 1) * 512], slice(c * 512, (c + 1) * 512)
                            mm = pe.matmul(out, h_hi_, hi[:, k, cs], start=(isinstance(step, int) and e == 0 and k == 0), stop=False,
                                           skip_group_check=True)
                            if k == 0 and t == 0 and c == 0:
                                carry(mm)
                            pe.matmul(out, h_hi_, lo[:, k, cs], start=False, stop=False, skip_group_check=True)
                            mm = pe.matmul(out, h_lo_, hi[:, k, cs], start=False, stop=False, skip_group_check=True)
                mm.then_inc(hid_used, 1)
                state["owed"] = (first_moe + n) % SLOTS

            def experts(step):
                for n, (part, e) in enumerate(MOE_ORDER):
                    if isinstance(step, int) and n == 4:
                        weights_of_tokens()
                    if part == "D":
                        expert_out(step, n)
                    else:
                        expert_in(step, n)
                pe.wait_ge(hid_used, step * EXPERT_STEP + (EXPERT_STEP + 2))
                pe.sem_inc(used[state["owed"]], 1)
                state["owed"] = None

            def weights_of_tokens():
                pe.wait_ge(comb_ready, 1)
                transpose4("combT", [comb[:, t, :] for t in range(TT)])
                jobs.wait_drained(pe, "combT")
                for i in range(8):
                    jobs.claim(pe, ("combB", i))
                    for e in range(2):
                        mm = pe.matmul(jobs.out(("combB", i))[:, e * T:(e + 1) * T], bc(ident[0:16, 2 * i + e:2 * i + e + 1], [16, P]),
                                       combT[0:16, :], start=True, stop=True)
                    jobs.fill(mm, ("combB", i))

            for r in range(4):
                pe.wait_ge(drained[f"a{r}"], jobs.sum[f"a{r}"])
            experts(0)
            with pe.Fori(1, EXPERTS // EXPERT_STEP) as step:
                experts(step)

        @block.scalar
        def _(act):
            order = Signal(a_order)

            def copy_out(name, dst, src=None, scale=1.0, func=ACT.Copy):
                jobs.wait_filled(act, name)
                jobs.drain(act.activation(dst, jobs.out(name) if src is None else src, func, scale=scale), name)

            act.dma_start(cols[:, :], cols_dram).then_inc(params, 16)
            act.dma_start(rows[:, 4 * D:], rows_dram[:, 4 * D:].to_broadcast([P, N_ROWS2 - 4 * D])).then_inc(params, 16)
            for c in range(2):
                for t in range(TT):
                    copy_out(("q", c, t), q[:, t, c * 512:(c + 1) * 512])
            act.dma_start(rows[:, 0:4 * D], rows_dram[:, 0:4 * D].to_broadcast([P, 4 * D])).then_inc(ln_rows, 16)
            act.wait_ge(params, 32)
            act.activation(expA, R("alog"), ACT.Exp).then_inc(a_ready, 1)
            act.wait_ge(dt_neg, 1)
            act.activation(tmp_b[:, :, :], tmp_b[:, :, :], ACT.Exp).then_inc(dt_exp, 1)
            act.wait_ge(dt_u, 1)
            act.activation(tmp_a[:, :, :], tmp_a[:, :, :], ACT.Ln).then_inc(dt_ln, 1)
            for i in range(SEQ_TILES):
                copy_out(("kv", i), kv[:, i, :])
            for b in range(DX + 1):
                if b < DX:
                    jobs.wait_filled(act, ("xbc", b))
                    dst = xbc_xs[:, b, :] if b < 8 else bcf[:, b - 8, :]
                    act.activation(dst, jobs.out(("xbc", b)), ACT.Identity, scale=C("conv_w", 5 * b + 2, 5 * b + 3),
                                   bias=C("conv_b", b, b + 1)).then_inc(conv_init, 1)
                if b >= 1:
                    dst = xbc_xs[:, b - 1, :] if b - 1 < 8 else bcf[:, b - 9, :]
                    jobs.wait_drained(act, ("xbc", b - 1))
                    act.activation(dst, dst, ACT.Silu).then_inc(xbc_ready, 1)
            act.wait_ge(diff_ready, 1)
            act.activation(dec[:, :, :], acs[:, :, 32:64], ACT.Exp).then_inc(decays, 1)
            act.activation(ea[:, :, :], acs[:, :, 0:32], ACT.Exp).then_inc(decays, 1)
            act.activation(dw[:, :, :], dw[:, :, :], ACT.Exp).then_inc(decays, 1)
            copy_out("aT", aT[0:32, :, :], jobs.out("aT")[0:32, 0:2 * P].rearrange("p (t q) -> p t q", t=2))
            for i in range(SEQ_TILES):
                for half in range(2):
                    copy_out(("xsT", i, half), xs[:, i, half * 512:(half + 1) * 512])
                copy_out(("bT", i), bt[:, i, :], jobs.out(("bT", i))[:, 0:256])
            for t in range(TT):
                copy_out(("z", 0, t), z[:, t, 0:512], func=ACT.Silu)
            for b in range(2):
                copy_out(("kT", b), kT[:, b, :])

            for n in range(len(UNITS)):
                for d in range(2):
                    act.wait_ge(aq_diff, 2 * n + d + 1)
                    act.activation(m[:, (2 * n + d) % 4, :], m[:, (2 * n + d) % 4, :], ACT.Exp).then_inc(aq_exp, 1)
                if n == 2:
                    for t in range(TT):
                        copy_out(("z", 1, t), z[:, t, 512:1024], func=ACT.Silu)
            for t in range(TT):
                for h in range(2):
                    copy_out(("qT", t, h), qT[:, 4 * h:4 * h + 4, t * P:(t + 1) * P], jobs.out(("qT", t, h)).rearrange("p (b t) -> p b t", b=4), 0.125)
            for n in range(len(HEAD_ITEMS) + 1):
                if n < len(HEAD_ITEMS):
                    if n >= 2:
                        jobs.wait_filled(act, ("PT", n - 2))
                    act.wait_ge(nmax_ready, n + 1)
                    name = ("S", n)
                    jobs.wait_filled(act, name)
                    jobs.drain(act.activation(p[:, n % 2, :], jobs.out(name), ACT.Exp, bias=nm[:, n:n + 1], accum_out=dn[:, n:n + 1]), name)
                if n >= 1 and (n - 1) % 2 == 0:
                    copy_out(("PT", n - 1), pt[:, (n - 1) % 2, :])
            for t in range(TT):
                act.wait_ge(y_gated, t + 1)
                if t:
                    act.wait_ge(y_sq, 2 * t)
                for g in range(2):
                    act.activation(wx[:, g, 0:512], y[:, t, g * 512:(g + 1) * 512], ACT.Square, accum_out=yss[:, 2 * t + g:2 * t + g + 1]).then_inc(y_sq, 1)
            for t in range(TT):
                for h in (2, 3):
                    copy_out(("mixT", h, t), mixT[:, 4 * h:4 * h + 4, t * P:(t + 1) * P], jobs.out(("mixT", h, t)).rearrange("p (b t) -> p b t", b=4))
            for v in range(2):
                for c in range(2):
                    copy_out(("gB", v, c), gB[:, v, c * 512:(c + 1) * 512])
            split_hi(act, 0, 0)
            split_hi(act, 0, 1)
            for n in range(4):
                c, t = divmod(n, TT)
                act.wait_ge(shifted, 8 + n + 1)
                act.activation(hfS[:, 0, 4 * c:4 * c + 4, t * P:(t + 1) * P], hf[:, 4 * c:4 * c + 4, t * P:(t + 1) * P], ACT.Copy).then_inc(h_hi, 1)
            split_hi(act, 0, 2)

            def silu(step, e):
                wait_expert(act, step, "G", e, "filled")
                act.wait_ge(hid_raw, step * EXPERT_STEP + (e + 1))
                act.activation(gated[:, e % 2, :], expert_bank("G", e), ACT.Silu).then_inc(drained[expert_regions(e)[0]], 1)

            def hidden_hi(step, e):
                act.wait_ge(hid_raw, step * EXPERT_STEP + (e + 3))
                act.wait_ge(hid_used, step * EXPERT_STEP + (e + 1))
                act.activation(hidS[:, e % 2, 0, :], hid[:, e % 2, :], ACT.Copy).then_inc(hid_hi, 1)

            act.wait_ge(r_logits, 1)
            act.activation(r8a[:, :, :], r8a[:, :, :], ACT.Exp).then_inc(r_exp, 1)
            act.activation(es[:, :, :], es[:, :, :], ACT.Exp).then_inc(r_exp, 1)
            split_hi(act, 0, 3)
            silu(0, 0)
            split_hi(act, 0, 4)
            split_hi(act, 0, 5)
            silu(0, 1)
            split_hi(act, 0, 6)
            copy_out("combT", combT[0:16, :], jobs.out("combT")[0:16, 0:T])
            for i in range(8):
                copy_out(("combB", i), combB[:, 2 * i:2 * i + 2, :], jobs.out(("combB", i)).rearrange("p (e t) -> p e t", e=2))
            hidden_hi(0, 0)
            hidden_hi(0, 1)

            def last_two(step):
                split_hi(act, step, 7)
                silu(step, 2)
                split_hi(act, step, 8)
                hidden_hi(step, 2)
                split_hi(act, step, 9)
                split_hi(act, step, 10)
                silu(step, 3)
                split_hi(act, step, 11)
                hidden_hi(step, 3)

            last_two(0)
            with act.Fori(1, EXPERTS // EXPERT_STEP) as step:
                for n in range(3):
                    split_hi(act, step, n)
                silu(step, 0)
                split_hi(act, step, 3)
                hidden_hi(step, 0)
                split_hi(act, step, 4)
                silu(step, 1)
                split_hi(act, step, 5)
                hidden_hi(step, 1)
                split_hi(act, step, 6)
                last_two(step)

        @block.vector
        def _(dve):
            order = Signal(v_order)

            def chain(ins):
                order.up(ins)
                order.here(dve)

            def tt(out, a, b, op):
                chain(dve.tensor_tensor(out, a, b, op))

            dve.tensor_scalar(modT[:, 8:16, :], modT[:, 8:16, :], 1.0, None, ALU.add).then_inc(mod_ready, 1)
            dve.tensor_scalar(modT[:, 32:40, :], modT[:, 32:40, :], 1.0, None, ALU.add).then_inc(mod_ready, 1)
            dve.wait_ge(mod_ready, 2)

            def scale_in(name, dst, block, v):
                jobs.wait_filled(dve, name)
                jobs.drain(dve.tensor_tensor(dst, jobs.out(name).rearrange("p (b t) -> p b t", b=4),
                                             bc(modT[:, block:block + 4, v:v + 1], [P, 4, P]), ALU.mult), name)

            for s in (1, 0):
                for c in range(2):
                    for t in range(TT):
                        scale_in(("in", s, c, t), hT[:, 4 * c:4 * c + 4, (2 * s + t) * P:(2 * s + t + 1) * P], 8 + 4 * c, 1 - s)
            jobs.wait_filled(dve, "dt")
            dve.wait_ge(params, 32)
            jobs.drain(dve.tensor_tensor(dtr[:, :, :], jobs.out("dt")[:, 0:128].rearrange("p (i h) -> p i h", i=4),
                                         bc(R("dtb").unsqueeze(1), [P, 4, 32]), ALU.add), "dt")
            jobs.wait_drained(dve, "dt")
            chain(dve.tensor_scalar(tmp_b[:, :, :], dtr[:, :, :], -1.0, None, ALU.mult))
            dve.tensor_tensor(tmp_b[:, :, :], tmp_b[:, :, :], dtr[:, :, :], ALU.min).then_inc(dt_neg, 1)

            dve.wait_ge(dt_exp, 1)
            chain(dve.tensor_scalar(tmp_a[:, :, :], tmp_b[:, :, :], 1.0, None, ALU.add))
            chain(dve.tensor_scalar(dt[:, :, :], tmp_a[:, :, :], -1.0, None, ALU.add))
            chain(dve.tensor_scalar(dtA[:, :, :], dt[:, :, :], 0.0, None, ALU.is_equal))
            dve.tensor_tensor(dt[:, :, :], dt[:, :, :], dtA[:, :, :], ALU.add).then_inc(dt_u, 1)
            dve.wait_ge(dt_u, 1)
            chain(dve.reciprocal(dt[:, :, :], dt[:, :, :]))
            tt(dt[:, :, :], dt[:, :, :], tmp_b[:, :, :], ALU.mult)
            dve.wait_ge(dt_ln, 1)
            tt(tmp_a[:, :, :], tmp_a[:, :, :], dtA[:, :, :], ALU.add)
            tt(dt[:, :, :], dt[:, :, :], tmp_a[:, :, :], ALU.mult)
            chain(dve.scalar_tensor_tensor(out=dt[:, :, :], in0=dtr[:, :, :], scalar=0.0, in1=dt[:, :, :], op0=ALU.max, op1=ALU.add))
            dve.wait_ge(a_ready, 1)
            chain(dve.tensor_scalar(expA, expA, -1.0, None, ALU.mult))
            dve.tensor_tensor(dtA[:, :, :], dt[:, :, :], bc(expA.unsqueeze(1), [P, 4, 32]), ALU.mult).then_inc(dt_ready, 1)
            tmpw = qT[:, 0:4, :].rearrange("p a n -> p (a n)")
            tmpv = pt[:, :, :].rearrange("p a n -> p (a n)")

            def head_norm(v, n_heads, ssum, rs, turn, g, tiles, tab):
                tn = len(tiles)
                w4 = tmpw.rearrange("p (t c) -> p t c", t=tn)
                tt(w4, v, v, ALU.mult)
                dve.tensor_reduce(ssum, w4.rearrange("p t (h d) -> p t h d", d=DH), AX_X, ALU.add).then_inc(qk_sum, 1)
                dve.wait_ge(qk_std, turn)
                for i in range(tn):
                    v3 = v[:, i, :].rearrange("p (h d) -> p h d", d=DH)
                    order.up(dve.tensor_tensor(v3, v3, bc(rs[:, i, :].unsqueeze(2), [P, n_heads, DH]), ALU.mult))
                order.here(dve)
                for i in range(tn):
                    v3 = v[:, i, :].rearrange("p (h d) -> p h d", d=DH)
                    order.up(dve.tensor_tensor(v3, v3, bc(g.unsqueeze(1), [P, n_heads, DH]), ALU.mult))
                order.here(dve)
                for i, tile in enumerate(tiles):
                    if tile is None:
                        continue
                    cos, sin, nsin = (K("axial", 64 * s + 32 * tile, 64 * s + 32 * tile + 32) for s in range(3))
                    v3 = v[:, i, :].rearrange("p (h d) -> p h d", d=32)
                    w3 = tmpw[:, 0:64 * n_heads].rearrange("p (h r d) -> p h r d", r=2, d=32)
                    v4 = v[:, i, :].rearrange("p (h r d) -> p h r d", r=2, d=32)
                    for r, tb in ((0, nsin), (1, sin)):
                        order.up(dve.tensor_tensor(w3[:, :, r, :], v4[:, :, 1 - r, :], bc(tb.unsqueeze(1), [P, n_heads, 32]), ALU.mult))
                    tt(tmpv[:, 0:64 * n_heads].rearrange("p (h d) -> p h d", d=32), v3, bc(cos.unsqueeze(1), [P, 2 * n_heads, 32]), ALU.mult)
                    tt(v[:, i, :], tmpw[:, 0:64 * n_heads], tmpv[:, 0:64 * n_heads], ALU.add)

            def k_norm():
                for i in range(SEQ_TILES):
                    jobs.wait_drained(dve, ("kv", i))
                head_norm(kv[:, :, 0:256], 4, kss.rearrange("p (t h) -> p t h", t=4), krs.rearrange("p (t h) -> p t h", t=4), 1, R("kn"),
                          [None, None, 0, 1], None)
                dve.tensor_copy(kss[:, 0:1], krs[:, 0:1]).then_inc(qk_ready, 1)

            def q_norm(t):
                for c in range(2):
                    jobs.wait_drained(dve, ("q", c, t))
                head_norm(q[:, t:t + 1, :], 16, qss[:, t:t + 1, :], qrs[:, t:t + 1, :], 2 + t, R("qn"), [t], None)
                dve.tensor_copy(qss[:, t, 0:1], qrs[:, t, 0:1]).then_inc(qk_ready, 1)

            def taps(b):
                dve.wait_ge(conv_init, b + 1)
                dst = (xbc_xs[:, b, :] if b < 8 else bcf[:, b - 8, :]).rearrange("p (s t) -> p s t", s=2)
                src = jobs.out(("xbc", b)).rearrange("p (s t) -> p s t", s=2)
                for n, k in enumerate((0, 1, 3, 4)):
                    sh = k - 2
                    lo, hi = max(0, -sh), T - max(0, sh)
                    ins = dve.scalar_tensor_tensor(out=dst[:, :, lo:hi], in0=src[:, :, lo + sh:hi + sh], scalar=C("conv_w", 5 * b + k, 5 * b + k + 1),
                                                   in1=dst[:, :, lo:hi], op0=ALU.mult, op1=ALU.add)
                    if n < 3:
                        chain(ins)
                    else:
                        jobs.drain(ins, ("xbc", b))

            for b in range(DX):
                taps(b)
                if b == 2:
                    k_norm()
                if b in (5, 8):
                    q_norm((b - 5) // 3)
            jobs.wait_filled(dve, "cum")
            jobs.drain(dve.tensor_copy(acs[:, :, :], jobs.out("cum")[:, 0:256].rearrange("p (i h) -> p i h", i=4)), "cum")
            jobs.wait_drained(dve, "cum")
            dve.tensor_tensor(dw[:, :, :], acs[:, :, 32:64], acs[:, :, 0:32], ALU.subtract).then_inc(diff_ready, 1)

            dve.wait_ge(decays, 3)
            dve.tensor_tensor(dw[:, :, :], dw[:, :, :], dt[:, :, :], ALU.mult).then_inc(dw_ready, 1)
            for t in range(TT):
                jobs.wait_filled(dve, ("cb", t))
                src = jobs.out(("cb", t))[:, 0:256].rearrange("p (g q) -> p g q", g=2)
                order.up(dve.tensor_tensor(cb[:, t, 0, :, :], src, bc(K("tri_u").unsqueeze(1), [P, 2, P]), ALU.mult))
                jobs.drain(dve.tensor_tensor(cb[:, t, 1, :, :], src, bc(K("tri_l").unsqueeze(1), [P, 2, P]), ALU.mult), ("cb", t))

            slot = {0: 0, 1: 0, 2: 1, 3: 3, 4: 3, 5: 2}
            prev = {1: 0, 2: 0, 4: 3, 5: 3}
            for n, (i, d) in enumerate(STATES):
                for g in range(2):
                    name = ("st", n, g)
                    dst = H[:, slot[n], g * 512:(g + 1) * 512]
                    jobs.wait_filled(dve, name)
                    if n in prev:
                        src = H[:, prev[n], g * 512:(g + 1) * 512].rearrange("p (h c) -> p h c", c=DH)
                        chain(dve.tensor_tensor(dst.rearrange("p (h c) -> p h c", c=DH), src,
                                                bc(dec[:, i, 16 * d + 8 * g:16 * d + 8 * g + 8].unsqueeze(2), [P, 8, DH]), ALU.mult))
                        jobs.drain(dve.tensor_tensor(dst, dst, jobs.out(name), ALU.add), name)
                    else:
                        jobs.drain(dve.tensor_copy(dst, jobs.out(name)), name)
                    jobs.wait_drained(dve, name)
                    dve.sem_inc(h_ready, 1)

            def decay_diffs(n):
                t, g, quad = UNITS[n]
                for d in range(2):
                    name = ("aq", t, g, quad, d)
                    if 2 * n + d >= 4:
                        if UNITS[n - 2][2] == 0:
                            dve.wait_ge(m_used, (n - 2) // 2 + 1)
                        else:
                            jobs.wait_filled(dve, ("yd", *UNITS[n - 2][:2]))
                    jobs.wait_filled(dve, name)
                    for h in range(4):
                        head = 16 * d + 8 * g + 4 * quad + h
                        ins = dve.tensor_scalar(m[:, (2 * n + d) % 4, h * P:(h + 1) * P], jobs.out(name)[:, h * P:(h + 1) * P],
                                                acs[:, 2 + t, head:head + 1], 0.0, ALU.subtract, ALU.min)
                        if h < 3:
                            order.up(ins)
                        else:
                            jobs.drain(ins, name)
                    jobs.wait_drained(dve, name)
                    dve.sem_inc(aq_diff, 1)

            def gather_y(t, g):
                yy = y[:, t, g * 512:(g + 1) * 512]
                if g == 0:
                    dve.wait_ge(skip_ready, t + 1)
                name = ("yd", t, g)
                jobs.wait_filled(dve, name)
                jobs.drain(dve.tensor_tensor(yy, jobs.out(name), yy, ALU.add), name)
                jobs.wait_drained(dve, name)
                for d in range(2):
                    name = ("yo", t, g, d)
                    jobs.wait_filled(dve, name)
                    tb = wx[:, d, 0:512]
                    jobs.drain(dve.tensor_tensor(tb.rearrange("p (h c) -> p h c", c=DH), jobs.out(name).rearrange("p (h c) -> p h c", c=DH),
                                                 bc(ea[:, 2 + t, 16 * d + 8 * g:16 * d + 8 * g + 8].unsqueeze(2), [P, 8, DH]), ALU.mult), name)
                    jobs.wait_drained(dve, name)
                    tt(yy, yy, tb, ALU.add)
                if g == 1:
                    for c in range(2):
                        jobs.wait_drained(dve, ("z", c, t))
                    dve.tensor_tensor(y[:, t, :], y[:, t, :], z[:, t, :], ALU.mult).then_inc(y_gated, 1)

            for n in range(len(UNITS) + 1):
                if n < len(UNITS):
                    decay_diffs(n)
                if n >= 1 and UNITS[n - 1][2] == 1:
                    gather_y(*UNITS[n - 1][:2])

            for n in range(len(HEAD_ITEMS) + 2):
                if n < len(HEAD_ITEMS):
                    jobs.wait_filled(dve, ("S", n))
                    dve.tensor_reduce(nm[:, n:n + 1], jobs.out(("S", n)), AX_X, ALU.max, negate=True).then_inc(nmax_ready, 1)
                if n <= len(HEAD_ITEMS) and (n - 1) % 2 == 1 and n >= 1:
                    name = ("PT", n - 1)
                    jobs.wait_filled(dve, name)
                    jobs.drain(dve.tensor_copy(pt[:, (n - 1) % 2, :], jobs.out(name)), name)
                if n >= 2:
                    t, b, g = HEAD_ITEMS[n - 2]
                    if b % 4 == 3 and g == 1:
                        name = ("O", t, b // 4)
                        h0 = n - 2 - 7
                        jobs.wait_drained(dve, ("S", n - 2))
                        chain(dve.reciprocal(rden[:, h0:h0 + 8], dn[:, h0:h0 + 8]))
                        jobs.wait_filled(dve, name)
                        jobs.drain(dve.tensor_tensor(q[:, t, (b // 4) * 512:(b // 4 + 1) * 512].rearrange("p (h c) -> p h c", c=DH),
                                                     jobs.out(name).rearrange("p (h c) -> p h c", c=DH),
                                                     bc(rden[:, h0:h0 + 8].unsqueeze(2), [P, 8, DH]), ALU.mult), name)
            for t in range(TT):
                dve.wait_ge(y_std, t + 1)
                for g in range(2):
                    ins = dve.tensor_scalar(y[:, t, g * 512:(g + 1) * 512], y[:, t, g * 512:(g + 1) * 512], yrs[:, 2 * t + g:2 * t + g + 1], None, ALU.mult)
                    if g == 0:
                        order.up(ins)
                    else:
                        ins.then_inc(y_norm, 1)
            dve.wait_ge(y_sq, 4)
            for v, block in enumerate((16, 40)):
                for b in range(8):
                    ins = dve.tensor_scalar(wx[:, v, b * P:(b + 1) * P], ident, modT[:, block + b, 0:1], None, ALU.mult)
                    if b < 7:
                        order.up(ins)
                    else:
                        ins.then_inc(diag_ready, 1)
            for t in range(TT):
                for h in range(2):
                    name = ("mixT", h, t)
                    jobs.wait_filled(dve, name)
                    jobs.drain(dve.tensor_tensor(mixT[:, 4 * h:4 * h + 4, t * P:(t + 1) * P], jobs.out(name).rearrange("p (b t) -> p b t", b=4),
                                                 bc(C("ssd_g", 4 * h, 4 * h + 4).unsqueeze(2), [P, 4, P]), ALU.mult), name)

            def residual(v, which, sources):
                for t in range(TT):
                    for c in range(2):
                        cs = slice(c * 512, (c + 1) * 512)
                        wait, src, done = sources(t, c)
                        wait()
                        done(dve.tensor_tensor(res[:, t, cs], src, gB[:, v, cs], ALU.mult))
                        chain(dve.scalar_tensor_tensor(out=res[:, t, cs], in0=x[:, t, cs], scalar=ALPHA, in1=res[:, t, cs], op0=ALU.mult, op1=ALU.add))
                        chain(dve.bn_stats(stats[:, t, c, :], res[:, t, cs]))
                    dve.bn_aggr(mv[:, t, :], stats[:, t, :, :].rearrange("p c s -> p (c s)")).then_inc(ln_stat, 1)
                for t in range(TT):
                    dve.wait_ge(ln_std, v * TT + t + 1)
                    chain(dve.tensor_scalar(x[:, t, :], res[:, t, :], mv[:, t, 0:1], lstd[:, t:t + 1], ALU.subtract, ALU.mult))
                    tt(x[:, t, :], x[:, t, :], R(f"ln{v + 1}_g"), ALU.mult)
                    dve.tensor_tensor(x[:, t, :], x[:, t, :], R(f"ln{v + 1}_b"), ALU.add).then_inc(x_normed, 1)

            def out_source(t, c):
                name = ("out", t, c)

                def wait():
                    jobs.wait_filled(dve, name)

                def done(ins):
                    jobs.drain(ins, name)
                    jobs.wait_drained(dve, name)
                return wait, jobs.out(name), done

            for n in range(2):
                split_lo(dve, 0, n)
            for c in range(2):
                jobs.wait_drained(dve, ("gB", 1, c))
            dve.wait_ge(ln_rows, 16)
            residual(0, "out", out_source)
            for n in range(4):
                c, t = divmod(n, TT)
                scale_in(("hf", c, t), hf[:, 4 * c:4 * c + 4, t * P:(t + 1) * P], 32 + 4 * c, 0)
            for n in range(4):
                c, t = divmod(n, TT)
                dve.wait_ge(h_hi, n + 1)
                part = hfS[:, :, 4 * c:4 * c + 4, t * P:(t + 1) * P]
                dve.tensor_tensor(part[:, 1, :, :], hf[:, 4 * c:4 * c + 4, t * P:(t + 1) * P], part[:, 0, :, :].bitcast(F32),
                                  ALU.subtract).then_inc(h_lo, 1)
            dve.sem_inc(hid_raw, 2)
            dve.sem_inc(hid_hi, 2)
            dve.sem_inc(hid_ready, 2)
            split_lo(dve, 0, 2)

            jobs.wait_filled(dve, "route")
            jobs.drain(dve.tensor_tensor(lg[:, :, :], jobs.out("route")[:, 0:40].rearrange("p (t n) -> p t n", t=2),
                                         bc(R("br").unsqueeze(1), [P, 2, 20]), ALU.add), "route")
            jobs.wait_drained(dve, "route")
            four = bc(K("four").unsqueeze(1), [P, 2, 4])

            def first_max(oh, v, vmax, scratch):
                chain(dve.tensor_reduce(vmax, v, AX_X, ALU.max))
                tt(oh, v, bc(vmax.unsqueeze(2), [P, 2, 4]), ALU.is_equal)
                tt(oh, oh, four, ALU.mult)
                chain(dve.tensor_reduce(scratch, oh, AX_X, ALU.max))
                tt(oh, oh, bc(scratch.unsqueeze(2), [P, 2, 4]), ALU.is_equal)

            first_max(goh[:, :, :], lg[:, :, 0:4], gm, r2a)
            tt(r8a[:, :, :], lg[:, :, 0:4], bc(gm.unsqueeze(2), [P, 2, 4]), ALU.subtract)
            el = lg[:, :, 4:20].rearrange("p t (g e) -> p t g e", g=4)
            for t in range(TT):
                order.up(dve.tensor_tensor(r32[:, t, :, :], el[:, t, :, :], bc(goh[:, t, :].unsqueeze(2), [P, 4, 4]), ALU.mult))
            order.here(dve)
            chain(dve.tensor_reduce(es[:, :, :], r32[:, :, :, :].rearrange("p t g e -> p t e g"), AX_X, ALU.add))
            chain(dve.tensor_reduce(r2b, es[:, :, :], AX_X, ALU.max))
            dve.tensor_tensor(es[:, :, :], es[:, :, :], bc(r2b.unsqueeze(2), [P, 2, 4]), ALU.subtract).then_inc(r_logits, 1)
            split_lo(dve, 0, 3)
            dve.wait_ge(r_exp, 2)
            chain(dve.tensor_reduce(gs, r8a[:, :, :], AX_X, ALU.add))
            chain(dve.reciprocal(gval, gs))
            chain(dve.tensor_reduce(r2a, es[:, :, :], AX_X, ALU.add))
            chain(dve.reciprocal(r2b, r2a))
            tt(pe_[:, :, :], es[:, :, :], bc(r2b.unsqueeze(2), [P, 2, 4]), ALU.mult)
            first_max(oh1[:, :, :], pe_[:, :, :], r2a, r2c)
            chain(dve.scalar_tensor_tensor(out=pm[:, :, :], in0=oh1[:, :, :], scalar=-2.0, in1=pe_[:, :, :], op0=ALU.mult, op1=ALU.add))
            first_max(oh2[:, :, :], pm[:, :, :], r2b, r2c)
            tt(r2c, r2a, r2b, ALU.add)
            chain(dve.reciprocal(r2c, r2c))
            tt(r2c, r2c, gval, ALU.mult)
            tt(wgt[:, :, :], oh1[:, :, :], oh2[:, :, :], ALU.add)
            tt(wgt[:, :, :], wgt[:, :, :], pe_[:, :, :], ALU.mult)
            tt(wgt[:, :, :], wgt[:, :, :], bc(r2c.unsqueeze(2), [P, 2, 4]), ALU.mult)
            for t in range(TT):
                ins = dve.tensor_tensor(comb[:, t, :].rearrange("p (g e) -> p g e", g=4), bc(goh[:, t, :].unsqueeze(2), [P, 4, 4]),
                                        bc(wgt[:, t, :].unsqueeze(1), [P, 4, 4]), ALU.mult)
                if t == 0:
                    chain(ins)
                else:
                    ins.then_inc(comb_ready, 1)

            def times_up(step, e):
                wait_expert(dve, step, "U", e, "filled")
                wait_expert(dve, step, "G", e, "drained")
                dve.tensor_tensor(gated[:, e % 2, :], gated[:, e % 2, :], expert_bank("U", e), ALU.mult).then_inc(drained[expert_regions(e)[1]], 1)

            def weight(step, e):
                wait_expert(dve, step, "U", e, "drained")
                dve.wait_ge(hid_ready, step * EXPERT_STEP + (e + 1))
                comb_e = combB[:, bass.ds(step * EXPERT_STEP + e, 1), :]
                dve.tensor_tensor(hid[:, e % 2, :].rearrange("p (b t) -> p b t", b=2), gated[:, e % 2, :].rearrange("p (b t) -> p b t", b=2),
                                  bc(comb_e, [P, 2, T]), ALU.mult).then_inc(hid_raw, 1)

            def hidden_lo(step, e):
                dve.wait_ge(hid_hi, step * EXPERT_STEP + (e + 3))
                dve.tensor_tensor(hidS[:, e % 2, 1, :], hid[:, e % 2, :], hidS[:, e % 2, 0, :].bitcast(F32), ALU.subtract).then_inc(hid_ready, 1)

            def last_two(step):
                split_lo(dve, step, 7)
                split_lo(dve, step, 8)
                times_up(step, 2)
                weight(step, 2)
                hidden_lo(step, 2)
                split_lo(dve, step, 9)
                split_lo(dve, step, 10)
                split_lo(dve, step, 11)
                times_up(step, 3)
                weight(step, 3)
                hidden_lo(step, 3)

            times_up(0, 0)
            split_lo(dve, 0, 4)
            split_lo(dve, 0, 5)
            times_up(0, 1)
            split_lo(dve, 0, 6)
            for i in range(8):
                jobs.wait_drained(dve, ("combB", i))
            for e in range(2):
                weight(0, e)
                hidden_lo(0, e)
            last_two(0)
            with dve.Fori(1, EXPERTS // EXPERT_STEP) as step:
                for n in range(4):
                    split_lo(dve, step, n)
                times_up(step, 0)
                weight(step, 0)
                hidden_lo(step, 0)
                split_lo(dve, step, 4)
                split_lo(dve, step, 5)
                times_up(step, 1)
                weight(step, 1)
                hidden_lo(step, 1)
                split_lo(dve, step, 6)
                last_two(step)
            dve.wait_ge(hid_used, EXPERTS + 2)

            def moe_source(t, c):
                def done(ins):
                    chain(ins)
                return (lambda: None), psum[:, (2 * t + c) * 512:(2 * t + c + 1) * 512], done

            residual(1, "moe", moe_source)

        @block.gpsimd
        def _(pool):
            order = Signal(g_order)

            def chain(ins):
                order.up(ins)
                order.here(pool)

            pool.wait_ge(mod_ready, 2)
            for s in (1, 0):
                for c in range(2):
                    for t in range(TT):
                        jobs.wait_drained(pool, ("in", s, c, t))
                        dst = hT[:, 4 * c:4 * c + 4, (2 * s + t) * P:(2 * s + t + 1) * P]
                        pool.tensor_tensor(dst, dst, bc(modT[:, 4 * c:4 * c + 4, 1 - s:2 - s], [P, 4, P]), ALU.add).then_inc(shifted, 1)

            def inv_roots(turn, dst, total, n, sig, eps=EPS, scratch=None):
                w = dst.shape[1]
                chain(pool.tensor_scalar(scratch[:, 0:w], total, 1.0 / n, eps, ALU.mult, ALU.add))
                pool.tensor_tensor(dst, scratch[:, 0:w], K("mhalf", 0, w), ALU.pow).then_inc(sig, 1)
                pool.wait_ge(sig, turn)

            pool.wait_ge(qk_sum, 1)
            inv_roots(1, krs, kss, DH, qk_std, scratch=ssq)
            for t in range(TT):
                pool.wait_ge(qk_sum, 2 + t)
                inv_roots(2 + t, qrs[:, t, :], qss[:, t, :], DH, qk_std, scratch=ssq)
            pool.wait_ge(dt_ready, 1)
            for i in range(4):
                for half in range(2):
                    jobs.wait_filled(pool, ("xsT", i, half))
            for i in (2, 3):
                for half in range(2):
                    jobs.wait_drained(pool, ("xsT", i, half))
            for t in range(TT):
                for d in range(2):
                    pool.tensor_tensor(xdt[:, 2 * t + d, :].rearrange("p (h c) -> p h c", c=DH), xs[:, 2 + t, :].rearrange("p (h c) -> p h c", c=DH),
                                       bc(dt[:, 2 + t, 16 * d:16 * d + 16].unsqueeze(2), [P, 16, DH]), ALU.mult).then_inc(xdt_ready, 1)
                pool.tensor_tensor(y[:, t, :].rearrange("p (h c) -> p h c", c=DH), xs[:, 2 + t, :].rearrange("p (h c) -> p h c", c=DH),
                                   bc(R("skip").unsqueeze(2), [P, 16, DH]), ALU.mult).then_inc(skip_ready, 1)
            pool.wait_ge(dw_ready, 1)
            for n, (i, d) in enumerate(STATES):
                for half in range(2):
                    jobs.wait_drained(pool, ("xsT", i, half))
                if n >= 2:
                    for g in range(2):
                        jobs.wait_filled(pool, ("st", n - 2, g))
                pool.tensor_tensor(wx[:, n % 2, :].rearrange("p (h c) -> p h c", c=DH), xs[:, i, :].rearrange("p (h c) -> p h c", c=DH),
                                   bc(dw[:, i, 16 * d:16 * d + 16].unsqueeze(2), [P, 16, DH]), ALU.mult).then_inc(xw_ready, 1)
            for t in range(TT):
                jobs.wait_drained(pool, ("cb", t))
            for n, (t, g, quad) in enumerate(UNITS):
                for d in range(2):
                    pool.wait_ge(aq_exp, 2 * n + d + 1)
                    m3 = m[:, (2 * n + d) % 4, :].rearrange("p (h q) -> p h q", h=4)
                    pool.tensor_tensor(m3, m3, bc(cb[:, t, d, g, :].unsqueeze(1), [P, 4, P]), ALU.mult).then_inc(m_ready, 1)
            for t in range(TT):
                pool.wait_ge(y_sq, 2 * t + 2)
                inv_roots(t + 1, yrs[:, 2 * t:2 * t + 2], yss[:, 2 * t:2 * t + 2], 512, y_std, scratch=ssq)

            def ln_roots(v):
                for t in range(TT):
                    pool.wait_ge(ln_stat, v * TT + t + 1)
                    chain(pool.tensor_scalar(lms[:, 0:1], mv[:, t, 1:2], 1.0, LN_EPS, ALU.mult, ALU.add))
                    pool.tensor_tensor(lstd[:, t:t + 1], lms[:, 0:1], K("mhalf", 0, 1), ALU.pow).then_inc(ln_std, 1)
                    pool.wait_ge(ln_std, v * TT + t + 1)

            ln_roots(0)
            for c in range(2):
                for t in range(TT):
                    jobs.wait_drained(pool, ("hf", c, t))
                    dst = hf[:, 4 * c:4 * c + 4, t * P:(t + 1) * P]
                    pool.tensor_tensor(dst, dst, bc(modT[:, 24 + 4 * c:28 + 4 * c, 0:1], [P, 4, P]), ALU.add).then_inc(shifted, 1)
            ln_roots(1)


MEM = dict(
    hT=(KD, T), small=(200,), mrow=(2, 512), cols=(N_COLS,), rows=(N_ROWS,),
    kblk=(32,), hidv=(2, P), bglu=(4, T + TAPS - 1), cpad=(4, 16 + T),
)
MEM_TM, MEM_BR1 = [("tm", (TT, D), F32)], [("br1", (2, 4, T), F32R)]
MEM_MIX = [("gates", (8192,), F32), ("brS", (2, 3, 4, T), F32R)]
MEM_ATT = [
    ("qTs", (3, 4, T), F32), ("proj", (TT, 2048), F32), ("sc", (2, 4, T), F32), ("pt", (2, 2, 4, P), F32), ("rkT", (3, T), F32),
    ("vblk", (512,), F32), ("acc", (4, T), F32), ("tmp", (2, 512), F32), ("hidk", (2, 2, 16), F32), ("csc", (2, P), F32),
    ("cpT", (2, P), F32),
]
MEM_UP = [("split2", (2, 2, CH), F32R), ("mixS", (2, KD, T), F32R)]
MEM_FFN = dict(hq=(2, 1024), f32=(T,))
MEM_FFN_SPLIT = dict(split=(SPLITS, 2, CH), hfT=(2, KD, T), fT=(2, FB, T))


def build_program(nc, x_in, ctx_in, cond, weights, cols, rows, cols2, rows2, const, out):
    with ExitStack() as ctx:
        keep = dict(x=(TT, D), const=(N_CONST,), cond=(16 + MODS,), cvec=(16,), modT=(MODS, 2))
        mem = {k: ctx.enter_context(nc.sbuf_tensor(f"sb_{k}", [P, *s], F32)) for k, s in keep.items()}
        ring = ctx.enter_context(nc.sbuf_tensor("ring", [P, SLOTS, CH], F32))
        psum = ctx.enter_context(nc.psum_tensor("psum", [P, 4096], F32))
        landed = [ctx.enter_context(nc.semaphore(f"landed_{s}")) for s in range(SLOTS)]
        used = [ctx.enter_context(nc.semaphore(f"used_{s}")) for s in range(SLOTS)]
        loaded = ctx.enter_context(nc.semaphore("loaded"))
        conditioned = ctx.enter_context(nc.semaphore("conditioned"))
        zeroed = ctx.enter_context(nc.semaphore("zeroed"))

        with ExitStack() as first:
            mem1 = {**mem, **{k: first.enter_context(nc.sbuf_tensor(f"sb_{k}", [P, *s], F32)) for k, s in MEM.items()}}

            def place(stack, fields):
                for k, s, dtype in fields:
                    mem1[k] = stack.enter_context(nc.sbuf_tensor(f"sb_{k}", [P, *s], dtype))

            with ExitStack() as phase:
                place(phase, MEM_TM)
            place(first, MEM_BR1)
            with ExitStack() as phase:
                place(phase, MEM_MIX)
                with ExitStack() as attention:
                    place(attention, MEM_ATT)
                place(phase, MEM_UP)
            for fields, dtype in ((MEM_FFN_SPLIT, F32R), (MEM_FFN, F32)):
                for k, s in fields.items():
                    mem1[k] = first.enter_context(nc.sbuf_tensor(f"sb_{k}", [P, *s], dtype))

            with nc.Block() as block:
                @block.sync
                def _(sp):
                    sp.dma_start(mem["cond"][:, :], cond).then_inc(conditioned, 16)
                    for s in range(SLOTS):
                        sp.dma_start(ring[:, s, :], weights[s]).then_inc(landed[s], 16)
                        if s == 0:
                            sp.dma_start(mem["x"][:, :, :], x_in.rearrange("(t p) d -> p t d", p=P)).then_inc(loaded, 16)
                            sp.dma_start(mem["const"][:, :], const).then_inc(loaded, 16)

                @block.scalar
                def _(act):
                    act.wait_ge(conditioned, 16)
                    act.activation(mem["cvec"][:, :], mem["cond"][:, 0:16], ACT.Silu).then_inc(zeroed, 1)

                @block.gpsimd
                def _(pool):
                    pool.memset(mem1["hidv"][:, :, :], 0.0).then_inc(zeroed, 1)
                    pool.memset(mem1["kblk"][:, :], 0.0).then_inc(zeroed, 1)
                    pool.memset(mem1["bglu"][:, :, 0:TAPS - 1], 0.0).then_inc(zeroed, 1)
                    pool.memset(mem1["cpad"][:, :, 0:16], 0.0).then_inc(zeroed, 1)
                    pool.wait_ge(zeroed, 5)

            layer_sems = []

            def sems(name):
                s = first.enter_context(nc.semaphore(name))
                layer_sems.append(s)
                return s

            with nc.Fori(0, LAYERS) as l:
                layer_block(nc, l, mem1, ring, landed, used, weights, psum, sems, cols, rows, loaded)
                nums = [s.num for s in layer_sems]
                assert nums == list(range(nums[0], nums[-1] + 1))
                nc.all_engine_barrier(sems_to_clear=range(nums[0], nums[-1] + 1))

        with ExitStack() as second:
            mem2 = {**mem, **{k: second.enter_context(nc.sbuf_tensor(f"sb2_{k}", [P, *s], F32)) for k, s in MEM2.items()}}
            with ExitStack() as phase:
                for k, s in MEM2_MIX.items():
                    mem2[k] = phase.enter_context(nc.sbuf_tensor(f"sb2_{k}", [P, *s], F32))
            for fields, dtype in ((MEM2_MOE_SPLIT, F32R), (MEM2_MOE, F32)):
                for k, s in fields.items():
                    mem2[k] = second.enter_context(nc.sbuf_tensor(f"sb2_{k}", [P, *s], dtype))

            def sems2(name):
                return second.enter_context(nc.semaphore(name))

            block2(nc, mem2, ring, landed, used, weights, psum, sems2, cols2, rows2, ctx_in, out)


HEADS_IN_PAIRS = [4 * g + j for j in range(4) for g in range(2)]


def pairs(a, width, axis=-1):
    idx = np.concatenate([np.arange(h * width, (h + 1) * width) for h in HEADS_IN_PAIRS])
    return np.take(a, idx, axis=axis)


def to_cols(v):
    return v.reshape(-1, P).T


def k_split(w):
    return w.reshape(2, 4, P, 512).transpose(0, 2, 1, 3).reshape(2, P, CH)


def n_split(w):
    return w.reshape(KD, P, -1, 256).transpose(2, 1, 0, 3).reshape(-1, P, CH)


def rows_split(w):
    return w.reshape(-1, 2, P, D).transpose(0, 2, 1, 3).reshape(-1, P, CH)


def layer_inputs(l, i):
    mod = [k_split(i["w_mod_2"][0][:, (l * MOD_STEPS + j) * 512:(l * MOD_STEPS + j + 1) * 512]) for j in range(MOD_STEPS)]
    w = i["w_in"][l]
    kv = w[:, 512:1280]
    gate_val = i["ffn_w_up"][l].reshape(D, 2, FB, P).transpose(0, 2, 1, 3).reshape(D, 2 * DFF)
    br = i["w_branch"][l]
    br = {0: pairs(br[0], DH, 0), 1: br[1], 2: br[2], 3: pairs(br[3], DH, 0)}
    chunks = [
        *(mod[j] for j in EARLY_MODS), k_split(kv[:, 0:512]), k_split(np.concatenate([kv[:, 512:768], w[:, 1816:2072]], 1)),
        k_split(pairs(w[:, 0:512], DH)), k_split(pairs(w[:, 1304:1816], DH)),
        n_split(w[:, 3096:3608]), n_split(w[:, 2072:2584]),
        i["nsa_cmp_w1"][l].reshape(2, 2, 8, P, 256).transpose(0, 1, 3, 2, 4).reshape(4, P, CH),
        n_split(w[:, 2584:3096]),
        n_split(i["w_gate"][l]),
        *[br[n].reshape(4, P, 2, 512).transpose(2, 1, 0, 3).reshape(2, P, CH) for n in BRANCH_ORDER],
        k_split(i["w_o"][l][:, 0:512]), k_split(i["w_o"][l][:, 512:1024]), *(mod[j] for j in LATE_MODS),
        n_split(gate_val), rows_split(i["ffn_w_down"][l]), *(mod[j] for j in END_MODS), np.zeros((1, P, CH), np.float32),
    ]
    pos = i["nsa_cmp_pos"][l].reshape(2, 16, 2, DH).transpose(2, 3, 0, 1).reshape(P, 32)
    w2 = i["nsa_cmp_w2"][l].reshape(2, 2, P, DH).transpose(2, 0, 1, 3).reshape(P, 256)
    fields = dict(
        g_mix=to_cols(i["norm_mix_pre"][l]), g_ffn=to_cols(i["norm_ffn_pre"][l]), pos=pos, w2=w2,
        conv_w=i["conv_w"][l].reshape(TAPS, 4, P).transpose(2, 1, 0), conv_b=to_cols(i["conv_b"][l]),
        ln_g=to_cols(i["conv_ln_g"][l]), ln_b=to_cols(i["conv_ln_b"][l]),
        pool_w=i["pool_w"][l].transpose(1, 0, 2), pool_s=to_cols(i["pool_scale"][l]),
        fw=i["ffn_conv_w"][l].reshape(3, 2, FB, P).transpose(3, 2, 1, 0),
        fb=i["ffn_conv_b"][l].reshape(2, FB, P).transpose(2, 1, 0),
        w_ga=w[:, 1280:1304].reshape(KD, P, 3, 2, 4).transpose(1, 0, 2, 4, 3),
    )
    packed = np.concatenate([fields[name].reshape(P, width) for name, (_, width) in COLS.items()], 1)
    row = np.concatenate([i["norm_mix_post"][l], i["norm_ffn_post"][l], pairs(i["swa_sinks"][l], 1)])
    return np.concatenate(chunks), packed, row[None, :]


def block2_inputs(i):
    pick = lambda a, idx, axis=-1: np.take(a, np.concatenate([np.atleast_1d(v) for v in idx]), axis=axis)
    inner = np.concatenate([np.arange(0, DH, 2), np.arange(1, DH, 2)])
    w = i["w_in_2"][0]
    k_cols = [3616 + h * DH + inner for h in range(4)]
    q_heads = [4 * (2 * (b // 4) + g) + b % 4 for b in range(8) for g in range(2)]
    q_cols = [1024 + h * DH + inner for h in q_heads]
    wo = i["w_out_2"][0]
    o_rows = [np.arange(1024)] + [1024 + h * DH + np.arange(DH) for h in q_heads]
    q = pick(w, q_cols)
    chunks = [k_split(q[:, 0:512]), k_split(q[:, 512:1024]), k_split(np.concatenate([pick(w, k_cols), w[:, 3872:4128]], 1)),
              n_split(w[:, 2048:3584]), k_split(w[:, 0:512]), k_split(w[:, 512:1024]),
              rows_split(pick(wo, o_rows, 0))]
    for e0 in range(0, EXPERTS, EXPERT_STEP):
        gu = [[n_split(i[k][0, e]) for k in ("w_gate_2", "w_up_2")] for e in range(e0, e0 + EXPERT_STEP)]
        down = [rows_split(i["w_down_2"][0, e]) for e in range(e0, e0 + EXPERT_STEP)]
        chunks += [*gu[0], *gu[1], down[0], *gu[2], down[1], *gu[3], down[2], down[3]]
    k_pack = lambda a: a.reshape(KD, P, -1).transpose(1, 0, 2)
    fields = dict(
        conv_w=i["conv_w_2"][0].reshape(5, DX, P).transpose(2, 1, 0), conv_b=to_cols(i["conv_b_2"][0]),
        ssd_g=to_cols(i["ssd_norm_g_2"][0]),
        w_dt=k_pack(w[:, 3584:3616]), w_r=k_pack(np.concatenate([i["w_rg_2"][0], i["w_re_2"][0]], 1)),
    )
    packed = np.concatenate([fields[name].reshape(P, width) for name, (_, width) in COLS2.items()], 1)
    row = np.concatenate([i["ln1_g_2"][0], i["ln1_b_2"][0], i["ln2_g_2"][0], i["ln2_b_2"][0], i["dt_bias_2"][0].reshape(-1),
                          i["a_log_2"][0].reshape(-1), i["q_norm_g_2"][0][inner], i["k_norm_g_2"][0][inner],
                          i["b_rg_2"][0], i["b_re_2"][0], i["d_skip_2"][0]])
    return np.concatenate(chunks), packed, row[None, :]


def lay_out(i):
    layers = [layer_inputs(l, i) for l in range(LAYERS)]
    chunks2, packed2, row2 = block2_inputs(i)
    return dict(
        cond=np.concatenate([np.stack([to_cols(i["c_2"][0]), to_cols(i["c_ctx_2"])], -1).reshape(P, 16), to_cols(i["b_mod_2"][0])], 1),
        x_in=i["x"][0], ctx_in=i["ctx_2"][0], weights=np.concatenate([layers[0][0], layers[1][0], chunks2]),
        cols=np.stack([v[1] for v in layers]), rows=np.stack([v[2] for v in layers]), cols2=packed2, rows2=row2, const=constants(),
    )


def kernel(**inputs):
    import concourse.bacc as bacc
    from concourse.bass_utils import run_bass_kernel_spmd

    arrays = {k: np.ascontiguousarray(v) for k, v in lay_out({k: np.asarray(v) for k, v in inputs.items()}).items()}
    nc = bacc.Bacc("TRN2", target_bir_lowering=False, num_devices=1)
    args = {k: nc.dram_tensor(k, v.shape, F32, kind="ExternalInput").ap() for k, v in arrays.items()}
    out = nc.dram_tensor("out", (T, D), F32, kind="ExternalOutput").ap()
    build_program(nc, out=out, **args)
    result = run_bass_kernel_spmd(nc, [arrays], core_ids=[0])
    return result.results[0]["out"].reshape(1, T, D)
```
